# Optimizing a Trainium2 kernel written in Bass

```python
import math
import jax
import jax.numpy as jnp
from jax import lax
import numpy as np

D_MODEL = 1024
BATCH = 1
SEQ = 1024
DEPTH = 2
DEC_BATCH = 8
DEC_SEQ = 1
PAST_LEN = 4096
PAGE_SIZE = 128

HEAD_DIM = 64
N_RET_HEADS = 4
N_MLSTM_HEADS = 4
N_GDN_HEADS = 4
N_NSA_HEADS = 4
D_RET = N_RET_HEADS * HEAD_DIM
D_MLSTM = N_MLSTM_HEADS * HEAD_DIM
D_GDN = N_GDN_HEADS * HEAD_DIM
D_NSA = N_NSA_HEADS * HEAD_DIM
D_MIX = D_RET + D_MLSTM + D_GDN + D_NSA
CHUNK = 64
GDN_CONV = 4
NSA_KV_ROWS = 6
NSA_CACHE_ROWS = 4
CMP_STRIDE = 16
CMP_LEN = 2 * CMP_STRIDE
SLC_BLOCK = 64
SLC_TOPK = 16
WINDOW = 512
Q_BLOCK = 128
T5_BUCKETS = 32
T5_MAX_DIST = 1024
ROPE_BASE = 10000.0
D_FF = 2816
FFN_CONV = 3
EPS = 1e-6
IN_WIDTHS = (D_RET, D_RET, D_RET, D_RET,
             D_MLSTM, D_MLSTM, D_MLSTM, N_MLSTM_HEADS, N_MLSTM_HEADS, D_MLSTM,
             3 * D_GDN, N_GDN_HEADS, N_GDN_HEADS, D_GDN,
             D_NSA, NSA_KV_ROWS * HEAD_DIM, 3 * N_NSA_HEADS)
D_IN = sum(IN_WIDTHS)
IN_SPLITS = tuple(int(s) for s in np.cumsum(IN_WIDTHS)[:-1])
STATE_KEYS = ('nsa', 'swa', 'ret', 'ml_C', 'ml_n', 'ml_m', 'gdn', 'gdn_conv', 'ffn_conv')

kernel_name = 'hybrid_retention_mlstm_gdn_nsa_step'

def _rmsnorm(x, g):
    x32 = x.astype(jnp.float32)
    y = x32 * lax.rsqrt(jnp.mean(x32 * x32, axis=-1, keepdims=True) + EPS)
    return (y * g.astype(jnp.float32)).astype(x.dtype)

def _head_rmsnorm(o, g):
    B, L, H, dh = o.shape
    o32 = o.astype(jnp.float32)
    y = o32 * lax.rsqrt(jnp.mean(o32 * o32, axis=-1, keepdims=True) + EPS)
    return y.reshape(B, L, H * dh) * g.astype(jnp.float32)

def _l2norm(x):
    return x * lax.rsqrt(jnp.sum(x * x, axis=-1, keepdims=True) + EPS)

def _causal_dwconv(buf, x, w):
    width = w.shape[0]
    L = x.shape[1]
    xp = jnp.concatenate([buf.astype(x.dtype), x], axis=1)
    out = sum(xp[:, j:j + L] * w[j].astype(x.dtype) for j in range(width))
    return out, xp[:, L:]

def _rope(x, pos):
    half = x.shape[-1] // 2
    inv = ROPE_BASE ** (-jnp.linspace(0.0, 1.0, half, dtype=jnp.float32))
    ang = pos.astype(jnp.float32)[:, None] * inv[None, :]
    cos = jnp.cos(ang)[None, :, None, :]
    sin = jnp.sin(ang)[None, :, None, :]
    x1, x2 = x[..., :half], x[..., half:]
    return jnp.concatenate([x1 * cos - x2 * sin, x1 * sin + x2 * cos], axis=-1)

def _chunk_len(L):
    return CHUNK if L % CHUNK == 0 else L

def _to_chunks(t, C):
    B, L = t.shape[:2]
    return jnp.moveaxis(t.reshape((B, L // C, C) + t.shape[2:]), 1, 0)

def _from_chunks(t):
    n, B, C = t.shape[:3]
    return jnp.moveaxis(t, 0, 1).reshape((B, n * C) + t.shape[3:])

def _retention(q, k, v, S0):
    H, L = q.shape[2], q.shape[1]
    C = _chunk_len(L)
    log_g = jnp.log(1.0 - 2.0 ** (-5.0 - jnp.arange(H, dtype=jnp.float32)))
    idx = jnp.arange(C, dtype=jnp.float32)
    diff = idx[:, None] - idx[None, :]
    causal = diff >= 0
    dmat = jnp.where(causal[None], jnp.exp(log_g[:, None, None] * jnp.where(causal, diff, 0.0)[None]), 0.0)
    xi = jnp.exp(log_g[None, :] * (idx[:, None] + 1.0))
    zeta = jnp.exp(log_g[None, :] * (C - 1.0 - idx[:, None]))
    g_chunk = jnp.exp(log_g * C)

    def step(S, inp):
        qc, kc, vc = inp
        s = jnp.einsum('bihd,bjhd->bhij', qc, kc) * dmat[None]
        o = (jnp.einsum('bhij,bjhe->bihe', s, vc)
             + jnp.einsum('bihd,bhde->bihe', qc * xi[None, :, :, None], S))
        S = S * g_chunk[None, :, None, None] + jnp.einsum('bjhd,bjhe->bhde', kc * zeta[None, :, :, None], vc)
        return S, o

    S, o = lax.scan(step, S0, (_to_chunks(q, C), _to_chunks(k, C), _to_chunks(v, C)))
    return _from_chunks(o), S

def _mlstm(q, k, v, i_pre, f_pre, C0, n0, m0):
    L = q.shape[1]
    Cn = _chunk_len(L)
    log_f = jax.nn.log_sigmoid(f_pre)
    tri = jnp.tril(jnp.ones((Cn, Cn), dtype=bool))[None, :, :, None]

    def step(carry, inp):
        Cm, nv, m = carry
        qc, kc, vc, ic, fc = inp
        b = jnp.cumsum(fc, axis=1)
        dlog = jnp.where(tri, b[:, :, None, :] - b[:, None, :, :] + ic[:, None, :, :], -jnp.inf)
        inter = b + m[:, None, :]
        m_t = jnp.maximum(inter, jnp.max(dlog, axis=2))
        w = jnp.exp(dlog - m_t[:, :, None, :])
        g_in = jnp.exp(inter - m_t)
        qk = jnp.einsum('bthd,bshd->btsh', qc, kc) * w
        num = (jnp.einsum('btsh,bshe->bthe', qk, vc)
               + g_in[..., None] * jnp.einsum('bthd,bhde->bthe', qc, Cm))
        den = jnp.sum(qk, axis=2) + g_in * jnp.einsum('bthd,bhd->bth', qc, nv)
        h = num / jnp.maximum(jnp.abs(den), jnp.exp(-m_t))[..., None]
        m_end = m_t[:, -1]
        w_end = jnp.exp(b[:, -1:, :] - b + ic - m_end[:, None, :])
        g_end = jnp.exp(inter[:, -1] - m_end)
        Cm = g_end[:, :, None, None] * Cm + jnp.einsum('bsh,bshd,bshe->bhde', w_end, kc, vc)
        nv = g_end[:, :, None] * nv + jnp.einsum('bsh,bshd->bhd', w_end, kc)
        return (Cm, nv, m_end), h

    xs = (_to_chunks(q, Cn), _to_chunks(k, Cn), _to_chunks(v, Cn), _to_chunks(i_pre, Cn), _to_chunks(log_f, Cn))
    (Cm, nv, m), h = lax.scan(step, (C0, n0, m0), xs)
    return _from_chunks(h), Cm, nv, m

def _gated_delta(q, k, v, g, beta, S0):
    L = q.shape[1]
    Cn = _chunk_len(L)
    incl = jnp.tril(jnp.ones((Cn, Cn), dtype=bool))
    strict = jnp.tril(jnp.ones((Cn, Cn), dtype=bool), -1)
    eye = jnp.eye(Cn, dtype=jnp.float32)

    def step(S, inp):
        qc, kc, vc, gc, bc = inp
        G = jnp.cumsum(gc, axis=1)
        Gh = jnp.moveaxis(G, 2, 1)
        decay = jnp.exp(jnp.where(incl, Gh[..., :, None] - Gh[..., None, :], -jnp.inf))
        kk = jnp.einsum('bthd,bshd->bhts', kc, kc)
        bh = jnp.moveaxis(bc, 2, 1)
        tmat = jnp.where(strict, bh[..., :, None] * kk * decay, 0.0) + eye
        rhs_v = jnp.moveaxis(vc * bc[..., None], 2, 1)
        rhs_k = jnp.moveaxis(kc * (bc * jnp.exp(G))[..., None], 2, 1)
        u = lax.linalg.triangular_solve(tmat, rhs_v, left_side=True, lower=True, unit_diagonal=True)
        w = lax.linalg.triangular_solve(tmat, rhs_k, left_side=True, lower=True, unit_diagonal=True)
        delta = u - jnp.einsum('bhtd,bhde->bhte', w, S)
        qk = jnp.einsum('bthd,bshd->bhts', qc, kc) * decay
        o = (jnp.einsum('bhts,bhse->bthe', qk, delta)
             + jnp.einsum('bthd,bhde->bthe', qc * jnp.exp(G)[..., None], S))
        g_end = Gh[..., -1]
        w_end = jnp.exp(g_end[..., None] - Gh)
        S = jnp.exp(g_end)[..., None, None] * S + jnp.einsum('bhs,bshd,bhse->bhde', w_end, kc, delta)
        return S, o

    xs = (_to_chunks(q, Cn), _to_chunks(k, Cn), _to_chunks(v, Cn), _to_chunks(g, Cn), _to_chunks(beta, Cn))
    S, o = lax.scan(step, S0, xs)
    return _from_chunks(o), S

def _t5_bias(rel_bias, dist):
    n = jnp.maximum(dist, 0)
    exact = T5_BUCKETS // 2
    large = exact + (jnp.log(jnp.maximum(n, 1).astype(jnp.float32) / exact)
                     / math.log(T5_MAX_DIST / exact) * (T5_BUCKETS - exact)).astype(jnp.int32)
    bucket = jnp.where(n < exact, n, jnp.minimum(large, T5_BUCKETS - 1))
    return rel_bias[bucket].astype(jnp.float32)

def _masked_softmax(s, valid):
    s = jnp.where(valid, s, -jnp.inf)
    m = jnp.max(s, axis=-1, keepdims=True)
    m = jnp.where(jnp.isfinite(m), m, 0.0)
    p = jnp.exp(s - m)
    den = jnp.sum(p, axis=-1, keepdims=True)
    return p / jnp.where(den > 0, den, 1.0)

def _nsa(q, gates, kv_new, kv_past, swa_buf, pos0, cmp_pe, cmp_w, rel_bias):
    B, L, H, dh = q.shape
    scale = dh ** -0.5
    full = jnp.concatenate([kv_past.astype(kv_new.dtype), kv_new[:, :, :NSA_CACHE_ROWS]], axis=1)
    T = full.shape[1]
    n16 = T // CMP_STRIDE
    rows = full[:, :n16 * CMP_STRIDE, :2].reshape(B, n16, CMP_STRIDE, 2, dh)
    part_a = jnp.einsum('bnjcd,cjde->bnce', rows, cmp_w[:, :CMP_STRIDE])
    part_b = jnp.einsum('bnjcd,cjde->bnce', rows, cmp_w[:, CMP_STRIDE:])
    pe_term = jnp.einsum('jcd,cjde->ce', cmp_pe, cmp_w)
    kv_cmp = part_a[:, :-1] + part_b[:, 1:] + pe_term
    n_cmp = kv_cmp.shape[1]
    cmp_start = jnp.arange(n_cmp) * CMP_STRIDE
    cmp_end = cmp_start + (CMP_LEN - 1)
    n_slc = -(-T // SLC_BLOCK)
    slc = jnp.pad(full[:, :, 2:4], ((0, 0), (0, n_slc * SLC_BLOCK - T), (0, 0), (0, 0)))
    slc = slc.reshape(B, n_slc, SLC_BLOCK, 2, dh)
    slc_start = jnp.arange(n_slc) * SLC_BLOCK
    overlap = ((cmp_start[:, None] < slc_start[None, :] + SLC_BLOCK)
               & (cmp_start[:, None] + CMP_LEN > slc_start[None, :])).astype(jnp.float32)
    topk = min(SLC_TOPK, n_slc)
    swa = jnp.concatenate([swa_buf.astype(kv_new.dtype), kv_new[:, :, 4:6]], axis=1)
    qb_len = Q_BLOCK if L % Q_BLOCK == 0 else L
    nb = L // qb_len
    band = WINDOW + qb_len
    jidx = jnp.arange(n_slc)

    def block(inp):
        bi, qb, gb = inp
        start = bi * qb_len
        qpos = pos0 + start + jnp.arange(qb_len)
        s_c = (jnp.einsum('bqhd,bnd->bhqn', qb, kv_cmp[:, :, 0]).astype(jnp.float32) * scale
               + jnp.moveaxis(_t5_bias(rel_bias, qpos[:, None] - cmp_end[None, :]), -1, 0)[None])
        p_c = _masked_softmax(s_c, (cmp_end[None, :] <= qpos[:, None])[None, None])
        o_c = jnp.einsum('bhqn,bnd->bqhd', p_c, kv_cmp[:, :, 1])
        imp = jnp.einsum('bhqn,nj->bqj', p_c, overlap)
        cur = qpos // SLC_BLOCK
        forced = (jidx[None] == 0) | (jidx[None] == cur[:, None]) | (jidx[None] == cur[:, None] - 1)
        score = jnp.where(forced[None], jnp.inf, imp)
        score = jnp.where((jidx[None] > cur[:, None])[None], -jnp.inf, score)
        top_s, top_i = lax.top_k(score, topk)
        sel = jax.vmap(lambda r, i: r[i])(slc, top_i)
        kpos = top_i[..., None] * SLC_BLOCK + jnp.arange(SLC_BLOCK)
        ok_s = (top_s > -jnp.inf)[..., None] & (kpos <= qpos[None, :, None, None])
        s_s = (jnp.einsum('bqhd,bqkjd->bhqkj', qb, sel[..., 0, :]).astype(jnp.float32) * scale
               + jnp.moveaxis(_t5_bias(rel_bias, qpos[None, :, None, None] - kpos), -1, 1))
        p_s = _masked_softmax(s_s.reshape(B, H, qb_len, topk * SLC_BLOCK),
                              ok_s.reshape(B, 1, qb_len, topk * SLC_BLOCK))
        o_s = jnp.einsum('bhqk,bqkd->bqhd', p_s, sel[..., 1, :].reshape(B, qb_len, topk * SLC_BLOCK, dh))
        kw = lax.dynamic_slice_in_dim(swa, start, band, axis=1)
        kwpos = pos0 - WINDOW + start + jnp.arange(band)
        dist = qpos[:, None] - kwpos[None, :]
        ok_w = (dist >= 0) & (dist < WINDOW) & (kwpos[None, :] >= 0)
        s_w = (jnp.einsum('bqhd,bkd->bhqk', qb, kw[:, :, 0]).astype(jnp.float32) * scale
               + jnp.moveaxis(_t5_bias(rel_bias, dist), -1, 0)[None])
        p_w = _masked_softmax(s_w, ok_w[None, None])
        o_w = jnp.einsum('bhqk,bkd->bqhd', p_w, kw[:, :, 1])
        gb = gb.astype(jnp.float32)
        return gb[..., 0:1] * o_c + gb[..., 1:2] * o_s + gb[..., 2:3] * o_w

    o = lax.map(block, (jnp.arange(nb), _to_chunks(q, qb_len), _to_chunks(gates, qb_len)))
    return _from_chunks(o), swa[:, L:]

def _layer(x, pos0, l, st, prm):
    B, L, _ = x.shape
    dt = x.dtype
    f32 = jnp.float32
    pos = pos0 + jnp.arange(L)
    scale = HEAD_DIM ** -0.5
    h = _rmsnorm(x, prm['norm_pre_mix'][l])
    z = h @ prm['w_in'][l]
    (rq, rk, rv, rg, mq, mk, mv, mi, mf, mo, gqkv, ga, gbeta, gg, nq, nkv, ngate) = jnp.split(z, IN_SPLITS, axis=-1)
    heads = lambda t: t.reshape(B, L, -1, HEAD_DIM).astype(f32)
    o_ret, ret_S = _retention(_rope(heads(rq), pos), _rope(heads(rk), pos) * scale, heads(rv), st['ret'].astype(f32))
    y_ret = _head_rmsnorm(o_ret, prm['ret_norm'][l]) * jax.nn.silu(rg.astype(f32))
    o_ml, ml_C, ml_n, ml_m = _mlstm(heads(mq), heads(mk) * scale, heads(mv),
                                    (mi + prm['mlstm_b_i'][l]).astype(f32), (mf + prm['mlstm_b_f'][l]).astype(f32),
                                    st['ml_C'].astype(f32), st['ml_n'].astype(f32), st['ml_m'].astype(f32))
    y_ml = _head_rmsnorm(jax.nn.sigmoid(heads(mo)) * o_ml, prm['mlstm_norm'][l])
    gconv, gdn_conv = _causal_dwconv(st['gdn_conv'], gqkv, prm['gdn_conv_w'][l])
    gq, gk, gv = jnp.split(jax.nn.silu(gconv), 3, axis=-1)
    decay = -jnp.exp(prm['gdn_A_log'][l].astype(f32)) * jax.nn.softplus(ga.astype(f32) + prm['gdn_dt_bias'][l].astype(f32))
    o_g, gdn_S = _gated_delta(_l2norm(heads(gq)) * scale, _l2norm(heads(gk)), heads(gv), decay,
                              jax.nn.sigmoid(gbeta.astype(f32)), st['gdn'].astype(f32))
    y_gdn = _head_rmsnorm(o_g, prm['gdn_norm'][l]) * jax.nn.silu(gg.astype(f32))
    nkv = nkv.reshape(B, L, NSA_KV_ROWS, HEAD_DIM)
    o_n, swa_new = _nsa(nq.reshape(B, L, N_NSA_HEADS, HEAD_DIM),
                        jax.nn.sigmoid(ngate.reshape(B, L, N_NSA_HEADS, 3).astype(f32)),
                        nkv, st['nsa_past'], st['swa'], pos0,
                        prm['nsa_cmp_pe'][l], prm['nsa_cmp_w'][l], prm['rel_bias'])
    y_nsa = o_n.reshape(B, L, D_NSA)
    y = jnp.concatenate([y_ret, y_ml, y_gdn, y_nsa], axis=-1).astype(dt)
    x = x + _rmsnorm(y @ prm['w_out'][l], prm['norm_post_mix'][l])
    h2 = _rmsnorm(x, prm['norm_pre_ffn'][l])
    gate, ffn_conv = _causal_dwconv(st['ffn_conv'], h2 @ prm['w_ffn_gate'][l], prm['ffn_conv_w'][l])
    f = (jax.nn.gelu(gate, approximate=True) * (h2 @ prm['w_ffn_up'][l])) @ prm['w_ffn_down'][l]
    x = x + _rmsnorm(f, prm['norm_post_ffn'][l])
    new = {'nsa': nkv[:, :, :NSA_CACHE_ROWS], 'swa': swa_new.astype(st['swa'].dtype),
           'ret': ret_S.astype(st['ret'].dtype), 'ml_C': ml_C.astype(st['ml_C'].dtype),
           'ml_n': ml_n.astype(st['ml_n'].dtype), 'ml_m': ml_m.astype(st['ml_m'].dtype),
           'gdn': gdn_S.astype(st['gdn'].dtype), 'gdn_conv': gdn_conv, 'ffn_conv': ffn_conv}
    return x, new

def _trunk(x, pos0, states, prm):
    new_states = []
    for l in range(DEPTH):
        x, new = _layer(x, pos0, l, states[l], prm)
        new_states.append(new)
    return x, {k: jnp.stack([s[k] for s in new_states]) for k in STATE_KEYS}

def _zero_states(B, dt):
    return {'nsa_past': jnp.zeros((B, 0, NSA_CACHE_ROWS, HEAD_DIM), dt),
            'swa': jnp.zeros((B, WINDOW, 2, HEAD_DIM), dt),
            'ret': jnp.zeros((B, N_RET_HEADS, HEAD_DIM, HEAD_DIM), dt),
            'ml_C': jnp.zeros((B, N_MLSTM_HEADS, HEAD_DIM, HEAD_DIM), dt),
            'ml_n': jnp.zeros((B, N_MLSTM_HEADS, HEAD_DIM), dt),
            'ml_m': jnp.zeros((B, N_MLSTM_HEADS), dt),
            'gdn': jnp.zeros((B, N_GDN_HEADS, HEAD_DIM, HEAD_DIM), dt),
            'gdn_conv': jnp.zeros((B, GDN_CONV - 1, 3 * D_GDN), dt),
            'ffn_conv': jnp.zeros((B, FFN_CONV - 1, D_FF), dt)}

def setup_inputs(seed: int = 0) -> dict:
    key = jax.random.key(seed)
    ks = iter(jax.random.split(key, 48))
    nrm = lambda shape, s=1.0: s * jax.random.normal(next(ks), shape, jnp.float32)
    gain = lambda shape: 1.0 + nrm(shape, 0.05)
    n_pages = PAST_LEN // PAGE_SIZE
    used = DEC_BATCH * n_pages
    n_pool = used + max(1, used // 4)
    page_table = jax.random.permutation(next(ks), n_pool)[:used].reshape(DEC_BATCH, n_pages).astype(jnp.int32)
    return {
        'x_prompt': nrm((BATCH, SEQ, D_MODEL)),
        'x_sample': nrm((DEC_BATCH, DEC_SEQ, D_MODEL)),
        'cache_nsa_kv': nrm((DEPTH, n_pool, PAGE_SIZE, NSA_CACHE_ROWS, HEAD_DIM)),
        'cache_swa_kv': nrm((DEPTH, DEC_BATCH, WINDOW, 2, HEAD_DIM)),
        'state_ret': nrm((DEPTH, DEC_BATCH, N_RET_HEADS, HEAD_DIM, HEAD_DIM), 0.1),
        'state_mlstm_C': nrm((DEPTH, DEC_BATCH, N_MLSTM_HEADS, HEAD_DIM, HEAD_DIM), 0.1),
        'state_mlstm_n': nrm((DEPTH, DEC_BATCH, N_MLSTM_HEADS, HEAD_DIM), 0.5),
        'state_mlstm_m': nrm((DEPTH, DEC_BATCH, N_MLSTM_HEADS)),
        'state_gdn': nrm((DEPTH, DEC_BATCH, N_GDN_HEADS, HEAD_DIM, HEAD_DIM), 0.1),
        'state_gdn_conv': nrm((DEPTH, DEC_BATCH, GDN_CONV - 1, 3 * D_GDN)),
        'state_ffn_conv': nrm((DEPTH, DEC_BATCH, FFN_CONV - 1, D_FF)),
        'page_table': page_table,
        'rel_bias': nrm((T5_BUCKETS, N_NSA_HEADS), 0.5),
        'norm_pre_mix': gain((DEPTH, D_MODEL)),
        'w_in': nrm((DEPTH, D_MODEL, D_IN), D_MODEL ** -0.5),
        'mlstm_b_i': nrm((DEPTH, N_MLSTM_HEADS), 0.1),
        'mlstm_b_f': jnp.linspace(3.0, 6.0, N_MLSTM_HEADS, dtype=jnp.float32)[None] + nrm((DEPTH, N_MLSTM_HEADS), 0.1),
        'gdn_conv_w': nrm((DEPTH, GDN_CONV, 3 * D_GDN), 0.5),
        'gdn_A_log': jnp.log(jax.random.uniform(next(ks), (DEPTH, N_GDN_HEADS), jnp.float32, 1.0, 16.0)),
        'gdn_dt_bias': jnp.log(jnp.expm1(jax.random.uniform(next(ks), (DEPTH, N_GDN_HEADS), jnp.float32, 0.001, 0.1))),
        'nsa_cmp_pe': nrm((DEPTH, CMP_LEN, 2, HEAD_DIM), 0.02),
        'nsa_cmp_w': nrm((DEPTH, 2, CMP_LEN, HEAD_DIM, HEAD_DIM), (CMP_LEN * HEAD_DIM) ** -0.5),
        'ret_norm': gain((DEPTH, D_RET)),
        'mlstm_norm': gain((DEPTH, D_MLSTM)),
        'gdn_norm': gain((DEPTH, D_GDN)),
        'w_out': nrm((DEPTH, D_MIX, D_MODEL), D_MIX ** -0.5),
        'norm_post_mix': gain((DEPTH, D_MODEL)),
        'norm_pre_ffn': gain((DEPTH, D_MODEL)),
        'w_ffn_gate': nrm((DEPTH, D_MODEL, D_FF), D_MODEL ** -0.5),
        'w_ffn_up': nrm((DEPTH, D_MODEL, D_FF), D_MODEL ** -0.5),
        'ffn_conv_w': nrm((DEPTH, FFN_CONV, D_FF), 0.5),
        'w_ffn_down': nrm((DEPTH, D_FF, D_MODEL), D_FF ** -0.5),
        'norm_post_ffn': gain((DEPTH, D_MODEL)),
    }

def reference(x_prompt, x_sample, cache_nsa_kv, cache_swa_kv, state_ret, state_mlstm_C, state_mlstm_n,
              state_mlstm_m, state_gdn, state_gdn_conv, state_ffn_conv, page_table, rel_bias, norm_pre_mix,
              w_in, mlstm_b_i, mlstm_b_f, gdn_conv_w, gdn_A_log, gdn_dt_bias, nsa_cmp_pe, nsa_cmp_w,
              ret_norm, mlstm_norm, gdn_norm, w_out, norm_post_mix, norm_pre_ffn, w_ffn_gate, w_ffn_up,
              ffn_conv_w, w_ffn_down, norm_post_ffn):
    prm = {'rel_bias': rel_bias, 'norm_pre_mix': norm_pre_mix, 'w_in': w_in, 'mlstm_b_i': mlstm_b_i,
           'mlstm_b_f': mlstm_b_f, 'gdn_conv_w': gdn_conv_w, 'gdn_A_log': gdn_A_log, 'gdn_dt_bias': gdn_dt_bias,
           'nsa_cmp_pe': nsa_cmp_pe, 'nsa_cmp_w': nsa_cmp_w, 'ret_norm': ret_norm, 'mlstm_norm': mlstm_norm,
           'gdn_norm': gdn_norm, 'w_out': w_out, 'norm_post_mix': norm_post_mix, 'norm_pre_ffn': norm_pre_ffn,
           'w_ffn_gate': w_ffn_gate, 'w_ffn_up': w_ffn_up, 'ffn_conv_w': ffn_conv_w, 'w_ffn_down': w_ffn_down,
           'norm_post_ffn': norm_post_ffn}
    p_init = [_zero_states(x_prompt.shape[0], x_prompt.dtype) for _ in range(DEPTH)]
    y_prompt, p_st = _trunk(x_prompt, 0, p_init, prm)
    dec_b = x_sample.shape[0]
    past_len = page_table.shape[1] * PAGE_SIZE
    s_init = [{'nsa_past': cache_nsa_kv[l][page_table].reshape(dec_b, past_len, NSA_CACHE_ROWS, HEAD_DIM),
               'swa': cache_swa_kv[l], 'ret': state_ret[l], 'ml_C': state_mlstm_C[l], 'ml_n': state_mlstm_n[l],
               'ml_m': state_mlstm_m[l], 'gdn': state_gdn[l], 'gdn_conv': state_gdn_conv[l],
               'ffn_conv': state_ffn_conv[l]} for l in range(DEPTH)]
    y_sample, s_st = _trunk(x_sample, past_len, s_init, prm)
    return (y_prompt, y_sample,
            p_st['nsa'], p_st['swa'], p_st['ret'], p_st['ml_C'], p_st['ml_n'], p_st['ml_m'],
            p_st['gdn'], p_st['gdn_conv'], p_st['ffn_conv'],
            s_st['nsa'], s_st['swa'], s_st['ret'], s_st['ml_C'], s_st['ml_n'], s_st['ml_m'],
            s_st['gdn'], s_st['gdn_conv'], s_st['ffn_conv'])


_drawn_inputs = setup_inputs


def setup_inputs(seed=0):
    import zlib

    import numpy as np

    out = dict(_drawn_inputs(seed))
    spreads = {}
    factors = {}
    for name, (base, spread) in spreads.items():
        noise = np.random.default_rng([zlib.crc32(name.encode()), seed]).standard_normal(out[name].shape)
        drawn = base * np.exp(spread * noise) if base else spread * noise
        out[name] = jnp.asarray(drawn.astype(out[name].dtype))
    for name, factor in factors.items():
        out[name] = (out[name] * factor).astype(out[name].dtype)
    return out
```

```python
import math
from contextlib import ExitStack

import numpy as np

import concourse.bass as bass
from concourse import mybir

F32 = mybir.dt.float32
I32 = mybir.dt.int32
ALU = mybir.AluOpType
ACT = mybir.ActivationFunctionType
AX = mybir.AxisListType
ds = bass.ds

P = 128
D = 1024
KD = D // P
SEQ = 1024
NB = 8
DEPTH = 2
NT = SEQ // P
TT = NT + 1
TOK = SEQ + NB
ROWS = TT * P
XROWS = ROWS + P
PADROWS = 8
DIN = 3740
ZC = 374
NZ = DIN // ZC
DFF = 2816
NF = DFF // P
SEG = TOK // 3
DQ = 256
HD = 64
H = 4
NEG = -1.0e30
EPS = 1e-6
PAST = 4096
PAGES = 32
NPOOL = 320
WIN = 512
RQ, RK, RV, RG = 0, 256, 512, 768
MQ, MK, MV, MI, MF, MO = 1024, 1280, 1536, 1792, 1796, 1800
GX, GA, GB, GG = 2056, 2824, 2828, 2832
NQ, NKV, NG = 3088, 3344, 3728


class Link:

    def __init__(self, eng, own):
        self.eng, self.own, self.n = eng, own, {}

    def __call__(self, ins, signal=None):
        s = self.own if signal is None else signal
        self.n[s.num] = self.n.get(s.num, 0) + 1
        ins.then_inc(s, 1)
        self.eng.wait_ge(s, self.n[s.num])


class Loads:

    def __init__(self, eng, sem):
        self.eng, self.sem, self.n = eng, sem, 0

    def __call__(self, out, in_, slow=False):
        self.eng.dma_start(out, in_, allow_slow_non_contiguous=slow).then_inc(self.sem, 16)
        self.n += 16

    def all_in(self):
        self.eng.wait_ge(self.sem, self.n)


class Kit:

    def __init__(self, nc, ctx):
        self.nc, self.ctx, self.sems = nc, ctx, {}

    def sem(self, name):
        if name not in self.sems:
            self.sems[name] = self.ctx.enter_context(self.nc.semaphore(name))
        return self.sems[name]

    def clear(self):
        nums = sorted(s.num for s in self.sems.values())
        self.nc.gpsimd.sem_clear(range(nums[0], nums[-1] + 1))
        self.nc.all_engine_barrier(sem_only=True)


def program(nc, io):
    with ExitStack() as ctx:
        kit = Kit(nc, ctx)
        S = kit.sem

        def sb(c, name, shape, dt=F32):
            return c.enter_context(nc.sbuf_tensor(name, shape, dt))

        ps = ctx.enter_context(nc.psum_tensor("ps", [P, 8, 512], F32))
        ident = sb(ctx, "ident", [P, P])
        mhalf = sb(ctx, "mhalf", [P, 16])
        zrow = sb(ctx, "zrow", [P, 1024])
        x_cur = nc.dram_tensor("x_cur", (XROWS, D), F32, kind="Internal").ap()
        z = nc.dram_tensor("z", (PADROWS + ROWS, DIN), F32, kind="Internal").ap()
        y_mix = nc.dram_tensor("y_mix", (XROWS, D), F32, kind="Internal").ap()
        wdist = nc.dram_tensor("wdist", (H, P, TWC), F32, kind="Internal").ap()
        env = dict(locals())

        with nc.Block() as b:
            @b.vector
            def _(dve):
                link = Link(dve, S("v"))
                link(nc.vector.memset(zrow[:], 0.0))
                link(nc.vector.memset(mhalf[:], -0.5), S("zeroed"))

            @b.sync
            def _(sp):
                ld = Loads(sp, S("ld"))
                ld(ident[:], io["c_ident"])
                ld(x_cur[0:SEQ, :], io["x_prompt"][0])
                ld(x_cur[SEQ:TOK, :], io["x_sample"][:, 0, :])
                sp.wait_ge(S("zeroed"), 1)
                ld(x_cur[TOK:TOK + P, :], zrow[:])
                ld(x_cur[TOK + P:XROWS, :], zrow[0:XROWS - TOK - P, :])
                ld(y_mix[TOK:TOK + P, :], zrow[:])
                ld(y_mix[TOK + P:XROWS, :], zrow[0:XROWS - TOK - P, :])
                for c in range(0, DIN, 1024):
                    n = min(1024, DIN - c)
                    ld(z[0:PADROWS, c:c + n], zrow[0:PADROWS, 0:n])
                ld.all_in()
        kit.clear()
        bias_tables(kit, env, io)

        with nc.Fori(0, DEPTH) as l:
            with ExitStack() as c:
                hT = sb(c, "hT", [P, KD, ROWS])
                norm_to_hT(kit, env, io, l, "norm_pre_mix", hT)
                project_in(kit, env, io, l, hT)
            if io.get("mixers", True):
                mixers(kit, env, io, l)
            with ExitStack() as c:
                fT = sb(c, "fT", [P, NF, TOK])
                with ExitStack() as c2:
                    hT = sb(c2, "hT2", [P, KD, ROWS])
                    project_out(kit, env, io, l, hT)
                    ffn_up(kit, env, io, l, hT, fT)
                ffn_down(kit, env, io, l, fT)

        with nc.Block() as b:
            @b.sync
            def _(sp):
                st = Loads(sp, S("st"))
                st(io["y_prompt"][0], x_cur[0:SEQ, :])
                st(io["y_sample"][:, 0, :], x_cur[SEQ:TOK, :])
                st.all_in()


def rows(t, n=P):
    return ds(t * P, n)


def norm_to_hT(kit, env, io, l, gain, hT):
    nc, S, ps, ident, mhalf, x_cur = kit.nc, kit.sem, env["ps"], env["ident"], env["mhalf"], env["x_cur"]
    with ExitStack() as c:
        xt = c.enter_context(nc.sbuf_tensor("n_x", [P, 2, D], F32))
        xn = c.enter_context(nc.sbuf_tensor("n_xn", [P, D], F32))
        junk = c.enter_context(nc.sbuf_tensor("n_junk", [P, D], F32))
        gT = c.enter_context(nc.sbuf_tensor("n_g", [P, KD], F32))
        ss = c.enter_context(nc.sbuf_tensor("n_ss", [P, 3], F32))
        with nc.Block() as b:
            @b.sync
            def _(sp):
                ld = Loads(sp, S("ld"))
                ld(gT[:], io[gain][ds(l, 1), :].rearrange("a (k p) -> p (a k)", p=P), slow=True)
                ld(xt[:, 0, :], x_cur[0:P, :])
                ld.all_in()
        kit.clear()
        with nc.Fori(0, TT) as t:
            with nc.Block(no_gpsimd_drain=True) as b:
                @b.sync
                def _(sp):
                    ld = Loads(sp, S("next_x"))
                    ld(xt[:, ds((t + 1) % 2, 1), :], x_cur[ds(t * P + P, P), :].rearrange("p (a n) -> p a n", a=1))
                    ld.all_in()

                @b.scalar
                def _(act):
                    nc.scalar.activation(junk[:], xt[:, ds(t % 2, 1), :].rearrange("p a n -> p (a n)"), ACT.Square,
                                         scale=1.0 / 32.0, accum_out=ss[:, 0:1]).then_inc(S("summed"), 1)

                @b.gpsimd
                def _(pool):
                    pool.wait_ge(S("eps_added"), 1)
                    nc.gpsimd.tensor_tensor(ss[:, 2:3], ss[:, 1:2], mhalf[:, 0:1], ALU.pow).then_inc(S("r_ready"), 1)

                @b.vector
                def _(dve):
                    dve.wait_ge(S("summed"), 1)
                    nc.vector.tensor_scalar(ss[:, 1:2], ss[:, 0:1], EPS, None, ALU.add).then_inc(S("eps_added"), 1)
                    dve.wait_ge(S("r_ready"), 1)
                    nc.vector.tensor_scalar(xn[:], xt[:, ds(t % 2, 1), :].rearrange("p a n -> p (a n)"),
                                            ss[:, 2:3], None, ALU.mult).then_inc(S("normed"), 1)
                    for half in range(2):
                        dve.wait_ge(S("turned"), half + 1)
                        nc.vector.tensor_tensor(hT[:, 4 * half:4 * half + 4, rows(t)],
                                                ps[:, half, :].rearrange("p (k n) -> p k n", k=4),
                                                gT[:, 4 * half:4 * half + 4].unsqueeze(2).to_broadcast([P, 4, P]),
                                                ALU.mult).then_inc(S("h_ready"), 1)

                @b.tensor
                def _(pe):
                    pe.wait_ge(S("normed"), 1)
                    for k in range(KD):
                        m = nc.tensor.transpose(ps[:, k // 4, (k % 4) * P:(k % 4) * P + P], xn[:, k * P:k * P + P], ident[:])
                        if k % 4 == 3:
                            m.then_inc(S("turned"), 1)
            kit.clear()


def project_in(kit, env, io, l, hT):
    nc, S, ps, z = kit.nc, kit.sem, env["ps"], env["z"]

    def chunk(i):
        return io["w_in"][ds(l, 1), :, ds(i * ZC, ZC)].rearrange("a (k p) n -> p (a k) n", p=P)

    with ExitStack() as c:
        w = c.enter_context(nc.sbuf_tensor("zi_w", [P, 2, KD, ZC], F32))
        zo = c.enter_context(nc.sbuf_tensor("zi_z", [P, TT, ZC], F32))
        with nc.Block() as b:
            @b.sync
            def _(sp):
                ld = Loads(sp, S("ld"))
                ld(w[:, 0], io["w_in"][ds(l, 1), :, 0:ZC].rearrange("a (k p) n -> p (a k) n", p=P))
                ld.all_in()
        kit.clear()
        with nc.Fori(0, NZ) as i:
            with nc.Block(no_gpsimd_drain=True) as b:
                @b.sync
                def _(sp):
                    ld = Loads(sp, S("next_w"))
                    nxt = (i + 1) % NZ
                    ld(w[:, ds((i + 1) % 2, 1), :, :].rearrange("p a k n -> p (a k) n"), chunk(nxt))
                    st = Loads(sp, S("z_stored"))
                    for t in range(TT):
                        sp.wait_ge(S("z_even") if t % 2 == 0 else S("z_odd"), t // 2 + 1)
                        st(z[PADROWS + t * P:PADROWS + t * P + P, ds(i * ZC, ZC)], zo[:, t, :])
                    ld.all_in()
                    st.all_in()

                @b.tensor
                def _(pe):
                    for t in range(TT):
                        if t == 8:
                            pe.wait_ge(S("z_even"), 1)
                        for k in range(KD):
                            m = nc.tensor.matmul(ps[:, t % 8, 0:ZC], hT[:, k, t * P:t * P + P],
                                                 w[:, ds(i % 2, 1), k, :].rearrange("p a n -> p (a n)"),
                                                 start=(k == 0), stop=(k == KD - 1))
                        m.then_inc(S("z_summed"), 1)

                @b.scalar
                def _(act):
                    for t in range(0, TT, 2):
                        act.wait_ge(S("z_summed"), t + 1)
                        nc.scalar.activation(zo[:, t, :], ps[:, t % 8, 0:ZC], ACT.Copy).then_inc(S("z_even"), 1)

                @b.vector
                def _(dve):
                    for t in range(1, TT, 2):
                        dve.wait_ge(S("z_summed"), t + 1)
                        nc.vector.tensor_copy(zo[:, t, :], ps[:, t % 8, 0:ZC]).then_inc(S("z_odd"), 1)
            kit.clear()


def project_out(kit, env, io, l, hT):
    nc, S, ps, ident, mhalf = kit.nc, kit.sem, env["ps"], env["ident"], env["mhalf"]
    x_cur, y_mix = env["x_cur"], env["y_mix"]
    with ExitStack() as c:
        def sb(name, shape):
            return c.enter_context(nc.sbuf_tensor(name, shape, F32))
        w = sb("po_w", [P, KD, D])
        yt = sb("po_y", [P, 2, D])
        xt = sb("po_x", [P, 2, D])
        ys = sb("po_ys", [P, D])
        yT = sb("po_yT", [P, KD, P])
        gb = sb("po_gb", [P, D])
        gT = sb("po_gT", [P, KD])
        xn = sb("po_xn", [P, D])
        x2 = sb("po_x2", [P, D])
        junk = sb("po_j", [P, D])
        ss = sb("po_ss", [P, 8])
        with nc.Block() as b:
            @b.sync
            def _(sp):
                ld = Loads(sp, S("ld"))
                ld(w[:], io["w_out"][ds(l, 1), :, :].rearrange("a (k p) n -> p (a k) n", p=P))
                ld(gb[:], io["norm_post_mix"][ds(l, 1), :].rearrange("a n -> (a n)").partition_broadcast(P))
                ld(gT[:], io["norm_pre_ffn"][ds(l, 1), :].rearrange("a (k p) -> p (a k)", p=P), slow=True)
                ld(xt[:, 0, :], x_cur[0:P, :])
                ld(yt[:, 0, :], y_mix[0:P, :])
                ld.all_in()
        kit.clear()
        with nc.Fori(0, TT) as t:
            xin = xt[:, ds(t % 2, 1), :].rearrange("p a n -> p (a n)")
            with nc.Block(no_gpsimd_drain=True) as b:
                @b.sync
                def _(sp):
                    ld = Loads(sp, S("next_x"))
                    for buf, src in ((xt, x_cur), (yt, y_mix)):
                        ld(buf[:, ds((t + 1) % 2, 1), :], src[ds(t * P + P, P), :].rearrange("p (a n) -> p a n", a=1))
                    sp.wait_ge(S("x2_ready"), 1)
                    st = Loads(sp, S("x_stored"))
                    st(x_cur[rows(t), :], x2[:])
                    ld.all_in()
                    st.all_in()

                @b.tensor
                def _(pe):
                    pe.wait_ge(S("y_here"), 1)
                    for k in range(KD):
                        m = nc.tensor.transpose(ps[:, 2 + k // 4, (k % 4) * P:(k % 4) * P + P],
                                                ys[:, k * P:k * P + P], ident[:])
                    m.then_inc(S("y_turned"), 1)
                    pe.wait_ge(S("yT_ready"), 2)
                    for n in range(2):
                        for k in range(KD):
                            m = nc.tensor.matmul(ps[:, n, :], yT[:, k, :], w[:, k, n * 512:n * 512 + 512],
                                                 start=(k == 0), stop=(k == KD - 1))
                    m.then_inc(S("mixed"), 1)
                    pe.wait_ge(S("xn_ready"), 1)
                    for k in range(KD):
                        m = nc.tensor.transpose(ps[:, 4 + k // 4, (k % 4) * P:(k % 4) * P + P],
                                                xn[:, k * P:k * P + P], ident[:])
                    m.then_inc(S("x_turned"), 1)

                @b.scalar
                def _(act):
                    nc.scalar.activation(ys[:], yt[:, ds(t % 2, 1), :].rearrange("p a n -> p (a n)"), ACT.Copy).then_inc(S("y_here"), 1)
                    act.wait_ge(S("y_turned"), 1)
                    nc.scalar.activation(yT[:, 4:8, :].rearrange("p k n -> p (k n)"), ps[:, 3, :], ACT.Copy).then_inc(S("yT_ready"), 1)
                    act.wait_ge(S("mixed"), 1)
                    nc.scalar.activation(junk[:], ps[:, 0:2, :].rearrange("p a n -> p (a n)"), ACT.Square,
                                         scale=1.0 / 32.0, accum_out=ss[:, 0:1]).then_inc(S("summed"), 1)
                    act.wait_ge(S("x2_ready"), 1)
                    act.wait_ge(S("summed"), 1)
                    nc.scalar.activation(junk[:], x2[:], ACT.Square,
                                         scale=1.0 / 32.0, accum_out=ss[:, 3:4]).then_inc(S("summed"), 1)

                @b.gpsimd
                def _(pool):
                    pool.wait_ge(S("eps_added"), 1)
                    nc.gpsimd.tensor_tensor(ss[:, 2:3], ss[:, 1:2], mhalf[:, 0:1], ALU.pow).then_inc(S("r_ready"), 1)
                    pool.wait_ge(S("eps_added"), 2)
                    nc.gpsimd.tensor_tensor(ss[:, 5:6], ss[:, 4:5], mhalf[:, 0:1], ALU.pow).then_inc(S("r_ready"), 1)

                @b.vector
                def _(dve):
                    link = Link(dve, S("v"))
                    dve.wait_ge(S("y_turned"), 1)
                    nc.vector.tensor_copy(yT[:, 0:4, :].rearrange("p k n -> p (k n)"), ps[:, 2, :]).then_inc(S("yT_ready"), 1)
                    dve.wait_ge(S("summed"), 1)
                    nc.vector.tensor_scalar(ss[:, 1:2], ss[:, 0:1], EPS, None, ALU.add).then_inc(S("eps_added"), 1)
                    dve.wait_ge(S("r_ready"), 1)
                    link(nc.vector.scalar_tensor_tensor(x2[:], ps[:, 0:2, :].rearrange("p a n -> p (a n)"), ss[:, 2:3],
                                                        gb[:], ALU.mult, ALU.mult))
                    link(nc.vector.tensor_tensor(x2[:], x2[:], xin, ALU.add), S("x2_ready"))
                    dve.wait_ge(S("summed"), 2)
                    nc.vector.tensor_scalar(ss[:, 4:5], ss[:, 3:4], EPS, None, ALU.add).then_inc(S("eps_added"), 1)
                    dve.wait_ge(S("r_ready"), 2)
                    nc.vector.tensor_scalar(xn[:], x2[:], ss[:, 5:6], None, ALU.mult).then_inc(S("xn_ready"), 1)
                    dve.wait_ge(S("x_turned"), 1)
                    for half in range(2):
                        nc.vector.tensor_tensor(hT[:, 4 * half:4 * half + 4, rows(t)],
                                                ps[:, 4 + half, :].rearrange("p (k n) -> p k n", k=4),
                                                gT[:, 4 * half:4 * half + 4].unsqueeze(2).to_broadcast([P, 4, P]),
                                                ALU.mult).then_inc(S("h_ready"), 1)

            kit.clear()


def ffn_up(kit, env, io, l, hT, fT):
    nc, S, ps, ident = kit.nc, kit.sem, env["ps"], env["ident"]
    with ExitStack() as c:
        def sb(name, shape):
            return c.enter_context(nc.sbuf_tensor(name, shape, F32))
        rows_in = sb("fu_rin", [19, DFF])
        rows_out = sb("fu_rout", [10, DFF])
        side = sb("fu_side", [P, NF, 19])
        w = [sb(f"fu_w{q}", [P, 2, KD, P]) for q in range(2)]
        g = sb("fu_g", [P, 2, 2 + TOK])
        cv = sb("fu_c", [P, 2, TOK])

        def load_w(ld, q, f):
            for j, name in enumerate(("w_ffn_gate", "w_ffn_up")):
                ld(w[q][:, j], io[name][ds(l, 1), :, f].rearrange("a (k p) n -> p (a k) n", p=P))

        with nc.Block() as b:
            @b.sync
            def _(sp):
                ld = Loads(sp, S("ld"))
                ld(rows_in[0:16, :], io["state_ffn_conv"][ds(l, 1)].rearrange("a b r n -> (a b r) n"))
                ld(rows_in[16:19, :], io["ffn_conv_w"][ds(l, 1)].rearrange("a r n -> (a r) n"))
                load_w(ld, 0, slice(0, P))
                ld.all_in()

            @b.tensor
            def _(pe):
                pe.wait_ge(S("ld"), 16 * 4)
                for f in range(NF):
                    m = nc.tensor.transpose(ps[:, 0, f * 19:f * 19 + 19], rows_in[:, f * P:f * P + P], ident[0:19, 0:19])
                m.then_inc(S("turned"), 1)

            @b.vector
            def _(dve):
                nc.vector.memset(g[:, :, 0:2], 0.0).then_inc(S("v"), 1)
                dve.wait_ge(S("turned"), 1)
                nc.vector.tensor_copy(side[:].rearrange("p f r -> p (f r)"), ps[:, 0, 0:NF * 19]).then_inc(S("v"), 1)
        kit.clear()

        with nc.Fori(0, NF // 2) as i:
            with nc.Block(no_gpsimd_drain=True) as b:
                @b.sync
                def _(sp):
                    ld = Loads(sp, S("w1_loaded"))
                    load_w(ld, 1, ds(i * 2 * P + P, P))
                    nxt = Loads(sp, S("next_w0"))
                    sp.wait_ge(S("summed"), 6)
                    load_w(nxt, 0, ds(((i + 1) % (NF // 2)) * 2 * P, P))
                    ld.all_in()
                    nxt.all_in()

                @b.tensor
                def _(pe):
                    m8 = 0
                    for q in range(2):
                        if q == 1:
                            pe.wait_ge(S("w1_loaded"), 32)
                        for j in range(2):
                            for s in range(3):
                                if m8 in (8, 9, 10):
                                    pe.wait_ge(S("gate_read"), m8 - 7)
                                if m8 == 11:
                                    pe.wait_ge(S("f_done"), 1)
                                for k in range(KD):
                                    m = nc.tensor.matmul(ps[:, m8 % 8, 0:SEG], w[q][:, j, k, :],
                                                         hT[:, k, s * SEG:s * SEG + SEG],
                                                         start=(k == 0), stop=(k == KD - 1))
                                m.then_inc(S("summed"), 1)
                                m8 += 1
                    pe.wait_ge(S("f_done"), 2)
                    pe.wait_ge(S("gate_read"), 6)
                    for q in range(2):
                        m = nc.tensor.transpose(ps[0:10, 5, q * P:q * P + P], g[:, q, SEQ:SEQ + 10], ident[:])
                    m.then_inc(S("rows_turned"), 1)

                @b.scalar
                def _(act):
                    for q in range(2):
                        for s in range(3):
                            act.wait_ge(S("summed"), 6 * q + s + 1)
                            nc.scalar.activation(g[:, q, 2 + s * SEG:2 + s * SEG + SEG], ps[:, (6 * q + s) % 8, 0:SEG],
                                                 ACT.Copy).then_inc(S("gate_read"), 1)
                        act.wait_ge(S("conved"), q + 1)
                        nc.scalar.activation(cv[:, q, :], cv[:, q, :], ACT.Gelu_apprx_tanh).then_inc(S("gelu"), 1)
                    act.wait_ge(S("rows_turned"), 1)
                    nc.scalar.activation(rows_out[:, ds(i * 2 * P, 2 * P)], ps[0:10, 5, 0:2 * P], ACT.Copy).then_inc(S("rows_ready"), 1)

                @b.vector
                def _(dve):
                    link = Link(dve, S("v"))
                    for q in range(2):
                        def cw(r):
                            return side[:, ds(2 * i + q, 1), r:r + 1].rearrange("p a b -> p (a b)")
                        past = side[:, ds(2 * i + q, 1), 0:16].rearrange("p a (b r) -> p (a b) r", r=2)
                        cp, cs = cv[:, q, 0:SEQ], cv[:, q, SEQ:TOK]
                        dve.wait_ge(S("gate_read"), 3 * q + 3)
                        link(nc.vector.tensor_scalar(cp, g[:, q, 0:SEQ], cw(16), None, ALU.mult))
                        link(nc.vector.scalar_tensor_tensor(cp, g[:, q, 1:1 + SEQ], cw(17), cp, ALU.mult, ALU.add))
                        link(nc.vector.scalar_tensor_tensor(cp, g[:, q, 2:2 + SEQ], cw(18), cp, ALU.mult, ALU.add))
                        link(nc.vector.tensor_scalar(cs, past[:, :, 0], cw(16), None, ALU.mult))
                        link(nc.vector.scalar_tensor_tensor(cs, past[:, :, 1], cw(17), cs, ALU.mult, ALU.add))
                        link(nc.vector.scalar_tensor_tensor(cs, g[:, q, 2 + SEQ:2 + TOK], cw(18), cs, ALU.mult, ALU.add), S("conved"))
                        dve.wait_ge(S("gelu"), q + 1)
                        for s in range(3):
                            dve.wait_ge(S("summed"), 6 * q + 3 + s + 1)
                            m = nc.vector.tensor_tensor(
                                fT[:, ds(2 * i + q, 1), s * SEG:s * SEG + SEG].rearrange("p a n -> p (a n)"),
                                cv[:, q, s * SEG:s * SEG + SEG], ps[:, (6 * q + 3 + s) % 8, 0:SEG], ALU.mult)
                            if s == 2:
                                m.then_inc(S("f_done"), 1)
            kit.clear()
        with nc.Block() as b:
            @b.sync
            def _(sp):
                st = Loads(sp, S("st"))
                st(io["p_ffn_conv"][ds(l, 1)].rearrange("a b r n -> (a b r) n"), rows_out[0:2, :])
                st(io["s_ffn_conv"][ds(l, 1), :, 1, :].rearrange("a b n -> (a b) n"), rows_out[2:10, :])
                st(io["s_ffn_conv"][ds(l, 1), :, 0, :], io["state_ffn_conv"][ds(l, 1), :, 1, :])
                st.all_in()
        kit.clear()


def ffn_down(kit, env, io, l, fT):
    nc, S, ps, mhalf, x_cur = kit.nc, kit.sem, env["ps"], env["mhalf"], env["x_cur"]
    with ExitStack() as c:
        def sb(name, shape):
            return c.enter_context(nc.sbuf_tensor(name, shape, F32))
        y = sb("fd_y", [P, TT, D])
        gb = sb("fd_gb", [P, D])
        with ExitStack() as c2:
            w = c2.enter_context(nc.sbuf_tensor("fd_w", [P, 2, NF, DQ], F32))

            def quarter(i):
                return io["w_ffn_down"][ds(l, 1), :, ds(i * DQ, DQ)].rearrange("a (f p) n -> p (a f) n", p=P)

            with nc.Block() as b:
                @b.vector
                def _(dve):
                    nc.vector.memset(y[:, NT, :], 0.0).then_inc(S("v"), 1)

                @b.sync
                def _(sp):
                    ld = Loads(sp, S("ld"))
                    ld(w[:, 0], io["w_ffn_down"][ds(l, 1), :, 0:DQ].rearrange("a (f p) n -> p (a f) n", p=P))
                    ld(gb[:], io["norm_post_ffn"][ds(l, 1), :].rearrange("a n -> (a n)").partition_broadcast(P))
                    ld.all_in()
            kit.clear()
            with nc.Fori(0, D // DQ) as i:
                with nc.Block(no_gpsimd_drain=True) as b:
                    @b.sync
                    def _(sp):
                        ld = Loads(sp, S("next_w"))
                        ld(w[:, ds((i + 1) % 2, 1), :, :].rearrange("p a f n -> p (a f) n"), quarter((i + 1) % (D // DQ)))
                        ld.all_in()

                    @b.tensor
                    def _(pe):
                        for t in range(TT):
                            n = min(P, TOK - t * P)
                            if t == 8:
                                pe.wait_ge(S("y_even"), 1)
                            for f in range(NF):
                                m = nc.tensor.matmul(ps[0:n, t % 8, 0:DQ], fT[:, f, t * P:t * P + n],
                                                     w[:, ds(i % 2, 1), f, :].rearrange("p a n -> p (a n)"),
                                                     start=(f == 0), stop=(f == NF - 1))
                            m.then_inc(S("summed"), 1)

                    @b.scalar
                    def _(act):
                        for t in range(0, TT, 2):
                            n = min(P, TOK - t * P)
                            act.wait_ge(S("summed"), t + 1)
                            nc.scalar.activation(y[0:n, t, ds(i * DQ, DQ)], ps[0:n, t % 8, 0:DQ], ACT.Copy).then_inc(S("y_even"), 1)

                    @b.vector
                    def _(dve):
                        for t in range(1, TT, 2):
                            dve.wait_ge(S("summed"), t + 1)
                            nc.vector.tensor_copy(y[:, t, ds(i * DQ, DQ)], ps[:, t % 8, 0:DQ]).then_inc(S("y_odd"), 1)
                kit.clear()
        xt = sb("fd_x", [P, 2, D])
        x2 = sb("fd_x2", [P, D])
        junk = sb("fd_j", [P, D])
        ss = sb("fd_ss", [P, 3])
        with nc.Block() as b:
            @b.sync
            def _(sp):
                ld = Loads(sp, S("ld"))
                ld(xt[:, 0, :], x_cur[0:P, :])
                ld.all_in()
        kit.clear()
        with nc.Fori(0, TT) as t:
            yin = y[:, ds(t, 1), :].rearrange("p a n -> p (a n)")
            with nc.Block(no_gpsimd_drain=True) as b:
                @b.sync
                def _(sp):
                    ld = Loads(sp, S("next_x"))
                    ld(xt[:, ds((t + 1) % 2, 1), :], x_cur[ds(t * P + P, P), :].rearrange("p (a n) -> p a n", a=1))
                    sp.wait_ge(S("x2_ready"), 1)
                    st = Loads(sp, S("x_stored"))
                    st(x_cur[rows(t), :], x2[:])
                    ld.all_in()
                    st.all_in()

                @b.scalar
                def _(act):
                    nc.scalar.activation(junk[:], yin, ACT.Square, scale=1.0 / 32.0, accum_out=ss[:, 0:1]).then_inc(S("summed"), 1)

                @b.gpsimd
                def _(pool):
                    pool.wait_ge(S("eps_added"), 1)
                    nc.gpsimd.tensor_tensor(ss[:, 2:3], ss[:, 1:2], mhalf[:, 0:1], ALU.pow).then_inc(S("r_ready"), 1)

                @b.vector
                def _(dve):
                    link = Link(dve, S("v"))
                    dve.wait_ge(S("summed"), 1)
                    nc.vector.tensor_scalar(ss[:, 1:2], ss[:, 0:1], EPS, None, ALU.add).then_inc(S("eps_added"), 1)
                    dve.wait_ge(S("r_ready"), 1)
                    link(nc.vector.scalar_tensor_tensor(x2[:], yin, ss[:, 2:3], gb[:], ALU.mult, ALU.mult))
                    link(nc.vector.tensor_tensor(x2[:], x2[:], xt[:, ds(t % 2, 1), :].rearrange("p a n -> p (a n)"), ALU.add), S("x2_ready"))
            kit.clear()


def bc(ap, n, shape):
    return ap.unsqueeze(2).to_broadcast(shape)


def recurrent_prompt(kit, env, io, l):
    nc, S, ps, ident, mhalf = kit.nc, kit.sem, env["ps"], env["ident"], env["mhalf"]
    z, y_mix = env["z"], env["y_mix"]
    V = nc.vector
    A = nc.scalar
    W3 = 3 * H * HD
    LEV = 7
    with ExitStack() as c:
        def sb(name, shape):
            return c.enter_context(nc.sbuf_tensor(name, shape, F32))
        zt = sb("r_z", [P, 2, GG + 256])
        zs = sb("r_zs", [P, 2, 3, W3])
        rope = sb("r_rope", [P, 2, 64])
        retD = sb("r_retD", [P, H, P])
        xi = sb("r_xi", [P, 3, H])
        upper = sb("r_upper", [P, P])
        mask = sb("r_mask", [P, P])
        maskT = sb("r_maskT", [P, P])
        last = sb("r_last", [P, P])
        ones = sb("r_ones", [P, P])
        lev = sb("r_lev", [P, LEV, P])
        levT = sb("r_levT", [P, LEV, P])
        gains = sb("r_gains", [P, 3, 256])
        gates = sb("r_gates", [P, 16])
        cw = sb("r_cw", [P, 4, W3])
        Sret = sb("r_S", [HD, H, HD])
        Caug = sb("r_C", [HD, H, HD + 1])
        Sgdn = sb("r_G", [HD, H, HD])
        mprev = sb("r_m", [P, H])
        qk = sb("r_qk", [P, 2 * H, HD])
        qkw = sb("r_qkw", [P, 2, 2 * H, HD // 2])
        kb = sb("r_kb", [P, H, HD])
        qT = sb("r_qT", [HD, H, P])
        kT = sb("r_kT", [HD, H, P])
        kbT = sb("r_kbT", [HD, H, P])
        v = sb("r_v", [P, H, HD + 1])
        pT = sb("r_pT", [P, H, P])
        w1 = sb("r_w1", [P, H, P])
        w2 = sb("r_w2", [P, H, P])
        kz = sb("r_kz", [P, H, HD])
        o = sb("r_o", [P, H, HD + 1])
        sq = sb("r_sq", [P, H, HD])
        sig = sb("r_sig", [P, 3, 256])
        sm = sb("r_sm", [P, 32, H])
        X = sb("r_X", [P, H, P])
        XT = sb("r_XT", [P, H, P])
        NLT = sb("r_NT", [P, H, P])
        NM = sb("r_NM", [P, H, P])
        Y = sb("r_Y", [P, H, P])
        rk = sb("r_rk", [P, H, HD])
        rv = sb("r_rv", [P, H, HD])
        wTn = sb("r_wTn", [HD, H, P])
        dl = sb("r_dl", [P, H, HD])
        xc = sb("r_xc", [P, W3])
        xc2 = sb("r_xc2", [P, W3])
        y = sb("r_y", [P, 3, 256])

        def loads(ld, t, q):
            ld(zt[:, q, :].rearrange("p a n -> p (a n)"), z[ds(t * P + PADROWS, P), 0:GG + 256])
            for j in range(3):
                ld(zs[:, q, j, :].rearrange("p a n -> p (a n)"), z[ds(t * P + PADROWS - 3 + j, P), GX:GX + W3])
            ld(rope[:, q, :].rearrange("p a n -> p (a n)"), io["c_rope"][ds(t * P, P), :])

        with nc.Block() as b:
            @b.sync
            def _(sp):
                ld = Loads(sp, S("ld"))
                ld(retD[:].rearrange("p h n -> p (h n)"), io["c_retD"])
                ld(xi[:].rearrange("p a h -> p (a h)"), io["c_xi"])
                ld(upper[:], io["c_upper"])
                ld(mask[:], io["c_mask"])
                ld(maskT[:], io["c_maskT"])
                ld(last[:], io["c_last"])
                ld(lev[:].rearrange("p a n -> p (a n)"), io["c_lev"])
                ld(levT[:].rearrange("p a n -> p (a n)"), io["c_levT"])
                for j, name in enumerate(("ret_norm", "mlstm_norm", "gdn_norm")):
                    ld(gains[:, j, :], io[name][ds(l, 1), :].rearrange("a n -> (a n)").partition_broadcast(P))
                for j, name in enumerate(("mlstm_b_i", "mlstm_b_f", "gdn_dt_bias", "gdn_A_log")):
                    ld(gates[:, 4 * j:4 * j + 4], io[name][ds(l, 1), :].rearrange("a n -> (a n)").partition_broadcast(P))
                ld(cw[:].rearrange("p a n -> p (a n)"), io["gdn_conv_w"][ds(l, 1)].rearrange("a j n -> (a j n)").partition_broadcast(P))
                loads(ld, 0, slice(0, 1))
                ld.all_in()

            @b.vector
            def _(dve):
                link = Link(dve, S("v"))
                link(V.memset(Sret[:], 0.0))
                link(V.memset(Caug[:], 0.0))
                link(V.memset(Sgdn[:], 0.0))
                link(V.memset(mprev[:], 0.0))
                link(V.memset(ones[:], 1.0))
                link(V.memset(v[:], 1.0))
                dve.wait_ge(S("aexp"), 1)
                link(V.tensor_scalar(gates[:, 12:16], gates[:, 12:16], -1.0, None, ALU.mult))

            @b.scalar
            def _(act):
                act.wait_ge(S("ld"), 16 * 21)
                A.activation(gates[:, 12:16], gates[:, 12:16], ACT.Exp).then_inc(S("aexp"), 1)
        kit.clear()

        with nc.Fori(0, NT) as t:
            par = ds(t % 2, 1)

            def zv(a, n=256):
                return zt[:, par, a:a + n].rearrange("p a n -> p (a n)")

            def heads(a, n=H):
                return zt[:, par, a:a + n * HD].rearrange("p a (h d) -> p (a h) d", d=HD)

            def s4(i):
                return sm[:, i, :]

            def b64(ap):
                return bc(ap, H, [P, H, HD])

            def flat(ap):
                return ap.rearrange("p h n -> p (h n)")

            def bank(i):
                return ps[:, i, :].rearrange("p (h n) -> p h n", h=H)

            def b512(ap):
                return ap.unsqueeze(1).to_broadcast([P, H, P])

            (R_SS, R_R, IC, LF, E1, BC, CC, MX, MU, MM, GIN, EM, DEN, RD, WEND, GEND, G, BETA, GCOL, EG, GE, EGE,
             WE, BEG, NGC, R_SS2, MEND, ABS, MIN0, TMP) = range(30)
            l2 = y[:, 0, 0:8]

            with nc.Block(no_gpsimd_drain=True) as b:
                @b.sync
                def _(sp):
                    ld = Loads(sp, S("next_z"))
                    t1 = (t + 1) % NT
                    loads(ld, t1, ds((t + 1) % 2, 1))
                    sp.wait_ge(S("y_ready"), 3)
                    st = Loads(sp, S("y_stored"))
                    st(y_mix[rows(t), 0:768], y[:].rearrange("p a n -> p (a n)"))
                    ld.all_in()
                    st.all_in()

                @b.gpsimd
                def _(pool):
                    for j, (src, dst) in enumerate(((sm[:, R_SS, :], sm[:, R_R, :]), (sm[:, R_SS, :], sm[:, R_R, :]),
                                                    (xc2[:, 0:8], xc2[:, 8:16]), (sm[:, R_SS, :], sm[:, R_R, :]))):
                        pool.wait_ge(S("squares"), j + 1)
                        n = 8 if j == 2 else 4
                        nc.gpsimd.tensor_tensor(dst, src, mhalf[:, 0:n], ALU.pow).then_inc(S("r_ready"), 1)

                @b.tensor
                def _(pe):
                    def turn(n, src, count):
                        for h in range(H):
                            m = nc.tensor.transpose(ps[0:HD, n, h * P:h * P + P], src[:, h, :], ident[:])
                        m.then_inc(S("turned"), 1)

                    def mm4(out, lhs, rhs, signal, start=True, stop=True):
                        for h in range(H):
                            m = nc.tensor.matmul(out(h), lhs(h), rhs(h), start=start, stop=stop)
                        m.then_inc(signal, 1)
                    pe.wait_ge(S("roped"), 1)
                    turn(0, qk[:, 0:4, :], 1)
                    turn(1, qk[:, 4:8, :], 1)
                    pe.wait_ge(S("qkT"), 2)
                    mm4(lambda h: ps[:, 2, h * P:h * P + P], lambda h: kT[:, h, :], lambda h: qT[:, h, :], S("scores"))
                    mm4(lambda h: ps[:, 6, h * HD:h * HD + HD], lambda h: qT[:, h, :], lambda h: Sret[:, h, :], S("inter"))
                    pe.wait_ge(S("p_ready"), 1)
                    pe.wait_ge(S("v_ready"), 1)
                    mm4(lambda h: ps[:, 3, h * HD:h * HD + HD], lambda h: pT[:, h, :], lambda h: v[:, h, 0:HD], S("intra"))
                    pe.wait_ge(S("kz_ready"), 1)
                    mm4(lambda h: ps[0:HD, 4, h * HD:h * HD + HD], lambda h: kz[:, h, :], lambda h: v[:, h, 0:HD], S("dstate"))
                    pe.wait_ge(S("gates_in"), 1)
                    nc.tensor.matmul(ps[:, 5, 0:4], upper[:], s4(LF), start=True, stop=True).then_inc(S("bcol"), 1)
                    pe.wait_ge(S("ccol"), 1)
                    mm4(lambda h: ps[:, 6, h * P:h * P + P], lambda h: w1[:, h, :], lambda h: ident[:], S("crow"))
                    pe.wait_ge(S("mucol"), 1)
                    nc.tensor.matmul(ps[:, 5, 16:24], last[:], sm[:, MU:MU + 2, :].rearrange("p a h -> p (a h)"), start=True, stop=True).then_inc(S("mend"), 1)
                    mm4(lambda h: ps[:, 7, h * P:h * P + P], lambda h: w2[:, h, :], lambda h: ident[:], S("murow"))
                    pe.wait_ge(S("qk_ml"), 1)
                    turn(0, qk[:, 0:4, :], 1)
                    turn(1, qk[:, 4:8, :], 1)
                    pe.wait_ge(S("qkT"), 4)
                    mm4(lambda h: ps[:, 2, h * P:h * P + P], lambda h: kT[:, h, :], lambda h: qT[:, h, :], S("scores"))
                    pe.wait_ge(S("ret_out"), 1)
                    mm4(lambda h: ps[:, 4, h * (HD + 1):(h + 1) * (HD + 1)], lambda h: qT[:, h, :], lambda h: Caug[:, h, :], S("inter"))
                    pe.wait_ge(S("p_ready"), 2)
                    pe.wait_ge(S("v_ready"), 2)
                    mm4(lambda h: ps[:, 3, h * (HD + 1):(h + 1) * (HD + 1)], lambda h: pT[:, h, :], lambda h: v[:, h, :], S("intra"))
                    pe.wait_ge(S("kz_ready"), 2)
                    pe.wait_ge(S("maxed"), 1)
                    mm4(lambda h: ps[0:HD, 6, h * (HD + 1):(h + 1) * (HD + 1)], lambda h: kz[:, h, :], lambda h: v[:, h, :], S("dstate"))
                    pe.wait_ge(S("g_ready"), 1)
                    nc.tensor.matmul(ps[:, 5, 0:4], upper[:], s4(G), start=True, stop=True)
                    nc.tensor.matmul(ps[:, 5, 4:8], ones[:], s4(G), start=True, stop=True).then_inc(S("gcol"), 1)
                    mm4(lambda h: ps[:, 7, h * P:h * P + P], lambda h: w1[:, h, :], lambda h: upper[:], S("grow"))
                    pe.wait_ge(S("qk_gdn"), 1)
                    turn(0, qk[:, 0:4, :], 1)
                    turn(1, qk[:, 4:8, :], 1)
                    pe.wait_ge(S("p_ready"), 2)
                    turn(2, kb, 1)
                    pe.wait_ge(S("qkT"), 7)
                    pe.wait_ge(S("ml_read"), 1)
                    mm4(lambda h: ps[:, 3, h * P:h * P + P], lambda h: kbT[:, h, :], lambda h: kT[:, h, :], S("nn"))
                    mm4(lambda h: ps[:, 4, h * P:h * P + P], lambda h: kT[:, h, :], lambda h: kbT[:, h, :], S("nn"))
                    mm4(lambda h: ps[:, 0, h * P:h * P + P], lambda h: kT[:, h, :], lambda h: qT[:, h, :], S("nn"))
                    for s in range(1, LEV):
                        pe.wait_ge(S("nm"), s)
                        pe.wait_ge(S("xt"), s)
                        mm4(lambda h: ps[:, 1, h * P:h * P + P], lambda h: NM[:, h, :], lambda h: X[:, h, :], S("ylev"))
                        pe.wait_ge(S("ysb"), s)
                        if s < LEV - 1:
                            mm4(lambda h: ps[:, 2, h * P:h * P + P], lambda h: XT[:, h, :], lambda h: Y[:, h, :], S("xy"))
                        mm4(lambda h: ps[:, 6, h * P:h * P + P], lambda h: Y[:, h, :], lambda h: XT[:, h, :], S("xy"))
                    pe.wait_ge(S("xt"), LEV)
                    pe.wait_ge(S("rhs"), 1)
                    mm4(lambda h: ps[0:HD, 7, h * P:h * P + P], lambda h: rk[:, h, :], lambda h: XT[:, h, :], S("wt"))
                    pe.wait_ge(S("wtn"), 1)
                    for h in range(H):
                        nc.tensor.matmul(ps[:, 1, h * HD:h * HD + HD], XT[:, h, :], rv[:, h, :], start=True, stop=False)
                        m = nc.tensor.matmul(ps[:, 1, h * HD:h * HD + HD], wTn[:, h, :], Sgdn[:, h, :], start=False, stop=True)
                    m.then_inc(S("delta"), 1)
                    mm4(lambda h: ps[:, 5, h * HD:h * HD + HD], lambda h: qT[:, h, :], lambda h: Sgdn[:, h, :], S("inter"))
                    pe.wait_ge(S("dl"), 1)
                    mm4(lambda h: ps[:, 3, h * HD:h * HD + HD], lambda h: pT[:, h, :], lambda h: dl[:, h, :], S("intra"))
                    mm4(lambda h: ps[0:HD, 4, h * HD:h * HD + HD], lambda h: kz[:, h, :], lambda h: dl[:, h, :], S("dstate"))

                @b.scalar
                def _(act):
                    link = Link(act, S("a"))
                    for j, a in enumerate((RG, MO, GG)):
                        link(A.activation(sig[:, j, :], zv(a), ACT.Exp, scale=-1.0))
                    nc.scalar.activation(sig[:], sig[:], ACT.Copy, bias=1.0).then_inc(S("sig_exp"), 1)
                    A.activation(v[:, :, 0:HD], heads(RV), ACT.Copy).then_inc(S("v_ready"), 1)
                    act.wait_ge(S("turned"), 1)
                    A.activation(flat(qT[:]), ps[0:HD, 0, :], ACT.Copy).then_inc(S("qkT"), 1)
                    act.wait_ge(S("turned"), 2)
                    A.activation(flat(kT[:]), ps[0:HD, 1, :], ACT.Copy).then_inc(S("qkT"), 1)
                    act.wait_ge(S("gate_abs"), 1)
                    link(A.activation(s4(E1), s4(ABS), ACT.Exp, scale=-1.0))
                    link(A.activation(s4(E1), s4(E1), ACT.Ln, bias=1.0), S("softplus"))
                    act.wait_ge(S("shifted"), 1)
                    for h in range(H):
                        m = A.activation(w2[:, h, :], w2[:, h, :], ACT.Exp, bias=sm[:, CC, h:h + 1])
                    m.then_inc(S("weights"), 1)
                    act.wait_ge(S("exps_in"), 1)
                    link(A.activation(s4(GIN), s4(GIN), ACT.Exp))
                    link(A.activation(s4(EM), s4(MM), ACT.Exp, scale=-1.0))
                    link(A.activation(s4(WEND), s4(WEND), ACT.Exp))
                    link(A.activation(s4(GEND), s4(GEND), ACT.Exp), S("exps_out"))
                    act.wait_ge(S("turned"), 3)
                    A.activation(flat(qT[:]), ps[0:HD, 0, :], ACT.Copy).then_inc(S("qkT"), 1)
                    act.wait_ge(S("turned"), 4)
                    A.activation(flat(kT[:]), ps[0:HD, 1, :], ACT.Copy).then_inc(S("qkT"), 1)
                    act.wait_ge(S("dstate"), 1)
                    A.activation(v[:, :, 0:HD], heads(MV), ACT.Copy).then_inc(S("v_ready"), 1)
                    act.wait_ge(S("conved"), 1)
                    link(A.activation(xc2[:], xc[:], ACT.Exp, scale=-1.0))
                    link(A.activation(xc2[:], xc2[:], ACT.Copy, bias=1.0))
                    link(A.activation(s4(BETA), zv(GB, 4), ACT.Exp, scale=-1.0), S("silu_exp"))
                    act.wait_ge(S("gate_abs"), 2)
                    link(A.activation(s4(E1), s4(ABS), ACT.Exp, scale=-1.0))
                    link(A.activation(s4(E1), s4(E1), ACT.Ln, bias=1.0), S("softplus"))
                    act.wait_ge(S("gexp_in"), 1)
                    link(A.activation(s4(EG), s4(GCOL), ACT.Exp))
                    link(A.activation(s4(EGE), s4(GE), ACT.Exp))
                    link(A.activation(s4(WE), s4(WE), ACT.Exp), S("gexp_out"))
                    act.wait_ge(S("turned"), 5)
                    act.wait_ge(S("inter"), 2)
                    A.activation(flat(qT[:]), ps[0:HD, 0, :], ACT.Copy).then_inc(S("qkT"), 1)
                    act.wait_ge(S("turned"), 6)
                    A.activation(flat(kT[:]), ps[0:HD, 1, :], ACT.Copy).then_inc(S("qkT"), 1)
                    act.wait_ge(S("turned"), 7)
                    A.activation(flat(kbT[:]), ps[0:HD, 2, :], ACT.Copy).then_inc(S("qkT"), 1)
                    act.wait_ge(S("shifted"), 2)
                    for h in range(H):
                        A.activation(w1[:, h, :], w1[:, h, :], ACT.Exp, bias=sm[:, GCOL, h:h + 1])
                        m = A.activation(w2[:, h, :], w2[:, h, :], ACT.Exp, bias=sm[:, NGC, h:h + 1])
                    m.then_inc(S("weights"), 1)
                    for s in range(1, LEV):
                        act.wait_ge(S("ylev"), s)
                        A.activation(flat(Y[:]), ps[:, 1, :], ACT.Copy).then_inc(S("ysb"), 1)
                    act.wait_ge(S("wt"), 1)
                    A.activation(flat(wTn[:]), ps[0:HD, 7, :], ACT.Copy, scale=-1.0).then_inc(S("wtn"), 1)
                    act.wait_ge(S("delta"), 1)
                    A.activation(flat(dl[:]), ps[:, 1, 0:256], ACT.Copy).then_inc(S("dl"), 1)

                @b.vector
                def _(dve):
                    link = Link(dve, S("v"))

                    def head_norm(j, gate, rn):
                        oo = o[:, :, 0:HD]
                        link(V.tensor_tensor(sq[:], oo, oo, ALU.mult))
                        link(V.tensor_reduce(s4(R_SS), sq[:], AX.X, ALU.add))
                        link(V.tensor_scalar(s4(R_SS), s4(R_SS), 1.0 / HD, EPS, ALU.mult, ALU.add), S("squares"))
                        dve.wait_ge(S("r_ready"), rn)
                        link(V.tensor_tensor(sq[:], oo, b64(s4(R_R)), ALU.mult))
                        if gate is None:
                            link(V.tensor_tensor(y[:, j, :], flat(sq[:]), gains[:, j, :], ALU.mult), S("y_ready"))
                        else:
                            link(V.tensor_tensor(y[:, j, :], flat(sq[:]), gains[:, j, :], ALU.mult))
                            link(V.tensor_tensor(y[:, j, :], y[:, j, :], gate, ALU.mult), S("y_ready"))

                    x12 = heads(RQ, 8)
                    cos = rope[:, par, 0:32].to_broadcast([P, 8, 32])
                    sin = rope[:, par, 32:64].to_broadcast([P, 8, 32])
                    lo, hi = slice(0, 32), slice(32, 64)
                    link(V.tensor_tensor(qkw[:, 0], x12[:, :, lo], cos, ALU.mult))
                    link(V.tensor_tensor(qkw[:, 1], x12[:, :, hi], sin, ALU.mult))
                    link(V.tensor_tensor(qk[:, :, lo], qkw[:, 0], qkw[:, 1], ALU.subtract))
                    link(V.tensor_tensor(qkw[:, 0], x12[:, :, lo], sin, ALU.mult))
                    link(V.tensor_tensor(qkw[:, 1], x12[:, :, hi], cos, ALU.mult))
                    link(V.tensor_tensor(qk[:, :, hi], qkw[:, 0], qkw[:, 1], ALU.add), S("roped"))
                    link(V.tensor_tensor(kz[:], qk[:, 4:8, :], b64(xi[:, 1, :]), ALU.mult), S("kz_ready"))
                    link(V.tensor_tensor(s4(IC), zv(MI, 4), gates[:, 0:4], ALU.add))
                    link(V.tensor_tensor(s4(LF), zv(MF, 4), gates[:, 4:8], ALU.add))
                    link(V.tensor_scalar(s4(MIN0), s4(LF), 0.0, None, ALU.min))
                    link(V.scalar_tensor_tensor(s4(ABS), s4(LF), -1.0, s4(LF), ALU.mult, ALU.max), S("gate_abs"))
                    dve.wait_ge(S("sig_exp"), 1)
                    link(V.reciprocal(sig[:], sig[:]))
                    link(V.tensor_tensor(sig[:, 0, :], sig[:, 0, :], zv(RG), ALU.mult))
                    link(V.tensor_tensor(sig[:, 2, :], sig[:, 2, :], zv(GG), ALU.mult))
                    dve.wait_ge(S("scores"), 1)
                    link(V.tensor_tensor(pT[:], bank(2), retD[:], ALU.mult), S("p_ready"))
                    dve.wait_ge(S("inter"), 1)
                    qs3 = ps[:, 6, 0:256].rearrange("p (h d) -> p h d", d=HD)
                    qs5 = ps[:, 5, 0:256].rearrange("p (h d) -> p h d", d=HD)
                    o3 = ps[:, 3, 0:256].rearrange("p (h d) -> p h d", d=HD)
                    link(V.tensor_tensor(o[:, :, 0:HD], qs3, b64(xi[:, 0, :]), ALU.mult))
                    dve.wait_ge(S("intra"), 1)
                    link(V.tensor_tensor(o[:, :, 0:HD], o[:, :, 0:HD], o3, ALU.add))
                    link(V.tensor_tensor(Sret[:], Sret[:], bc(xi[0:HD, 2, :], H, [HD, H, HD]), ALU.mult))
                    dve.wait_ge(S("dstate"), 1)
                    link(V.tensor_tensor(Sret[:], Sret[:], ps[0:HD, 4, 0:256].rearrange("p (h d) -> p h d", d=HD), ALU.add), S("ret_out"))
                    head_norm(0, sig[:, 0, :], 1)
                    dve.wait_ge(S("turned"), 2)
                    link(V.tensor_copy(qk[:], heads(MQ, 8)), S("qk_ml"))
                    dve.wait_ge(S("softplus"), 1)
                    link(V.tensor_tensor(s4(LF), s4(MIN0), s4(E1), ALU.subtract), S("gates_in"))
                    dve.wait_ge(S("bcol"), 1)
                    link(V.tensor_copy(s4(BC), ps[:, 5, 0:4]))
                    link(V.tensor_tensor(s4(CC), s4(IC), s4(BC), ALU.subtract))
                    link(V.tensor_copy(w1[:], bc(s4(CC), H, [P, H, P])), S("ccol"))
                    dve.wait_ge(S("crow"), 1)
                    link(V.tensor_tensor(w2[:], bank(6), b512(mask[:]), ALU.add), S("maxed"))
                    link(V.tensor_reduce(s4(MX), w2[:], AX.X, ALU.max))
                    link(V.tensor_tensor(s4(MU), s4(MX), mprev[:], ALU.max))
                    link(V.tensor_tensor(s4(MM), s4(MU), s4(BC), ALU.add))
                    link(V.tensor_copy(w2[:], bc(s4(MU), H, [P, H, P])), S("mucol"))
                    dve.wait_ge(S("mend"), 1)
                    link(V.tensor_copy(sm[:, MEND, :], ps[:, 5, 20:24]))
                    link(V.tensor_tensor(s4(GIN), mprev[:], s4(MU), ALU.subtract))
                    link(V.tensor_tensor(s4(WEND), s4(CC), ps[:, 5, 16:20], ALU.subtract))
                    link(V.tensor_tensor(s4(GEND), mprev[:], ps[:, 5, 16:20], ALU.subtract), S("exps_in"))
                    dve.wait_ge(S("murow"), 1)
                    link(V.scalar_tensor_tensor(w2[:], bank(7), -1.0, b512(maskT[:]), ALU.mult, ALU.add), S("shifted"))
                    link(V.tensor_copy(mprev[:], sm[:, MEND, :]))
                    dve.wait_ge(S("exps_out"), 1)
                    link(V.tensor_scalar(s4(WEND), s4(WEND), 0.125, None, ALU.mult))
                    link(V.tensor_tensor(kz[:], qk[:, 4:8, :], b64(s4(WEND)), ALU.mult), S("kz_ready"))
                    dve.wait_ge(S("scores"), 2)
                    dve.wait_ge(S("weights"), 1)
                    link(V.scalar_tensor_tensor(pT[:], bank(2), 0.125, w2[:], ALU.mult, ALU.mult), S("p_ready"))
                    dve.wait_ge(S("inter"), 2)
                    oa = ps[:, 4, 0:260].rearrange("p (h d) -> p h d", d=HD + 1)
                    ob = ps[:, 3, 0:260].rearrange("p (h d) -> p h d", d=HD + 1)
                    link(V.tensor_tensor(o[:], oa, bc(s4(GIN), H, [P, H, HD + 1]), ALU.mult))
                    dve.wait_ge(S("intra"), 2)
                    link(V.tensor_tensor(o[:], o[:], ob, ALU.add), S("ml_read"))
                    link(V.scalar_tensor_tensor(s4(DEN), o[:, :, HD], -1.0, o[:, :, HD], ALU.mult, ALU.max))
                    link(V.tensor_tensor(s4(DEN), s4(DEN), s4(EM), ALU.max))
                    link(V.reciprocal(s4(RD), s4(DEN)))
                    link(V.tensor_tensor(o[:, :, 0:HD], o[:, :, 0:HD], b64(s4(RD)), ALU.mult))
                    link(V.tensor_tensor(o[:, :, 0:HD], o[:, :, 0:HD], sig[:, 1, :].rearrange("p (h d) -> p h d", d=HD), ALU.mult))
                    link(V.tensor_tensor(Caug[:], Caug[:], bc(sm[0:HD, GEND, :], H, [HD, H, HD + 1]), ALU.mult))
                    dve.wait_ge(S("dstate"), 2)
                    link(V.tensor_tensor(Caug[:], Caug[:], ps[0:HD, 6, 0:260].rearrange("p (h d) -> p h d", d=HD + 1), ALU.add))
                    head_norm(1, None, 2)
                    link(V.tensor_tensor(xc[:], zv(GX, W3), cw[:, 3, :], ALU.mult))
                    for j in range(3):
                        link(V.tensor_tensor(xc2[:], zs[:, par, j, :].rearrange("p a n -> p (a n)"), cw[:, j, :], ALU.mult))
                        link(V.tensor_tensor(xc[:], xc[:], xc2[:], ALU.add), S("conved") if j == 2 else None)
                    link(V.tensor_tensor(s4(G), zv(GA, 4), gates[:, 8:12], ALU.add))
                    link(V.tensor_scalar(s4(MIN0), s4(G), 0.0, None, ALU.max))
                    link(V.scalar_tensor_tensor(s4(ABS), s4(G), -1.0, s4(G), ALU.mult, ALU.max), S("gate_abs"))
                    dve.wait_ge(S("silu_exp"), 1)
                    link(V.reciprocal(xc2[:], xc2[:]))
                    link(V.tensor_tensor(xc[:], xc[:], xc2[:], ALU.mult))
                    link(V.tensor_scalar(s4(BETA), s4(BETA), 1.0, None, ALU.add))
                    link(V.reciprocal(s4(BETA), s4(BETA)))
                    xh = xc[:].rearrange("p (h d) -> p h d", d=HD)
                    sq8 = Y[:].rearrange("p h n -> p (h n)").rearrange("p (h d) -> p h d", d=HD)
                    link(V.tensor_tensor(sq8, xh[:, 0:8, :], xh[:, 0:8, :], ALU.mult))
                    link(V.tensor_reduce(xc2[:, 0:8], sq8, AX.X, ALU.add))
                    link(V.tensor_scalar(xc2[:, 0:8], xc2[:, 0:8], EPS, None, ALU.add), S("squares"))
                    dve.wait_ge(S("softplus"), 2)
                    link(V.tensor_tensor(s4(G), s4(MIN0), s4(E1), ALU.add))
                    link(V.tensor_tensor(s4(G), s4(G), gates[:, 12:16], ALU.mult))
                    link(V.tensor_copy(w1[:], bc(s4(G), H, [P, H, P])), S("g_ready"))
                    dve.wait_ge(S("r_ready"), 3)
                    link(V.tensor_scalar(xc2[:, 8:12], xc2[:, 8:12], 0.125, None, ALU.mult))
                    dve.wait_ge(S("turned"), 4)
                    link(V.tensor_tensor(qk[:], xh[:, 0:8, :], bc(xc2[:, 8:16], 8, [P, 8, HD]), ALU.mult))
                    link(V.tensor_tensor(kb[:], qk[:, 4:8, :], b64(s4(BETA)), ALU.mult), S("qk_gdn"))
                    link(V.tensor_tensor(rv[:], xh[:, 8:12, :], b64(s4(BETA)), ALU.mult))
                    dve.wait_ge(S("gcol"), 1)
                    link(V.tensor_copy(s4(GCOL), ps[:, 5, 0:4]))
                    link(V.tensor_copy(s4(GE), ps[:, 5, 4:8]))
                    link(V.tensor_tensor(s4(WE), s4(GE), s4(GCOL), ALU.subtract))
                    link(V.tensor_scalar(s4(NGC), s4(GCOL), -1.0, None, ALU.mult), S("gexp_in"))
                    dve.wait_ge(S("grow"), 1)
                    link(V.scalar_tensor_tensor(w1[:], bank(7), -1.0, b512(mask[:]), ALU.mult, ALU.add))
                    link(V.tensor_tensor(w2[:], bank(7), b512(maskT[:]), ALU.add), S("shifted"))
                    dve.wait_ge(S("gexp_out"), 1)
                    link(V.tensor_tensor(rk[:], kb[:], b64(s4(EG)), ALU.mult), S("rhs"))
                    link(V.tensor_tensor(kz[:], qk[:, 4:8, :], b64(s4(WE)), ALU.mult))
                    dve.wait_ge(S("weights"), 2)
                    dve.wait_ge(S("nn"), 3)
                    link(V.tensor_tensor(w1[:], bank(3), w1[:], ALU.mult))
                    link(V.tensor_tensor(NLT[:], bank(4), w2[:], ALU.mult))
                    link(V.tensor_tensor(pT[:], bank(0), w2[:], ALU.mult))
                    link(V.tensor_tensor(X[:], w1[:], b512(lev[:, 0, :]), ALU.mult))
                    link(V.scalar_tensor_tensor(X[:], X[:], -1.0, b512(ident[:]), ALU.mult, ALU.add))
                    link(V.tensor_tensor(XT[:], NLT[:], b512(levT[:, 0, :]), ALU.mult))
                    link(V.scalar_tensor_tensor(XT[:], XT[:], -1.0, b512(ident[:]), ALU.mult, ALU.add), S("xt"))
                    for s in range(1, LEV):
                        if s > 1:
                            dve.wait_ge(S("ylev"), s - 1)
                        link(V.tensor_tensor(NM[:], NLT[:], b512(levT[:, s, :]), ALU.mult), S("nm"))
                        if s < LEV - 1:
                            dve.wait_ge(S("xy"), 2 * s - 1)
                            dve.wait_ge(S("xy"), 2 * s)
                            link(V.tensor_tensor(X[:], X[:], bank(2), ALU.subtract))
                        else:
                            dve.wait_ge(S("xy"), 2 * s - 1)
                        link(V.tensor_tensor(XT[:], XT[:], bank(6), ALU.subtract), S("xt"))
                    dve.wait_ge(S("inter"), 3)
                    link(V.tensor_tensor(o[:, :, 0:HD], qs5, b64(s4(EG)), ALU.mult))
                    dve.wait_ge(S("intra"), 3)
                    link(V.tensor_tensor(o[:, :, 0:HD], o[:, :, 0:HD], o3, ALU.add))
                    link(V.tensor_tensor(Sgdn[:], Sgdn[:], bc(sm[0:HD, EGE, :], H, [HD, H, HD]), ALU.mult))
                    dve.wait_ge(S("dstate"), 3)
                    link(V.tensor_tensor(Sgdn[:], Sgdn[:], ps[0:HD, 4, 0:256].rearrange("p (h d) -> p h d", d=HD), ALU.add))
                    head_norm(2, sig[:, 2, :], 4)
            kit.clear()

        with nc.Block() as b:
            @b.sync
            def _(sp):
                st = Loads(sp, S("st"))
                st(io["p_ret"][ds(l, 1), 0].rearrange("a h d e -> d (a h) e"), Sret[:])
                st(io["p_C"][ds(l, 1), 0].rearrange("a h d e -> d (a h) e"), Caug[:, :, 0:HD])
                st(io["p_n"][ds(l, 1), 0].rearrange("a h (d o) -> d (a h) o", o=1), Caug[:, :, HD:HD + 1], slow=True)
                st(io["p_gdn"][ds(l, 1), 0].rearrange("a h d e -> d (a h) e"), Sgdn[:])
                st(io["p_m"][ds(l, 1), 0], mprev[0:1, :])
                st.all_in()
        kit.clear()


def copy_states(kit, env, io, l):
    nc, S, z = kit.nc, kit.sem, env["z"]
    with nc.Block() as b:
        @b.sync
        def _(sp):
            st = Loads(sp, S("st"))
            p0, s0 = PADROWS, PADROWS + SEQ
            st(io["p_nsa"][ds(l, 1), 0].rearrange("a t r d -> (a t) (r d)"), z[p0:p0 + SEQ, NKV:NKV + 256])
            st(io["p_swa"][ds(l, 1), 0].rearrange("a t r d -> (a t) (r d)"), z[p0 + SEQ - WIN:p0 + SEQ, NKV + 256:NKV + 384])
            st(io["p_gconv"][ds(l, 1), 0].rearrange("a r n -> (a r) n"), z[p0 + SEQ - 3:p0 + SEQ, GX:GX + 768])
            st(io["s_nsa"][ds(l, 1), :, 0].rearrange("a b r d -> (a b) (r d)"), z[s0:s0 + NB, NKV:NKV + 256])
            st(io["s_swa"][ds(l, 1), :, WIN - 1].rearrange("a b r d -> (a b) (r d)"), z[s0:s0 + NB, NKV + 256:NKV + 384])
            st(io["s_swa"][ds(l, 1), :, 0:WIN - 1].rearrange("a b t r d -> (a b) (t r d)"),
               io["cache_swa_kv"][ds(l, 1), :, 1:WIN].rearrange("a b t r d -> (a b) (t r d)"))
            st(io["s_gconv"][ds(l, 1), :, 2].rearrange("a b n -> (a b) n"), z[s0:s0 + NB, GX:GX + 768])
            st(io["s_gconv"][ds(l, 1), :, 0:2], io["state_gdn_conv"][ds(l, 1), :, 1:3])
            st.all_in()
    kit.clear()


def sample_heads(ld, io, z, dst, a, groups, pitch=256):
    s0 = PADROWS + SEQ
    for h in range(H):
        src = z[s0:s0 + NB, a + h * HD:a + h * HD + pitch * (groups - 1) + HD] if groups == 1 else \
            z[s0:s0 + NB, a:a + pitch * groups].rearrange("b (g n) -> b g n", n=pitch)[:, :, h * HD:h * HD + HD]
        ld(dst[h * NB:h * NB + NB], src)


def recurrent_sample(kit, env, io, l):
    nc, S, mhalf = kit.nc, kit.sem, env["mhalf"]
    z, y_mix = env["z"], env["y_mix"]
    V, A = nc.vector, nc.scalar
    R = H * NB
    s0 = PADROWS + SEQ
    with ExitStack() as c:
        def sb(name, shape):
            return c.enter_context(nc.sbuf_tensor(name, shape, F32))
        rz = sb("d_rz", [R, 4, HD])
        mz = sb("d_mz", [R, 3, HD])
        mo = sb("d_mo", [R, HD])
        taps = sb("d_taps", [R, 4, 3, HD])
        cw = sb("d_cw", [R, 4, 3, HD])
        gg = sb("d_gg", [R, HD])
        sc = sb("d_sc", [R, 4])
        par = sb("d_par", [R, 4])
        gains = sb("d_gains", [R, 3, HD])
        rope = sb("d_rope", [R, HD])
        dec = sb("d_dec", [R, 1])
        st3 = [sb(f"d_st{j}", [R, HD, HD]) for j in range(3)]
        nst = sb("d_n", [R, HD])
        mst = sb("d_m", [R, 1])
        tmp = sb("d_tmp", [R, HD, HD])
        q = sb("d_q", [R, HD])
        k = sb("d_k", [R, HD])
        xc = sb("d_xc", [R, 3, HD])
        xe = sb("d_xe", [R, 3, HD])
        sg = sb("d_sg", [R, 3, HD])
        t4 = sb("d_t4", [R, 4, HD])
        o = sb("d_o", [R, HD])
        col = sb("d_col", [R, 24])
        y = sb("d_y", [R, 3, HD])
        n_loads = [0]

        with nc.Block() as b:
            @b.sync
            def _(sp):
                ld = Loads(sp, S("ld"))
                sample_heads(ld, io, z, rz, RQ, 4)
                sample_heads(ld, io, z, mz, MQ, 3)
                sample_heads(ld, io, z, mo, MO, 1)
                sample_heads(ld, io, z, taps[:, 3], GX, 3)
                sample_heads(ld, io, z, gg, GG, 1)
                for h in range(H):
                    hb = slice(h * NB, h * NB + NB)
                    for j, a in enumerate((MI, MF, GA, GB)):
                        ld(sc[hb, j:j + 1], z[s0:s0 + NB, a + h:a + h + 1], slow=True)
                    for j, name in enumerate(("mlstm_b_i", "mlstm_b_f", "gdn_dt_bias", "gdn_A_log")):
                        ld(par[hb, j:j + 1], io[name][ds(l, 1), h:h + 1].rearrange("a n -> (a n)").partition_broadcast(NB))
                    for j, name in enumerate(("ret_norm", "mlstm_norm", "gdn_norm")):
                        ld(gains[hb, j], io[name][ds(l, 1), h * HD:h * HD + HD].rearrange("a n -> (a n)").partition_broadcast(NB))
                    for j in range(4):
                        ld(cw[hb, j], io["gdn_conv_w"][ds(l, 1), j].rearrange("a (g n) -> (a g) n", g=3)[:, h * HD:h * HD + HD].partition_broadcast(NB))
                    for j in range(3):
                        ld(taps[hb, j], io["state_gdn_conv"][ds(l, 1), :, j].rearrange("a b (g n) -> (a b) g n", g=3)[:, :, h * HD:h * HD + HD])
                    for j, name in enumerate(("state_ret", "state_mlstm_C", "state_gdn")):
                        ld(st3[j][hb], io[name][ds(l, 1), :, h].rearrange("a b d e -> (a b) d e"))
                    ld(nst[hb], io["state_mlstm_n"][ds(l, 1), :, h].rearrange("a b d -> (a b) d"))
                    ld(mst[hb], io["state_mlstm_m"][ds(l, 1), :, h:h + 1].rearrange("a b d -> (a b) d"), slow=True)
                ld(rope[:], io["c_rope"][SEQ:SEQ + 1, :].rearrange("a n -> (a n)").partition_broadcast(R))
                ld(dec[:], io["c_dec"])
                n_loads[0] = ld.n
                ld.all_in()
        kit.clear()

        with nc.Block() as b:
            LFC, ABS, MN, E1, MT, WI, GI, EM, DEN, SS, RR, GD, BT, EGD, SS2, RR2, EA, IP = range(18)

            def cc(i, n=1):
                return col[:, i:i + n]

            @b.gpsimd
            def _(pool):
                for j, (src, dst, n) in enumerate(((SS, RR, 1), (SS, RR, 1), (18, 20, 2), (SS, RR, 1))):
                    pool.wait_ge(S("squares"), j + 1)
                    nc.gpsimd.tensor_tensor(cc(dst, n), cc(src, n), mhalf[0:R, 0:n], ALU.pow).then_inc(S("r_ready"), 1)

            @b.scalar
            def _(act):
                link = Link(act, S("a"))
                for j, src in enumerate((rz[:, 3, :], mo[:], gg[:])):
                    link(A.activation(sg[:, j], src, ACT.Exp, scale=-1.0))
                link(A.activation(cc(EA), par[:, 3:4], ACT.Exp))
                link(A.activation(cc(BT), sc[:, 3:4], ACT.Exp, scale=-1.0), S("sig_exp"))
                act.wait_ge(S("abs"), 1)
                link(A.activation(cc(E1), cc(ABS), ACT.Exp, scale=-1.0))
                link(A.activation(cc(E1), cc(E1), ACT.Ln, bias=1.0), S("softplus"))
                act.wait_ge(S("mt"), 1)
                link(A.activation(cc(WI), cc(WI), ACT.Exp))
                link(A.activation(cc(GI), cc(GI), ACT.Exp))
                link(A.activation(cc(EM), cc(MT), ACT.Exp, scale=-1.0), S("mexp"))
                act.wait_ge(S("conved"), 1)
                link(A.activation(xe[:], xc[:], ACT.Exp, scale=-1.0), S("silu_exp"))
                act.wait_ge(S("abs"), 2)
                link(A.activation(cc(E1), cc(ABS), ACT.Exp, scale=-1.0))
                link(A.activation(cc(E1), cc(E1), ACT.Ln, bias=1.0), S("softplus"))
                act.wait_ge(S("gd"), 1)
                link(A.activation(cc(EGD), cc(GD), ACT.Exp), S("gexp"))

            @b.vector
            def _(dve):
                link = Link(dve, S("v"))

                def outer(kk, vv):
                    link(V.tensor_tensor(tmp[:], kk.unsqueeze(2).to_broadcast([R, HD, HD]),
                                         vv.unsqueeze(1).to_broadcast([R, HD, HD]), ALU.mult))

                def dot(out, vec, st):
                    link(V.tensor_tensor(tmp[:], st[:], vec.unsqueeze(2).to_broadcast([R, HD, HD]), ALU.mult))
                    link(V.tensor_reduce(out, tmp[:].rearrange("p d e -> p e d"), AX.X, ALU.add))

                def head_norm(j, gate, n):
                    link(V.tensor_tensor_reduce(t4[:, 0], o[:], o[:], 1.0, 0.0, ALU.mult, ALU.add, cc(SS)))
                    link(V.tensor_scalar(cc(SS), cc(SS), 1.0 / HD, EPS, ALU.mult, ALU.add), S("squares"))
                    dve.wait_ge(S("r_ready"), n)
                    link(V.scalar_tensor_tensor(y[:, j], o[:], cc(RR), gains[:, j], ALU.mult, ALU.mult))
                    if gate is not None:
                        link(V.tensor_tensor(y[:, j], y[:, j], gate, ALU.mult))

                dve.wait_ge(S("sig_exp"), 1)
                link(V.tensor_scalar(sg[:], sg[:], 1.0, None, ALU.add))
                link(V.reciprocal(sg[:], sg[:]))
                link(V.tensor_tensor(sg[:, 0], sg[:, 0], rz[:, 3], ALU.mult))
                link(V.tensor_tensor(sg[:, 2], sg[:, 2], gg[:], ALU.mult))
                link(V.tensor_scalar(cc(BT), cc(BT), 1.0, None, ALU.add))
                link(V.reciprocal(cc(BT), cc(BT)))
                lo, hi = slice(0, 32), slice(32, 64)
                for j, out in ((0, q), (1, k)):
                    link(V.tensor_tensor(t4[:, 0, 0:32], rz[:, j, lo], rope[:, lo], ALU.mult))
                    link(V.tensor_tensor(t4[:, 1, 0:32], rz[:, j, hi], rope[:, hi], ALU.mult))
                    link(V.tensor_tensor(out[:, lo], t4[:, 0, 0:32], t4[:, 1, 0:32], ALU.subtract))
                    link(V.tensor_tensor(t4[:, 0, 0:32], rz[:, j, lo], rope[:, hi], ALU.mult))
                    link(V.tensor_tensor(t4[:, 1, 0:32], rz[:, j, hi], rope[:, lo], ALU.mult))
                    link(V.tensor_tensor(out[:, hi], t4[:, 0, 0:32], t4[:, 1, 0:32], ALU.add))
                link(V.tensor_scalar(k[:], k[:], 0.125, None, ALU.mult))
                outer(k[:], rz[:, 2])
                link(V.scalar_tensor_tensor(st3[0][:], st3[0][:], dec[:, 0:1], tmp[:], ALU.mult, ALU.add))
                dot(o[:], q[:], st3[0])
                head_norm(0, sg[:, 0], 1)
                link(V.tensor_tensor(cc(LFC), sc[:, 1:2], par[:, 1:2], ALU.add))
                link(V.tensor_tensor(cc(IP), sc[:, 0:1], par[:, 0:1], ALU.add))
                link(V.tensor_scalar(cc(MN), cc(LFC), 0.0, None, ALU.min))
                link(V.scalar_tensor_tensor(cc(ABS), cc(LFC), -1.0, cc(LFC), ALU.mult, ALU.max), S("abs"))
                dve.wait_ge(S("softplus"), 1)
                link(V.tensor_tensor(cc(LFC), cc(MN), cc(E1), ALU.subtract))
                link(V.tensor_tensor(cc(LFC), cc(LFC), mst[:], ALU.add))
                link(V.tensor_tensor(cc(MT), cc(LFC), cc(IP), ALU.max))
                link(V.tensor_tensor(cc(WI), cc(IP), cc(MT), ALU.subtract))
                link(V.tensor_tensor(cc(GI), cc(LFC), cc(MT), ALU.subtract), S("mt"))
                dve.wait_ge(S("mexp"), 1)
                link(V.tensor_scalar(k[:], mz[:, 1], cc(WI), 0.125, ALU.mult, ALU.mult))
                outer(k[:], mz[:, 2])
                link(V.scalar_tensor_tensor(st3[1][:], st3[1][:], cc(GI), tmp[:], ALU.mult, ALU.add))
                link(V.scalar_tensor_tensor(nst[:], nst[:], cc(GI), k[:], ALU.mult, ALU.add))
                dot(o[:], mz[:, 0], st3[1])
                link(V.tensor_tensor_reduce(t4[:, 0], mz[:, 0], nst[:], 1.0, 0.0, ALU.mult, ALU.add, cc(DEN)))
                link(V.scalar_tensor_tensor(cc(DEN), cc(DEN), -1.0, cc(DEN), ALU.mult, ALU.max))
                link(V.tensor_tensor(cc(DEN), cc(DEN), cc(EM), ALU.max))
                link(V.reciprocal(cc(DEN), cc(DEN)))
                link(V.scalar_tensor_tensor(o[:], o[:], cc(DEN), sg[:, 1], ALU.mult, ALU.mult))
                head_norm(1, None, 2)
                link(V.tensor_tensor(taps[:], taps[:], cw[:], ALU.mult))
                link(V.tensor_tensor(taps[:, 0], taps[:, 0], taps[:, 1], ALU.add))
                link(V.tensor_tensor(taps[:, 2], taps[:, 2], taps[:, 3], ALU.add))
                link(V.tensor_tensor(xc[:], taps[:, 0], taps[:, 2], ALU.add), S("conved"))
                link(V.tensor_tensor(cc(GD), sc[:, 2:3], par[:, 2:3], ALU.add))
                link(V.tensor_scalar(cc(MN), cc(GD), 0.0, None, ALU.max))
                link(V.scalar_tensor_tensor(cc(ABS), cc(GD), -1.0, cc(GD), ALU.mult, ALU.max), S("abs"))
                dve.wait_ge(S("silu_exp"), 1)
                link(V.tensor_scalar(xe[:], xe[:], 1.0, None, ALU.add))
                link(V.reciprocal(xe[:], xe[:]))
                link(V.tensor_tensor(xc[:], xc[:], xe[:], ALU.mult))
                for j in range(2):
                    link(V.tensor_tensor_reduce(t4[:, 0], xc[:, j], xc[:, j], 1.0, 0.0, ALU.mult, ALU.add, cc(18 + j)))
                link(V.tensor_scalar(cc(18, 2), cc(18, 2), EPS, None, ALU.add), S("squares"))
                dve.wait_ge(S("softplus"), 2)
                link(V.tensor_tensor(cc(GD), cc(MN), cc(E1), ALU.add))
                link(V.scalar_tensor_tensor(cc(GD), cc(GD), -1.0, cc(EA), ALU.mult, ALU.mult), S("gd"))
                dve.wait_ge(S("r_ready"), 3)
                link(V.tensor_scalar(q[:], xc[:, 0], cc(20), 0.125, ALU.mult, ALU.mult))
                link(V.tensor_scalar(k[:], xc[:, 1], cc(21), None, ALU.mult))
                dve.wait_ge(S("gexp"), 1)
                link(V.tensor_scalar(st3[2][:], st3[2][:], cc(EGD), None, ALU.mult))
                dot(o[:], k[:], st3[2])
                link(V.tensor_tensor(o[:], xc[:, 2], o[:], ALU.subtract))
                link(V.tensor_scalar(o[:], o[:], cc(BT), None, ALU.mult))
                outer(k[:], o[:])
                link(V.tensor_tensor(st3[2][:], st3[2][:], tmp[:], ALU.add))
                dot(o[:], q[:], st3[2])
                head_norm(2, sg[:, 2], 4)
        kit.clear()

        with nc.Block() as b:
            @b.sync
            def _(sp):
                st = Loads(sp, S("st"))
                for h in range(H):
                    hb = slice(h * NB, h * NB + NB)
                    for j, name in enumerate(("s_ret", "s_C", "s_gdn")):
                        st(io[name][ds(l, 1), :, h].rearrange("a b d e -> (a b) d e"), st3[j][hb])
                    st(io["s_n"][ds(l, 1), :, h].rearrange("a b d -> (a b) d"), nst[hb])
                    st(io["s_m"][ds(l, 1), :, h:h + 1].rearrange("a b d -> (a b) d"), col[hb, 4:5], slow=True)
                    st(y_mix[SEQ:TOK, 0:768].rearrange("b (j n) -> b j n", j=3)[:, :, h * HD:h * HD + HD], y[hb])
                st.all_in()
        kit.clear()


TL = 1152
WL = 768
TWC = TL + WL


def bias_tables(kit, env, io):
    nc, S, ps = kit.nc, kit.sem, env["ps"]
    V, A = nc.vector, nc.scalar
    with ExitStack() as c:
        def sb(name, shape):
            return c.enter_context(nc.sbuf_tensor(name, shape, F32))
        rel = sb("b_rel", [33, H])
        relb = sb("b_relb", [33, H, P])
        oneh = sb("b_oneh", [33, TWC])
        rows_sb = sb("b_rows", [P, H, TWC])
        with nc.Block() as b:
            @b.sync
            def _(sp):
                ld = Loads(sp, S("ld"))
                ld(rel[0:32, :], io["rel_bias"])
                ld(oneh[:], io["c_onehot"])
                sp.wait_ge(S("rows_ready"), H)
                ld(env["wdist"].rearrange("h p n -> p h n"), rows_sb[:])
                ld.all_in()

            @b.vector
            def _(dve):
                link = Link(dve, S("v"))
                link(V.memset(relb[:], 1.0))
                dve.wait_ge(S("ld"), 32)
                link(V.tensor_copy(relb[0:32], bc(rel[0:32, :], H, [32, H, P])), S("rel_ready"))
                for h in range(H):
                    dve.wait_ge(S("looked_up"), h + 1)
                    link(V.tensor_copy(rows_sb[:, h, :].rearrange("p (a n) -> p a n", a=4), ps[:, 0:4, 0:TWC // 4]), S("rows_ready"))

            @b.tensor
            def _(pe):
                pe.wait_ge(S("rel_ready"), 1)
                for h in range(H):
                    if h:
                        pe.wait_ge(S("rows_ready"), h)
                    for a in range(4):
                        m = nc.tensor.matmul(ps[:, a, 0:TWC // 4], relb[:, h, :], oneh[:, a * (TWC // 4):(a + 1) * (TWC // 4)],
                                             start=True, stop=True)
                    m.then_inc(S("looked_up"), 1)
        kit.clear()


def compress_weights(kit, env, io, l, wb, peadd, c):
    nc, S, ps, ident = kit.nc, kit.sem, env["ps"], env["ident"]
    V, A = nc.vector, nc.scalar
    with ExitStack() as c2:
        pe_in = c2.enter_context(nc.sbuf_tensor("cw_pe", [32, P], F32))
        peT = c2.enter_context(nc.sbuf_tensor("cw_peT", [P, 32], F32))
        with nc.Block() as b:
            @b.sync
            def _(sp):
                ld = Loads(sp, S("pe_in"))
                ld(pe_in[:], io["nsa_cmp_pe"][ds(l, 1)].rearrange("a j c d -> (a j) (c d)"))
                ld.all_in()
                ld2 = Loads(sp, S("wb_in"))
                sp.wait_ge(S("wb_zero"), 1)
                for cc in range(2):
                    ld2(wb[cc * HD:cc * HD + HD, :, cc * HD:cc * HD + HD],
                        io["nsa_cmp_w"][ds(l, 1), cc].rearrange("a j d e -> d (a j) e"))
                ld2.all_in()

            @b.vector
            def _(dve):
                V.memset(wb[:], 0.0).then_inc(S("wb_zero"), 1)
                dve.wait_ge(S("turned"), 1)
                V.tensor_copy(peT[:], ps[:, 0, 0:32]).then_inc(S("peT"), 1)
                dve.wait_ge(S("pe_summed"), 1)
                V.tensor_copy(peadd[:], ps[:, 1, 0:1]).then_inc(S("v"), 1)

            @b.tensor
            def _(pe):
                pe.wait_ge(S("pe_in"), 16)
                nc.tensor.transpose(ps[:, 0, 0:32], pe_in[:], ident[0:32, 0:32]).then_inc(S("turned"), 1)
                pe.wait_ge(S("peT"), 1)
                pe.wait_ge(S("wb_in"), 32)
                for j in range(32):
                    m = nc.tensor.matmul(ps[:, 1, 0:1], wb[:, j, :], peT[:, j:j + 1], start=(j == 0), stop=(j == 31))
                m.then_inc(S("pe_summed"), 1)
        kit.clear()


def nsa_prompt(kit, env, io, l, wb, peadd):
    nc, S, ps, ident = kit.nc, kit.sem, env["ps"], env["ident"]
    z, y_mix = env["z"], env["y_mix"]
    V, A = nc.vector, nc.scalar
    NC = SEQ // 16 - 1
    WT = WIN // P
    with ExitStack() as c:
        def sb(name, shape):
            return c.enter_context(nc.sbuf_tensor(name, shape, F32))
        kTs = sb("p_kTs", [HD, SEQ])
        kTw = sb("p_kTw", [HD, SEQ])
        qT = sb("p_qT", [HD, H, SEQ])
        kc = sb("p_kc", [P, 64])
        vc = sb("p_vc", [64, HD])
        zk = sb("p_zk", [P, NT, 384])
        ng = sb("p_ng", [P, NT, H, 3])
        T = sb("p_T", [P, H, SEQ])
        TW = sb("p_TW", [P, H, WIN + P])
        valid = sb("p_valid", [P, NT])
        y = sb("p_y", [P, 2, 256])
        with ExitStack() as c2:
            zq = c2.enter_context(nc.sbuf_tensor("p_zq", [P, NT, 256], F32))
            cT = c2.enter_context(nc.sbuf_tensor("p_cT", [P, SEQ], F32))
            with nc.Block() as b:
                @b.sync
                def _(sp):
                    ld = Loads(sp, S("ld"))
                    zr = z[PADROWS:PADROWS + SEQ, :]
                    ld(zk[:], zr[:, NKV:NKV + 384].rearrange("(t p) n -> p t n", p=P))
                    ld(zq[:], zr[:, NQ:NQ + 256].rearrange("(t p) n -> p t n", p=P))
                    ld2 = Loads(sp, S("ld2"))
                    ld2(ng[:].rearrange("p t h b -> p t (h b)"), zr[:, NG:NG + 12].rearrange("(t p) n -> p t n", p=P))
                    wt = env["wdist"].tensor
                    for h in range(H):
                        base = h * P * TWC + P - 1
                        ld2(T[:, h, :], bass.AP(wt, base, [[TWC - 1, P], [1, SEQ]]))
                        ld2(TW[:, h, :], bass.AP(wt, base + TL, [[TWC - 1, P], [1, WIN + P]]))
                    ld2(valid[:], io["c_valid"])
                    ld2.all_in()

                @b.tensor
                def _(pe):
                    pe.wait_ge(S("ld"), 32)
                    g = 0
                    for kind in range(3 + H):
                        for half in range(2):
                            if g >= 4:
                                pe.wait_ge(S("even" if g % 2 == 0 else "odd"), (g - 4) // 2 + 1)
                            for i in range(4):
                                t = 4 * half + i
                                if kind == 0:
                                    m = nc.tensor.transpose(ps[:, g % 4, i * P:i * P + P], zk[:, t, 0:P], ident[:])
                                else:
                                    src = zk[:, t, P:P + HD] if kind == 1 else zk[:, t, 256:256 + HD] if kind == 2 else \
                                        zq[:, t, (kind - 3) * HD:(kind - 2) * HD]
                                    m = nc.tensor.transpose(ps[0:HD, g % 4, i * P:i * P + P], src, ident[:])
                            m.then_inc(S("turned"), 1)
                            g += 1
                    pe.wait_ge(S("even"), 1)
                    pe.wait_ge(S("odd"), 1)
                    for j in range(32):
                        m = nc.tensor.matmul(ps[:, 4, 0:NC], wb[:, j, :], cT[:, j:j + 16 * (NC - 1) + 1:16],
                                             start=(j == 0), stop=(j == 31))
                    m.then_inc(S("compressed"), 1)
                    pe.wait_ge(S("kc"), 1)
                    nc.tensor.transpose(ps[0:64, 5, 0:P], kc[:], ident[:]).then_inc(S("vc_turned"), 1)

                def dests():
                    out = []
                    for kind in range(3 + H):
                        for half in range(2):
                            cols = slice(512 * half, 512 * half + 512)
                            out.append((cT[:, cols], P) if kind == 0 else (kTs[:, cols], HD) if kind == 1 else
                                       (kTw[:, cols], HD) if kind == 2 else (qT[:, kind - 3, cols], HD))
                    return out

                @b.scalar
                def _(act):
                    for g, (dst, n) in enumerate(dests()):
                        if g % 2 == 0:
                            act.wait_ge(S("turned"), g + 1)
                            A.activation(dst, ps[0:n, g % 4, :], ACT.Copy, scale=0.125 if g >= 6 else 1.0).then_inc(S("even"), 1)
                    act.wait_ge(S("ld2"), 16 * 10)
                    A.activation(ng[:], ng[:], ACT.Exp, scale=-1.0).then_inc(S("gexp"), 1)

                @b.vector
                def _(dve):
                    link = Link(dve, S("v"))
                    link(V.memset(kc[:], 0.0))
                    for g, (dst, n) in enumerate(dests()):
                        if g % 2 == 1:
                            dve.wait_ge(S("turned"), g + 1)
                            V.tensor_scalar(dst, ps[0:n, g % 4, :], 0.125 if g >= 6 else 1.0, None, ALU.mult).then_inc(S("odd"), 1)
                    dve.wait_ge(S("gexp"), 1)
                    link(V.tensor_scalar(ng[:], ng[:], 1.0, None, ALU.add))
                    link(V.reciprocal(ng[:], ng[:]))
                    dve.wait_ge(S("compressed"), 1)
                    link(V.tensor_scalar(kc[:, 0:NC], ps[:, 4, 0:NC], peadd[:, 0:1], None, ALU.add), S("kc"))
                    dve.wait_ge(S("vc_turned"), 1)
                    link(V.tensor_copy(vc[:], ps[0:64, 5, HD:P]))
            kit.clear()

        CW, CC = SEQ, SEQ + 640
        s = sb("p_s", [P, 2, CC + 64])
        pT = sb("p_pT", [P, 2, 14, P])
        stat = sb("p_stat", [P, 2, 4, 3])
        bits = sb("p_bits", [P, HD])
        for t in range(NT):
            nk = (t + 1) * P
            w0 = max(0, t - WT) * P
            nw = nk - w0
            ncm = 8 * t + 7
            blocks = [(1, i * P, P, zk[:, i, 192:256]) for i in range(t + 1)]
            blocks += [(2, CW + i * P, P, zk[:, w0 // P + i, 320:384]) for i in range(nw // P)]
            blocks += [(0, CC, ncm, vc[0:ncm, :])]
            groups = [blocks[i:i + 4] for i in range(0, len(blocks), 4)]
            NGr = len(groups)

            def turn_wait(eng, g):
                eng.wait_ge(S("even" if g % 2 == 0 else "odd"), g // 2 + 1)

            def copy_group(op, h, gi, grp, g, name):
                k = len(grp)
                whole = k if grp[-1][0] != 0 else k - 1
                m = None
                if whole:
                    m = op(pT[:, h % 2, 4 * gi:4 * gi + whole, :].rearrange("p a n -> p (a n)"), ps[:, 4 + g % 2, 0:whole * P])
                if whole < k:
                    n = grp[-1][2]
                    m = op(pT[0:n, h % 2, 4 * gi + whole, :], ps[0:n, 4 + g % 2, whole * P:k * P])
                m.then_inc(S(name), 1)

            with nc.Block(no_gpsimd_drain=True) as b:
                @b.tensor
                def _(pe):
                    def scores(h):
                        if h:
                            pe.wait_ge(S("biased"), h)
                        q = qT[:, h, t * P:t * P + P]
                        for n0 in range(0, nk, 512):
                            n = min(512, nk - n0)
                            nc.tensor.matmul(ps[:, n0 // 512, 0:n], q, kTs[:, n0:n0 + n], start=True, stop=True)
                        n = min(512, nw)
                        nc.tensor.matmul(ps[:, 2, 0:n], q, kTw[:, w0:w0 + n], start=True, stop=True)
                        if nw > 512:
                            nc.tensor.matmul(ps[:, 3, 0:P], q, kTw[:, w0 + 512:w0 + nw], start=True, stop=True)
                        nc.tensor.matmul(ps[:, 3, P:P + ncm], q, kc[0:HD, 0:ncm], start=True, stop=True).then_inc(S("scored"), 1)

                    scores(0)
                    for h in range(H):
                        if h + 1 < H:
                            scores(h + 1)
                        pe.wait_ge(S("exped"), h + 1)
                        for gi, grp in enumerate(groups):
                            g = h * NGr + gi
                            if g >= 2:
                                turn_wait(pe, g - 2)
                            for i, (br, col, n, v) in enumerate(grp):
                                m = nc.tensor.transpose(ps[0:n, 4 + g % 2, i * P:i * P + P], s[:, h % 2, col:col + n], ident[:])
                            m.then_inc(S("turned"), 1)
                        for g in (h * NGr + NGr - 2, h * NGr + NGr - 1):
                            if g >= 0:
                                turn_wait(pe, g)
                        if h >= 2:
                            pe.wait_ge(S("combined"), h - 1)
                        first = set()
                        for bi, (br, col, n, v) in enumerate(blocks):
                            lastb = bi + 1 == len(blocks) or blocks[bi + 1][0] != br
                            m = nc.tensor.matmul(ps[:, 6 + h % 2, br * HD:br * HD + HD], pT[0:n, h % 2, bi, :], v,
                                                 start=br not in first, stop=lastb)
                            first.add(br)
                        m.then_inc(S("pv"), 1)

                @b.vector
                def _(dve):
                    link = Link(dve, S("v"))

                    def biases(h):
                        dve.wait_ge(S("scored"), h + 1)
                        if h >= 2:
                            dve.wait_ge(S("turned"), (h - 1) * NGr)
                        sp_, hp = s[:, h % 2], h % 2
                        off = SEQ - nk
                        for n0 in range(0, nk, 512):
                            n = min(512, nk - n0)
                            link(V.tensor_tensor(sp_[:, n0:n0 + n], ps[:, n0 // 512, 0:n], T[:, h, off + n0:off + n0 + n], ALU.add))
                        wo = WIN + P - nw
                        n = min(512, nw)
                        link(V.tensor_tensor(sp_[:, CW:CW + n], ps[:, 2, 0:n], TW[:, h, wo:wo + n], ALU.add))
                        if nw > 512:
                            link(V.tensor_tensor(sp_[:, CW + 512:CW + nw], ps[:, 3, 0:P], TW[:, h, 512:512 + P], ALU.add))
                        co = 927 - P * t
                        link(V.tensor_tensor(sp_[:, CC:CC + ncm], ps[:, 3, P:P + ncm], T[:, h, co:co + 16 * (ncm - 1) + 1:16], ALU.add), S("biased"))
                        for br, (a, n) in enumerate(((CC, ncm), (0, nk), (CW, nw))):
                            link(V.tensor_reduce(stat[:, hp, 0, br:br + 1], sp_[:, a:a + n], AX.X, ALU.max, negate=True), S("maxed") if br == 2 else None)

                    def copies(h):
                        if h >= 2:
                            dve.wait_ge(S("pv"), h - 1)
                        for gi, grp in enumerate(groups):
                            g = h * NGr + gi
                            if g % 2 == 1:
                                dve.wait_ge(S("turned"), g + 1)
                                copy_group(nc.vector.tensor_copy, h, gi, grp, g, "odd")

                    def combine(h):
                        hp = h % 2
                        dve.wait_ge(S("exped"), h + 1)
                        link(V.reciprocal(stat[:, hp, 2, :], stat[:, hp, 1, :]))
                        link(V.tensor_tensor(stat[:, hp, 3, :], stat[:, hp, 2, :], ng[:, t, h, :], ALU.mult))
                        link(V.tensor_tensor(stat[:, hp, 3, 0:1], stat[:, hp, 3, 0:1], valid[:, t:t + 1], ALU.mult))
                        dve.wait_ge(S("pv"), h + 1)
                        yh = y[:, t % 2, h * HD:h * HD + HD]
                        link(V.tensor_scalar(yh, ps[:, 6 + hp, 0:HD], stat[:, hp, 3, 0:1], None, ALU.mult))
                        link(V.scalar_tensor_tensor(yh, ps[:, 6 + hp, HD:2 * HD], stat[:, hp, 3, 1:2], yh, ALU.mult, ALU.add))
                        link(V.scalar_tensor_tensor(yh, ps[:, 6 + hp, 2 * HD:3 * HD], stat[:, hp, 3, 2:3], yh, ALU.mult, ALU.add), S("combined"))

                    biases(0)
                    for h in range(H):
                        if h + 1 < H:
                            biases(h + 1)
                        copies(h)
                        combine(h)

                @b.scalar
                def _(act):
                    def exps(h):
                        act.wait_ge(S("maxed"), h + 1)
                        hp = h % 2
                        if h >= 2:
                            act.wait_ge(S("combined"), h - 1)
                        for br, (a, n) in enumerate(((CC, ncm), (0, nk), (CW, nw))):
                            m = A.activation(s[:, hp, a:a + n], s[:, hp, a:a + n], ACT.Exp, bias=stat[:, hp, 0, br:br + 1],
                                             accum_out=stat[:, hp, 1, br:br + 1])
                        m.then_inc(S("exped"), 1)

                    exps(0)
                    for h in range(H):
                        if h + 1 < H:
                            exps(h + 1)
                        if h >= 2:
                            act.wait_ge(S("pv"), h - 1)
                        for gi, grp in enumerate(groups):
                            g = h * NGr + gi
                            if g % 2 == 0:
                                act.wait_ge(S("turned"), g + 1)
                                copy_group(lambda o_, i_: A.activation(o_, i_, ACT.Copy), h, gi, grp, g, "even")

                @b.sync
                def _(sp):
                    sp.wait_ge(S("combined"), H)
                    st = Loads(sp, S("st"))
                    st(y_mix[t * P:t * P + P, 768:1024], y[:, t % 2, :])
                    st.all_in()
            kit.clear()


def nsa(kit, env, io, l):
    nc = kit.nc
    with ExitStack() as c:
        wb = c.enter_context(nc.sbuf_tensor("c_wb", [P, 32, P], F32))
        peadd = c.enter_context(nc.sbuf_tensor("c_peadd", [P, 1], F32))
        compress_weights(kit, env, io, l, wb, peadd, c)
        nsa_prompt(kit, env, io, l, wb, peadd)
        if NSA_SAMPLE:
            nsa_sample(kit, env, io, l, wb, peadd)


NSA_SAMPLE = True


SL, SCM, SWN, SNW = 0, PAST, PAST + 256, PAST + 256 + WIN
NDEC = SNW + 8


def nsa_sample(kit, env, io, l, wb, peadd):
    nc, S, ps, ident = kit.nc, kit.sem, env["ps"], env["ident"]
    z, y_mix = env["z"], env["y_mix"]
    V, A = nc.vector, nc.scalar
    R = H * NB
    s0 = PADROWS + SEQ
    G4 = 4
    NCH = PAGES // G4
    with ExitStack() as c:
        def sb(name, shape, dt=F32):
            return c.enter_context(nc.sbuf_tensor(name, shape, dt))
        q = sb("e_q", [R, HD])
        qT = sb("e_qT", [HD, R])
        qpad = sb("e_qpad", [HD, NB, R])
        qb = sb("e_qb", [HD, 2, R])
        kvn = sb("e_kvn", [R, 6, HD])
        ng = sb("e_ng", [R, 3])
        same = sb("e_same", [R, R])
        own = sb("e_own", [R, NB])
        new = sb("e_new", [R, 16])
        sall = sb("e_sall", [R, PAST + 4])
        scm = sb("e_scm", [R, 256])
        ptab = sb("e_ptab", [1, NB * PAGES], I32)
        t64 = sb("e_t64", [R, HD])
        st = sb("e_st", [R, 16])
        ob = sb("e_ob", [R, NB, HD])
        o = sb("e_o", [R, 3, HD])
        y = sb("e_y", [R, HD])

        with ExitStack() as c2:
            def sb2(name, shape):
                return c2.enter_context(nc.sbuf_tensor(name, shape, F32))
            win = sb2("e_win", [P, NB, WIN // P, P])
            kTw = sb2("e_kTw", [HD, NB, WIN])
            swn = sb2("e_swn", [R, WIN + 1])
            pTw = sb2("e_pTw", [P, WIN // P, R])
            oneh = sb2("e_oneh", [33, NDEC])
            rel = sb2("e_rel", [33, H])
            relq = sb2("e_relq", [33, H, NB])
            with nc.Block() as b:
                @b.sync
                def _(sp):
                    ld = Loads(sp, S("ld"))
                    sample_heads(ld, io, z, q, NQ, 1)
                    for h in range(H):
                        hb = slice(h * NB, h * NB + NB)
                        ld(kvn[hb].rearrange("p a n -> p (a n)"), z[s0:s0 + NB, NKV:NKV + 384])
                        ld(ng[hb], z[s0:s0 + NB, NG + 3 * h:NG + 3 * h + 3])
                    ld(rel[0:32, :], io["rel_bias"])
                    ld(oneh[:], io["c_onehot_dec"])
                    ld(same[:], io["c_same"])
                    ld(own[:], io["c_own"])
                    ld(ptab[:], io["page_table"].rearrange("b n -> (b n)").rearrange("(a n) -> a n", a=1))
                    ld2 = Loads(sp, S("win_in"))
                    for bb in range(NB):
                        ld2(win[:, bb], io["cache_swa_kv"][ds(l, 1), bb].rearrange("a (t p) r d -> p (a t) (r d)", p=P))
                    ld.all_in()
                    ld2.all_in()

                @b.vector
                def _(dve):
                    link = Link(dve, S("v"))
                    link(V.memset(qpad[:], 0.0))
                    link(V.memset(relq[:], 1.0))
                    dve.wait_ge(S("ld"), 16 * 17)
                    link(V.tensor_scalar(q[:], q[:], 0.125, None, ALU.mult), S("q_ready"))
                    link(V.tensor_copy(relq[0:32], bc(rel[0:32, :], H, [32, H, NB])), S("rel_ready"))
                    dve.wait_ge(S("q_turned"), 1)
                    link(V.tensor_copy(qT[:], ps[0:HD, 0, 0:R]))
                    for bb in range(NB):
                        link(V.tensor_copy(qpad[:, bb, bb::NB], qT[:, bb::NB]), S("qpad") if bb == NB - 1 else None)
                    for bb in range(NB):
                        dve.wait_ge(S("kw_turned"), bb + 1)
                        link(V.tensor_copy(kTw[:, bb, :], ps[0:HD, 1 + bb % 2, :]), S("kw_ready"))
                    dve.wait_ge(S("biases"), 1)
                    link(V.tensor_copy(scm[:], ps[0:R, 4, 0:256]))
                    link(V.tensor_copy(swn[:, 0:WIN], ps[0:R, 5, :]))
                    link(V.tensor_copy(new[:, 0:1], ps[0:R, 6, 0:1]), S("bias_read"))
                    for ch in range(NCH):
                        dve.wait_ge(S("slc_bias"), ch + 1)
                        link(V.tensor_copy(sall[:, ch * 512:ch * 512 + 512], ps[0:R, 4 + ch % 2, :]), S("bias_read"))
                    for j, r in enumerate((2, 4)):
                        link(V.tensor_tensor_reduce(t64[:], q[:], kvn[:, r, :], 1.0, 0.0, ALU.mult, ALU.add, new[:, 1 + j:2 + j]))
                        link(V.tensor_tensor(new[:, 1 + j:2 + j], new[:, 1 + j:2 + j], new[:, 0:1], ALU.add))
                    link(V.tensor_copy(sall[:, PAST:PAST + 1], new[:, 1:2]))
                    link(V.tensor_copy(swn[:, WIN:WIN + 1], new[:, 2:3]))
                    dve.wait_ge(S("gexp"), 1)
                    link(V.tensor_scalar(ng[:], ng[:], 1.0, None, ALU.add))
                    link(V.reciprocal(ng[:], ng[:]))
                    dve.wait_ge(S("w_scored"), 1)
                    link(V.tensor_tensor(swn[:, 0:WIN], swn[:, 0:WIN], ps[0:R, 7, :], ALU.add))
                    link(V.tensor_reduce(st[:, 0:1], swn[:], AX.X, ALU.max, negate=True), S("w_max"))
                    dve.wait_ge(S("pw_turned"), 1)
                    link(V.tensor_copy(pTw[:].rearrange("p a n -> p (a n)"), ps[:, 0, 0:4 * R]), S("pw_ready"))
                    dve.wait_ge(S("w_pv"), 1)
                    link(V.tensor_tensor(ob[:], ps[0:R, 1, :].rearrange("p (b d) -> p b d", b=NB), bc(own[:], NB, [R, NB, HD]), ALU.mult))
                    link(V.tensor_reduce(o[:, 2, :], ob[:].rearrange("p b d -> p d b"), AX.X, ALU.add))
                    link(V.scalar_tensor_tensor(o[:, 2, :], kvn[:, 5, :], swn[:, WIN:WIN + 1], o[:, 2, :], ALU.mult, ALU.add))
                    link(V.reciprocal(st[:, 8:9], st[:, 1:2]))
                    link(V.tensor_scalar(o[:, 2, :], o[:, 2, :], st[:, 8:9], ng[:, 2:3], ALU.mult, ALU.mult))

                @b.scalar
                def _(act):
                    act.wait_ge(S("ld"), 16 * 17)
                    A.activation(ng[:], ng[:], ACT.Exp, scale=-1.0).then_inc(S("gexp"), 1)
                    act.wait_ge(S("w_max"), 1)
                    A.activation(swn[:], swn[:], ACT.Exp, bias=st[:, 0:1], accum_out=st[:, 1:2]).then_inc(S("w_exp"), 1)

                @b.tensor
                def _(pe):
                    pe.wait_ge(S("q_ready"), 1)
                    nc.tensor.transpose(ps[0:HD, 0, 0:R], q[:], ident[0:R, 0:R]).then_inc(S("q_turned"), 1)
                    pe.wait_ge(S("win_in"), 16 * NB)
                    for bb in range(NB):
                        if bb >= 2:
                            pe.wait_ge(S("kw_ready"), bb - 1)
                        for i in range(4):
                            m = nc.tensor.transpose(ps[0:HD, 1 + bb % 2, i * P:i * P + P], win[:, bb, i, 0:HD], ident[:])
                        m.then_inc(S("kw_turned"), 1)
                    pe.wait_ge(S("rel_ready"), 1)
                    rq = relq[:].rearrange("p h b -> p (h b)")
                    nc.tensor.matmul(ps[0:R, 4, 0:256], rq, oneh[:, SCM:SCM + 256], start=True, stop=True)
                    nc.tensor.matmul(ps[0:R, 5, :], rq, oneh[:, SWN:SWN + WIN], start=True, stop=True)
                    nc.tensor.matmul(ps[0:R, 6, 0:8], rq, oneh[:, SNW:SNW + 8], start=True, stop=True).then_inc(S("biases"), 1)
                    for ch in range(NCH):
                        pe.wait_ge(S("bias_read"), max(1, ch))
                        nc.tensor.matmul(ps[0:R, 4 + ch % 2, :], rq, oneh[:, ch * 512:ch * 512 + 512], start=True, stop=True).then_inc(S("slc_bias"), 1)
                    pe.wait_ge(S("qpad"), 1)
                    pe.wait_ge(S("kw_ready"), NB)
                    for bb in range(NB):
                        m = nc.tensor.matmul(ps[0:R, 7, :], qpad[:, bb, :], kTw[:, bb, :], start=(bb == 0), stop=(bb == NB - 1))
                    m.then_inc(S("w_scored"), 1)
                    pe.wait_ge(S("w_exp"), 1)
                    for i in range(4):
                        m = nc.tensor.transpose(ps[:, 0, i * R:i * R + R], swn[:, i * P:i * P + P], ident[0:R, 0:R])
                    m.then_inc(S("pw_turned"), 1)
                    pe.wait_ge(S("pw_ready"), 1)
                    for i in range(4):
                        m = nc.tensor.matmul(ps[0:R, 1, :], pTw[:, i, :], win[:, :, i, HD:P], start=(i == 0), stop=(i == 3))
                    m.then_inc(S("w_pv"), 1)
            kit.clear()

        with ExitStack() as c2:
            vall = c2.enter_context(nc.sbuf_tensor("e_vall", [P, NB, PAGES, HD], F32))
            vcm = c2.enter_context(nc.sbuf_tensor("e_vcm", [P, NB, 2, HD], F32))
            with ExitStack() as c3:
                pages = [c3.enter_context(nc.sbuf_tensor(f"e_pg{j}", [P, PAGES, 256], F32)) for j in range(2)]
                pT = c3.enter_context(nc.sbuf_tensor("e_pT", [P, PAST], F32))
                kT = c3.enter_context(nc.sbuf_tensor("e_kT", [HD, 2, 512], F32))
                kvT = c3.enter_context(nc.sbuf_tensor("e_kvT", [P, 256], F32))

                def load_pages(sp, buf, bb, sem):
                    with sp.Fori(0, PAGES) as i:
                        page = sp.value_load(ptab[0:1, ds(bb * PAGES + i, 1)], min_val=0, max_val=NPOOL - 1)
                        sp.dma_start(buf[:, ds(i, 1), :],
                                     io["cache_nsa_kv"][ds(l, 1), ds(page, 1)].rearrange("a g t r d -> t (a g) (r d)")).then_inc(sem, 16)

                with nc.Block() as b:
                    @b.sync
                    def _(sp):
                        load_pages(sp, pages[0], 0, S("ld"))
                        sp.wait_ge(S("ld"), 16 * PAGES)

                    @b.vector
                    def _(dve):
                        V.memset(kvT[:], 0.0).then_inc(S("v"), 1)
                kit.clear()

                with nc.Fori(0, NB // 2) as g:
                    with nc.Block(no_gpsimd_drain=True) as b:
                        @b.sync
                        def _(sp):
                            load_pages(sp, pages[1], g * 2 + 1, S("odd_in"))
                            sp.wait_ge(S("k_turned"), NCH)
                            sp.wait_ge(S("v_kept"), 1)
                            load_pages(sp, pages[0], (g * 2 + 2) % NB, S("next_in"))
                            sp.wait_ge(S("odd_in"), 16 * PAGES)
                            sp.wait_ge(S("next_in"), 16 * PAGES)

                        @b.tensor
                        def _(pe):
                            def score(pe, j, ch):
                                n = NCH * j + ch
                                pe.wait_ge(S("qb"), j + 1)
                                pe.wait_ge(S("kT"), n + 1)
                                if n >= 2:
                                    pe.wait_ge(S("added"), n - 1)
                                nc.tensor.matmul(ps[0:R, 4 + ch % 2, :], qb[:, j, :], kT[:, ch % 2, :], start=True, stop=True).then_inc(S("scored"), 1)

                            for j in range(2):
                                pg = pages[j]
                                if j:
                                    pe.wait_ge(S("odd_in"), 16 * PAGES)
                                for ch in range(NCH):
                                    n = NCH * j + ch
                                    if n >= 2:
                                        pe.wait_ge(S("pT"), n - 1)
                                    for i in range(G4):
                                        m = nc.tensor.transpose(ps[:, ch % 2, i * P:i * P + P], pg[:, ch * G4 + i, 0:P], ident[:])
                                    m.then_inc(S("kv_turned"), 1)
                                    if n >= 2:
                                        pe.wait_ge(S("kT"), n - 1)
                                    for i in range(G4):
                                        m = nc.tensor.transpose(ps[0:HD, 2 + ch % 2, i * P:i * P + P], pg[:, ch * G4 + i, P:P + HD], ident[:])
                                    m.then_inc(S("k_turned"), 1)
                                    if ch:
                                        score(pe, j, ch - 1)
                                score(pe, j, NCH - 1)
                                if j:
                                    pe.wait_ge(S("c_added"), 1)
                                pe.wait_ge(S("pT"), NCH * (j + 1))
                                for k in range(32):
                                    m = nc.tensor.matmul(ps[:, 6, 0:255], wb[:, k, :], pT[:, k:k + 16 * 254 + 1:16],
                                                         start=(k == 0), stop=(k == 31))
                                m.then_inc(S("compressed"), 1)
                                pe.wait_ge(S("kvT"), j + 1)
                                for i in range(2):
                                    m = nc.tensor.transpose(ps[:, 7, i * P:i * P + P], kvT[:, i * P:i * P + P], ident[:])
                                m.then_inc(S("vc_turned"), 1)
                                nc.tensor.matmul(ps[0:R, 6, 0:255], qb[:, j, :], kvT[0:HD, 0:255], start=True, stop=True).then_inc(S("c_scored"), 1)

                        @b.scalar
                        def _(act):
                            for j in range(2):
                                for ch in range(NCH):
                                    n = NCH * j + ch
                                    act.wait_ge(S("kv_turned"), n + 1)
                                    if n == NCH:
                                        act.wait_ge(S("compressed"), 1)
                                    A.activation(pT[:, ch * 512:ch * 512 + 512], ps[:, ch % 2, :], ACT.Copy).then_inc(S("pT"), 1)
                                A.activation(vall[:, ds(2 * g + j, 1)].rearrange("p a n d -> p (a n) d"), pages[j][:, :, 192:256], ACT.Copy).then_inc(S("v_kept"), 1)

                        @b.vector
                        def _(dve):
                            link = Link(dve, S("v"))
                            for j in range(2):
                                link(V.tensor_copy(qb[:, j, :], qpad[:, ds(2 * g + j, 1), :].rearrange("p a n -> p (a n)")), S("qb"))
                                for ch in range(NCH + 1):
                                    n = NCH * j + ch
                                    if ch < NCH:
                                        dve.wait_ge(S("k_turned"), n + 1)
                                        if n >= 2:
                                            dve.wait_ge(S("scored"), n - 1)
                                        link(V.tensor_copy(kT[:, ch % 2, :], ps[0:HD, 2 + ch % 2, :]), S("kT"))
                                    if ch:
                                        dve.wait_ge(S("scored"), n)
                                        sc = sall[:, (ch - 1) * 512:ch * 512]
                                        link(V.tensor_tensor(sc, sc, ps[0:R, 4 + (ch - 1) % 2, :], ALU.add), S("added"))
                                dve.wait_ge(S("compressed"), j + 1)
                                link(V.tensor_scalar(kvT[:, 0:255], ps[:, 6, 0:255], peadd[:, 0:1], None, ALU.add), S("kvT"))
                                dve.wait_ge(S("vc_turned"), j + 1)
                                link(V.tensor_copy(vcm[:, ds(2 * g + j, 1)].rearrange("p a n d -> p (a n) d"),
                                                   ps[:, 7, 0:256].rearrange("p (n d) -> p n d", n=2)[:, :, HD:P]))
                                dve.wait_ge(S("c_scored"), j + 1)
                                link(V.tensor_tensor(scm[:, 0:255], scm[:, 0:255], ps[0:R, 6, 0:255], ALU.add), S("c_added"))
                    kit.clear()

            with ExitStack() as c3:
                def sb3(name, shape):
                    return c3.enter_context(nc.sbuf_tensor(name, shape, F32))
                pcT = sb3("e_pcT", [P, 2, R])
                psT = sb3("e_psT", [P, PAGES, R])
                pwT = None
                imp = sb3("e_imp", [R, 64])
                score_ = sb3("e_score", [R, 72])
                top = sb3("e_top", [R, 16])
                with nc.Block() as b:
                    @b.vector
                    def _(dve):
                        link = Link(dve, S("v"))
                        link(V.tensor_reduce(st[:, 2:3], scm[:], AX.X, ALU.max, negate=True), S("c_max"))
                        dve.wait_ge(S("c_exp"), 1)
                        link(V.reciprocal(st[:, 4:5], st[:, 3:4]))
                        link(V.tensor_scalar(scm[:], scm[:], st[:, 4:5], None, ALU.mult), S("p_c"))
                        link(V.tensor_reduce(imp[:], scm[:].rearrange("p (j n) -> p j n", n=4), AX.X, ALU.add))
                        link(V.tensor_tensor(imp[:, 1:64], imp[:, 1:64], scm[:, 3:252:4], ALU.add), S("imp"))
                        link(V.memset(score_[:], 1.0e30))
                        dve.wait_ge(S("imp_summed"), 1)
                        link(V.tensor_copy(score_[:, 1:63], ps[0:R, 0, 1:63]))
                        link(V.max(top[:, 0:8], score_[:, 0:65]))
                        link(V.match_replace(score_[:, 0:65], top[:, 0:8], score_[:, 0:65], -1.0e30))
                        link(V.max(top[:, 8:16], score_[:, 0:65]))
                        link(V.match_replace(score_[:, 0:65], top[:, 8:16], score_[:, 0:65], -1.0e30))
                        link(V.tensor_scalar(score_[:, 0:65], score_[:, 0:65], -5.0e29, NEG, ALU.is_gt, ALU.mult))
                        s3 = sall[:, 0:PAST].rearrange("p (j n) -> p j n", n=HD)
                        link(V.tensor_tensor(s3, s3, score_[:, 0:64].unsqueeze(2).to_broadcast([R, 64, HD]), ALU.add))
                        link(V.tensor_reduce(st[:, 5:6], sall[:, 0:PAST + 1], AX.X, ALU.max, negate=True), S("s_max"))
                        dve.wait_ge(S("pc_turned"), 1)
                        link(V.tensor_copy(pcT[:].rearrange("p a n -> p (a n)"), ps[:, 1, 0:2 * R]), S("pcT"))
                        for k in range(2):
                            dve.wait_ge(S("ps_turned"), k + 1)
                            link(V.tensor_copy(psT[:, 16 * k:16 * k + 16, :].rearrange("p a n -> p (a n)"), ps[:, 2 + k, :]), S("psT"))

                        def own_part(acc, br):
                            link(V.tensor_tensor(ob[:], acc.rearrange("p (b d) -> p b d", b=NB), bc(own[:], NB, [R, NB, HD]), ALU.mult))
                            link(V.tensor_reduce(o[:, br, :], ob[:].rearrange("p b d -> p d b"), AX.X, ALU.add))

                        dve.wait_ge(S("c_pv"), 1)
                        own_part(ps[0:R, 4, :], 0)
                        dve.wait_ge(S("s_pv"), 1)
                        own_part(ps[0:R, 5, :], 1)
                        link(V.scalar_tensor_tensor(o[:, 1, :], kvn[:, 3, :], sall[:, PAST:PAST + 1], o[:, 1, :], ALU.mult, ALU.add))
                        link(V.reciprocal(st[:, 7:8], st[:, 6:7]))
                        link(V.tensor_tensor(st[:, 7:8], st[:, 7:8], ng[:, 1:2], ALU.mult))
                        link(V.scalar_tensor_tensor(y[:], o[:, 1, :], st[:, 7:8], o[:, 2, :], ALU.mult, ALU.add))
                        link(V.scalar_tensor_tensor(y[:], o[:, 0, :], ng[:, 0:1], y[:], ALU.mult, ALU.add), S("y_ready"))

                    @b.scalar
                    def _(act):
                        act.wait_ge(S("c_max"), 1)
                        A.activation(scm[:], scm[:], ACT.Exp, bias=st[:, 2:3], accum_out=st[:, 3:4]).then_inc(S("c_exp"), 1)
                        act.wait_ge(S("s_max"), 1)
                        A.activation(sall[:, 0:PAST + 1], sall[:, 0:PAST + 1], ACT.Exp, bias=st[:, 5:6], accum_out=st[:, 6:7]).then_inc(S("s_exp"), 1)

                    @b.tensor
                    def _(pe):
                        pe.wait_ge(S("imp"), 1)
                        nc.tensor.matmul(ps[0:R, 0, 0:64], same[:], imp[:], start=True, stop=True).then_inc(S("imp_summed"), 1)
                        for i in range(2):
                            m = nc.tensor.transpose(ps[:, 1, i * R:i * R + R], scm[:, i * P:i * P + P], ident[0:R, 0:R])
                        m.then_inc(S("pc_turned"), 1)
                        pe.wait_ge(S("pcT"), 1)
                        for i in range(2):
                            m = nc.tensor.matmul(ps[0:R, 4, :], pcT[:, i, :], vcm[:, :, i, :], start=(i == 0), stop=(i == 1))
                        m.then_inc(S("c_pv"), 1)
                        pe.wait_ge(S("s_exp"), 1)
                        for k in range(2):
                            for i in range(16):
                                m = nc.tensor.transpose(ps[:, 2 + k, i * R:i * R + R], sall[:, (16 * k + i) * P:(16 * k + i) * P + P], ident[0:R, 0:R])
                            m.then_inc(S("ps_turned"), 1)
                        pe.wait_ge(S("psT"), 2)
                        for i in range(PAGES):
                            m = nc.tensor.matmul(ps[0:R, 5, :], psT[:, i, :], vall[:, :, i, :], start=(i == 0), stop=(i == PAGES - 1))
                        m.then_inc(S("s_pv"), 1)

                    @b.sync
                    def _(sp):
                        sp.wait_ge(S("y_ready"), 1)
                        so = Loads(sp, S("st"))
                        for h in range(H):
                            so(y_mix[SEQ:TOK, 768 + h * HD:768 + h * HD + HD], y[h * NB:h * NB + NB, :])
                        so.all_in()
                kit.clear()


def mixers(kit, env, io, l):
    copy_states(kit, env, io, l)
    recurrent_prompt(kit, env, io, l)
    recurrent_sample(kit, env, io, l)
    nsa(kit, env, io, l)


OUTS = [("y_prompt", (1, SEQ, D)), ("y_sample", (NB, 1, D)),
        ("p_nsa", (2, 1, SEQ, 4, HD)), ("p_swa", (2, 1, WIN, 2, HD)), ("p_ret", (2, 1, 4, HD, HD)),
        ("p_C", (2, 1, 4, HD, HD)), ("p_n", (2, 1, 4, HD)), ("p_m", (2, 1, 4)), ("p_gdn", (2, 1, 4, HD, HD)),
        ("p_gconv", (2, 1, 3, 768)), ("p_ffn_conv", (2, 1, 2, DFF)),
        ("s_nsa", (2, NB, 1, 4, HD)), ("s_swa", (2, NB, WIN, 2, HD)), ("s_ret", (2, NB, 4, HD, HD)),
        ("s_C", (2, NB, 4, HD, HD)), ("s_n", (2, NB, 4, HD)), ("s_m", (2, NB, 4)), ("s_gdn", (2, NB, 4, HD, HD)),
        ("s_gconv", (2, NB, 3, 768)), ("s_ffn_conv", (2, NB, 2, DFF))]


def buckets(n):
    f = np.float32
    big = 16 + (np.log(np.maximum(n, 1).astype(f) / f(16)) / f(math.log(64)) * f(16)).astype(np.int32)
    return np.where(n < 16, n, np.minimum(big, 31))


def onehot(dist, ok):
    out = np.zeros((33, len(dist)), np.float32)
    out[buckets(np.maximum(dist, 0)), np.arange(len(dist))] = ok
    out[32] = np.where(ok, 0.0, NEG)
    return out


def constants():
    f = np.float32
    i = np.arange(P)
    lo = i[:, None] >= i[None, :]
    pos = np.concatenate([np.arange(SEQ), [PAST]]).astype(f)
    inv = f(10000.0) ** (-np.linspace(0.0, 1.0, HD // 2, dtype=f))
    ang = (pos[:, None] * inv[None, :]).astype(f).astype(np.float64)
    log_g = np.log(1.0 - 2.0 ** (-5.0 - np.arange(H)))
    dist = (i[None, :] - i[:, None])
    ret = np.where(dist[:, None, :] >= 0, np.exp(log_g[None, :, None] * np.maximum(dist, 0)[:, None, :]), 0.0) * 0.125
    xi = np.stack([np.exp(log_g[None] * (i[:, None] + 1.0)), 0.125 * np.exp(log_g[None] * (P - 1.0 - i[:, None])),
                   np.broadcast_to(np.exp(log_g * P), (P, H))], 1)
    lev = []
    for s in range(7):
        w = 1 << s
        lev.append((i[:, None] // (2 * w) == i[None, :] // (2 * w)) & (i[:, None] // w % 2 == 1) & (i[None, :] // w % 2 == 0))
    lev = np.stack(lev, 1)
    last = np.zeros((P, P), f)
    last[P - 1] = 1.0
    d1, d2 = 1023 - np.arange(TL), 639 - np.arange(WL)
    return {
        "c_ident": np.eye(P, dtype=f),
        "c_rope": np.concatenate([np.cos(ang), np.sin(ang)], 1).astype(f),
        "c_retD": ret.astype(f).reshape(P, H * P),
        "c_xi": xi.astype(f).reshape(P, 3 * H),
        "c_dec": np.repeat(1.0 - 2.0 ** (-5.0 - np.arange(H)), NB).astype(f)[:, None],
        "c_onehot": np.concatenate([onehot(d1, d1 >= 0), onehot(d2, (d2 >= 0) & (d2 < WIN))], 1),
        "c_onehot_dec": np.concatenate([onehot(x, ok) for x, ok in (
            (PAST - np.arange(PAST), np.arange(PAST) >= 0),
            (PAST - (16 * np.arange(256) + 31), np.arange(256) < 255),
            (WIN - np.arange(WIN), np.arange(WIN) > 0),
            (np.zeros(8, int), np.arange(8) < 8))], 1),
        "c_same": (np.arange(H * NB)[:, None] % NB == np.arange(H * NB)[None] % NB).astype(f),
        "c_own": (np.arange(H * NB)[:, None] % NB == np.arange(NB)[None]).astype(f),
        "c_valid": (np.arange(SEQ) >= 31).astype(f).reshape(NT, P).T.copy(),
        "c_upper": lo.T.astype(f),
        "c_mask": np.where(lo, 0.0, NEG).astype(f),
        "c_maskT": np.where(lo.T, 0.0, NEG).astype(f),
        "c_last": last,
        "c_lev": lev.astype(f).reshape(P, 7 * P),
        "c_levT": lev.transpose(2, 1, 0).astype(f).reshape(P, 7 * P),
    }


def kernel(**inputs):
    import concourse.bacc as bacc
    from concourse.bass_utils import run_bass_kernel_spmd

    nc = bacc.Bacc("TRN2", target_bir_lowering=False, num_devices=1)
    arrays, io = {}, {}
    for name, a in {**inputs, **constants()}.items():
        arrays[name] = np.ascontiguousarray(a)
        io[name] = nc.dram_tensor(name, a.shape, mybir.dt.from_np(np.asarray(a).dtype), kind="ExternalInput").ap()
    for name, shape in OUTS:
        io[name] = nc.dram_tensor(name, shape, F32, kind="ExternalOutput").ap()
    program(nc, io)
    r = run_bass_kernel_spmd(nc, [arrays], core_ids=[0])
    return tuple(r.results[0][name] for name, _ in OUTS)
```

```python
import math
from contextlib import ExitStack

import numpy as np

import concourse.bass as bass
from concourse import mybir

F32 = mybir.dt.float32
I32 = mybir.dt.int32
ALU = mybir.AluOpType
ACT = mybir.ActivationFunctionType
AX = mybir.AxisListType
ds = bass.ds

P = 128
D = 1024
KD = D // P
SEQ = 1024
NB = 8
DEPTH = 2
NT = SEQ // P
TT = NT + 1
TOK = SEQ + NB
ROWS = TT * P
XROWS = ROWS + P
PADROWS = 8
DIN = 3740
ZC = 374
NZ = DIN // ZC
DFF = 2816
NF = DFF // P
SEG = TOK // 3
DQ = 256
HD = 64
H = 4
NEG = -1.0e30
EPS = 1e-6
PAST = 4096
PAGES = 32
NPOOL = 320
WIN = 512
RQ, RK, RV, RG = 0, 256, 512, 768
MQ, MK, MV, MI, MF, MO = 1024, 1280, 1536, 1792, 1796, 1800
GX, GA, GB, GG = 2056, 2824, 2828, 2832
NQ, NKV, NG = 3088, 3344, 3728


class Link:

    def __init__(self, eng, own):
        self.eng, self.own, self.n = eng, own, {}

    def __call__(self, ins, signal=None):
        s = self.own if signal is None else signal
        self.n[s.num] = self.n.get(s.num, 0) + 1
        ins.then_inc(s, 1)
        self.eng.wait_ge(s, self.n[s.num])


class Loads:

    def __init__(self, eng, sem):
        self.eng, self.sem, self.n = eng, sem, 0

    def __call__(self, out, in_, slow=False):
        self.eng.dma_start(out, in_, allow_slow_non_contiguous=slow).then_inc(self.sem, 16)
        self.n += 16

    def all_in(self):
        self.eng.wait_ge(self.sem, self.n)


class Kit:

    def __init__(self, nc, ctx):
        self.nc, self.ctx = nc, ctx
        self.sems, self.stage_ctx, self.nums = {}, ExitStack(), set()

    def sem(self, name):
        if name not in self.sems:
            self.sems[name] = self.stage_ctx.enter_context(self.nc.semaphore(name))
            self.nums.add(self.sems[name].num)
        return self.sems[name]

    def next_stage(self):
        self.stage_ctx.close()
        self.sems, self.stage_ctx = {}, ExitStack()

    def clear(self):
        self.nc.gpsimd.sem_clear(range(min(self.nums), max(self.nums) + 1))
        self.nc.all_engine_barrier(sem_only=True)


def program(nc, io):
    with ExitStack() as ctx:
        kit = Kit(nc, ctx)
        S = kit.sem

        def sb(c, name, shape, dt=F32):
            return c.enter_context(nc.sbuf_tensor(name, shape, dt))

        ps = ctx.enter_context(nc.psum_tensor("ps", [P, 8, 512], F32))
        ident = sb(ctx, "ident", [P, P])
        mhalf = sb(ctx, "mhalf", [P, 16])
        zrow = sb(ctx, "zrow", [P, 1024])
        x_cur = nc.dram_tensor("x_cur", (XROWS, D), F32, kind="Internal").ap()
        z = nc.dram_tensor("z", (PADROWS + ROWS, DIN), F32, kind="Internal").ap()
        y_mix = nc.dram_tensor("y_mix", (XROWS, D), F32, kind="Internal").ap()
        wdist = nc.dram_tensor("wdist", (H, P, TWC), F32, kind="Internal").ap()
        env = dict(locals())

        with nc.Block() as b:
            @b.vector
            def _(dve):
                link = Link(dve, S("v"))
                link(nc.vector.memset(zrow[:], 0.0))
                link(nc.vector.memset(mhalf[:], -0.5), S("zeroed"))

            @b.sync
            def _(sp):
                ld = Loads(sp, S("ld"))
                ld(ident[:], io["c_ident"])
                ld(x_cur[0:SEQ, :], io["x_prompt"][0])
                ld(x_cur[SEQ:TOK, :], io["x_sample"][:, 0, :])
                sp.wait_ge(S("zeroed"), 1)
                ld(x_cur[TOK:TOK + P, :], zrow[:])
                ld(x_cur[TOK + P:XROWS, :], zrow[0:XROWS - TOK - P, :])
                ld(y_mix[TOK:TOK + P, :], zrow[:])
                ld(y_mix[TOK + P:XROWS, :], zrow[0:XROWS - TOK - P, :])
                for c in range(0, DIN, 1024):
                    n = min(1024, DIN - c)
                    ld(z[0:PADROWS, c:c + n], zrow[0:PADROWS, 0:n])
                ld.all_in()
        kit.clear()
        bias_tables(kit, env, io)
        kit.next_stage()

        with nc.Fori(0, DEPTH) as l:
            with ExitStack() as c:
                hT = sb(c, "hT", [P, KD, ROWS])
                norm_to_hT(kit, env, io, l, "norm_pre_mix", hT)
                project_in(kit, env, io, l, hT)
            kit.next_stage()
            if io.get("mixers", True):
                mixers(kit, env, io, l)
            with ExitStack() as c:
                fT = sb(c, "fT", [P, NF, TOK])
                with ExitStack() as c2:
                    hT = sb(c2, "hT2", [P, KD, ROWS])
                    project_out(kit, env, io, l, hT)
                    ffn_up(kit, env, io, l, hT, fT)
                ffn_down(kit, env, io, l, fT)
            kit.next_stage()

        with nc.Block() as b:
            @b.sync
            def _(sp):
                st = Loads(sp, S("st"))
                st(io["y_prompt"][0], x_cur[0:SEQ, :])
                st(io["y_sample"][:, 0, :], x_cur[SEQ:TOK, :])
                st.all_in()


def rows(t, n=P):
    return ds(t * P, n)


def norm_to_hT(kit, env, io, l, gain, hT):
    nc, S, ps, ident, mhalf, x_cur = kit.nc, kit.sem, env["ps"], env["ident"], env["mhalf"], env["x_cur"]
    with ExitStack() as c:
        xt = c.enter_context(nc.sbuf_tensor("n_x", [P, 2, D], F32))
        xn = c.enter_context(nc.sbuf_tensor("n_xn", [P, D], F32))
        junk = c.enter_context(nc.sbuf_tensor("n_junk", [P, D], F32))
        gT = c.enter_context(nc.sbuf_tensor("n_g", [P, KD], F32))
        ss = c.enter_context(nc.sbuf_tensor("n_ss", [P, 3], F32))
        with nc.Block() as b:
            @b.sync
            def _(sp):
                ld = Loads(sp, S("ld"))
                ld(gT[:], io[gain][ds(l, 1), :].rearrange("a (k p) -> p (a k)", p=P), slow=True)
                ld(xt[:, 0, :], x_cur[0:P, :])
                ld.all_in()
        kit.clear()
        with nc.Fori(0, TT) as t:
            with nc.Block(no_gpsimd_drain=True) as b:
                @b.sync
                def _(sp):
                    ld = Loads(sp, S("next_x"))
                    ld(xt[:, ds((t + 1) % 2, 1), :], x_cur[ds(t * P + P, P), :].rearrange("p (a n) -> p a n", a=1))
                    ld.all_in()

                @b.scalar
                def _(act):
                    nc.scalar.activation(junk[:], xt[:, ds(t % 2, 1), :].rearrange("p a n -> p (a n)"), ACT.Square,
                                         scale=1.0 / 32.0, accum_out=ss[:, 0:1]).then_inc(S("summed"), 1)

                @b.gpsimd
                def _(pool):
                    pool.wait_ge(S("eps_added"), 1)
                    nc.gpsimd.tensor_tensor(ss[:, 2:3], ss[:, 1:2], mhalf[:, 0:1], ALU.pow).then_inc(S("r_ready"), 1)

                @b.vector
                def _(dve):
                    dve.wait_ge(S("summed"), 1)
                    nc.vector.tensor_scalar(ss[:, 1:2], ss[:, 0:1], EPS, None, ALU.add).then_inc(S("eps_added"), 1)
                    dve.wait_ge(S("r_ready"), 1)
                    nc.vector.tensor_scalar(xn[:], xt[:, ds(t % 2, 1), :].rearrange("p a n -> p (a n)"),
                                            ss[:, 2:3], None, ALU.mult).then_inc(S("normed"), 1)
                    for half in range(2):
                        dve.wait_ge(S("turned"), half + 1)
                        nc.vector.tensor_tensor(hT[:, 4 * half:4 * half + 4, rows(t)],
                                                ps[:, half, :].rearrange("p (k n) -> p k n", k=4),
                                                gT[:, 4 * half:4 * half + 4].unsqueeze(2).to_broadcast([P, 4, P]),
                                                ALU.mult).then_inc(S("h_ready"), 1)

                @b.tensor
                def _(pe):
                    pe.wait_ge(S("normed"), 1)
                    for k in range(KD):
                        m = nc.tensor.transpose(ps[:, k // 4, (k % 4) * P:(k % 4) * P + P], xn[:, k * P:k * P + P], ident[:])
                        if k % 4 == 3:
                            m.then_inc(S("turned"), 1)
            kit.clear()


def project_in(kit, env, io, l, hT):
    nc, S, ps, z = kit.nc, kit.sem, env["ps"], env["z"]

    def chunk(i):
        return io["w_in"][ds(l, 1), :, ds(i * ZC, ZC)].rearrange("a (k p) n -> p (a k) n", p=P)

    with ExitStack() as c:
        w = c.enter_context(nc.sbuf_tensor("zi_w", [P, 2, KD, ZC], F32))
        zo = c.enter_context(nc.sbuf_tensor("zi_z", [P, TT, ZC], F32))
        with nc.Block() as b:
            @b.sync
            def _(sp):
                ld = Loads(sp, S("ld"))
                ld(w[:, 0], io["w_in"][ds(l, 1), :, 0:ZC].rearrange("a (k p) n -> p (a k) n", p=P))
                ld.all_in()
        kit.clear()
        with nc.Fori(0, NZ) as i:
            with nc.Block(no_gpsimd_drain=True) as b:
                @b.sync
                def _(sp):
                    ld = Loads(sp, S("next_w"))
                    nxt = (i + 1) % NZ
                    ld(w[:, ds((i + 1) % 2, 1), :, :].rearrange("p a k n -> p (a k) n"), chunk(nxt))
                    st = Loads(sp, S("z_stored"))
                    for t in range(TT):
                        sp.wait_ge(S("z_even") if t % 2 == 0 else S("z_odd"), t // 2 + 1)
                        st(z[PADROWS + t * P:PADROWS + t * P + P, ds(i * ZC, ZC)], zo[:, t, :])
                    ld.all_in()
                    st.all_in()

                @b.tensor
                def _(pe):
                    for t in range(TT):
                        if t == 8:
                            pe.wait_ge(S("z_even"), 1)
                        for k in range(KD):
                            m = nc.tensor.matmul(ps[:, t % 8, 0:ZC], hT[:, k, t * P:t * P + P],
                                                 w[:, ds(i % 2, 1), k, :].rearrange("p a n -> p (a n)"),
                                                 start=(k == 0), stop=(k == KD - 1))
                        m.then_inc(S("z_summed"), 1)

                @b.scalar
                def _(act):
                    for t in range(0, TT, 2):
                        act.wait_ge(S("z_summed"), t + 1)
                        nc.scalar.activation(zo[:, t, :], ps[:, t % 8, 0:ZC], ACT.Copy).then_inc(S("z_even"), 1)

                @b.vector
                def _(dve):
                    for t in range(1, TT, 2):
                        dve.wait_ge(S("z_summed"), t + 1)
                        nc.vector.tensor_copy(zo[:, t, :], ps[:, t % 8, 0:ZC]).then_inc(S("z_odd"), 1)
            kit.clear()


def project_out(kit, env, io, l, hT):
    nc, S, ps, ident, mhalf = kit.nc, kit.sem, env["ps"], env["ident"], env["mhalf"]
    x_cur, y_mix = env["x_cur"], env["y_mix"]
    with ExitStack() as c:
        def sb(name, shape):
            return c.enter_context(nc.sbuf_tensor(name, shape, F32))
        w = sb("po_w", [P, KD, D])
        yt = sb("po_y", [P, 2, D])
        xt = sb("po_x", [P, 2, D])
        ys = sb("po_ys", [P, D])
        yT = sb("po_yT", [P, KD, P])
        gb = sb("po_gb", [P, D])
        gT = sb("po_gT", [P, KD])
        xn = sb("po_xn", [P, D])
        x2 = sb("po_x2", [P, D])
        junk = sb("po_j", [P, D])
        ss = sb("po_ss", [P, 8])
        with nc.Block() as b:
            @b.sync
            def _(sp):
                ld = Loads(sp, S("ld"))
                ld(w[:], io["w_out"][ds(l, 1), :, :].rearrange("a (k p) n -> p (a k) n", p=P))
                ld(gb[:], io["norm_post_mix"][ds(l, 1), :].rearrange("a n -> (a n)").partition_broadcast(P))
                ld(gT[:], io["norm_pre_ffn"][ds(l, 1), :].rearrange("a (k p) -> p (a k)", p=P), slow=True)
                ld(xt[:, 0, :], x_cur[0:P, :])
                ld(yt[:, 0, :], y_mix[0:P, :])
                ld.all_in()
        kit.clear()
        with nc.Fori(0, TT) as t:
            xin = xt[:, ds(t % 2, 1), :].rearrange("p a n -> p (a n)")
            with nc.Block(no_gpsimd_drain=True) as b:
                @b.sync
                def _(sp):
                    ld = Loads(sp, S("next_x"))
                    for buf, src in ((xt, x_cur), (yt, y_mix)):
                        ld(buf[:, ds((t + 1) % 2, 1), :], src[ds(t * P + P, P), :].rearrange("p (a n) -> p a n", a=1))
                    sp.wait_ge(S("x2_ready"), 1)
                    st = Loads(sp, S("x_stored"))
                    st(x_cur[rows(t), :], x2[:])
                    ld.all_in()
                    st.all_in()

                @b.tensor
                def _(pe):
                    pe.wait_ge(S("y_here"), 1)
                    for k in range(KD):
                        m = nc.tensor.transpose(ps[:, 2 + k // 4, (k % 4) * P:(k % 4) * P + P],
                                                ys[:, k * P:k * P + P], ident[:])
                    m.then_inc(S("y_turned"), 1)
                    pe.wait_ge(S("yT_ready"), 2)
                    for n in range(2):
                        for k in range(KD):
                            m = nc.tensor.matmul(ps[:, n, :], yT[:, k, :], w[:, k, n * 512:n * 512 + 512],
                                                 start=(k == 0), stop=(k == KD - 1))
                    m.then_inc(S("mixed"), 1)
                    pe.wait_ge(S("xn_ready"), 1)
                    for k in range(KD):
                        m = nc.tensor.transpose(ps[:, 4 + k // 4, (k % 4) * P:(k % 4) * P + P],
                                                xn[:, k * P:k * P + P], ident[:])
                    m.then_inc(S("x_turned"), 1)

                @b.scalar
                def _(act):
                    nc.scalar.activation(ys[:], yt[:, ds(t % 2, 1), :].rearrange("p a n -> p (a n)"), ACT.Copy).then_inc(S("y_here"), 1)
                    act.wait_ge(S("y_turned"), 1)
                    nc.scalar.activation(yT[:, 4:8, :].rearrange("p k n -> p (k n)"), ps[:, 3, :], ACT.Copy).then_inc(S("yT_ready"), 1)
                    act.wait_ge(S("mixed"), 1)
                    nc.scalar.activation(junk[:], ps[:, 0:2, :].rearrange("p a n -> p (a n)"), ACT.Square,
                                         scale=1.0 / 32.0, accum_out=ss[:, 0:1]).then_inc(S("summed"), 1)
                    act.wait_ge(S("x2_ready"), 1)
                    act.wait_ge(S("summed"), 1)
                    nc.scalar.activation(junk[:], x2[:], ACT.Square,
                                         scale=1.0 / 32.0, accum_out=ss[:, 3:4]).then_inc(S("summed"), 1)

                @b.gpsimd
                def _(pool):
                    pool.wait_ge(S("eps_added"), 1)
                    nc.gpsimd.tensor_tensor(ss[:, 2:3], ss[:, 1:2], mhalf[:, 0:1], ALU.pow).then_inc(S("r_ready"), 1)
                    pool.wait_ge(S("eps_added"), 2)
                    nc.gpsimd.tensor_tensor(ss[:, 5:6], ss[:, 4:5], mhalf[:, 0:1], ALU.pow).then_inc(S("r_ready"), 1)

                @b.vector
                def _(dve):
                    link = Link(dve, S("v"))
                    dve.wait_ge(S("y_turned"), 1)
                    nc.vector.tensor_copy(yT[:, 0:4, :].rearrange("p k n -> p (k n)"), ps[:, 2, :]).then_inc(S("yT_ready"), 1)
                    dve.wait_ge(S("summed"), 1)
                    nc.vector.tensor_scalar(ss[:, 1:2], ss[:, 0:1], EPS, None, ALU.add).then_inc(S("eps_added"), 1)
                    dve.wait_ge(S("r_ready"), 1)
                    link(nc.vector.scalar_tensor_tensor(x2[:], ps[:, 0:2, :].rearrange("p a n -> p (a n)"), ss[:, 2:3],
                                                        gb[:], ALU.mult, ALU.mult))
                    link(nc.vector.tensor_tensor(x2[:], x2[:], xin, ALU.add), S("x2_ready"))
                    dve.wait_ge(S("summed"), 2)
                    nc.vector.tensor_scalar(ss[:, 4:5], ss[:, 3:4], EPS, None, ALU.add).then_inc(S("eps_added"), 1)
                    dve.wait_ge(S("r_ready"), 2)
                    nc.vector.tensor_scalar(xn[:], x2[:], ss[:, 5:6], None, ALU.mult).then_inc(S("xn_ready"), 1)
                    dve.wait_ge(S("x_turned"), 1)
                    for half in range(2):
                        nc.vector.tensor_tensor(hT[:, 4 * half:4 * half + 4, rows(t)],
                                                ps[:, 4 + half, :].rearrange("p (k n) -> p k n", k=4),
                                                gT[:, 4 * half:4 * half + 4].unsqueeze(2).to_broadcast([P, 4, P]),
                                                ALU.mult).then_inc(S("h_ready"), 1)

            kit.clear()


def ffn_up(kit, env, io, l, hT, fT):
    nc, S, ps, ident = kit.nc, kit.sem, env["ps"], env["ident"]
    with ExitStack() as c:
        def sb(name, shape):
            return c.enter_context(nc.sbuf_tensor(name, shape, F32))
        rows_in = sb("fu_rin", [19, DFF])
        rows_out = sb("fu_rout", [10, DFF])
        side = sb("fu_side", [P, NF, 19])
        w = [sb(f"fu_w{q}", [P, 2, KD, P]) for q in range(2)]
        g = sb("fu_g", [P, 2, 2 + TOK])
        cv = sb("fu_c", [P, 2, TOK])

        def load_w(ld, q, f):
            for j, name in enumerate(("w_ffn_gate", "w_ffn_up")):
                ld(w[q][:, j], io[name][ds(l, 1), :, f].rearrange("a (k p) n -> p (a k) n", p=P))

        with nc.Block() as b:
            @b.sync
            def _(sp):
                ld = Loads(sp, S("ld"))
                ld(rows_in[0:16, :], io["state_ffn_conv"][ds(l, 1)].rearrange("a b r n -> (a b r) n"))
                ld(rows_in[16:19, :], io["ffn_conv_w"][ds(l, 1)].rearrange("a r n -> (a r) n"))
                load_w(ld, 0, slice(0, P))
                ld.all_in()

            @b.tensor
            def _(pe):
                pe.wait_ge(S("ld"), 16 * 4)
                for f in range(NF):
                    m = nc.tensor.transpose(ps[:, 0, f * 19:f * 19 + 19], rows_in[:, f * P:f * P + P], ident[0:19, 0:19])
                m.then_inc(S("turned"), 1)

            @b.vector
            def _(dve):
                nc.vector.memset(g[:, :, 0:2], 0.0).then_inc(S("v"), 1)
                dve.wait_ge(S("turned"), 1)
                nc.vector.tensor_copy(side[:].rearrange("p f r -> p (f r)"), ps[:, 0, 0:NF * 19]).then_inc(S("v"), 1)
        kit.clear()

        with nc.Fori(0, NF // 2) as i:
            with nc.Block(no_gpsimd_drain=True) as b:
                @b.sync
                def _(sp):
                    ld = Loads(sp, S("w1_loaded"))
                    load_w(ld, 1, ds(i * 2 * P + P, P))
                    nxt = Loads(sp, S("next_w0"))
                    sp.wait_ge(S("summed"), 6)
                    load_w(nxt, 0, ds(((i + 1) % (NF // 2)) * 2 * P, P))
                    ld.all_in()
                    nxt.all_in()

                @b.tensor
                def _(pe):
                    m8 = 0
                    for q in range(2):
                        if q == 1:
                            pe.wait_ge(S("w1_loaded"), 32)
                        for j in range(2):
                            for s in range(3):
                                if m8 in (8, 9, 10):
                                    pe.wait_ge(S("gate_read"), m8 - 7)
                                if m8 == 11:
                                    pe.wait_ge(S("f_done"), 1)
                                for k in range(KD):
                                    m = nc.tensor.matmul(ps[:, m8 % 8, 0:SEG], w[q][:, j, k, :],
                                                         hT[:, k, s * SEG:s * SEG + SEG],
                                                         start=(k == 0), stop=(k == KD - 1))
                                m.then_inc(S("summed"), 1)
                                m8 += 1
                    pe.wait_ge(S("f_done"), 2)
                    pe.wait_ge(S("gate_read"), 6)
                    for q in range(2):
                        m = nc.tensor.transpose(ps[0:10, 5, q * P:q * P + P], g[:, q, SEQ:SEQ + 10], ident[:])
                    m.then_inc(S("rows_turned"), 1)

                @b.scalar
                def _(act):
                    for q in range(2):
                        for s in range(3):
                            act.wait_ge(S("summed"), 6 * q + s + 1)
                            nc.scalar.activation(g[:, q, 2 + s * SEG:2 + s * SEG + SEG], ps[:, (6 * q + s) % 8, 0:SEG],
                                                 ACT.Copy).then_inc(S("gate_read"), 1)
                        act.wait_ge(S("conved"), q + 1)
                        nc.scalar.activation(cv[:, q, :], cv[:, q, :], ACT.Gelu_apprx_tanh).then_inc(S("gelu"), 1)
                    act.wait_ge(S("rows_turned"), 1)
                    nc.scalar.activation(rows_out[:, ds(i * 2 * P, 2 * P)], ps[0:10, 5, 0:2 * P], ACT.Copy).then_inc(S("rows_ready"), 1)

                @b.vector
                def _(dve):
                    link = Link(dve, S("v"))
                    for q in range(2):
                        def cw(r):
                            return side[:, ds(2 * i + q, 1), r:r + 1].rearrange("p a b -> p (a b)")
                        past = side[:, ds(2 * i + q, 1), 0:16].rearrange("p a (b r) -> p (a b) r", r=2)
                        cp, cs = cv[:, q, 0:SEQ], cv[:, q, SEQ:TOK]
                        dve.wait_ge(S("gate_read"), 3 * q + 3)
                        link(nc.vector.tensor_scalar(cp, g[:, q, 0:SEQ], cw(16), None, ALU.mult))
                        link(nc.vector.scalar_tensor_tensor(cp, g[:, q, 1:1 + SEQ], cw(17), cp, ALU.mult, ALU.add))
                        link(nc.vector.scalar_tensor_tensor(cp, g[:, q, 2:2 + SEQ], cw(18), cp, ALU.mult, ALU.add))
                        link(nc.vector.tensor_scalar(cs, past[:, :, 0], cw(16), None, ALU.mult))
                        link(nc.vector.scalar_tensor_tensor(cs, past[:, :, 1], cw(17), cs, ALU.mult, ALU.add))
                        link(nc.vector.scalar_tensor_tensor(cs, g[:, q, 2 + SEQ:2 + TOK], cw(18), cs, ALU.mult, ALU.add), S("conved"))
                        dve.wait_ge(S("gelu"), q + 1)
                        for s in range(3):
                            dve.wait_ge(S("summed"), 6 * q + 3 + s + 1)
                            m = nc.vector.tensor_tensor(
                                fT[:, ds(2 * i + q, 1), s * SEG:s * SEG + SEG].rearrange("p a n -> p (a n)"),
                                cv[:, q, s * SEG:s * SEG + SEG], ps[:, (6 * q + 3 + s) % 8, 0:SEG], ALU.mult)
                            if s == 2:
                                m.then_inc(S("f_done"), 1)
            kit.clear()
        with nc.Block() as b:
            @b.sync
            def _(sp):
                st = Loads(sp, S("st"))
                st(io["p_ffn_conv"][ds(l, 1)].rearrange("a b r n -> (a b r) n"), rows_out[0:2, :])
                st(io["s_ffn_conv"][ds(l, 1), :, 1, :].rearrange("a b n -> (a b) n"), rows_out[2:10, :])
                st(io["s_ffn_conv"][ds(l, 1), :, 0, :], io["state_ffn_conv"][ds(l, 1), :, 1, :])
                st.all_in()
        kit.clear()


def ffn_down(kit, env, io, l, fT):
    nc, S, ps, mhalf, x_cur = kit.nc, kit.sem, env["ps"], env["mhalf"], env["x_cur"]
    with ExitStack() as c:
        def sb(name, shape):
            return c.enter_context(nc.sbuf_tensor(name, shape, F32))
        y = sb("fd_y", [P, TT, D])
        gb = sb("fd_gb", [P, D])
        with ExitStack() as c2:
            w = c2.enter_context(nc.sbuf_tensor("fd_w", [P, 2, NF, DQ], F32))

            def quarter(i):
                return io["w_ffn_down"][ds(l, 1), :, ds(i * DQ, DQ)].rearrange("a (f p) n -> p (a f) n", p=P)

            with nc.Block() as b:
                @b.vector
                def _(dve):
                    nc.vector.memset(y[:, NT, :], 0.0).then_inc(S("v"), 1)

                @b.sync
                def _(sp):
                    ld = Loads(sp, S("ld"))
                    ld(w[:, 0], io["w_ffn_down"][ds(l, 1), :, 0:DQ].rearrange("a (f p) n -> p (a f) n", p=P))
                    ld(gb[:], io["norm_post_ffn"][ds(l, 1), :].rearrange("a n -> (a n)").partition_broadcast(P))
                    ld.all_in()
            kit.clear()
            with nc.Fori(0, D // DQ) as i:
                with nc.Block(no_gpsimd_drain=True) as b:
                    @b.sync
                    def _(sp):
                        ld = Loads(sp, S("next_w"))
                        ld(w[:, ds((i + 1) % 2, 1), :, :].rearrange("p a f n -> p (a f) n"), quarter((i + 1) % (D // DQ)))
                        ld.all_in()

                    @b.tensor
                    def _(pe):
                        for t in range(TT):
                            n = min(P, TOK - t * P)
                            if t == 8:
                                pe.wait_ge(S("y_even"), 1)
                            for f in range(NF):
                                m = nc.tensor.matmul(ps[0:n, t % 8, 0:DQ], fT[:, f, t * P:t * P + n],
                                                     w[:, ds(i % 2, 1), f, :].rearrange("p a n -> p (a n)"),
                                                     start=(f == 0), stop=(f == NF - 1))
                            m.then_inc(S("summed"), 1)

                    @b.scalar
                    def _(act):
                        for t in range(0, TT, 2):
                            n = min(P, TOK - t * P)
                            act.wait_ge(S("summed"), t + 1)
                            nc.scalar.activation(y[0:n, t, ds(i * DQ, DQ)], ps[0:n, t % 8, 0:DQ], ACT.Copy).then_inc(S("y_even"), 1)

                    @b.vector
                    def _(dve):
                        for t in range(1, TT, 2):
                            dve.wait_ge(S("summed"), t + 1)
                            nc.vector.tensor_copy(y[:, t, ds(i * DQ, DQ)], ps[:, t % 8, 0:DQ]).then_inc(S("y_odd"), 1)
                kit.clear()
        xt = sb("fd_x", [P, 2, D])
        x2 = sb("fd_x2", [P, D])
        junk = sb("fd_j", [P, D])
        ss = sb("fd_ss", [P, 3])
        with nc.Block() as b:
            @b.sync
            def _(sp):
                ld = Loads(sp, S("ld"))
                ld(xt[:, 0, :], x_cur[0:P, :])
                ld.all_in()
        kit.clear()
        with nc.Fori(0, TT) as t:
            yin = y[:, ds(t, 1), :].rearrange("p a n -> p (a n)")
            with nc.Block(no_gpsimd_drain=True) as b:
                @b.sync
                def _(sp):
                    ld = Loads(sp, S("next_x"))
                    ld(xt[:, ds((t + 1) % 2, 1), :], x_cur[ds(t * P + P, P), :].rearrange("p (a n) -> p a n", a=1))
                    sp.wait_ge(S("x2_ready"), 1)
                    st = Loads(sp, S("x_stored"))
                    st(x_cur[rows(t), :], x2[:])
                    ld.all_in()
                    st.all_in()

                @b.scalar
                def _(act):
                    nc.scalar.activation(junk[:], yin, ACT.Square, scale=1.0 / 32.0, accum_out=ss[:, 0:1]).then_inc(S("summed"), 1)

                @b.gpsimd
                def _(pool):
                    pool.wait_ge(S("eps_added"), 1)
                    nc.gpsimd.tensor_tensor(ss[:, 2:3], ss[:, 1:2], mhalf[:, 0:1], ALU.pow).then_inc(S("r_ready"), 1)

                @b.vector
                def _(dve):
                    link = Link(dve, S("v"))
                    dve.wait_ge(S("summed"), 1)
                    nc.vector.tensor_scalar(ss[:, 1:2], ss[:, 0:1], EPS, None, ALU.add).then_inc(S("eps_added"), 1)
                    dve.wait_ge(S("r_ready"), 1)
                    link(nc.vector.scalar_tensor_tensor(x2[:], yin, ss[:, 2:3], gb[:], ALU.mult, ALU.mult))
                    link(nc.vector.tensor_tensor(x2[:], x2[:], xt[:, ds(t % 2, 1), :].rearrange("p a n -> p (a n)"), ALU.add), S("x2_ready"))
            kit.clear()


def bc(ap, n, shape):
    return ap.unsqueeze(2).to_broadcast(shape)


def recurrent_prompt(kit, env, io, l):
    nc, S, ps, ident, mhalf = kit.nc, kit.sem, env["ps"], env["ident"], env["mhalf"]
    z, y_mix = env["z"], env["y_mix"]
    V, A, G_ = nc.vector, nc.scalar, nc.gpsimd
    W3 = 3 * H * HD
    LEV = 7
    IC, LF, G, MN, MX, AB, AB2, BC, GC, CC, EG, EGE, WE, BETA, BETAH, NEGG, TMP = range(17)
    with ExitStack() as c:
        def sb(name, shape):
            return c.enter_context(nc.sbuf_tensor(name, shape, F32))
        zt = sb("r_z", [P, 2, 6 * H * HD])
        zs = sb("r_zs", [P, 4, W3])
        rope = sb("r_rope", [P, 2, 64])
        retD = sb("r_retD", [P, H, P])
        xi = sb("r_xi", [P, 3, H])
        upper = sb("r_upper", [P, P])
        mask = sb("r_mask", [P, P])
        maskT = sb("r_maskT", [P, P])
        last = sb("r_last", [P, P])
        ones = sb("r_ones", [P, P])
        lev = sb("r_lev", [P, P])
        levT = sb("r_levT", [P, LEV, P])
        qkscale = sb("r_qks", [P, 8])
        gates = sb("r_gates", [P, 16])
        cw = sb("r_cw", [P, 4, W3])
        qa = sb("r_qa", [P, 17, NT, H])
        gain = sb("r_gain", [P, NT, 3, 256])
        smo = sb("r_smo", [P, NT, 256])
        Sret = sb("r_S", [HD, H, HD])
        Caug = sb("r_C", [HD, H, HD + 1])
        Sgdn = sb("r_G", [HD, H, HD])
        mprev = sb("r_m", [P, H])
        xc = sb("r_xc", [P, 2, W3])

        def tiles(a, n):
            return z[PADROWS:PADROWS + SEQ, a:a + n].rearrange("(t p) n -> p t n", p=P)

        def loads(ld, t, q):
            ld(zt[:, q, 0:768].rearrange("p a n -> p (a n)"), z[ds(t * P + PADROWS, P), RQ:RQ + 768])
            ld(zt[:, q, 768:1536].rearrange("p a n -> p (a n)"), z[ds(t * P + PADROWS, P), MQ:MQ + 768])
            ld(rope[:, q, :].rearrange("p a n -> p (a n)"), io["c_rope"][ds(t * P, P), :])

        def conv_loads(ld, t):
            for j in range(4):
                ld(zs[:, j, :], z[ds(t * P + PADROWS - 3 + j, P), GX:GX + W3])

        def conv(link, out):
            for j in range(4):
                link(G_.tensor_tensor(zs[:, j, :], zs[:, j, :], cw[:, j, :], ALU.mult))
            link(G_.tensor_tensor(zs[:, 0, :], zs[:, 0, :], zs[:, 1, :], ALU.add))
            link(G_.tensor_tensor(zs[:, 2, :], zs[:, 2, :], zs[:, 3, :], ALU.add))
            link(G_.tensor_tensor(zs[:, 0, :], zs[:, 0, :], zs[:, 2, :], ALU.add), S("conved"))

        with ExitStack() as c2:
            def sb2(name, shape):
                return c2.enter_context(nc.sbuf_tensor(name, shape, F32))
            zg = sb2("r_zg", [P, 3, NT, 256])
            zsm = sb2("r_zsm", [P, 2, NT, 8])
            gains = sb2("r_gains", [P, 3, 256])
            sg = sb2("r_sg", [P, NT, 256])
            with nc.Block() as b:
                @b.sync
                def _(sp):
                    ld = Loads(sp, S("ld"))
                    for j, name in enumerate(("mlstm_b_i", "mlstm_b_f", "gdn_dt_bias", "gdn_A_log")):
                        ld(gates[:, 4 * j:4 * j + 4], io[name][ds(l, 1), :].rearrange("a n -> (a n)").partition_broadcast(P))
                    ld(zsm[:, 0], tiles(MI, 8))
                    ld(zsm[:, 1], tiles(GA, 8))
                    ld(upper[:], io["c_upper"])
                    ldc = Loads(sp, S("conv_in"))
                    ldc(cw[:].rearrange("p a n -> p (a n)"), io["gdn_conv_w"][ds(l, 1)].rearrange("a j n -> (a j n)").partition_broadcast(P))
                    conv_loads(ldc, 0)
                    ldg = Loads(sp, S("gates_in"))
                    for j, a in enumerate((RG, MO, GG)):
                        ldg(zg[:, j], tiles(a, 256))
                    for j, name in enumerate(("ret_norm", "mlstm_norm", "gdn_norm")):
                        ldg(gains[:, j, :], io[name][ds(l, 1), :].rearrange("a n -> (a n)").partition_broadcast(P))
                    ld2 = Loads(sp, S("ld2"))
                    ld2(retD[:].rearrange("p h n -> p (h n)"), io["c_retD"])
                    ld2(xi[:].rearrange("p a h -> p (a h)"), io["c_xi"])
                    ld2(mask[:], io["c_mask"])
                    ld2(maskT[:], io["c_maskT"])
                    ld2(last[:], io["c_last"])
                    ld2(lev[:], io["c_lev"][:, 0:P])
                    ld2(levT[:].rearrange("p a n -> p (a n)"), io["c_levT"])
                    ld2(qkscale[:], io["c_qkscale"])
                    loads(ld2, 0, slice(0, 1))
                    for x in (ld, ldc, ldg, ld2):
                        x.all_in()

                @b.gpsimd
                def _(pool):
                    link = Link(pool, S("p"))
                    pool.wait_ge(S("conv_in"), 16 * 5)
                    conv(link, 0)

                @b.scalar
                def _(act):
                    link = Link(act, S("a"))
                    act.wait_ge(S("ld"), 16 * 7)
                    link(A.activation(gates[:, 12:16], gates[:, 12:16], ACT.Exp))
                    link(A.activation(qa[:, BETA], zsm[:, 1, :, 4:8], ACT.Exp, scale=-1.0))
                    act.wait_ge(S("abs"), 1)
                    link(A.activation(qa[:, AB:AB2 + 1], qa[:, AB:AB2 + 1], ACT.Exp, scale=-1.0))
                    link(A.activation(qa[:, AB:AB2 + 1], qa[:, AB:AB2 + 1], ACT.Ln, bias=1.0), S("softplus"))
                    act.wait_ge(S("cols"), 1)
                    link(A.activation(qa[:, EG:WE + 1], qa[:, EG:WE + 1], ACT.Exp), S("exps"))
                    act.wait_ge(S("gates_in"), 16 * 6)
                    for j, dst in ((1, smo[:]), (0, gain[:, :, 0, :]), (2, gain[:, :, 2, :])):
                        link(A.activation(dst, zg[:, j], ACT.Tanh, scale=0.5), S("tanh"))
                    act.wait_ge(S("conved"), 1)
                    link(A.activation(xc[:, 0, :], zs[:, 0, :], ACT.Tanh, scale=0.5), S("xtanh"))

                @b.tensor
                def _(pe):
                    pe.wait_ge(S("lf_g"), 1)
                    nc.tensor.matmul(ps[:, 0, 0:64], upper[:], qa[:, LF:G + 1].rearrange("p a t h -> p (a t h)"), start=True, stop=True)
                    nc.tensor.matmul(ps[:, 0, 64:96], ones[:], qa[:, G].rearrange("p t h -> p (t h)"), start=True, stop=True).then_inc(S("sums"), 1)

                @b.vector
                def _(dve):
                    link = Link(dve, S("v"))
                    for x in (Sret, Caug, Sgdn, mprev):
                        link(V.memset(x[:], 0.0))
                    link(V.memset(ones[:], 1.0))
                    dve.wait_ge(S("ld"), 16 * 7)

                    def bias(j):
                        return gates[:, 4 * j:4 * j + 4].unsqueeze(1).to_broadcast([P, NT, H])
                    dve.wait_ge(S("a"), 2)
                    link(V.tensor_tensor(qa[:, IC], zsm[:, 0, :, 0:4], bias(0), ALU.add))
                    link(V.tensor_tensor(qa[:, LF], zsm[:, 0, :, 4:8], bias(1), ALU.add))
                    link(V.tensor_tensor(qa[:, G], zsm[:, 1, :, 0:4], bias(2), ALU.add))
                    link(V.tensor_scalar(qa[:, MN], qa[:, LF], 0.0, None, ALU.min))
                    link(V.tensor_scalar(qa[:, MX], qa[:, G], 0.0, None, ALU.max))
                    link(V.scalar_tensor_tensor(qa[:, AB:AB2 + 1], qa[:, LF:G + 1], -1.0, qa[:, LF:G + 1], ALU.mult, ALU.max), S("abs"))
                    link(V.tensor_scalar(qa[:, BETA], qa[:, BETA], 1.0, None, ALU.add))
                    link(V.reciprocal(qa[:, BETA], qa[:, BETA]))
                    link(V.tensor_scalar(qa[:, BETAH], qa[:, BETA], 0.5, None, ALU.mult))
                    dve.wait_ge(S("softplus"), 1)
                    link(V.tensor_tensor(qa[:, LF], qa[:, MN], qa[:, AB], ALU.subtract))
                    link(V.tensor_tensor(qa[:, G], qa[:, MX], qa[:, AB2], ALU.add))
                    link(V.scalar_tensor_tensor(qa[:, G], qa[:, G], -1.0, bias(3), ALU.mult, ALU.mult), S("lf_g"))
                    link(V.tensor_scalar(qa[:, NEGG], qa[:, G], -1.0, None, ALU.mult))
                    dve.wait_ge(S("sums"), 1)
                    link(V.tensor_copy(qa[:, BC:GC + 1].rearrange("p a t h -> p (a t h)"), ps[:, 0, 0:64]))
                    link(V.tensor_copy(qa[:, EGE].rearrange("p t h -> p (t h)"), ps[:, 0, 64:96]))
                    link(V.tensor_tensor(qa[:, CC], qa[:, IC], qa[:, BC], ALU.subtract))
                    link(V.tensor_copy(qa[:, EG], qa[:, GC]))
                    link(V.tensor_tensor(qa[:, WE], qa[:, EGE], qa[:, GC], ALU.subtract), S("cols"))
                    dve.wait_ge(S("tanh"), 1)
                    link(V.tensor_scalar(smo[:], smo[:], 0.5, 0.5, ALU.mult, ALU.add))
                    for n, j in ((2, 0), (3, 2)):
                        dve.wait_ge(S("tanh"), n)
                        gj = gains[:, j, :].unsqueeze(1).to_broadcast([P, NT, 256])
                        link(V.tensor_scalar(sg[:], gain[:, :, j, :], 0.5, 0.5, ALU.mult, ALU.add))
                        link(V.tensor_tensor(sg[:], sg[:], zg[:, j], ALU.mult))
                        link(V.tensor_tensor(gain[:, :, j, :], sg[:], gj, ALU.mult))
                    link(V.tensor_copy(gain[:, :, 1, :], gains[:, 1, :].unsqueeze(1).to_broadcast([P, NT, 256])))
                    dve.wait_ge(S("xtanh"), 1)
                    link(V.scalar_tensor_tensor(xc[:, 0, :], xc[:, 0, :], 1.0, zs[:, 0, :], ALU.add, ALU.mult))
            kit.clear()

        qk = sb("r_qk", [P, 2 * H, HD])
        qkw = sb("r_qkw", [P, 2, 2 * H, HD // 2])
        qkm = sb("r_qkm", [P, 2 * H, HD])
        qkg = sb("r_qkg", [P, 2 * H, HD])
        kb = sb("r_kb", [P, H, HD])
        qTr, kTr, qTm, kTm, qTg, kTg, kbT, wTn = [sb(f"r_T{i}", [HD, H, P]) for i in range(8)]
        vr = sb("r_vr", [P, H, HD])
        vm = sb("r_vm", [P, H, HD + 1])
        pTr, pTm, pTg, w1, w2, wm, dgm, dgg, dmu = [sb(f"r_W{i}", [P, H, P]) for i in range(9)]
        kzr, kzm, kzg, rk, rv, dl = [sb(f"r_K{i}", [P, H, HD]) for i in range(6)]
        om = sb("r_om", [P, H, HD + 1])
        o3 = sb("r_o3", [P, 3, H, HD])
        sq = sb("r_sq", [P, 3, H, HD])
        y = sb("r_y", [P, 3 * H, HD])
        sm = sb("r_sm", [P, 12, H])
        ss8 = sb("r_ss8", [P, 2, 8])
        ss12 = sb("r_ss12", [P, 2, 3 * H])
        X = sb("r_X", [P, H, P])
        XT = sb("r_XT", [P, H, P])
        NLT = sb("r_NT", [P, H, P])
        NM = [sb(f"r_NM{i}", [P, H, P]) for i in range(1, LEV)]
        Y = sb("r_Y", [P, H, P])
        with nc.Block() as b:
            @b.vector
            def _(dve):
                V.memset(vm[:], 1.0).then_inc(S("v"), 1)
        kit.clear()

        with nc.Fori(0, NT) as t:
            par = ds(t % 2, 1)
            nxt = ds((t + 1) % 2, 1)
            MXM, MU, MM, GIN, WEND, GEND, EM, MEND, DEN, RD = range(10)

            def gq(i, n=H):
                return qa[:, i, ds(t, 1), :].rearrange("p a h -> p (a h)")

            def heads(a, n=H):
                return zt[:, par, a:a + n * HD].rearrange("p a (h d) -> p (a h) d", d=HD)

            def s4(i):
                return sm[:, i, :]

            def b64(ap):
                return bc(ap, H, [P, H, HD])

            def b128(ap):
                return bc(ap, H, [P, H, P])

            def flat(ap):
                return ap.rearrange("p h n -> p (h n)")

            def bank(i):
                return ps[:, i, :].rearrange("p (h n) -> p h n", h=H)

            def bank64(i, n=HD, rows_=P):
                return ps[0:rows_, i, 0:H * n].rearrange("p (h d) -> p h d", d=n)

            def b512(ap):
                return ap.unsqueeze(1).to_broadcast([P, H, P])

            xh = xc[:, par, :].rearrange("p a (h d) -> p (a h) d", d=HD)
            halves = ((0, 1), (2, 3))

            def half(ap, k):
                return ap[:, 2 * k:2 * k + 2, :]

            with nc.Block(no_gpsimd_drain=True) as b:
                @b.sync
                def _(sp):
                    ldc = Loads(sp, S("conv_in"))
                    conv_loads(ldc, (t + 1) % NT)
                    ld = Loads(sp, S("next_z"))
                    loads(ld, (t + 1) % NT, nxt)
                    sp.wait_ge(S("y_ready"), 1)
                    st = Loads(sp, S("y_stored"))
                    st(y_mix[rows(t), 0:768], y[:].rearrange("p a n -> p (a n)"))
                    ldc.all_in()
                    ld.all_in()
                    st.all_in()

                @b.gpsimd
                def _(pool):
                    link = Link(pool, S("p"))
                    link(G_.tensor_tensor(dgm[:], b512(ident[:]), b128(gq(CC)), ALU.mult), S("m_diag"))
                    link(G_.tensor_tensor(dgg[:], b512(upper[:]), b128(gq(NEGG)), ALU.mult), S("g_diag"))
                    pool.wait_ge(S("g_squares"), 1)
                    link(G_.tensor_tensor(ss8[:, 1, :], ss8[:, 0, :], mhalf[:, 0:8], ALU.pow), S("g_r"))
                    pool.wait_ge(S("g_nlt"), 1)
                    for s in range(1, LEV):
                        link(G_.tensor_tensor(NM[s - 1][:], NLT[:], b512(levT[:, s, :]), ALU.mult), S("g_nm"))
                    pool.wait_ge(S("conv_in"), 16 * 4)
                    conv(link, nxt)
                    pool.wait_ge(S("squares"), 1)
                    link(G_.tensor_tensor(ss12[:, 1, :], ss12[:, 0, :], mhalf[:, 0:12], ALU.pow), S("r_all"))

                @b.tensor
                def _(pe):
                    def turn(n, src, signal):
                        for h in range(H):
                            m = nc.tensor.transpose(ps[0:HD, n, h * P:h * P + P], src[:, h, :], ident[:])
                        m.then_inc(signal, 1)

                    def mm4(out, lhs, rhs, signal, hs=range(H)):
                        for h in hs:
                            m = nc.tensor.matmul(out(h), lhs(h), rhs(h), start=True, stop=True)
                        m.then_inc(signal, 1)

                    def at(n, w=P, rows_=P):
                        return lambda h: ps[0:rows_, n, h * w:h * w + w]

                    def of(x, w=None):
                        return lambda h: x[:, h, :] if w is None else x[:, h, 0:w]

                    pe.wait_ge(S("m_qk"), 1)
                    turn(2, qkm[:, 0:4, :], S("m_turned"))
                    turn(3, qkm[:, 4:8, :], S("m_turned"))
                    pe.wait_ge(S("m_diag"), 1)
                    nc.tensor.matmul(ps[:, 4, :], ones[:], flat(dgm[:]), start=True, stop=True).then_inc(S("m_crow"), 1)
                    pe.wait_ge(S("g_diag"), 1)
                    nc.tensor.matmul(ps[:, 5, :], ones[:], flat(dgg[:]), start=True, stop=False)
                    nc.tensor.matmul(ps[:, 5, :], upper[:], b128(gq(G)), start=False, stop=True).then_inc(S("g_square"), 1)
                    pe.wait_ge(S("r_roped"), 1)
                    turn(0, qk[:, 0:4, :], S("r_turned"))
                    turn(1, qk[:, 4:8, :], S("r_turned"))
                    pe.wait_ge(S("g_qk"), 1)
                    pe.wait_ge(S("r_T"), 1)
                    turn(0, qkg[:, 0:4, :], S("g_turned"))
                    pe.wait_ge(S("r_T"), 2)
                    turn(1, qkg[:, 4:8, :], S("g_turned"))
                    pe.wait_ge(S("m_T"), 1)
                    turn(2, kb, S("g_turned"))
                    pe.wait_ge(S("m_T"), 2)
                    mm4(at(3), of(kTr), of(qTr), S("r_scores"))
                    pe.wait_ge(S("m_mu"), 1)
                    nc.tensor.matmul(ps[:, 4, :], ones[:], flat(dmu[:]), start=True, stop=False)
                    nc.tensor.matmul(ps[:, 4, :], ident[:], b128(gq(CC)), start=False, stop=True).then_inc(S("m_square"), 1)
                    nc.tensor.matmul(ps[:, 6, 0:8], last[:], sm[:, MU:MM + 1, :].rearrange("p a h -> p (a h)"), start=True, stop=True).then_inc(S("m_end"), 1)
                    pe.wait_ge(S("g_T"), 3)
                    pe.wait_ge(S("g_shifted"), 1)
                    mm4(at(5), of(kbT), of(kTg), S("g_nn"))
                    mm4(at(7), of(kTg), of(kbT), S("g_nn"))
                    mm4(at(0), of(kTg), of(qTg), S("g_nn"))

                    def level(s):
                        for k in range(2):
                            pe.wait_ge(S("g_x"), 2 * (s - 1) + k + 1)
                            if k == 0:
                                pe.wait_ge(S("g_nm"), s)
                            mm4(lambda h: ps[:, 1 + k, (h % 2) * P:(h % 2) * P + P], of(NM[s - 1]), of(X), S("g_y"), halves[k])
                        for k, n in ((0, 5), (1, 7)):
                            pe.wait_ge(S("g_ysb"), 2 * (s - 1) + k + 1)
                            if s < LEV - 1:
                                for h in halves[k]:
                                    nc.tensor.matmul(ps[:, n, (h % 2) * P:(h % 2) * P + P], XT[:, h, :], Y[:, h, :], start=True, stop=True)
                            for h in halves[k]:
                                m = nc.tensor.matmul(ps[:, n, 256 + (h % 2) * P:256 + (h % 2) * P + P], Y[:, h, :], XT[:, h, :], start=True, stop=True)
                            m.then_inc(S("g_xy"), 1)

                    level(1)
                    mm4(at(0, HD), of(qTr), of(Sret), S("r_inter"))
                    pe.wait_ge(S("m_end_read"), 1)
                    mm4(at(6, HD, HD), of(kzr), of(vr), S("r_dstate"))
                    level(2)
                    pe.wait_ge(S("r_p"), 1)
                    mm4(at(3, HD), of(pTr), of(vr), S("r_intra"))
                    pe.wait_ge(S("m_shifted"), 1)
                    mm4(at(4), of(kTm), of(qTm), S("m_scores"))
                    level(3)
                    pe.wait_ge(S("r_state"), 1)
                    mm4(at(0, HD + 1), of(qTm), of(Caug), S("m_inter"))
                    pe.wait_ge(S("m_kz"), 1)
                    mm4(at(6, HD + 1, HD), of(kzm), of(vm), S("m_dstate"))
                    level(4)
                    pe.wait_ge(S("m_p"), 1)
                    mm4(at(3, HD + 1), of(pTm), of(vm), S("m_intra"))
                    level(5)
                    pe.wait_ge(S("m_state"), 1)
                    mm4(at(0, HD), of(qTg), of(Sgdn), S("g_inter"))
                    level(6)
                    pe.wait_ge(S("g_x"), 2 * LEV)
                    mm4(at(4, P, HD), of(rk), of(XT), S("g_wt"))
                    pe.wait_ge(S("g_wtn"), 1)
                    for h in range(H):
                        nc.tensor.matmul(ps[:, 1, h * HD:h * HD + HD], XT[:, h, :], rv[:, h, :], start=True, stop=False)
                        m = nc.tensor.matmul(ps[:, 1, h * HD:h * HD + HD], wTn[:, h, :], Sgdn[:, h, :], start=False, stop=True)
                    m.then_inc(S("g_delta"), 1)
                    pe.wait_ge(S("g_dl"), 1)
                    pe.wait_ge(S("m_o"), 1)
                    mm4(at(3, HD), of(pTg), of(dl), S("g_intra"))
                    mm4(at(6, HD, HD), of(kzg), of(dl), S("g_dstate"))

                @b.scalar
                def _(act):
                    link = Link(act, S("a"))

                    def turned(dst, n, signal, at_, done):
                        act.wait_ge(signal, at_)
                        A.activation(flat(dst[:]), ps[0:HD, n, :], ACT.Copy).then_inc(done, 1)
                    A.activation(qkm[:], heads(768, 8), ACT.Copy).then_inc(S("m_qk"), 1)
                    A.activation(vr[:], heads(512), ACT.Copy).then_inc(S("v_ready"), 1)
                    A.activation(vm[:, :, 0:HD], heads(1280), ACT.Copy).then_inc(S("v_ready"), 1)
                    turned(qTm, 2, S("m_turned"), 1, S("m_T"))
                    turned(kTm, 3, S("m_turned"), 2, S("m_T"))
                    turned(qTr, 0, S("r_turned"), 1, S("r_T"))
                    turned(kTr, 1, S("r_turned"), 2, S("r_T"))
                    for i, x in enumerate((qTg, kTg, kbT)):
                        turned(x, i, S("g_turned"), i + 1, S("g_T"))
                    act.wait_ge(S("g_shifted"), 1)
                    A.activation(w1[:], w1[:], ACT.Exp).then_inc(S("g_weights"), 1)
                    A.activation(w2[:], w2[:], ACT.Exp).then_inc(S("g_weights"), 1)
                    act.wait_ge(S("m_exp_in"), 1)
                    A.activation(sm[:, GIN:EM + 1, :], sm[:, GIN:EM + 1, :], ACT.Exp).then_inc(S("m_exps"), 1)
                    act.wait_ge(S("m_shifted"), 1)
                    A.activation(wm[:], wm[:], ACT.Exp).then_inc(S("m_weights"), 1)
                    for s in range(1, LEV):
                        for k in range(2):
                            act.wait_ge(S("g_y"), 2 * (s - 1) + k + 1)
                            A.activation(flat(half(Y[:], k)), ps[:, 1 + k, 0:2 * P], ACT.Copy).then_inc(S("g_ysb"), 1)
                    act.wait_ge(S("g_wt"), 1)
                    A.activation(flat(wTn[:]), ps[0:HD, 4, :], ACT.Copy, scale=-1.0).then_inc(S("g_wtn"), 1)
                    act.wait_ge(S("g_delta"), 1)
                    A.activation(flat(dl[:]), ps[:, 1, 0:256], ACT.Copy).then_inc(S("g_dl"), 1)
                    act.wait_ge(S("conved"), 1)
                    A.activation(xc[:, nxt, :].rearrange("p a n -> p (a n)"), zs[:, 0, :], ACT.Tanh, scale=0.5).then_inc(S("xtanh"), 1)

                @b.vector
                def _(dve):
                    link = Link(dve, S("v"))
                    sq8 = sq[:, 0:2].rearrange("p a h d -> p (a h) d")
                    link(V.tensor_tensor(sq8, xh[:, 0:8, :], xh[:, 0:8, :], ALU.mult))
                    link(V.tensor_reduce(ss8[:, 0, :], sq8, AX.X, ALU.add))
                    link(V.tensor_scalar(ss8[:, 0, :], ss8[:, 0, :], 0.25, EPS, ALU.mult, ALU.add), S("g_squares"))
                    x12 = heads(0, 8)
                    cos = rope[:, par, 0:32].to_broadcast([P, 8, 32])
                    sin = rope[:, par, 32:64].to_broadcast([P, 8, 32])
                    lo, hi = slice(0, 32), slice(32, 64)
                    link(V.tensor_tensor(qkw[:, 0], x12[:, :, lo], cos, ALU.mult))
                    link(V.tensor_tensor(qkw[:, 1], x12[:, :, hi], sin, ALU.mult))
                    link(V.tensor_tensor(qk[:, :, lo], qkw[:, 0], qkw[:, 1], ALU.subtract))
                    link(V.tensor_tensor(qkw[:, 0], x12[:, :, lo], sin, ALU.mult))
                    link(V.tensor_tensor(qkw[:, 1], x12[:, :, hi], cos, ALU.mult))
                    link(V.tensor_tensor(qk[:, :, hi], qkw[:, 0], qkw[:, 1], ALU.add), S("r_roped"))
                    dve.wait_ge(S("g_r"), 1)
                    link(V.tensor_tensor(ss8[:, 1, :], ss8[:, 1, :], qkscale[:], ALU.mult))
                    link(V.tensor_tensor(qkg[:], xh[:, 0:8, :], bc(ss8[:, 1, :], 8, [P, 8, HD]), ALU.mult))
                    link(V.tensor_tensor(kb[:], qkg[:, 4:8, :], b64(gq(BETA)), ALU.mult), S("g_qk"))
                    dve.wait_ge(S("m_crow"), 1)
                    link(V.tensor_tensor(wm[:], bank(4), b512(mask[:]), ALU.add))
                    link(V.tensor_reduce(s4(MXM), wm[:], AX.X, ALU.max))
                    link(V.tensor_tensor(s4(MU), s4(MXM), mprev[:], ALU.max))
                    link(V.tensor_tensor(s4(MM), s4(MU), gq(BC), ALU.add))
                    link(V.scalar_tensor_tensor(dmu[:], b128(s4(MU)), -1.0, b512(ident[:]), ALU.mult, ALU.mult), S("m_mu"))
                    dve.wait_ge(S("g_square"), 1)
                    link(V.tensor_tensor(w1[:], bank(5), b512(mask[:]), ALU.add))
                    link(V.scalar_tensor_tensor(w2[:], bank(5), -1.0, b512(maskT[:]), ALU.mult, ALU.add), S("g_shifted"))
                    link(V.tensor_tensor(rk[:], kb[:], b64(gq(EG)), ALU.mult))
                    link(V.tensor_tensor(rv[:], xh[:, 8:12, :], b64(gq(BETAH)), ALU.mult))
                    link(V.tensor_tensor(kzg[:], qkg[:, 4:8, :], b64(gq(WE)), ALU.mult))
                    link(V.tensor_tensor(kzr[:], qk[:, 4:8, :], b64(xi[:, 1, :]), ALU.mult))
                    dve.wait_ge(S("m_end"), 1)
                    link(V.tensor_tensor(s4(GIN), mprev[:], s4(MU), ALU.subtract))
                    link(V.tensor_tensor(s4(WEND), gq(CC), ps[:, 6, 0:4], ALU.subtract))
                    link(V.tensor_tensor(s4(GEND), mprev[:], ps[:, 6, 0:4], ALU.subtract))
                    link(V.tensor_scalar(s4(EM), s4(MM), -1.0, None, ALU.mult), S("m_exp_in"))
                    link(V.tensor_copy(mprev[:], ps[:, 6, 4:8]), S("m_end_read"))
                    dve.wait_ge(S("m_square"), 1)
                    link(V.tensor_tensor(wm[:], bank(4), b512(maskT[:]), ALU.add), S("m_shifted"))
                    dve.wait_ge(S("g_weights"), 2)
                    dve.wait_ge(S("g_nn"), 2)
                    link(V.tensor_tensor(NLT[:], bank(7), w2[:], ALU.mult), S("g_nlt"))
                    link(V.tensor_tensor(w1[:], bank(5), w1[:], ALU.mult))
                    link(V.tensor_tensor(X[:], w1[:], b512(lev[:]), ALU.mult))
                    link(V.tensor_tensor(X[:], b512(ident[:]), X[:], ALU.subtract))
                    link(V.tensor_tensor(XT[:], NLT[:], b512(levT[:, 0, :]), ALU.mult))
                    dve.wait_ge(S("g_nn"), 3)
                    link(V.tensor_tensor(pTg[:], bank(0), w2[:], ALU.mult))
                    V.tensor_tensor(half(XT[:], 0), b512(ident[:])[:, 0:2, :], half(XT[:], 0), ALU.subtract).then_inc(S("g_x"), 1)
                    V.tensor_tensor(half(XT[:], 1), b512(ident[:])[:, 0:2, :], half(XT[:], 1), ALU.subtract).then_inc(S("g_x"), 1)

                    def level(s):
                        for k, n in ((0, 5), (1, 7)):
                            dve.wait_ge(S("g_xy"), 2 * (s - 1) + k + 1)
                            dve.wait_ge(S("g_x"), 2 * (s - 1) + k + 1)
                            if s < LEV - 1:
                                link(V.tensor_tensor(half(X[:], k), half(X[:], k), ps[:, n, 0:256].rearrange("p (h n) -> p h n", h=2), ALU.subtract))
                            V.tensor_tensor(half(XT[:], k), half(XT[:], k), ps[:, n, 256:512].rearrange("p (h n) -> p h n", h=2), ALU.subtract).then_inc(S("g_x"), 1)

                    link(V.tensor_tensor(pTr[:], bank(3), retD[:], ALU.mult), S("r_p"))
                    level(1)
                    dve.wait_ge(S("r_inter"), 1)
                    link(V.tensor_tensor(o3[:, 0], bank64(0), b64(xi[:, 0, :]), ALU.mult))
                    link(V.tensor_tensor(Sret[:], Sret[:], bc(xi[0:HD, 2, :], H, [HD, H, HD]), ALU.mult))
                    dve.wait_ge(S("m_exps"), 1)
                    link(V.scalar_tensor_tensor(kzm[:], qkm[:, 4:8, :], 0.125, b64(s4(WEND)), ALU.mult, ALU.mult), S("m_kz"))
                    level(2)
                    dve.wait_ge(S("r_dstate"), 1)
                    link(V.tensor_tensor(Sret[:], Sret[:], bank64(6, HD, HD), ALU.add), S("r_state"))
                    dve.wait_ge(S("r_intra"), 1)
                    link(V.tensor_tensor(o3[:, 0], o3[:, 0], bank64(3), ALU.add))
                    level(3)
                    dve.wait_ge(S("m_scores"), 1)
                    dve.wait_ge(S("m_weights"), 1)
                    link(V.scalar_tensor_tensor(pTm[:], bank(4), 0.125, wm[:], ALU.mult, ALU.mult), S("m_p"))
                    level(4)
                    dve.wait_ge(S("m_inter"), 1)
                    link(V.tensor_tensor(om[:], bank64(0, HD + 1), bc(s4(GIN), H, [P, H, HD + 1]), ALU.mult))
                    link(V.tensor_tensor(Caug[:], Caug[:], bc(sm[0:HD, GEND, :], H, [HD, H, HD + 1]), ALU.mult))
                    dve.wait_ge(S("m_dstate"), 1)
                    link(V.tensor_tensor(Caug[:], Caug[:], bank64(6, HD + 1, HD), ALU.add), S("m_state"))
                    level(5)
                    dve.wait_ge(S("m_intra"), 1)
                    link(V.tensor_tensor(om[:], om[:], bank64(3, HD + 1), ALU.add), S("m_o"))
                    link(V.scalar_tensor_tensor(s4(DEN), om[:, :, HD], -1.0, om[:, :, HD], ALU.mult, ALU.max))
                    link(V.tensor_tensor(s4(DEN), s4(DEN), s4(EM), ALU.max))
                    link(V.reciprocal(s4(RD), s4(DEN)))
                    link(V.tensor_tensor(o3[:, 1], om[:, :, 0:HD], b64(s4(RD)), ALU.mult))
                    link(V.tensor_tensor(o3[:, 1], o3[:, 1], smo[:, ds(t, 1), :].rearrange("p a (h d) -> p (a h) d", d=HD), ALU.mult))
                    level(6)
                    dve.wait_ge(S("g_inter"), 1)
                    link(V.tensor_tensor(o3[:, 2], bank64(0), b64(gq(EG)), ALU.mult))
                    link(V.tensor_tensor(sq[:, 0:2], o3[:, 0:2], o3[:, 0:2], ALU.mult))
                    link(V.tensor_reduce(ss12[:, 0, 0:8], sq[:, 0:2].rearrange("p a h d -> p (a h) d"), AX.X, ALU.add))
                    dve.wait_ge(S("g_delta"), 1)
                    link(V.tensor_tensor(Sgdn[:], Sgdn[:], qa[0:HD, EGE, ds(t, 1), :].rearrange("p a h -> p (a h)").unsqueeze(2).to_broadcast([HD, H, HD]), ALU.mult))
                    dve.wait_ge(S("g_intra"), 1)
                    link(V.tensor_tensor(o3[:, 2], o3[:, 2], bank64(3), ALU.add))
                    link(V.tensor_tensor(sq[:, 2], o3[:, 2], o3[:, 2], ALU.mult))
                    link(V.tensor_reduce(ss12[:, 0, 8:12], sq[:, 2], AX.X, ALU.add))
                    link(V.tensor_scalar(ss12[:, 0, :], ss12[:, 0, :], 1.0 / HD, EPS, ALU.mult, ALU.add), S("squares"))
                    dve.wait_ge(S("g_dstate"), 1)
                    link(V.tensor_tensor(Sgdn[:], Sgdn[:], bank64(6, HD, HD), ALU.add))
                    dve.wait_ge(S("r_all"), 1)
                    o12 = o3[:].rearrange("p a h d -> p (a h) d")
                    link(V.tensor_tensor(y[:], o12, bc(ss12[:, 1, :], 12, [P, 12, HD]), ALU.mult))
                    link(V.tensor_tensor(y[:].rearrange("p a d -> p (a d)"), y[:].rearrange("p a d -> p (a d)"),
                                         gain[:, ds(t, 1)].rearrange("p a j n -> p (a j n)"), ALU.mult), S("y_ready"))
                    dve.wait_ge(S("xtanh"), 1)
                    xn = xc[:, nxt, :].rearrange("p a n -> p (a n)")
                    link(V.scalar_tensor_tensor(xn, xn, 1.0, zs[:, 0, :], ALU.add, ALU.mult))
            kit.clear()

        with nc.Block() as b:
            @b.sync
            def _(sp):
                st = Loads(sp, S("st"))
                st(io["p_ret"][ds(l, 1), 0].rearrange("a h d e -> d (a h) e"), Sret[:])
                st(io["p_C"][ds(l, 1), 0].rearrange("a h d e -> d (a h) e"), Caug[:, :, 0:HD])
                st(io["p_n"][ds(l, 1), 0].rearrange("a h (d o) -> d (a h) o", o=1), Caug[:, :, HD:HD + 1], slow=True)
                st(io["p_gdn"][ds(l, 1), 0].rearrange("a h d e -> d (a h) e"), Sgdn[:])
                st(io["p_m"][ds(l, 1), 0], mprev[0:1, :])
                st.all_in()
        kit.clear()


def copy_states(kit, io, z, l, sp):
    st = Loads(sp, kit.sem("states_copied"))
    p0, s0 = PADROWS, PADROWS + SEQ
    st(io["p_nsa"][ds(l, 1), 0].rearrange("a t r d -> (a t) (r d)"), z[p0:p0 + SEQ, NKV:NKV + 256])
    st(io["p_swa"][ds(l, 1), 0].rearrange("a t r d -> (a t) (r d)"), z[p0 + SEQ - WIN:p0 + SEQ, NKV + 256:NKV + 384])
    st(io["p_gconv"][ds(l, 1), 0].rearrange("a r n -> (a r) n"), z[p0 + SEQ - 3:p0 + SEQ, GX:GX + 768])
    st(io["s_nsa"][ds(l, 1), :, 0].rearrange("a b r d -> (a b) (r d)"), z[s0:s0 + NB, NKV:NKV + 256])
    st(io["s_swa"][ds(l, 1), :, WIN - 1].rearrange("a b r d -> (a b) (r d)"), z[s0:s0 + NB, NKV + 256:NKV + 384])
    st(io["s_swa"][ds(l, 1), :, 0:WIN - 1].rearrange("a b t r d -> (a b) (t r d)"),
       io["cache_swa_kv"][ds(l, 1), :, 1:WIN].rearrange("a b t r d -> (a b) (t r d)"))
    st(io["s_gconv"][ds(l, 1), :, 2].rearrange("a b n -> (a b) n"), z[s0:s0 + NB, GX:GX + 768])
    st(io["s_gconv"][ds(l, 1), :, 0:2], io["state_gdn_conv"][ds(l, 1), :, 1:3])
    st.all_in()


def sample_heads(ld, io, z, dst, a, groups, pitch=256):
    s0 = PADROWS + SEQ
    for h in range(H):
        src = z[s0:s0 + NB, a + h * HD:a + h * HD + pitch * (groups - 1) + HD] if groups == 1 else \
            z[s0:s0 + NB, a:a + pitch * groups].rearrange("b (g n) -> b g n", n=pitch)[:, :, h * HD:h * HD + HD]
        ld(dst[h * NB:h * NB + NB], src)


def recurrent_sample(kit, env, io, l):
    nc, S, mhalf = kit.nc, kit.sem, env["mhalf"]
    z, y_mix = env["z"], env["y_mix"]
    V, A = nc.vector, nc.scalar
    R = H * NB
    s0 = PADROWS + SEQ
    with ExitStack() as c:
        def sb(name, shape):
            return c.enter_context(nc.sbuf_tensor(name, shape, F32))
        rz = sb("d_rz", [R, 4, HD])
        mz = sb("d_mz", [R, 3, HD])
        mo = sb("d_mo", [R, HD])
        taps = sb("d_taps", [R, 4, 3, HD])
        cw = sb("d_cw", [R, 4, 3, HD])
        gg = sb("d_gg", [R, HD])
        sc = sb("d_sc", [R, 4])
        par = sb("d_par", [R, 4])
        gains = sb("d_gains", [R, 3, HD])
        rope = sb("d_rope", [R, HD])
        dec = sb("d_dec", [R, 1])
        st3 = [sb(f"d_st{j}", [R, HD, HD]) for j in range(3)]
        nst = sb("d_n", [R, HD])
        mst = sb("d_m", [R, 1])
        tmp = sb("d_tmp", [R, HD, HD])
        q = sb("d_q", [R, HD])
        k = sb("d_k", [R, HD])
        xc = sb("d_xc", [R, 3, HD])
        xe = sb("d_xe", [R, 3, HD])
        sg = sb("d_sg", [R, 3, HD])
        t4 = sb("d_t4", [R, 4, HD])
        o = sb("d_o", [R, HD])
        col = sb("d_col", [R, 24])
        y = sb("d_y", [R, 3, HD])
        n_loads = [0]

        with nc.Block() as b:
            @b.sync
            def _(sp):
                ld = Loads(sp, S("ld"))
                sample_heads(ld, io, z, rz, RQ, 4)
                sample_heads(ld, io, z, mz, MQ, 3)
                sample_heads(ld, io, z, mo, MO, 1)
                sample_heads(ld, io, z, taps[:, 3], GX, 3)
                sample_heads(ld, io, z, gg, GG, 1)
                for h in range(H):
                    hb = slice(h * NB, h * NB + NB)
                    for j, a in enumerate((MI, MF, GA, GB)):
                        ld(sc[hb, j:j + 1], z[s0:s0 + NB, a + h:a + h + 1], slow=True)
                    for j, name in enumerate(("mlstm_b_i", "mlstm_b_f", "gdn_dt_bias", "gdn_A_log")):
                        ld(par[hb, j:j + 1], io[name][ds(l, 1), h:h + 1].rearrange("a n -> (a n)").partition_broadcast(NB))
                    for j, name in enumerate(("ret_norm", "mlstm_norm", "gdn_norm")):
                        ld(gains[hb, j], io[name][ds(l, 1), h * HD:h * HD + HD].rearrange("a n -> (a n)").partition_broadcast(NB))
                    for j in range(4):
                        ld(cw[hb, j], io["gdn_conv_w"][ds(l, 1), j].rearrange("a (g n) -> (a g) n", g=3)[:, h * HD:h * HD + HD].partition_broadcast(NB))
                    for j in range(3):
                        ld(taps[hb, j], io["state_gdn_conv"][ds(l, 1), :, j].rearrange("a b (g n) -> (a b) g n", g=3)[:, :, h * HD:h * HD + HD])
                    for j, name in enumerate(("state_ret", "state_mlstm_C", "state_gdn")):
                        ld(st3[j][hb], io[name][ds(l, 1), :, h].rearrange("a b d e -> (a b) d e"))
                    ld(nst[hb], io["state_mlstm_n"][ds(l, 1), :, h].rearrange("a b d -> (a b) d"))
                    ld(mst[hb], io["state_mlstm_m"][ds(l, 1), :, h:h + 1].rearrange("a b d -> (a b) d"), slow=True)
                ld(rope[:], io["c_rope"][SEQ:SEQ + 1, :].rearrange("a n -> (a n)").partition_broadcast(R))
                ld(dec[:], io["c_dec"])
                n_loads[0] = ld.n
                ld.all_in()
        kit.clear()

        with nc.Block() as b:
            LFC, ABS, MN, E1, MT, WI, GI, EM, DEN, SS, RR, GD, BT, EGD, SS2, RR2, EA, IP = range(18)

            def cc(i, n=1):
                return col[:, i:i + n]

            @b.sync
            def _(sp):
                copy_states(kit, io, z, l, sp)

            @b.gpsimd
            def _(pool):
                for j, (src, dst, n) in enumerate(((SS, RR, 1), (SS, RR, 1), (18, 20, 2), (SS, RR, 1))):
                    pool.wait_ge(S("squares"), j + 1)
                    nc.gpsimd.tensor_tensor(cc(dst, n), cc(src, n), mhalf[0:R, 0:n], ALU.pow).then_inc(S("r_ready"), 1)

            @b.scalar
            def _(act):
                link = Link(act, S("a"))
                for j, src in enumerate((rz[:, 3, :], mo[:], gg[:])):
                    link(A.activation(sg[:, j], src, ACT.Exp, scale=-1.0))
                link(A.activation(cc(EA), par[:, 3:4], ACT.Exp))
                link(A.activation(cc(BT), sc[:, 3:4], ACT.Exp, scale=-1.0), S("sig_exp"))
                act.wait_ge(S("abs"), 1)
                link(A.activation(cc(E1), cc(ABS), ACT.Exp, scale=-1.0))
                link(A.activation(cc(E1), cc(E1), ACT.Ln, bias=1.0), S("softplus"))
                act.wait_ge(S("mt"), 1)
                link(A.activation(cc(WI), cc(WI), ACT.Exp))
                link(A.activation(cc(GI), cc(GI), ACT.Exp))
                link(A.activation(cc(EM), cc(MT), ACT.Exp, scale=-1.0), S("mexp"))
                act.wait_ge(S("conved"), 1)
                link(A.activation(xe[:], xc[:], ACT.Exp, scale=-1.0), S("silu_exp"))
                act.wait_ge(S("abs"), 2)
                link(A.activation(cc(E1), cc(ABS), ACT.Exp, scale=-1.0))
                link(A.activation(cc(E1), cc(E1), ACT.Ln, bias=1.0), S("softplus"))
                act.wait_ge(S("gd"), 1)
                link(A.activation(cc(EGD), cc(GD), ACT.Exp), S("gexp"))

            @b.vector
            def _(dve):
                link = Link(dve, S("v"))

                def outer(kk, vv):
                    link(V.tensor_tensor(tmp[:], kk.unsqueeze(2).to_broadcast([R, HD, HD]),
                                         vv.unsqueeze(1).to_broadcast([R, HD, HD]), ALU.mult))

                def dot(out, vec, st):
                    link(V.tensor_tensor(tmp[:], st[:], vec.unsqueeze(2).to_broadcast([R, HD, HD]), ALU.mult))
                    link(V.tensor_reduce(out, tmp[:].rearrange("p d e -> p e d"), AX.X, ALU.add))

                def head_norm(j, gate, n):
                    link(V.tensor_tensor_reduce(t4[:, 0], o[:], o[:], 1.0, 0.0, ALU.mult, ALU.add, cc(SS)))
                    link(V.tensor_scalar(cc(SS), cc(SS), 1.0 / HD, EPS, ALU.mult, ALU.add), S("squares"))
                    dve.wait_ge(S("r_ready"), n)
                    link(V.scalar_tensor_tensor(y[:, j], o[:], cc(RR), gains[:, j], ALU.mult, ALU.mult))
                    if gate is not None:
                        link(V.tensor_tensor(y[:, j], y[:, j], gate, ALU.mult))

                dve.wait_ge(S("sig_exp"), 1)
                link(V.tensor_scalar(sg[:], sg[:], 1.0, None, ALU.add))
                link(V.reciprocal(sg[:], sg[:]))
                link(V.tensor_tensor(sg[:, 0], sg[:, 0], rz[:, 3], ALU.mult))
                link(V.tensor_tensor(sg[:, 2], sg[:, 2], gg[:], ALU.mult))
                link(V.tensor_scalar(cc(BT), cc(BT), 1.0, None, ALU.add))
                link(V.reciprocal(cc(BT), cc(BT)))
                lo, hi = slice(0, 32), slice(32, 64)
                for j, out in ((0, q), (1, k)):
                    link(V.tensor_tensor(t4[:, 0, 0:32], rz[:, j, lo], rope[:, lo], ALU.mult))
                    link(V.tensor_tensor(t4[:, 1, 0:32], rz[:, j, hi], rope[:, hi], ALU.mult))
                    link(V.tensor_tensor(out[:, lo], t4[:, 0, 0:32], t4[:, 1, 0:32], ALU.subtract))
                    link(V.tensor_tensor(t4[:, 0, 0:32], rz[:, j, lo], rope[:, hi], ALU.mult))
                    link(V.tensor_tensor(t4[:, 1, 0:32], rz[:, j, hi], rope[:, lo], ALU.mult))
                    link(V.tensor_tensor(out[:, hi], t4[:, 0, 0:32], t4[:, 1, 0:32], ALU.add))
                link(V.tensor_scalar(k[:], k[:], 0.125, None, ALU.mult))
                outer(k[:], rz[:, 2])
                link(V.scalar_tensor_tensor(st3[0][:], st3[0][:], dec[:, 0:1], tmp[:], ALU.mult, ALU.add))
                dot(o[:], q[:], st3[0])
                head_norm(0, sg[:, 0], 1)
                link(V.tensor_tensor(cc(LFC), sc[:, 1:2], par[:, 1:2], ALU.add))
                link(V.tensor_tensor(cc(IP), sc[:, 0:1], par[:, 0:1], ALU.add))
                link(V.tensor_scalar(cc(MN), cc(LFC), 0.0, None, ALU.min))
                link(V.scalar_tensor_tensor(cc(ABS), cc(LFC), -1.0, cc(LFC), ALU.mult, ALU.max), S("abs"))
                dve.wait_ge(S("softplus"), 1)
                link(V.tensor_tensor(cc(LFC), cc(MN), cc(E1), ALU.subtract))
                link(V.tensor_tensor(cc(LFC), cc(LFC), mst[:], ALU.add))
                link(V.tensor_tensor(cc(MT), cc(LFC), cc(IP), ALU.max))
                link(V.tensor_tensor(cc(WI), cc(IP), cc(MT), ALU.subtract))
                link(V.tensor_tensor(cc(GI), cc(LFC), cc(MT), ALU.subtract), S("mt"))
                dve.wait_ge(S("mexp"), 1)
                link(V.tensor_scalar(k[:], mz[:, 1], cc(WI), 0.125, ALU.mult, ALU.mult))
                outer(k[:], mz[:, 2])
                link(V.scalar_tensor_tensor(st3[1][:], st3[1][:], cc(GI), tmp[:], ALU.mult, ALU.add))
                link(V.scalar_tensor_tensor(nst[:], nst[:], cc(GI), k[:], ALU.mult, ALU.add))
                dot(o[:], mz[:, 0], st3[1])
                link(V.tensor_tensor_reduce(t4[:, 0], mz[:, 0], nst[:], 1.0, 0.0, ALU.mult, ALU.add, cc(DEN)))
                link(V.scalar_tensor_tensor(cc(DEN), cc(DEN), -1.0, cc(DEN), ALU.mult, ALU.max))
                link(V.tensor_tensor(cc(DEN), cc(DEN), cc(EM), ALU.max))
                link(V.reciprocal(cc(DEN), cc(DEN)))
                link(V.scalar_tensor_tensor(o[:], o[:], cc(DEN), sg[:, 1], ALU.mult, ALU.mult))
                head_norm(1, None, 2)
                link(V.tensor_tensor(taps[:], taps[:], cw[:], ALU.mult))
                link(V.tensor_tensor(taps[:, 0], taps[:, 0], taps[:, 1], ALU.add))
                link(V.tensor_tensor(taps[:, 2], taps[:, 2], taps[:, 3], ALU.add))
                link(V.tensor_tensor(xc[:], taps[:, 0], taps[:, 2], ALU.add), S("conved"))
                link(V.tensor_tensor(cc(GD), sc[:, 2:3], par[:, 2:3], ALU.add))
                link(V.tensor_scalar(cc(MN), cc(GD), 0.0, None, ALU.max))
                link(V.scalar_tensor_tensor(cc(ABS), cc(GD), -1.0, cc(GD), ALU.mult, ALU.max), S("abs"))
                dve.wait_ge(S("silu_exp"), 1)
                link(V.tensor_scalar(xe[:], xe[:], 1.0, None, ALU.add))
                link(V.reciprocal(xe[:], xe[:]))
                link(V.tensor_tensor(xc[:], xc[:], xe[:], ALU.mult))
                for j in range(2):
                    link(V.tensor_tensor_reduce(t4[:, 0], xc[:, j], xc[:, j], 1.0, 0.0, ALU.mult, ALU.add, cc(18 + j)))
                link(V.tensor_scalar(cc(18, 2), cc(18, 2), EPS, None, ALU.add), S("squares"))
                dve.wait_ge(S("softplus"), 2)
                link(V.tensor_tensor(cc(GD), cc(MN), cc(E1), ALU.add))
                link(V.scalar_tensor_tensor(cc(GD), cc(GD), -1.0, cc(EA), ALU.mult, ALU.mult), S("gd"))
                dve.wait_ge(S("r_ready"), 3)
                link(V.tensor_scalar(q[:], xc[:, 0], cc(20), 0.125, ALU.mult, ALU.mult))
                link(V.tensor_scalar(k[:], xc[:, 1], cc(21), None, ALU.mult))
                dve.wait_ge(S("gexp"), 1)
                link(V.tensor_scalar(st3[2][:], st3[2][:], cc(EGD), None, ALU.mult))
                dot(o[:], k[:], st3[2])
                link(V.tensor_tensor(o[:], xc[:, 2], o[:], ALU.subtract))
                link(V.tensor_scalar(o[:], o[:], cc(BT), None, ALU.mult))
                outer(k[:], o[:])
                link(V.tensor_tensor(st3[2][:], st3[2][:], tmp[:], ALU.add))
                dot(o[:], q[:], st3[2])
                head_norm(2, sg[:, 2], 4)
        kit.clear()

        with nc.Block() as b:
            @b.sync
            def _(sp):
                st = Loads(sp, S("st"))
                for h in range(H):
                    hb = slice(h * NB, h * NB + NB)
                    for j, name in enumerate(("s_ret", "s_C", "s_gdn")):
                        st(io[name][ds(l, 1), :, h].rearrange("a b d e -> (a b) d e"), st3[j][hb])
                    st(io["s_n"][ds(l, 1), :, h].rearrange("a b d -> (a b) d"), nst[hb])
                    st(io["s_m"][ds(l, 1), :, h:h + 1].rearrange("a b d -> (a b) d"), col[hb, 4:5], slow=True)
                    st(y_mix[SEQ:TOK, 0:768].rearrange("b (j n) -> b j n", j=3)[:, :, h * HD:h * HD + HD], y[hb])
                st.all_in()
        kit.clear()


TL = 1152
WL = 768
TWC = TL + WL


def bias_tables(kit, env, io):
    nc, S, ps = kit.nc, kit.sem, env["ps"]
    V, A = nc.vector, nc.scalar
    with ExitStack() as c:
        def sb(name, shape):
            return c.enter_context(nc.sbuf_tensor(name, shape, F32))
        rel = sb("b_rel", [33, H])
        relb = sb("b_relb", [33, H, P])
        oneh = sb("b_oneh", [33, TWC])
        rows_sb = sb("b_rows", [P, H, TWC])
        with nc.Block() as b:
            @b.sync
            def _(sp):
                ld = Loads(sp, S("ld"))
                ld(rel[0:32, :], io["rel_bias"])
                ld(oneh[:], io["c_onehot"])
                sp.wait_ge(S("rows_ready"), H)
                ld(env["wdist"].rearrange("h p n -> p h n"), rows_sb[:])
                ld.all_in()

            @b.vector
            def _(dve):
                link = Link(dve, S("v"))
                link(V.memset(relb[:], 1.0))
                dve.wait_ge(S("ld"), 32)
                link(V.tensor_copy(relb[0:32], bc(rel[0:32, :], H, [32, H, P])), S("rel_ready"))
                for h in range(H):
                    dve.wait_ge(S("looked_up"), h + 1)
                    link(V.tensor_copy(rows_sb[:, h, :].rearrange("p (a n) -> p a n", a=4), ps[:, 0:4, 0:TWC // 4]), S("rows_ready"))

            @b.tensor
            def _(pe):
                pe.wait_ge(S("rel_ready"), 1)
                for h in range(H):
                    if h:
                        pe.wait_ge(S("rows_ready"), h)
                    for a in range(4):
                        m = nc.tensor.matmul(ps[:, a, 0:TWC // 4], relb[:, h, :], oneh[:, a * (TWC // 4):(a + 1) * (TWC // 4)],
                                             start=True, stop=True)
                    m.then_inc(S("looked_up"), 1)
        kit.clear()


def compress_weights(kit, env, io, l, wb, peadd, c):
    nc, S, ps, ident = kit.nc, kit.sem, env["ps"], env["ident"]
    V, A = nc.vector, nc.scalar
    with ExitStack() as c2:
        pe_in = c2.enter_context(nc.sbuf_tensor("cw_pe", [32, P], F32))
        peT = c2.enter_context(nc.sbuf_tensor("cw_peT", [P, 32], F32))
        with nc.Block() as b:
            @b.sync
            def _(sp):
                ld = Loads(sp, S("pe_in"))
                ld(pe_in[:], io["nsa_cmp_pe"][ds(l, 1)].rearrange("a j c d -> (a j) (c d)"))
                ld.all_in()
                ld2 = Loads(sp, S("wb_in"))
                sp.wait_ge(S("wb_zero"), 1)
                for cc in range(2):
                    ld2(wb[cc * HD:cc * HD + HD, :, cc * HD:cc * HD + HD],
                        io["nsa_cmp_w"][ds(l, 1), cc].rearrange("a j d e -> d (a j) e"))
                ld2.all_in()

            @b.vector
            def _(dve):
                V.memset(wb[:], 0.0).then_inc(S("wb_zero"), 1)
                dve.wait_ge(S("turned"), 1)
                V.tensor_copy(peT[:], ps[:, 0, 0:32]).then_inc(S("peT"), 1)
                dve.wait_ge(S("pe_summed"), 1)
                V.tensor_copy(peadd[:], ps[:, 1, 0:1]).then_inc(S("v"), 1)

            @b.tensor
            def _(pe):
                pe.wait_ge(S("pe_in"), 16)
                nc.tensor.transpose(ps[:, 0, 0:32], pe_in[:], ident[0:32, 0:32]).then_inc(S("turned"), 1)
                pe.wait_ge(S("peT"), 1)
                pe.wait_ge(S("wb_in"), 32)
                for j in range(32):
                    m = nc.tensor.matmul(ps[:, 1, 0:1], wb[:, j, :], peT[:, j:j + 1], start=(j == 0), stop=(j == 31))
                m.then_inc(S("pe_summed"), 1)
        kit.clear()


def nsa_prompt(kit, env, io, l, wb, peadd):
    nc, S, ps, ident = kit.nc, kit.sem, env["ps"], env["ident"]
    z, y_mix = env["z"], env["y_mix"]
    V, A = nc.vector, nc.scalar
    NC = SEQ // 16 - 1
    WT = WIN // P
    with ExitStack() as c:
        def sb(name, shape):
            return c.enter_context(nc.sbuf_tensor(name, shape, F32))
        kTs = sb("p_kTs", [HD, SEQ])
        kTw = sb("p_kTw", [HD, SEQ])
        qT = sb("p_qT", [HD, H, SEQ])
        kc = sb("p_kc", [P, 64])
        vc = sb("p_vc", [64, HD])
        zk = sb("p_zk", [P, NT, 384])
        ng = sb("p_ng", [P, NT, H, 3])
        T = sb("p_T", [P, H, SEQ])
        TW = sb("p_TW", [P, H, WIN + P])
        valid = sb("p_valid", [P, NT])
        y = sb("p_y", [P, 2, 256])
        with ExitStack() as c2:
            zq = c2.enter_context(nc.sbuf_tensor("p_zq", [P, NT, 256], F32))
            cT = c2.enter_context(nc.sbuf_tensor("p_cT", [P, SEQ], F32))
            with nc.Block() as b:
                @b.sync
                def _(sp):
                    ld = Loads(sp, S("ld"))
                    zr = z[PADROWS:PADROWS + SEQ, :]
                    ld(zk[:], zr[:, NKV:NKV + 384].rearrange("(t p) n -> p t n", p=P))
                    ld(zq[:], zr[:, NQ:NQ + 256].rearrange("(t p) n -> p t n", p=P))
                    ld2 = Loads(sp, S("ld2"))
                    ld2(ng[:].rearrange("p t h b -> p t (h b)"), zr[:, NG:NG + 12].rearrange("(t p) n -> p t n", p=P))
                    wt = env["wdist"].tensor
                    for h in range(H):
                        base = h * P * TWC + P - 1
                        ld2(T[:, h, :], bass.AP(wt, base, [[TWC - 1, P], [1, SEQ]]))
                        ld2(TW[:, h, :], bass.AP(wt, base + TL, [[TWC - 1, P], [1, WIN + P]]))
                    ld2(valid[:], io["c_valid"])
                    ld2.all_in()

                @b.tensor
                def _(pe):
                    pe.wait_ge(S("ld"), 32)
                    g = 0
                    for kind in range(3 + H):
                        for half in range(2):
                            if g >= 4:
                                pe.wait_ge(S("even" if g % 2 == 0 else "odd"), (g - 4) // 2 + 1)
                            for i in range(4):
                                t = 4 * half + i
                                if kind == 0:
                                    m = nc.tensor.transpose(ps[:, g % 4, i * P:i * P + P], zk[:, t, 0:P], ident[:])
                                else:
                                    src = zk[:, t, P:P + HD] if kind == 1 else zk[:, t, 256:256 + HD] if kind == 2 else \
                                        zq[:, t, (kind - 3) * HD:(kind - 2) * HD]
                                    m = nc.tensor.transpose(ps[0:HD, g % 4, i * P:i * P + P], src, ident[:])
                            m.then_inc(S("turned"), 1)
                            g += 1
                    pe.wait_ge(S("even"), 1)
                    pe.wait_ge(S("odd"), 1)
                    for j in range(32):
                        m = nc.tensor.matmul(ps[:, 4, 0:NC], wb[:, j, :], cT[:, j:j + 16 * (NC - 1) + 1:16],
                                             start=(j == 0), stop=(j == 31))
                    m.then_inc(S("compressed"), 1)
                    pe.wait_ge(S("kc"), 1)
                    nc.tensor.transpose(ps[0:64, 5, 0:P], kc[:], ident[:]).then_inc(S("vc_turned"), 1)

                def dests():
                    out = []
                    for kind in range(3 + H):
                        for half in range(2):
                            cols = slice(512 * half, 512 * half + 512)
                            out.append((cT[:, cols], P) if kind == 0 else (kTs[:, cols], HD) if kind == 1 else
                                       (kTw[:, cols], HD) if kind == 2 else (qT[:, kind - 3, cols], HD))
                    return out

                @b.scalar
                def _(act):
                    for g, (dst, n) in enumerate(dests()):
                        if g % 2 == 0:
                            act.wait_ge(S("turned"), g + 1)
                            A.activation(dst, ps[0:n, g % 4, :], ACT.Copy, scale=0.125 if g >= 6 else 1.0).then_inc(S("even"), 1)
                    act.wait_ge(S("ld2"), 16 * 10)
                    A.activation(ng[:], ng[:], ACT.Exp, scale=-1.0).then_inc(S("gexp"), 1)

                @b.vector
                def _(dve):
                    link = Link(dve, S("v"))
                    link(V.memset(kc[:], 0.0))
                    for g, (dst, n) in enumerate(dests()):
                        if g % 2 == 1:
                            dve.wait_ge(S("turned"), g + 1)
                            V.tensor_scalar(dst, ps[0:n, g % 4, :], 0.125 if g >= 6 else 1.0, None, ALU.mult).then_inc(S("odd"), 1)
                    dve.wait_ge(S("gexp"), 1)
                    link(V.tensor_scalar(ng[:], ng[:], 1.0, None, ALU.add))
                    link(V.reciprocal(ng[:], ng[:]))
                    dve.wait_ge(S("compressed"), 1)
                    link(V.tensor_scalar(kc[:, 0:NC], ps[:, 4, 0:NC], peadd[:, 0:1], None, ALU.add), S("kc"))
                    dve.wait_ge(S("vc_turned"), 1)
                    link(V.tensor_copy(vc[:], ps[0:64, 5, HD:P]))
            kit.clear()

        CW, CC = SEQ, SEQ + 640
        s = sb("p_s", [P, 2, CC + 64])
        pT = sb("p_pT", [P, 2, 14, P])
        stat = sb("p_stat", [P, 2, 4, 3])
        bits = sb("p_bits", [P, HD])
        for t in range(NT):
            nk = (t + 1) * P
            w0 = max(0, t - WT) * P
            nw = nk - w0
            ncm = 8 * t + 7
            blocks = [(1, i * P, P, zk[:, i, 192:256]) for i in range(t + 1)]
            blocks += [(2, CW + i * P, P, zk[:, w0 // P + i, 320:384]) for i in range(nw // P)]
            blocks += [(0, CC, ncm, vc[0:ncm, :])]
            groups = [blocks[i:i + 4] for i in range(0, len(blocks), 4)]
            NGr = len(groups)

            def turn_wait(eng, g):
                eng.wait_ge(S("even" if g % 2 == 0 else "odd"), g // 2 + 1)

            def copy_group(op, h, gi, grp, g, name):
                k = len(grp)
                whole = k if grp[-1][0] != 0 else k - 1
                m = None
                if whole:
                    m = op(pT[:, h % 2, 4 * gi:4 * gi + whole, :].rearrange("p a n -> p (a n)"), ps[:, 4 + g % 2, 0:whole * P])
                if whole < k:
                    n = grp[-1][2]
                    m = op(pT[0:n, h % 2, 4 * gi + whole, :], ps[0:n, 4 + g % 2, whole * P:k * P])
                m.then_inc(S(name), 1)

            with nc.Block(no_gpsimd_drain=True) as b:
                @b.tensor
                def _(pe):
                    def scores(h):
                        if h:
                            pe.wait_ge(S("biased"), h)
                        q = qT[:, h, t * P:t * P + P]
                        for n0 in range(0, nk, 512):
                            n = min(512, nk - n0)
                            nc.tensor.matmul(ps[:, n0 // 512, 0:n], q, kTs[:, n0:n0 + n], start=True, stop=True)
                        n = min(512, nw)
                        nc.tensor.matmul(ps[:, 2, 0:n], q, kTw[:, w0:w0 + n], start=True, stop=True)
                        if nw > 512:
                            nc.tensor.matmul(ps[:, 3, 0:P], q, kTw[:, w0 + 512:w0 + nw], start=True, stop=True)
                        nc.tensor.matmul(ps[:, 3, P:P + ncm], q, kc[0:HD, 0:ncm], start=True, stop=True).then_inc(S("scored"), 1)

                    scores(0)
                    for h in range(H):
                        if h + 1 < H:
                            scores(h + 1)
                        pe.wait_ge(S("exped"), h + 1)
                        for gi, grp in enumerate(groups):
                            g = h * NGr + gi
                            if g >= 2:
                                turn_wait(pe, g - 2)
                            for i, (br, col, n, v) in enumerate(grp):
                                m = nc.tensor.transpose(ps[0:n, 4 + g % 2, i * P:i * P + P], s[:, h % 2, col:col + n], ident[:])
                            m.then_inc(S("turned"), 1)
                        for g in (h * NGr + NGr - 2, h * NGr + NGr - 1):
                            if g >= 0:
                                turn_wait(pe, g)
                        if h >= 2:
                            pe.wait_ge(S("combined"), h - 1)
                        first = set()
                        for bi, (br, col, n, v) in enumerate(blocks):
                            lastb = bi + 1 == len(blocks) or blocks[bi + 1][0] != br
                            m = nc.tensor.matmul(ps[:, 6 + h % 2, br * HD:br * HD + HD], pT[0:n, h % 2, bi, :], v,
                                                 start=br not in first, stop=lastb)
                            first.add(br)
                        m.then_inc(S("pv"), 1)

                @b.vector
                def _(dve):
                    link = Link(dve, S("v"))

                    def biases(h):
                        dve.wait_ge(S("scored"), h + 1)
                        if h >= 2:
                            dve.wait_ge(S("turned"), (h - 1) * NGr)
                        sp_, hp = s[:, h % 2], h % 2
                        off = SEQ - nk
                        for n0 in range(0, nk, 512):
                            n = min(512, nk - n0)
                            link(V.tensor_tensor(sp_[:, n0:n0 + n], ps[:, n0 // 512, 0:n], T[:, h, off + n0:off + n0 + n], ALU.add))
                        wo = WIN + P - nw
                        n = min(512, nw)
                        link(V.tensor_tensor(sp_[:, CW:CW + n], ps[:, 2, 0:n], TW[:, h, wo:wo + n], ALU.add))
                        if nw > 512:
                            link(V.tensor_tensor(sp_[:, CW + 512:CW + nw], ps[:, 3, 0:P], TW[:, h, 512:512 + P], ALU.add))
                        co = 927 - P * t
                        link(V.tensor_tensor(sp_[:, CC:CC + ncm], ps[:, 3, P:P + ncm], T[:, h, co:co + 16 * (ncm - 1) + 1:16], ALU.add), S("biased"))
                        for br, (a, n) in enumerate(((CC, ncm), (0, nk), (CW, nw))):
                            link(V.tensor_reduce(stat[:, hp, 0, br:br + 1], sp_[:, a:a + n], AX.X, ALU.max, negate=True), S("maxed") if br == 2 else None)

                    def copies(h):
                        if h >= 2:
                            dve.wait_ge(S("pv"), h - 1)
                        for gi, grp in enumerate(groups):
                            g = h * NGr + gi
                            if g % 2 == 1:
                                dve.wait_ge(S("turned"), g + 1)
                                copy_group(nc.vector.tensor_copy, h, gi, grp, g, "odd")

                    def combine(h):
                        hp = h % 2
                        dve.wait_ge(S("exped"), h + 1)
                        link(V.reciprocal(stat[:, hp, 2, :], stat[:, hp, 1, :]))
                        link(V.tensor_tensor(stat[:, hp, 3, :], stat[:, hp, 2, :], ng[:, t, h, :], ALU.mult))
                        link(V.tensor_tensor(stat[:, hp, 3, 0:1], stat[:, hp, 3, 0:1], valid[:, t:t + 1], ALU.mult))
                        dve.wait_ge(S("pv"), h + 1)
                        yh = y[:, t % 2, h * HD:h * HD + HD]
                        link(V.tensor_scalar(yh, ps[:, 6 + hp, 0:HD], stat[:, hp, 3, 0:1], None, ALU.mult))
                        link(V.scalar_tensor_tensor(yh, ps[:, 6 + hp, HD:2 * HD], stat[:, hp, 3, 1:2], yh, ALU.mult, ALU.add))
                        link(V.scalar_tensor_tensor(yh, ps[:, 6 + hp, 2 * HD:3 * HD], stat[:, hp, 3, 2:3], yh, ALU.mult, ALU.add), S("combined"))

                    biases(0)
                    for h in range(H):
                        if h + 1 < H:
                            biases(h + 1)
                        copies(h)
                        combine(h)

                @b.scalar
                def _(act):
                    def exps(h):
                        act.wait_ge(S("maxed"), h + 1)
                        hp = h % 2
                        if h >= 2:
                            act.wait_ge(S("combined"), h - 1)
                        for br, (a, n) in enumerate(((CC, ncm), (0, nk), (CW, nw))):
                            m = A.activation(s[:, hp, a:a + n], s[:, hp, a:a + n], ACT.Exp, bias=stat[:, hp, 0, br:br + 1],
                                             accum_out=stat[:, hp, 1, br:br + 1])
                        m.then_inc(S("exped"), 1)

                    exps(0)
                    for h in range(H):
                        if h + 1 < H:
                            exps(h + 1)
                        if h >= 2:
                            act.wait_ge(S("pv"), h - 1)
                        for gi, grp in enumerate(groups):
                            g = h * NGr + gi
                            if g % 2 == 0:
                                act.wait_ge(S("turned"), g + 1)
                                copy_group(lambda o_, i_: A.activation(o_, i_, ACT.Copy), h, gi, grp, g, "even")

                @b.sync
                def _(sp):
                    sp.wait_ge(S("combined"), H)
                    st = Loads(sp, S("st"))
                    st(y_mix[t * P:t * P + P, 768:1024], y[:, t % 2, :])
                    st.all_in()
            kit.clear()


def nsa(kit, env, io, l):
    nc = kit.nc
    with ExitStack() as c:
        wb = c.enter_context(nc.sbuf_tensor("c_wb", [P, 32, P], F32))
        peadd = c.enter_context(nc.sbuf_tensor("c_peadd", [P, 1], F32))
        compress_weights(kit, env, io, l, wb, peadd, c)
        nsa_prompt(kit, env, io, l, wb, peadd)
        if NSA_SAMPLE:
            nsa_sample(kit, env, io, l, wb, peadd)


NSA_SAMPLE = True


SL, SCM, SWN, SNW = 0, PAST, PAST + 256, PAST + 256 + WIN
NDEC = SNW + 8


def nsa_sample(kit, env, io, l, wb, peadd):
    nc, S, ps, ident = kit.nc, kit.sem, env["ps"], env["ident"]
    z, y_mix = env["z"], env["y_mix"]
    V, A = nc.vector, nc.scalar
    R = H * NB
    s0 = PADROWS + SEQ
    G4 = 4
    NCH = PAGES // G4
    with ExitStack() as c:
        def sb(name, shape, dt=F32):
            return c.enter_context(nc.sbuf_tensor(name, shape, dt))
        q = sb("e_q", [R, HD])
        qT = sb("e_qT", [HD, R])
        qpad = sb("e_qpad", [HD, NB, R])
        qb = sb("e_qb", [HD, 2, R])
        kvn = sb("e_kvn", [R, 6, HD])
        ng = sb("e_ng", [R, 3])
        same = sb("e_same", [R, R])
        own = sb("e_own", [R, NB])
        new = sb("e_new", [R, 16])
        sall = sb("e_sall", [R, PAST + 4])
        scm = sb("e_scm", [R, 256])
        ptab = sb("e_ptab", [1, NB * PAGES], I32)
        t64 = sb("e_t64", [R, HD])
        st = sb("e_st", [R, 16])
        ob = sb("e_ob", [R, NB, HD])
        o = sb("e_o", [R, 3, HD])
        y = sb("e_y", [R, HD])

        with ExitStack() as c2:
            def sb2(name, shape):
                return c2.enter_context(nc.sbuf_tensor(name, shape, F32))
            win = sb2("e_win", [P, NB, WIN // P, P])
            kTw = sb2("e_kTw", [HD, NB, WIN])
            swn = sb2("e_swn", [R, WIN + 1])
            pTw = sb2("e_pTw", [P, WIN // P, R])
            oneh = sb2("e_oneh", [33, NDEC])
            rel = sb2("e_rel", [33, H])
            relq = sb2("e_relq", [33, H, NB])
            with nc.Block() as b:
                @b.sync
                def _(sp):
                    ld = Loads(sp, S("ld"))
                    sample_heads(ld, io, z, q, NQ, 1)
                    for h in range(H):
                        hb = slice(h * NB, h * NB + NB)
                        ld(kvn[hb].rearrange("p a n -> p (a n)"), z[s0:s0 + NB, NKV:NKV + 384])
                        ld(ng[hb], z[s0:s0 + NB, NG + 3 * h:NG + 3 * h + 3])
                    ld(rel[0:32, :], io["rel_bias"])
                    ld(oneh[:], io["c_onehot_dec"])
                    ld(same[:], io["c_same"])
                    ld(own[:], io["c_own"])
                    ld(ptab[:], io["page_table"].rearrange("b n -> (b n)").rearrange("(a n) -> a n", a=1))
                    ld2 = Loads(sp, S("win_in"))
                    for bb in range(NB):
                        ld2(win[:, bb], io["cache_swa_kv"][ds(l, 1), bb].rearrange("a (t p) r d -> p (a t) (r d)", p=P))
                    ld.all_in()
                    ld2.all_in()

                @b.vector
                def _(dve):
                    link = Link(dve, S("v"))
                    link(V.memset(qpad[:], 0.0))
                    link(V.memset(relq[:], 1.0))
                    dve.wait_ge(S("ld"), 16 * 17)
                    link(V.tensor_scalar(q[:], q[:], 0.125, None, ALU.mult), S("q_ready"))
                    link(V.tensor_copy(relq[0:32], bc(rel[0:32, :], H, [32, H, NB])), S("rel_ready"))
                    dve.wait_ge(S("q_turned"), 1)
                    link(V.tensor_copy(qT[:], ps[0:HD, 0, 0:R]))
                    for bb in range(NB):
                        link(V.tensor_copy(qpad[:, bb, bb::NB], qT[:, bb::NB]), S("qpad") if bb == NB - 1 else None)
                    for bb in range(NB):
                        dve.wait_ge(S("kw_turned"), bb + 1)
                        link(V.tensor_copy(kTw[:, bb, :], ps[0:HD, 1 + bb % 2, :]), S("kw_ready"))
                    dve.wait_ge(S("biases"), 1)
                    link(V.tensor_copy(scm[:], ps[0:R, 4, 0:256]))
                    link(V.tensor_copy(swn[:, 0:WIN], ps[0:R, 5, :]))
                    link(V.tensor_copy(new[:, 0:1], ps[0:R, 6, 0:1]), S("bias_read"))
                    for ch in range(NCH):
                        dve.wait_ge(S("slc_bias"), ch + 1)
                        link(V.tensor_copy(sall[:, ch * 512:ch * 512 + 512], ps[0:R, 4 + ch % 2, :]), S("bias_read"))
                    for j, r in enumerate((2, 4)):
                        link(V.tensor_tensor_reduce(t64[:], q[:], kvn[:, r, :], 1.0, 0.0, ALU.mult, ALU.add, new[:, 1 + j:2 + j]))
                        link(V.tensor_tensor(new[:, 1 + j:2 + j], new[:, 1 + j:2 + j], new[:, 0:1], ALU.add))
                    link(V.tensor_copy(sall[:, PAST:PAST + 1], new[:, 1:2]))
                    link(V.tensor_copy(swn[:, WIN:WIN + 1], new[:, 2:3]))
                    dve.wait_ge(S("gexp"), 1)
                    link(V.tensor_scalar(ng[:], ng[:], 1.0, None, ALU.add))
                    link(V.reciprocal(ng[:], ng[:]))
                    dve.wait_ge(S("w_scored"), 1)
                    link(V.tensor_tensor(swn[:, 0:WIN], swn[:, 0:WIN], ps[0:R, 7, :], ALU.add))
                    link(V.tensor_reduce(st[:, 0:1], swn[:], AX.X, ALU.max, negate=True), S("w_max"))
                    dve.wait_ge(S("pw_turned"), 1)
                    link(V.tensor_copy(pTw[:].rearrange("p a n -> p (a n)"), ps[:, 0, 0:4 * R]), S("pw_ready"))
                    dve.wait_ge(S("w_pv"), 1)
                    link(V.tensor_tensor(ob[:], ps[0:R, 1, :].rearrange("p (b d) -> p b d", b=NB), bc(own[:], NB, [R, NB, HD]), ALU.mult))
                    link(V.tensor_reduce(o[:, 2, :], ob[:].rearrange("p b d -> p d b"), AX.X, ALU.add))
                    link(V.scalar_tensor_tensor(o[:, 2, :], kvn[:, 5, :], swn[:, WIN:WIN + 1], o[:, 2, :], ALU.mult, ALU.add))
                    link(V.reciprocal(st[:, 8:9], st[:, 1:2]))
                    link(V.tensor_scalar(o[:, 2, :], o[:, 2, :], st[:, 8:9], ng[:, 2:3], ALU.mult, ALU.mult))

                @b.scalar
                def _(act):
                    act.wait_ge(S("ld"), 16 * 17)
                    A.activation(ng[:], ng[:], ACT.Exp, scale=-1.0).then_inc(S("gexp"), 1)
                    act.wait_ge(S("w_max"), 1)
                    A.activation(swn[:], swn[:], ACT.Exp, bias=st[:, 0:1], accum_out=st[:, 1:2]).then_inc(S("w_exp"), 1)

                @b.tensor
                def _(pe):
                    pe.wait_ge(S("q_ready"), 1)
                    nc.tensor.transpose(ps[0:HD, 0, 0:R], q[:], ident[0:R, 0:R]).then_inc(S("q_turned"), 1)
                    pe.wait_ge(S("win_in"), 16 * NB)
                    for bb in range(NB):
                        if bb >= 2:
                            pe.wait_ge(S("kw_ready"), bb - 1)
                        for i in range(4):
                            m = nc.tensor.transpose(ps[0:HD, 1 + bb % 2, i * P:i * P + P], win[:, bb, i, 0:HD], ident[:])
                        m.then_inc(S("kw_turned"), 1)
                    pe.wait_ge(S("rel_ready"), 1)
                    rq = relq[:].rearrange("p h b -> p (h b)")
                    nc.tensor.matmul(ps[0:R, 4, 0:256], rq, oneh[:, SCM:SCM + 256], start=True, stop=True)
                    nc.tensor.matmul(ps[0:R, 5, :], rq, oneh[:, SWN:SWN + WIN], start=True, stop=True)
                    nc.tensor.matmul(ps[0:R, 6, 0:8], rq, oneh[:, SNW:SNW + 8], start=True, stop=True).then_inc(S("biases"), 1)
                    for ch in range(NCH):
                        pe.wait_ge(S("bias_read"), max(1, ch))
                        nc.tensor.matmul(ps[0:R, 4 + ch % 2, :], rq, oneh[:, ch * 512:ch * 512 + 512], start=True, stop=True).then_inc(S("slc_bias"), 1)
                    pe.wait_ge(S("qpad"), 1)
                    pe.wait_ge(S("kw_ready"), NB)
                    for bb in range(NB):
                        m = nc.tensor.matmul(ps[0:R, 7, :], qpad[:, bb, :], kTw[:, bb, :], start=(bb == 0), stop=(bb == NB - 1))
                    m.then_inc(S("w_scored"), 1)
                    pe.wait_ge(S("w_exp"), 1)
                    for i in range(4):
                        m = nc.tensor.transpose(ps[:, 0, i * R:i * R + R], swn[:, i * P:i * P + P], ident[0:R, 0:R])
                    m.then_inc(S("pw_turned"), 1)
                    pe.wait_ge(S("pw_ready"), 1)
                    for i in range(4):
                        m = nc.tensor.matmul(ps[0:R, 1, :], pTw[:, i, :], win[:, :, i, HD:P], start=(i == 0), stop=(i == 3))
                    m.then_inc(S("w_pv"), 1)
            kit.clear()

        with ExitStack() as c2:
            vall = c2.enter_context(nc.sbuf_tensor("e_vall", [P, NB, PAGES, HD], F32))
            vcm = c2.enter_context(nc.sbuf_tensor("e_vcm", [P, NB, 2, HD], F32))
            with ExitStack() as c3:
                pages = [c3.enter_context(nc.sbuf_tensor(f"e_pg{j}", [P, PAGES, 256], F32)) for j in range(2)]
                pT = c3.enter_context(nc.sbuf_tensor("e_pT", [P, PAST], F32))
                kT = c3.enter_context(nc.sbuf_tensor("e_kT", [HD, 2, 512], F32))
                kvT = c3.enter_context(nc.sbuf_tensor("e_kvT", [P, 256], F32))

                def load_pages(sp, buf, bb, sem):
                    with sp.Fori(0, PAGES) as i:
                        page = sp.value_load(ptab[0:1, ds(bb * PAGES + i, 1)], min_val=0, max_val=NPOOL - 1)
                        sp.dma_start(buf[:, ds(i, 1), :],
                                     io["cache_nsa_kv"][ds(l, 1), ds(page, 1)].rearrange("a g t r d -> t (a g) (r d)")).then_inc(sem, 16)

                with nc.Block() as b:
                    @b.sync
                    def _(sp):
                        load_pages(sp, pages[0], 0, S("ld"))
                        sp.wait_ge(S("ld"), 16 * PAGES)

                    @b.vector
                    def _(dve):
                        V.memset(kvT[:], 0.0).then_inc(S("v"), 1)
                kit.clear()

                with nc.Fori(0, NB // 2) as g:
                    with nc.Block(no_gpsimd_drain=True) as b:
                        @b.sync
                        def _(sp):
                            load_pages(sp, pages[1], g * 2 + 1, S("odd_in"))
                            sp.wait_ge(S("k_turned"), NCH)
                            sp.wait_ge(S("v_kept"), 1)
                            load_pages(sp, pages[0], (g * 2 + 2) % NB, S("next_in"))
                            sp.wait_ge(S("odd_in"), 16 * PAGES)
                            sp.wait_ge(S("next_in"), 16 * PAGES)

                        @b.tensor
                        def _(pe):
                            def score(pe, j, ch):
                                n = NCH * j + ch
                                pe.wait_ge(S("qb"), j + 1)
                                pe.wait_ge(S("kT"), n + 1)
                                if n >= 2:
                                    pe.wait_ge(S("added"), n - 1)
                                nc.tensor.matmul(ps[0:R, 4 + ch % 2, :], qb[:, j, :], kT[:, ch % 2, :], start=True, stop=True).then_inc(S("scored"), 1)

                            for j in range(2):
                                pg = pages[j]
                                if j:
                                    pe.wait_ge(S("odd_in"), 16 * PAGES)
                                for ch in range(NCH):
                                    n = NCH * j + ch
                                    if n >= 2:
                                        pe.wait_ge(S("pT"), n - 1)
                                    for i in range(G4):
                                        m = nc.tensor.transpose(ps[:, ch % 2, i * P:i * P + P], pg[:, ch * G4 + i, 0:P], ident[:])
                                    m.then_inc(S("kv_turned"), 1)
                                    if n >= 2:
                                        pe.wait_ge(S("kT"), n - 1)
                                    for i in range(G4):
                                        m = nc.tensor.transpose(ps[0:HD, 2 + ch % 2, i * P:i * P + P], pg[:, ch * G4 + i, P:P + HD], ident[:])
                                    m.then_inc(S("k_turned"), 1)
                                    if ch:
                                        score(pe, j, ch - 1)
                                score(pe, j, NCH - 1)
                                if j:
                                    pe.wait_ge(S("c_added"), 1)
                                pe.wait_ge(S("pT"), NCH * (j + 1))
                                for k in range(32):
                                    m = nc.tensor.matmul(ps[:, 6, 0:255], wb[:, k, :], pT[:, k:k + 16 * 254 + 1:16],
                                                         start=(k == 0), stop=(k == 31))
                                m.then_inc(S("compressed"), 1)
                                pe.wait_ge(S("kvT"), j + 1)
                                for i in range(2):
                                    m = nc.tensor.transpose(ps[:, 7, i * P:i * P + P], kvT[:, i * P:i * P + P], ident[:])
                                m.then_inc(S("vc_turned"), 1)
                                nc.tensor.matmul(ps[0:R, 6, 0:255], qb[:, j, :], kvT[0:HD, 0:255], start=True, stop=True).then_inc(S("c_scored"), 1)

                        @b.scalar
                        def _(act):
                            for j in range(2):
                                for ch in range(NCH):
                                    n = NCH * j + ch
                                    act.wait_ge(S("kv_turned"), n + 1)
                                    if n == NCH:
                                        act.wait_ge(S("compressed"), 1)
                                    A.activation(pT[:, ch * 512:ch * 512 + 512], ps[:, ch % 2, :], ACT.Copy).then_inc(S("pT"), 1)
                                A.activation(vall[:, ds(2 * g + j, 1)].rearrange("p a n d -> p (a n) d"), pages[j][:, :, 192:256], ACT.Copy).then_inc(S("v_kept"), 1)

                        @b.vector
                        def _(dve):
                            link = Link(dve, S("v"))
                            for j in range(2):
                                link(V.tensor_copy(qb[:, j, :], qpad[:, ds(2 * g + j, 1), :].rearrange("p a n -> p (a n)")), S("qb"))
                                for ch in range(NCH + 1):
                                    n = NCH * j + ch
                                    if ch < NCH:
                                        dve.wait_ge(S("k_turned"), n + 1)
                                        if n >= 2:
                                            dve.wait_ge(S("scored"), n - 1)
                                        link(V.tensor_copy(kT[:, ch % 2, :], ps[0:HD, 2 + ch % 2, :]), S("kT"))
                                    if ch:
                                        dve.wait_ge(S("scored"), n)
                                        sc = sall[:, (ch - 1) * 512:ch * 512]
                                        link(V.tensor_tensor(sc, sc, ps[0:R, 4 + (ch - 1) % 2, :], ALU.add), S("added"))
                                dve.wait_ge(S("compressed"), j + 1)
                                link(V.tensor_scalar(kvT[:, 0:255], ps[:, 6, 0:255], peadd[:, 0:1], None, ALU.add), S("kvT"))
                                dve.wait_ge(S("vc_turned"), j + 1)
                                link(V.tensor_copy(vcm[:, ds(2 * g + j, 1)].rearrange("p a n d -> p (a n) d"),
                                                   ps[:, 7, 0:256].rearrange("p (n d) -> p n d", n=2)[:, :, HD:P]))
                                dve.wait_ge(S("c_scored"), j + 1)
                                link(V.tensor_tensor(scm[:, 0:255], scm[:, 0:255], ps[0:R, 6, 0:255], ALU.add), S("c_added"))
                    kit.clear()

            with ExitStack() as c3:
                def sb3(name, shape):
                    return c3.enter_context(nc.sbuf_tensor(name, shape, F32))
                pcT = sb3("e_pcT", [P, 2, R])
                psT = sb3("e_psT", [P, PAGES, R])
                pwT = None
                imp = sb3("e_imp", [R, 64])
                score_ = sb3("e_score", [R, 72])
                top = sb3("e_top", [R, 16])
                with nc.Block() as b:
                    @b.vector
                    def _(dve):
                        link = Link(dve, S("v"))
                        link(V.tensor_reduce(st[:, 2:3], scm[:], AX.X, ALU.max, negate=True), S("c_max"))
                        dve.wait_ge(S("c_exp"), 1)
                        link(V.reciprocal(st[:, 4:5], st[:, 3:4]))
                        link(V.tensor_scalar(scm[:], scm[:], st[:, 4:5], None, ALU.mult), S("p_c"))
                        link(V.tensor_reduce(imp[:], scm[:].rearrange("p (j n) -> p j n", n=4), AX.X, ALU.add))
                        link(V.tensor_tensor(imp[:, 1:64], imp[:, 1:64], scm[:, 3:252:4], ALU.add), S("imp"))
                        link(V.memset(score_[:], 1.0e30))
                        dve.wait_ge(S("imp_summed"), 1)
                        link(V.tensor_copy(score_[:, 1:63], ps[0:R, 0, 1:63]))
                        link(V.max(top[:, 0:8], score_[:, 0:65]))
                        link(V.match_replace(score_[:, 0:65], top[:, 0:8], score_[:, 0:65], -1.0e30))
                        link(V.max(top[:, 8:16], score_[:, 0:65]))
                        link(V.match_replace(score_[:, 0:65], top[:, 8:16], score_[:, 0:65], -1.0e30))
                        link(V.tensor_scalar(score_[:, 0:65], score_[:, 0:65], -5.0e29, NEG, ALU.is_gt, ALU.mult))
                        s3 = sall[:, 0:PAST].rearrange("p (j n) -> p j n", n=HD)
                        link(V.tensor_tensor(s3, s3, score_[:, 0:64].unsqueeze(2).to_broadcast([R, 64, HD]), ALU.add))
                        link(V.tensor_reduce(st[:, 5:6], sall[:, 0:PAST + 1], AX.X, ALU.max, negate=True), S("s_max"))
                        dve.wait_ge(S("pc_turned"), 1)
                        link(V.tensor_copy(pcT[:].rearrange("p a n -> p (a n)"), ps[:, 1, 0:2 * R]), S("pcT"))
                        for k in range(2):
                            dve.wait_ge(S("ps_turned"), k + 1)
                            link(V.tensor_copy(psT[:, 16 * k:16 * k + 16, :].rearrange("p a n -> p (a n)"), ps[:, 2 + k, :]), S("psT"))

                        def own_part(acc, br):
                            link(V.tensor_tensor(ob[:], acc.rearrange("p (b d) -> p b d", b=NB), bc(own[:], NB, [R, NB, HD]), ALU.mult))
                            link(V.tensor_reduce(o[:, br, :], ob[:].rearrange("p b d -> p d b"), AX.X, ALU.add))

                        dve.wait_ge(S("c_pv"), 1)
                        own_part(ps[0:R, 4, :], 0)
                        dve.wait_ge(S("s_pv"), 1)
                        own_part(ps[0:R, 5, :], 1)
                        link(V.scalar_tensor_tensor(o[:, 1, :], kvn[:, 3, :], sall[:, PAST:PAST + 1], o[:, 1, :], ALU.mult, ALU.add))
                        link(V.reciprocal(st[:, 7:8], st[:, 6:7]))
                        link(V.tensor_tensor(st[:, 7:8], st[:, 7:8], ng[:, 1:2], ALU.mult))
                        link(V.scalar_tensor_tensor(y[:], o[:, 1, :], st[:, 7:8], o[:, 2, :], ALU.mult, ALU.add))
                        link(V.scalar_tensor_tensor(y[:], o[:, 0, :], ng[:, 0:1], y[:], ALU.mult, ALU.add), S("y_ready"))

                    @b.scalar
                    def _(act):
                        act.wait_ge(S("c_max"), 1)
                        A.activation(scm[:], scm[:], ACT.Exp, bias=st[:, 2:3], accum_out=st[:, 3:4]).then_inc(S("c_exp"), 1)
                        act.wait_ge(S("s_max"), 1)
                        A.activation(sall[:, 0:PAST + 1], sall[:, 0:PAST + 1], ACT.Exp, bias=st[:, 5:6], accum_out=st[:, 6:7]).then_inc(S("s_exp"), 1)

                    @b.tensor
                    def _(pe):
                        pe.wait_ge(S("imp"), 1)
                        nc.tensor.matmul(ps[0:R, 0, 0:64], same[:], imp[:], start=True, stop=True).then_inc(S("imp_summed"), 1)
                        for i in range(2):
                            m = nc.tensor.transpose(ps[:, 1, i * R:i * R + R], scm[:, i * P:i * P + P], ident[0:R, 0:R])
                        m.then_inc(S("pc_turned"), 1)
                        pe.wait_ge(S("pcT"), 1)
                        for i in range(2):
                            m = nc.tensor.matmul(ps[0:R, 4, :], pcT[:, i, :], vcm[:, :, i, :], start=(i == 0), stop=(i == 1))
                        m.then_inc(S("c_pv"), 1)
                        pe.wait_ge(S("s_exp"), 1)
                        for k in range(2):
                            for i in range(16):
                                m = nc.tensor.transpose(ps[:, 2 + k, i * R:i * R + R], sall[:, (16 * k + i) * P:(16 * k + i) * P + P], ident[0:R, 0:R])
                            m.then_inc(S("ps_turned"), 1)
                        pe.wait_ge(S("psT"), 2)
                        for i in range(PAGES):
                            m = nc.tensor.matmul(ps[0:R, 5, :], psT[:, i, :], vall[:, :, i, :], start=(i == 0), stop=(i == PAGES - 1))
                        m.then_inc(S("s_pv"), 1)

                    @b.sync
                    def _(sp):
                        sp.wait_ge(S("y_ready"), 1)
                        so = Loads(sp, S("st"))
                        for h in range(H):
                            so(y_mix[SEQ:TOK, 768 + h * HD:768 + h * HD + HD], y[h * NB:h * NB + NB, :])
                        so.all_in()
                kit.clear()


def mixers(kit, env, io, l):
    recurrent_prompt(kit, env, io, l)
    kit.next_stage()
    recurrent_sample(kit, env, io, l)
    kit.next_stage()
    nsa(kit, env, io, l)
    kit.next_stage()


OUTS = [("y_prompt", (1, SEQ, D)), ("y_sample", (NB, 1, D)),
        ("p_nsa", (2, 1, SEQ, 4, HD)), ("p_swa", (2, 1, WIN, 2, HD)), ("p_ret", (2, 1, 4, HD, HD)),
        ("p_C", (2, 1, 4, HD, HD)), ("p_n", (2, 1, 4, HD)), ("p_m", (2, 1, 4)), ("p_gdn", (2, 1, 4, HD, HD)),
        ("p_gconv", (2, 1, 3, 768)), ("p_ffn_conv", (2, 1, 2, DFF)),
        ("s_nsa", (2, NB, 1, 4, HD)), ("s_swa", (2, NB, WIN, 2, HD)), ("s_ret", (2, NB, 4, HD, HD)),
        ("s_C", (2, NB, 4, HD, HD)), ("s_n", (2, NB, 4, HD)), ("s_m", (2, NB, 4)), ("s_gdn", (2, NB, 4, HD, HD)),
        ("s_gconv", (2, NB, 3, 768)), ("s_ffn_conv", (2, NB, 2, DFF))]


def buckets(n):
    f = np.float32
    big = 16 + (np.log(np.maximum(n, 1).astype(f) / f(16)) / f(math.log(64)) * f(16)).astype(np.int32)
    return np.where(n < 16, n, np.minimum(big, 31))


def onehot(dist, ok):
    out = np.zeros((33, len(dist)), np.float32)
    out[buckets(np.maximum(dist, 0)), np.arange(len(dist))] = ok
    out[32] = np.where(ok, 0.0, NEG)
    return out


def constants():
    f = np.float32
    i = np.arange(P)
    lo = i[:, None] >= i[None, :]
    pos = np.concatenate([np.arange(SEQ), [PAST]]).astype(f)
    inv = f(10000.0) ** (-np.linspace(0.0, 1.0, HD // 2, dtype=f))
    ang = (pos[:, None] * inv[None, :]).astype(f).astype(np.float64)
    log_g = np.log(1.0 - 2.0 ** (-5.0 - np.arange(H)))
    dist = (i[None, :] - i[:, None])
    ret = np.where(dist[:, None, :] >= 0, np.exp(log_g[None, :, None] * np.maximum(dist, 0)[:, None, :]), 0.0) * 0.125
    xi = np.stack([np.exp(log_g[None] * (i[:, None] + 1.0)), 0.125 * np.exp(log_g[None] * (P - 1.0 - i[:, None])),
                   np.broadcast_to(np.exp(log_g * P), (P, H))], 1)
    lev = []
    for s in range(7):
        w = 1 << s
        lev.append((i[:, None] // (2 * w) == i[None, :] // (2 * w)) & (i[:, None] // w % 2 == 1) & (i[None, :] // w % 2 == 0))
    lev = np.stack(lev, 1)
    last = np.zeros((P, P), f)
    last[P - 1] = 1.0
    d1, d2 = 1023 - np.arange(TL), 639 - np.arange(WL)
    return {
        "c_ident": np.eye(P, dtype=f),
        "c_rope": np.concatenate([np.cos(ang), np.sin(ang)], 1).astype(f),
        "c_retD": ret.astype(f).reshape(P, H * P),
        "c_xi": xi.astype(f).reshape(P, 3 * H),
        "c_dec": np.repeat(1.0 - 2.0 ** (-5.0 - np.arange(H)), NB).astype(f)[:, None],
        "c_onehot": np.concatenate([onehot(d1, d1 >= 0), onehot(d2, (d2 >= 0) & (d2 < WIN))], 1),
        "c_onehot_dec": np.concatenate([onehot(x, ok) for x, ok in (
            (PAST - np.arange(PAST), np.arange(PAST) >= 0),
            (PAST - (16 * np.arange(256) + 31), np.arange(256) < 255),
            (WIN - np.arange(WIN), np.arange(WIN) > 0),
            (np.zeros(8, int), np.arange(8) < 8))], 1),
        "c_same": (np.arange(H * NB)[:, None] % NB == np.arange(H * NB)[None] % NB).astype(f),
        "c_own": (np.arange(H * NB)[:, None] % NB == np.arange(NB)[None]).astype(f),
        "c_qkscale": np.broadcast_to(np.repeat(np.array([0.0625, 0.5], f), H), (P, 8)).copy(),
        "c_valid": (np.arange(SEQ) >= 31).astype(f).reshape(NT, P).T.copy(),
        "c_upper": lo.T.astype(f),
        "c_mask": np.where(lo, 0.0, NEG).astype(f),
        "c_maskT": np.where(lo.T, 0.0, NEG).astype(f),
        "c_last": last,
        "c_lev": lev.astype(f).reshape(P, 7 * P),
        "c_levT": lev.transpose(2, 1, 0).astype(f).reshape(P, 7 * P),
    }


def kernel(**inputs):
    import concourse.bacc as bacc
    from concourse.bass_utils import run_bass_kernel_spmd

    nc = bacc.Bacc("TRN2", target_bir_lowering=False, num_devices=1)
    arrays, io = {}, {}
    for name, a in {**inputs, **constants()}.items():
        arrays[name] = np.ascontiguousarray(a)
        io[name] = nc.dram_tensor(name, a.shape, mybir.dt.from_np(np.asarray(a).dtype), kind="ExternalInput").ap()
    for name, shape in OUTS:
        io[name] = nc.dram_tensor(name, shape, F32, kind="ExternalOutput").ap()
    program(nc, io)
    r = run_bass_kernel_spmd(nc, [arrays], core_ids=[0])
    return tuple(r.results[0][name] for name, _ in OUTS)
```

```python
import math
from contextlib import ExitStack

import numpy as np

import concourse.bass as bass
from concourse import mybir

F32 = mybir.dt.float32
F32R = mybir.dt.float32r
I32 = mybir.dt.int32
ALU = mybir.AluOpType
ACT = mybir.ActivationFunctionType
AX = mybir.AxisListType
ds = bass.ds

P = 128
D = 1024
KD = D // P
SEQ = 1024
NB = 8
DEPTH = 2
NT = SEQ // P
TT = NT + 1
TOK = SEQ + NB
ROWS = TT * P
XROWS = ROWS + 3 * P
PADROWS = 8
DIN = 3740
ZC = 374
NZ = DIN // ZC
DFF = 2816
NF = DFF // P
SEG = TOK // 3
DQ = 256
HD = 64
H = 4
NEG = -1.0e30
EPS = 1e-6
PAST = 4096
PAGES = 32
NPOOL = 320
WIN = 512
RQ, RK, RV, RG = 0, 256, 512, 768
MQ, MK, MV, MI, MF, MO = 1024, 1280, 1536, 1792, 1796, 1800
GX, GA, GB, GG = 2056, 2824, 2828, 2832
NQ, NKV, NG = 3088, 3344, 3728


class Link:

    def __init__(self, eng, own):
        self.eng, self.own, self.n = eng, own, {}

    def __call__(self, ins, signal=None):
        s = self.own if signal is None else signal
        self.n[s.num] = self.n.get(s.num, 0) + 1
        ins.then_inc(s, 1)
        self.eng.wait_ge(s, self.n[s.num])


class Loads:

    def __init__(self, eng, sem):
        self.eng, self.sem, self.n = eng, sem, 0

    def __call__(self, out, in_, slow=False):
        self.eng.dma_start(out, in_, allow_slow_non_contiguous=slow).then_inc(self.sem, 16)
        self.n += 16

    def all_in(self):
        self.eng.wait_ge(self.sem, self.n)


class Kit:

    def __init__(self, nc, ctx):
        self.nc, self.ctx = nc, ctx
        self.sems, self.stage_ctx, self.nums = {}, ExitStack(), set()

    def sem(self, name):
        if name not in self.sems:
            self.sems[name] = self.stage_ctx.enter_context(self.nc.semaphore(name))
            self.nums.add(self.sems[name].num)
        return self.sems[name]

    def next_stage(self):
        self.stage_ctx.close()
        self.sems, self.stage_ctx = {}, ExitStack()

    def clear(self, kept=None):
        if kept is not None:
            self.nc.gpsimd.sem_clear(kept)
        self.nc.gpsimd.sem_clear(range(min(self.nums), max(self.nums) + 1))
        self.nc.all_engine_barrier(sem_only=True)


def program(nc, io):
    with ExitStack() as ctx:
        kit = Kit(nc, ctx)
        S = kit.sem

        def sb(c, name, shape, dt=F32):
            return c.enter_context(nc.sbuf_tensor(name, shape, dt))

        ps = ctx.enter_context(nc.psum_tensor("ps", [P, 8, 512], F32))
        ident = sb(ctx, "ident", [P, P])
        mhalf = sb(ctx, "mhalf", [P, 16])
        zrow = sb(ctx, "zrow", [P, 1024])
        x_cur = nc.dram_tensor("x_cur", (XROWS, D), F32, kind="Internal").ap()
        z = nc.dram_tensor("z", (PADROWS + ROWS, DIN), F32, kind="Internal").ap()
        y_mix = nc.dram_tensor("y_mix", (XROWS, D), F32, kind="Internal").ap()
        wdist = nc.dram_tensor("wdist", (H, P, TWC), F32, kind="Internal").ap()
        f_all = nc.dram_tensor("f_all", (NF, P, TOK), F32, kind="Internal").ap()
        kept = ctx.enter_context(nc.semaphore("kept"))
        env = dict(locals())

        with nc.Block() as b:
            @b.vector
            def _(dve):
                link = Link(dve, S("v"))
                link(nc.vector.memset(zrow[:], 0.0))
                link(nc.vector.memset(mhalf[:], -0.5), S("zeroed"))

            @b.sync
            def _(sp):
                ld = Loads(sp, S("ld"))
                ld(ident[:], io["c_ident"])
                ld(x_cur[0:SEQ, :], io["x_prompt"][0])
                ld(x_cur[SEQ:TOK, :], io["x_sample"][:, 0, :])
                sp.wait_ge(S("zeroed"), 1)
                for r in range(TOK, XROWS, P):
                    ld(x_cur[r:min(r + P, XROWS), :], zrow[0:min(P, XROWS - r), :])
                    ld(y_mix[r:min(r + P, XROWS), :], zrow[0:min(P, XROWS - r), :])
                for c in range(0, DIN, 1024):
                    n = min(1024, DIN - c)
                    ld(z[0:PADROWS, c:c + n], zrow[0:PADROWS, 0:n])
                ld.all_in()
        kit.clear()
        bias_tables(kit, env, io)
        kit.next_stage()

        with nc.Fori(0, DEPTH) as l:
            with ExitStack() as c:
                h_hi = sb(c, "h_hi", [P, KD, ROWS], F32R)
                h_lo = sb(c, "h_lo", [P, KD, ROWS], F32R)
                norm_to_hT(kit, env, io, l, "norm_pre_mix", h_hi, h_lo)
                kit.next_stage()
                project_in(kit, env, io, l, h_hi, h_lo)
            kit.next_stage()
            if io.get("mixers", True):
                mixers(kit, env, io, l)
            with ExitStack() as c:
                h_hi = sb(c, "h2_hi", [P, KD, ROWS], F32R)
                h_lo = sb(c, "h2_lo", [P, KD, ROWS], F32R)
                project_out(kit, env, io, l, h_hi, h_lo)
                kit.next_stage()
                ffn_up(kit, env, io, l, h_hi, h_lo)
                kit.next_stage()
            ffn_down(kit, env, io, l)
            kit.next_stage()

        with nc.Block() as b:
            @b.sync
            def _(sp):
                st = Loads(sp, S("st"))
                st(io["y_prompt"][0], x_cur[0:SEQ, :])
                st(io["y_sample"][:, 0, :], x_cur[SEQ:TOK, :])
                st.all_in()


def rows(t, n=P):
    return ds(t * P, n)


def norm_to_hT(kit, env, io, l, gain, h_hi, h_lo):
    nc, S, ps, ident, mhalf, x_cur = kit.nc, kit.sem, env["ps"], env["ident"], env["mhalf"], env["x_cur"]
    G = 3
    with ExitStack() as c:
        xt = c.enter_context(nc.sbuf_tensor("n_x", [P, 2, G, D], F32))
        xn = c.enter_context(nc.sbuf_tensor("n_xn", [P, G, D], F32))
        h = c.enter_context(nc.sbuf_tensor("n_h", [P, G, KD, P], F32))
        junk = c.enter_context(nc.sbuf_tensor("n_junk", [P, D], F32))
        gT = c.enter_context(nc.sbuf_tensor("n_g", [P, KD], F32))
        ss = c.enter_context(nc.sbuf_tensor("n_ss", [P, 3, G], F32))
        with nc.Block() as b:
            @b.sync
            def _(sp):
                ld = Loads(sp, S("ld"))
                ld(xt[:, 0], x_cur[0:G * P, :].rearrange("(g p) n -> p g n", p=P))
                ld(gT[:], io[gain][ds(l, 1), :].rearrange("a (k p) -> p (a k)", p=P), slow=True)
                ld.all_in()
        kit.clear()
        with nc.Fori(0, TT // G) as t:
            def x_in(g):
                return xt[:, ds(t % 2, 1), g, :].rearrange("p a n -> p (a n)")

            with nc.Block(no_gpsimd_drain=True) as b:
                @b.sync
                def _(sp):
                    ld = Loads(sp, S("next_x"))
                    ld(xt[:, ds((t + 1) % 2, 1), :, :].rearrange("p a g n -> p (a g) n"),
                       x_cur[ds((t + 1) * G * P, G * P), :].rearrange("(g p) n -> p g n", p=P))
                    ld.all_in()

                @b.scalar
                def _(act):
                    for g in range(G):
                        if g:
                            act.wait_ge(S("summed"), g)
                        nc.scalar.activation(junk[:], x_in(g), ACT.Square,
                                             scale=1.0 / 32.0, accum_out=ss[:, 0, g:g + 1]).then_inc(S("summed"), 1)
                    for g in range(G):
                        act.wait_ge(S("h_ready"), 2 * g + 2)
                        nc.scalar.activation(h_hi[:, :, ds(t * G * P + g * P, P)], h[:, g], ACT.Copy).then_inc(S("hi_ready"), 1)

                @b.gpsimd
                def _(pool):
                    pool.wait_ge(S("eps_added"), 1)
                    nc.gpsimd.tensor_tensor(ss[:, 2, :], ss[:, 1, :], mhalf[:, 0:G], ALU.pow).then_inc(S("r_ready"), 1)

                @b.vector
                def _(dve):
                    def low(g):
                        dve.wait_ge(S("hi_ready"), g + 1)
                        nc.vector.tensor_tensor(h_lo[:, :, ds(t * G * P + g * P, P)], h[:, g],
                                                h_hi[:, :, ds(t * G * P + g * P, P)].bitcast(F32),
                                                ALU.subtract).then_inc(S("lo_ready"), 1)
                    dve.wait_ge(S("summed"), G)
                    nc.vector.tensor_scalar(ss[:, 1, :], ss[:, 0, :], EPS, None, ALU.add).then_inc(S("eps_added"), 1)
                    dve.wait_ge(S("r_ready"), 1)
                    for g in range(G):
                        nc.vector.tensor_scalar(xn[:, g], x_in(g), ss[:, 2, g:g + 1], None, ALU.mult).then_inc(S("normed"), 1)
                    for g in range(G):
                        for half in range(2):
                            dve.wait_ge(S("turned"), 2 * g + half + 1)
                            nc.vector.tensor_tensor(h[:, g, 4 * half:4 * half + 4, :],
                                                    ps[:, 2 * g + half, :].rearrange("p (k n) -> p k n", k=4),
                                                    gT[:, 4 * half:4 * half + 4].unsqueeze(2).to_broadcast([P, 4, P]),
                                                    ALU.mult).then_inc(S("h_ready"), 1)
                        if g:
                            low(g - 1)
                    low(G - 1)

                @b.tensor
                def _(pe):
                    for g in range(G):
                        pe.wait_ge(S("normed"), g + 1)
                        for k in range(KD):
                            m = nc.tensor.transpose(ps[:, 2 * g + k // 4, (k % 4) * P:(k % 4) * P + P],
                                                    xn[:, g, k * P:k * P + P], ident[:])
                            if k % 4 == 3:
                                m.then_inc(S("turned"), 1)
            kit.clear()


def project_in(kit, env, io, l, h_hi, h_lo):
    nc, S, ps, z = kit.nc, kit.sem, env["ps"], env["z"]

    def chunk(i):
        return io["w_in"][ds(l, 1), :, ds(i * ZC, ZC)].rearrange("a (k p) n -> p (a k) n", p=P)

    with ExitStack() as c:
        raw = c.enter_context(nc.sbuf_tensor("zi_raw", [P, KD, ZC], F32))
        w_hi = c.enter_context(nc.sbuf_tensor("zi_whi", [P, 2, KD, ZC], F32R))
        w_lo = c.enter_context(nc.sbuf_tensor("zi_wlo", [P, 2, KD, ZC], F32R))
        zo = c.enter_context(nc.sbuf_tensor("zi_z", [P, 2, TT, ZC], F32))
        z_stored = env["kept"]
        with nc.Block() as b:
            @b.sync
            def _(sp):
                sp.dma_start(raw[:], io["w_in"][ds(l, 1), :, 0:ZC].rearrange("a (k p) n -> p (a k) n", p=P)).then_inc(z_stored, 16)
                sp.wait_ge(z_stored, 16)

            @b.scalar
            def _(act):
                act.wait_ge(z_stored, 16)
                nc.scalar.activation(w_hi[:, 0], raw[:], ACT.Copy).then_inc(S("hi_ready"), 1)

            @b.vector
            def _(dve):
                dve.wait_ge(S("hi_ready"), 1)
                nc.vector.tensor_tensor(w_lo[:, 0], raw[:], w_hi[:, 0].bitcast(F32), ALU.subtract).then_inc(S("lo_ready"), 1)
        kit.clear()
        with nc.Fori(0, NZ) as i:
            def buf(w, step, k):
                return w[:, ds((i + step) % 2, 1), k, :].rearrange("p a n -> p (a n)")

            def z_tile(t):
                return zo[:, ds(i % 2, 1), t, :].rearrange("p a n -> p (a n)")

            with nc.Block(no_gpsimd_drain=True) as b:
                @b.sync
                def _(sp):
                    ld = Loads(sp, S("next_w"))
                    ld(raw[:], chunk((i + 1) % NZ))
                    for t in range(TT):
                        sp.wait_ge(S("z_even") if t % 2 == 0 else S("z_odd"), t // 2 + 1)
                        if t == 0:
                            sp.wait_ge(z_stored, 16 + i * 16 * TT)
                        sp.dma_start(z[PADROWS + t * P:PADROWS + t * P + P, ds(i * ZC, ZC)], z_tile(t)).then_inc(z_stored, 16)
                    ld.all_in()

                @b.tensor
                def _(pe):
                    for t in range(TT):
                        if t == 8:
                            pe.wait_ge(S("z_even"), 1)
                        for k in range(KD):
                            rows_hi, rows_lo = h_hi[:, k, t * P:t * P + P], h_lo[:, k, t * P:t * P + P]
                            nc.tensor.matmul(ps[:, t % 8, 0:ZC], rows_hi, buf(w_hi, 0, k), start=(k == 0), stop=False)
                            nc.tensor.matmul(ps[:, t % 8, 0:ZC], rows_hi, buf(w_lo, 0, k), start=False, stop=False)
                            m = nc.tensor.matmul(ps[:, t % 8, 0:ZC], rows_lo, buf(w_hi, 0, k),
                                                 start=False, stop=(k == KD - 1))
                        m.then_inc(S("z_summed"), 1)

                @b.scalar
                def _(act):
                    for t in range(0, TT, 2):
                        act.wait_ge(S("z_summed"), t + 1)
                        nc.scalar.activation(z_tile(t), ps[:, t % 8, 0:ZC], ACT.Copy).then_inc(S("z_even"), 1)
                        if t < 8:
                            if t == 0:
                                act.wait_ge(S("next_w"), 16)
                            for k in (t, t + 1):
                                nc.scalar.activation(buf(w_hi, 1, k), raw[:, k], ACT.Copy).then_inc(S("hi_ready"), 1)

                @b.vector
                def _(dve):
                    for t in range(1, TT, 2):
                        dve.wait_ge(S("z_summed"), t + 1)
                        nc.vector.tensor_copy(z_tile(t), ps[:, t % 8, 0:ZC]).then_inc(S("z_odd"), 1)
                        for k in (t - 1, t):
                            dve.wait_ge(S("hi_ready"), k + 1)
                            nc.vector.tensor_tensor(buf(w_lo, 1, k), raw[:, k], buf(w_hi, 1, k).bitcast(F32),
                                                    ALU.subtract).then_inc(S("lo_ready"), 1)
            kit.clear()
        with nc.Block() as b:
            @b.sync
            def _(sp):
                sp.wait_ge(z_stored, 16 + NZ * TT * 16)
        kit.clear(kept=z_stored)


def project_out(kit, env, io, l, h_hi, h_lo):
    nc, S, ps, ident, mhalf = kit.nc, kit.sem, env["ps"], env["ident"], env["mhalf"]
    x_cur, y_mix = env["x_cur"], env["y_mix"]
    G = 3
    TURN = (6, 4, 6)
    with ExitStack() as c:
        def sb(name, shape):
            return c.enter_context(nc.sbuf_tensor(name, shape, F32))
        w = sb("po_w", [P, KD, D])
        yt = sb("po_y", [P, G, D])
        xt = sb("po_x", [P, G, D])
        yT = sb("po_yT", [P, G, KD, P])
        xn = sb("po_xn", [P, G, D])
        gb = sb("po_gb", [P, D])
        gT = sb("po_gT", [P, KD])
        junk = sb("po_j", [P, D])
        ss = sb("po_ss", [P, 6, G])
        with nc.Block() as b:
            @b.sync
            def _(sp):
                ld = Loads(sp, S("ld"))
                ld(yt[:], y_mix[0:G * P, :].rearrange("(g p) n -> p g n", p=P))
                ld(w[:], io["w_out"][ds(l, 1), :, :].rearrange("a (k p) n -> p (a k) n", p=P))
                ld(gb[:], io["norm_post_mix"][ds(l, 1), :].rearrange("a n -> (a n)").partition_broadcast(P))
                ld(gT[:], io["norm_pre_ffn"][ds(l, 1), :].rearrange("a (k p) -> p (a k)", p=P), slow=True)
                ld.all_in()
        kit.clear()
        with nc.Fori(0, TT // G) as t:
            def rows_of(g):
                return ds(t * G * P + g * P, P)

            with nc.Block(no_gpsimd_drain=True) as b:
                @b.sync
                def _(sp):
                    ld = Loads(sp, S("x_loaded"))
                    ld(xt[:], x_cur[ds(t * G * P, G * P), :].rearrange("(g p) n -> p g n", p=P))
                    nxt = Loads(sp, S("next_y"))
                    sp.wait_ge(S("y_turned"), G)
                    nxt(yt[:], y_mix[ds((t + 1) * G * P, G * P), :].rearrange("(g p) n -> p g n", p=P))
                    st = Loads(sp, S("x_stored"))
                    for g in range(G):
                        sp.wait_ge(S("x2_ready"), g + 1)
                        st(x_cur[rows_of(g), :], xt[:, g])
                    nxt.all_in()
                    st.all_in()

                @b.tensor
                def _(pe):
                    def turn_y(g):
                        for k in range(KD):
                            m = nc.tensor.transpose(ps[:, TURN[g] + k // 4, (k % 4) * P:(k % 4) * P + P],
                                                    yt[:, g, k * P:k * P + P], ident[:])
                        m.then_inc(S("y_turned"), 1)

                    def mix(g):
                        pe.wait_ge(S("yT_low"), g + 1)
                        pe.wait_ge(S("yT_high"), g + 1)
                        for n in range(2):
                            for k in range(KD):
                                m = nc.tensor.matmul(ps[:, 2 * g + n, :], yT[:, g, k, :], w[:, k, n * 512:n * 512 + 512],
                                                     start=(k == 0), stop=(k == KD - 1))
                        m.then_inc(S("mixed"), 1)

                    turn_y(0)
                    turn_y(1)
                    mix(0)
                    turn_y(2)
                    mix(1)
                    mix(2)
                    for g in range(G):
                        pe.wait_ge(S("xn_ready"), g + 1)
                        for k in range(KD):
                            m = nc.tensor.transpose(ps[:, 2 * g + k // 4, (k % 4) * P:(k % 4) * P + P],
                                                    xn[:, g, k * P:k * P + P], ident[:])
                        m.then_inc(S("x_turned"), 1)

                @b.scalar
                def _(act):
                    def take(g):
                        act.wait_ge(S("y_turned"), g + 1)
                        nc.scalar.activation(yT[:, g, 4:8, :].rearrange("p k n -> p (k n)"), ps[:, TURN[g] + 1, :],
                                             ACT.Copy).then_inc(S("yT_high"), 1)

                    def squares(g):
                        act.wait_ge(S("mixed"), g + 1)
                        nc.scalar.activation(junk[:], ps[:, 2 * g:2 * g + 2, :].rearrange("p a n -> p (a n)"), ACT.Square,
                                             scale=1.0 / 32.0, accum_out=ss[:, 0, g:g + 1]).then_inc(S("summed"), 1)
                        act.wait_ge(S("x2_ready"), g + 1)
                        act.wait_ge(S("summed"), 2 * g + 1)
                        nc.scalar.activation(junk[:], xt[:, g], ACT.Square,
                                             scale=1.0 / 32.0, accum_out=ss[:, 3, g:g + 1]).then_inc(S("summed"), 1)
                        act.wait_ge(S("summed"), 2 * g + 2)

                    take(0)
                    take(1)
                    take(2)
                    for g in range(G):
                        squares(g)
                    for g in range(G):
                        act.wait_ge(S("h_ready"), g + 1)
                        nc.scalar.activation(h_hi[:, :, rows_of(g)], yT[:, g], ACT.Copy).then_inc(S("hi_ready"), 1)

                @b.gpsimd
                def _(pool):
                    for g in range(G):
                        for j in range(2):
                            pool.wait_ge(S("eps_added"), 2 * g + j + 1)
                            nc.gpsimd.tensor_tensor(ss[:, 3 * j + 2, g:g + 1], ss[:, 3 * j + 1, g:g + 1], mhalf[:, 0:1],
                                                    ALU.pow).then_inc(S("r_ready"), 1)

                @b.vector
                def _(dve):
                    link = Link(dve, S("v"))

                    def take(g):
                        dve.wait_ge(S("y_turned"), g + 1)
                        nc.vector.tensor_copy(yT[:, g, 0:4, :].rearrange("p k n -> p (k n)"),
                                              ps[:, TURN[g], :]).then_inc(S("yT_low"), 1)

                    take(0)
                    take(1)
                    take(2)
                    for g in range(G):
                        dve.wait_ge(S("summed"), 2 * g + 1)
                        nc.vector.tensor_scalar(ss[:, 1, g:g + 1], ss[:, 0, g:g + 1], EPS, None, ALU.add).then_inc(S("eps_added"), 1)
                        dve.wait_ge(S("r_ready"), 2 * g + 1)
                        link(nc.vector.scalar_tensor_tensor(xn[:, g], ps[:, 2 * g:2 * g + 2, :].rearrange("p a n -> p (a n)"),
                                                            ss[:, 2, g:g + 1], gb[:], ALU.mult, ALU.mult))
                        if g == 0:
                            dve.wait_ge(S("x_loaded"), 16)
                        link(nc.vector.tensor_tensor(xt[:, g], xt[:, g], xn[:, g], ALU.add), S("x2_ready"))
                        dve.wait_ge(S("summed"), 2 * g + 2)
                        nc.vector.tensor_scalar(ss[:, 4, g:g + 1], ss[:, 3, g:g + 1], EPS, None, ALU.add).then_inc(S("eps_added"), 1)
                        dve.wait_ge(S("r_ready"), 2 * g + 2)
                        nc.vector.tensor_scalar(xn[:, g], xt[:, g], ss[:, 5, g:g + 1], None, ALU.mult).then_inc(S("xn_ready"), 1)
                    for g in range(G):
                        dve.wait_ge(S("x_turned"), g + 1)
                        link(nc.vector.tensor_tensor(yT[:, g], ps[:, 2 * g:2 * g + 2, :].rearrange("p a (k n) -> p (a k) n", k=4),
                                                     gT[:].unsqueeze(2).to_broadcast([P, KD, P]), ALU.mult), S("h_ready"))
                        dve.wait_ge(S("hi_ready"), g + 1)
                        nc.vector.tensor_tensor(h_lo[:, :, rows_of(g)], yT[:, g], h_hi[:, :, rows_of(g)].bitcast(F32),
                                                ALU.subtract).then_inc(S("lo_ready"), 1)
            kit.clear()


def ffn_up(kit, env, io, l, h_hi, h_lo):
    nc, S, ps, ident, f_all = kit.nc, kit.sem, env["ps"], env["ident"], env["f_all"]
    f_stored = env["kept"]
    with ExitStack() as c:
        def sb(name, shape, dt=F32):
            return c.enter_context(nc.sbuf_tensor(name, shape, dt))
        side = sb("fu_side", [P, NF, 19])
        raw = [sb(f"fu_raw{q}", [P, 2, KD, P]) for q in range(2)]
        w_hi = [sb(f"fu_hi{q}", [P, 2, KD, P], F32R) for q in range(2)]
        w_lo = [sb(f"fu_lo{q}", [P, 2, KD, P], F32R) for q in range(2)]
        g = sb("fu_g", [P, 2, 2 + TOK])
        cv = sb("fu_c", [P, 2, TOK])
        fo = sb("fu_f", [P, 2, 2, TOK])
        rows_in = sb("fu_rin", [19, DFF])
        rows_out = sb("fu_rout", [10, DFF])

        def load_w(ld, q, f):
            for j, name in enumerate(("w_ffn_gate", "w_ffn_up")):
                ld(raw[q][:, j], io[name][ds(l, 1), :, f].rearrange("a (k p) n -> p (a k) n", p=P))

        def high(q):
            nc.scalar.activation(w_hi[q][:], raw[q][:], ACT.Copy).then_inc(S("w_high"), 1)

        def low(q):
            nc.vector.tensor_tensor(w_lo[q][:], raw[q][:], w_hi[q][:].bitcast(F32), ALU.subtract).then_inc(S("w_low"), 1)

        with nc.Block() as b:
            @b.sync
            def _(sp):
                ld = Loads(sp, S("ld"))
                ld(rows_in[0:16, :], io["state_ffn_conv"][ds(l, 1)].rearrange("a b r n -> (a b r) n"))
                ld(rows_in[16:19, :], io["ffn_conv_w"][ds(l, 1)].rearrange("a r n -> (a r) n"))
                load_w(ld, 0, slice(0, P))
                for j, name in enumerate(("w_ffn_gate", "w_ffn_up")):
                    sp.dma_start(raw[1][:, j], io[name][ds(l, 1), :, P:2 * P].rearrange("a (k p) n -> p (a k) n", p=P)).then_inc(f_stored, 16)
                ld.all_in()
                sp.wait_ge(f_stored, 32)

            @b.tensor
            def _(pe):
                pe.wait_ge(S("ld"), 16 * 4)
                for f in range(NF):
                    m = nc.tensor.transpose(ps[:, 0, f * 19:f * 19 + 19], rows_in[:, f * P:f * P + P], ident[0:19, 0:19])
                m.then_inc(S("turned"), 1)

            @b.scalar
            def _(act):
                act.wait_ge(S("ld"), 16 * 4)
                high(0)

            @b.vector
            def _(dve):
                nc.vector.memset(g[:, :, 0:2], 0.0).then_inc(S("v"), 1)
                dve.wait_ge(S("turned"), 1)
                nc.vector.tensor_copy(side[:].rearrange("p f r -> p (f r)"), ps[:, 0, 0:NF * 19]).then_inc(S("v"), 1)
                dve.wait_ge(S("w_high"), 1)
                low(0)
        kit.clear()

        with nc.Fori(0, NF // 2) as i:
            def f_tile(q):
                return fo[:, ds(i % 2, 1), q, :].rearrange("p a n -> p (a n)")

            with nc.Block(no_gpsimd_drain=True) as b:
                @b.sync
                def _(sp):
                    nxt = Loads(sp, S("next_w"))
                    load_w(nxt, 0, ds(((i + 1) % (NF // 2)) * 2 * P, P))
                    sp.wait_ge(S("w_low"), 1)
                    last = Loads(sp, S("next_w1"))
                    load_w(last, 1, ds(((i + 1) % (NF // 2)) * 2 * P + P, P))
                    for q in range(2):
                        sp.wait_ge(S("f_done"), q + 1)
                        if q == 0:
                            sp.wait_ge(f_stored, 32 + i * 32)
                        sp.dma_start(f_all[ds(2 * i + q, 1), :, :].rearrange("a p n -> p (a n)"), f_tile(q)).then_inc(f_stored, 16)
                    nxt.all_in()
                    last.all_in()

                @b.tensor
                def _(pe):
                    m8 = 0
                    for q in range(2):
                        if q == 1:
                            pe.wait_ge(S("w_low"), 1)
                        for j in range(2):
                            for s in range(3):
                                if m8 in (8, 9, 10):
                                    pe.wait_ge(S("gate_read"), m8 - 7)
                                if m8 == 11:
                                    pe.wait_ge(S("f_done"), 1)
                                for k in range(KD):
                                    seg = slice(s * SEG, s * SEG + SEG)
                                    nc.tensor.matmul(ps[:, m8 % 8, 0:SEG], w_hi[q][:, j, k, :], h_hi[:, k, seg],
                                                     start=(k == 0), stop=False)
                                    nc.tensor.matmul(ps[:, m8 % 8, 0:SEG], w_hi[q][:, j, k, :], h_lo[:, k, seg],
                                                     start=False, stop=False)
                                    m = nc.tensor.matmul(ps[:, m8 % 8, 0:SEG], w_lo[q][:, j, k, :], h_hi[:, k, seg],
                                                         start=False, stop=(k == KD - 1))
                                m.then_inc(S("summed"), 1)
                                m8 += 1
                    pe.wait_ge(S("f_done"), 2)
                    pe.wait_ge(S("gate_read"), 6)
                    for q in range(2):
                        m = nc.tensor.transpose(ps[0:10, 5, q * P:q * P + P], g[:, q, SEQ:SEQ + 10], ident[:])
                    m.then_inc(S("rows_turned"), 1)

                @b.scalar
                def _(act):
                    high(1)
                    for q in range(2):
                        for s in range(3):
                            act.wait_ge(S("summed"), 6 * q + s + 1)
                            nc.scalar.activation(g[:, q, 2 + s * SEG:2 + s * SEG + SEG], ps[:, (6 * q + s) % 8, 0:SEG],
                                                 ACT.Copy).then_inc(S("gate_read"), 1)
                        act.wait_ge(S("conved"), q + 1)
                        nc.scalar.activation(cv[:, q, :], cv[:, q, :], ACT.Gelu_apprx_tanh).then_inc(S("gelu"), 1)
                        if q == 0:
                            act.wait_ge(S("summed"), 6)
                            act.wait_ge(S("next_w"), 32)
                            high(0)
                    act.wait_ge(S("rows_turned"), 1)
                    nc.scalar.activation(rows_out[:, ds(i * 2 * P, 2 * P)], ps[0:10, 5, 0:2 * P], ACT.Copy).then_inc(S("rows_ready"), 1)

                @b.vector
                def _(dve):
                    link = Link(dve, S("v"))
                    dve.wait_ge(S("w_high"), 1)
                    low(1)
                    for q in range(2):
                        def cw(r):
                            return side[:, ds(2 * i + q, 1), r:r + 1].rearrange("p a b -> p (a b)")
                        past = side[:, ds(2 * i + q, 1), 0:16].rearrange("p a (b r) -> p (a b) r", r=2)
                        cp, cs = cv[:, q, 0:SEQ], cv[:, q, SEQ:TOK]
                        dve.wait_ge(S("gate_read"), 3 * q + 3)
                        link(nc.vector.tensor_scalar(cp, g[:, q, 0:SEQ], cw(16), None, ALU.mult))
                        link(nc.vector.scalar_tensor_tensor(cp, g[:, q, 1:1 + SEQ], cw(17), cp, ALU.mult, ALU.add))
                        link(nc.vector.scalar_tensor_tensor(cp, g[:, q, 2:2 + SEQ], cw(18), cp, ALU.mult, ALU.add))
                        link(nc.vector.tensor_scalar(cs, past[:, :, 0], cw(16), None, ALU.mult))
                        link(nc.vector.scalar_tensor_tensor(cs, past[:, :, 1], cw(17), cs, ALU.mult, ALU.add))
                        link(nc.vector.scalar_tensor_tensor(cs, g[:, q, 2 + SEQ:2 + TOK], cw(18), cs, ALU.mult, ALU.add), S("conved"))
                        dve.wait_ge(S("gelu"), q + 1)
                        for s in range(3):
                            dve.wait_ge(S("summed"), 6 * q + 3 + s + 1)
                            m = nc.vector.tensor_tensor(f_tile(q)[:, s * SEG:s * SEG + SEG],
                                                        cv[:, q, s * SEG:s * SEG + SEG], ps[:, (6 * q + 3 + s) % 8, 0:SEG], ALU.mult)
                            if s == 2:
                                m.then_inc(S("f_done"), 1)
                        if q == 0:
                            dve.wait_ge(S("w_high"), 2)
                            low(0)
            kit.clear()
        with nc.Block() as b:
            @b.sync
            def _(sp):
                st = Loads(sp, S("st"))
                st(io["p_ffn_conv"][ds(l, 1)].rearrange("a b r n -> (a b r) n"), rows_out[0:2, :])
                st(io["s_ffn_conv"][ds(l, 1), :, 1, :].rearrange("a b n -> (a b) n"), rows_out[2:10, :])
                st(io["s_ffn_conv"][ds(l, 1), :, 0, :], io["state_ffn_conv"][ds(l, 1), :, 1, :])
                st.all_in()
                sp.wait_ge(f_stored, 32 + NF * 16)
        kit.clear(kept=f_stored)


def ffn_down(kit, env, io, l):
    nc, S, ps, mhalf, x_cur, f_all = kit.nc, kit.sem, env["ps"], env["mhalf"], env["x_cur"], env["f_all"]
    zrow = env["zrow"]
    G = 3
    NQ = D // DQ
    PAIRS = NF // 2
    RING = 3
    with ExitStack() as c:
        def sb(name, shape):
            return c.enter_context(nc.sbuf_tensor(name, shape, F32))
        y = sb("fd_y", [P, TT, D])
        gb = sb("fd_gb", [P, D])
        xt = sb("fd_x", [P, 2, G, D])
        with ExitStack() as c2:
            fT = c2.enter_context(nc.sbuf_tensor("fd_f", [P, NF, TOK], F32))
            raw = c2.enter_context(nc.sbuf_tensor("fd_raw", [P, RING, 2, DQ], F32))
            w_hi = c2.enter_context(nc.sbuf_tensor("fd_whi", [P, 2, DQ], F32R))
            w_lo = c2.enter_context(nc.sbuf_tensor("fd_wlo", [P, 2, DQ], F32R))
            f_hi = c2.enter_context(nc.sbuf_tensor("fd_fhi", [P, 2, TOK], F32R))
            f_lo = c2.enter_context(nc.sbuf_tensor("fd_flo", [P, 2, TOK], F32R))
            zr = c2.enter_context(nc.sbuf_tensor("fd_zero", [P, 2 * DQ], F32R))

            def load_pair(ld, p, i):
                ld(raw[:, p % RING], io["w_ffn_down"][ds(l, 1), p * 2 * P:(p + 1) * 2 * P, ds(i * DQ, DQ)]
                   .rearrange("a (f p) n -> p (a f) n", p=P))

            def quarter(i, first):
                with nc.Block(no_gpsimd_drain=True) as b:
                    @b.sync
                    def _(sp):
                        one = [Loads(sp, S(f"w_in{p}")) for p in range(PAIRS)]
                        other = Loads(sp, S("others"))
                        for p in range(PAIRS):
                            if p >= RING:
                                sp.wait_ge(S("w_low"), 2 * (p - RING) + 2)
                            if p >= 2 or first:
                                load_pair(one[p], p, i)
                            if first:
                                f_in = Loads(sp, S(f"f_in{p}"))
                                f_in(fT[:, 2 * p:2 * p + 2, :], f_all[2 * p:2 * p + 2].rearrange("f p n -> p f n"))
                        if first:
                            other(gb[:], io["norm_post_ffn"][ds(l, 1), :].rearrange("a n -> (a n)").partition_broadcast(P))
                            other(xt[:, 0], x_cur[0:G * P, :].rearrange("(g p) n -> p g n", p=P))
                        for p in range(2):
                            sp.wait_ge(S("w_low"), 2 * (PAIRS - 2 + p) + 2)
                            other(raw[:, p], io["w_ffn_down"][ds(l, 1), p * 2 * P:(p + 1) * 2 * P, ds(((i + 1) % NQ) * DQ, DQ)]
                               .rearrange("a (f p) n -> p (a f) n", p=P))
                        other.all_in()

                    @b.scalar
                    def _(act):
                        for f in range(NF):
                            p = f // 2
                            if f % 2 == 0 and (first or p >= 2):
                                act.wait_ge(S(f"w_in{p}"), 16)
                            if f % 2 == 0 and first:
                                act.wait_ge(S(f"f_in{p}"), 16)
                            if f >= 2:
                                act.wait_ge(S("used"), f - 1)
                            nc.scalar.activation(w_hi[:, f % 2], raw[:, p % RING, f % 2], ACT.Copy).then_inc(S("w_high"), 1)
                            nc.scalar.activation(f_hi[:, f % 2], fT[:, f, :], ACT.Copy).then_inc(S("f_high"), 1)
                        for q in (0, 2, 4):
                            n = P if q < 4 else TOK - NT * P
                            m = min(2, TT - 2 * q)
                            act.wait_ge(S("bank_done"), q + 1)
                            nc.scalar.activation(y[0:n, 2 * q:2 * q + m, ds(i * DQ, DQ)],
                                                 ps[0:n, q, 0:m * DQ].rearrange("p (t n) -> p t n", t=m), ACT.Copy).then_inc(S("y_even"), 1)

                    @b.vector
                    def _(dve):
                        if first:
                            nc.vector.memset(y[:, NT, :], 0.0).then_inc(S("zeroed"), 1)
                            nc.vector.tensor_copy(zr[:], zrow[:, 0:2 * DQ]).then_inc(S("zeroed"), 1)
                        for f in range(NF):
                            if f >= 2:
                                dve.wait_ge(S("used"), f - 1)
                            dve.wait_ge(S("w_high"), f + 1)
                            nc.vector.tensor_tensor(w_lo[:, f % 2], raw[:, (f // 2) % RING, f % 2], w_hi[:, f % 2].bitcast(F32),
                                                    ALU.subtract).then_inc(S("w_low"), 1)
                            dve.wait_ge(S("f_high"), f + 1)
                            nc.vector.tensor_tensor(f_lo[:, f % 2], fT[:, f, :], f_hi[:, f % 2].bitcast(F32),
                                                    ALU.subtract).then_inc(S("f_low"), 1)
                        for q in (1, 3):
                            dve.wait_ge(S("bank_done"), q + 1)
                            nc.vector.tensor_copy(y[:, 2 * q:2 * q + 2, ds(i * DQ, DQ)],
                                                  ps[:, q, 0:2 * DQ].rearrange("p (t n) -> p t n", t=2)).then_inc(S("y_odd"), 1)

                    @b.tensor
                    def _(pe):
                        if first:
                            pe.wait_ge(S("zeroed"), 2)
                        for f in range(NF):
                            pe.wait_ge(S("w_low"), f + 1)
                            pe.wait_ge(S("f_low"), f + 1)
                            for t in range(TT):
                                n = min(P, TOK - t * P)
                                out = ps[0:n, t // 2, (t % 2) * DQ:(t % 2) * DQ + DQ]
                                hi, lo = f_hi[:, f % 2, t * P:t * P + n], f_lo[:, f % 2, t * P:t * P + n]
                                alone = t == NT
                                if f == 0 and t % 2 == 0 and not alone:
                                    nc.tensor.matmul(ps[:, t // 2, :], zr[:, 0:P], zr[:], start=True, stop=False)
                                nc.tensor.matmul(out, hi, w_hi[:, f % 2], start=(f == 0 and alone), stop=False)
                                nc.tensor.matmul(out, hi, w_lo[:, f % 2], start=False, stop=False)
                                m = nc.tensor.matmul(out, lo, w_hi[:, f % 2], start=False,
                                                     stop=(f == NF - 1 and (t % 2 == 1 or t == TT - 1)))
                                if f == NF - 1 and (t % 2 == 1 or t == TT - 1):
                                    m.then_inc(S("bank_done"), 1)
                            if f < NF - 1:
                                m.then_inc(S("used"), 1)
                kit.clear()

            quarter(0, True)
            with nc.Fori(1, NQ) as i:
                quarter(i, False)
        kit.next_stage()
        x2 = sb("fd_x2", [P, G, D])
        junk = sb("fd_j", [P, D])
        ss = sb("fd_ss", [P, 3, G])
        with nc.Fori(0, TT // G) as t:
            def y_in(g):
                return y[:, ds(t * G + g, 1), :].rearrange("p a n -> p (a n)")

            with nc.Block(no_gpsimd_drain=True) as b:
                @b.sync
                def _(sp):
                    ld = Loads(sp, S("next_x"))
                    ld(xt[:, ds((t + 1) % 2, 1), :, :].rearrange("p a g n -> p (a g) n"),
                       x_cur[ds((t + 1) * G * P, G * P), :].rearrange("(g p) n -> p g n", p=P))
                    st = Loads(sp, S("x_stored"))
                    for g in range(G):
                        sp.wait_ge(S("x2_ready"), g + 1)
                        st(x_cur[ds(t * G * P + g * P, P), :], x2[:, g])
                    ld.all_in()
                    st.all_in()

                @b.scalar
                def _(act):
                    for g in range(G):
                        if g:
                            act.wait_ge(S("summed"), g)
                        nc.scalar.activation(junk[:], y_in(g), ACT.Square, scale=1.0 / 32.0,
                                             accum_out=ss[:, 0, g:g + 1]).then_inc(S("summed"), 1)

                @b.gpsimd
                def _(pool):
                    pool.wait_ge(S("eps_added"), 1)
                    nc.gpsimd.tensor_tensor(ss[:, 2, :], ss[:, 1, :], mhalf[:, 0:G], ALU.pow).then_inc(S("r_ready"), 1)

                @b.vector
                def _(dve):
                    link = Link(dve, S("v"))
                    dve.wait_ge(S("summed"), G)
                    nc.vector.tensor_scalar(ss[:, 1, :], ss[:, 0, :], EPS, None, ALU.add).then_inc(S("eps_added"), 1)
                    dve.wait_ge(S("r_ready"), 1)
                    for g in range(G):
                        link(nc.vector.scalar_tensor_tensor(x2[:, g], y_in(g), ss[:, 2, g:g + 1], gb[:], ALU.mult, ALU.mult))
                        link(nc.vector.tensor_tensor(x2[:, g], x2[:, g], xt[:, ds(t % 2, 1), g, :].rearrange("p a n -> p (a n)"),
                                                     ALU.add), S("x2_ready"))
            kit.clear()


def bc(ap, n, shape):
    return ap.unsqueeze(2).to_broadcast(shape)


def recurrent_prompt(kit, env, io, l, beside):
    nc, S, ps, ident, mhalf = kit.nc, kit.sem, env["ps"], env["ident"], env["mhalf"]
    z, y_mix = env["z"], env["y_mix"]
    V, A, G_ = nc.vector, nc.scalar, nc.gpsimd
    W3 = 3 * H * HD
    LEV = 7
    IC, LF, G, MN, MX, AB, AB2, BC, GC, CC, EG, EGE, WE, BETA, BETAH, NEGG, TMP = range(17)
    with ExitStack() as c:
        def sb(name, shape):
            return c.enter_context(nc.sbuf_tensor(name, shape, F32))
        zt = sb("r_z", [P, 2, 6 * H * HD])
        zs = sb("r_zs", [P, 4, W3])
        rope = sb("r_rope", [P, 2, 64])
        retD = sb("r_retD", [P, H, P])
        xi = sb("r_xi", [P, 3, H])
        upper = sb("r_upper", [P, P])
        mask = sb("r_mask", [P, P])
        maskT = sb("r_maskT", [P, P])
        last = sb("r_last", [P, P])
        ones = sb("r_ones", [P, P])
        lev = sb("r_lev", [P, P])
        levT = sb("r_levT", [P, LEV, P])
        qkscale = sb("r_qks", [P, 8])
        gates = sb("r_gates", [P, 16])
        cw = sb("r_cw", [P, 4, W3])
        qa = sb("r_qa", [P, 17, NT, H])
        gain = sb("r_gain", [P, NT, 3, 256])
        smo = sb("r_smo", [P, NT, 256])
        Sret = sb("r_S", [HD, H, HD])
        Caug = sb("r_C", [HD, H, HD + 1])
        Sgdn = sb("r_G", [HD, H, HD])
        mprev = sb("r_m", [P, H])
        xc = sb("r_xc", [P, 2, W3])

        def tiles(a, n):
            return z[PADROWS:PADROWS + SEQ, a:a + n].rearrange("(t p) n -> p t n", p=P)

        def loads(ld, t, q):
            ld(zt[:, q, 0:768].rearrange("p a n -> p (a n)"), z[ds(t * P + PADROWS, P), RQ:RQ + 768])
            ld(zt[:, q, 768:1536].rearrange("p a n -> p (a n)"), z[ds(t * P + PADROWS, P), MQ:MQ + 768])
            ld(rope[:, q, :].rearrange("p a n -> p (a n)"), io["c_rope"][ds(t * P, P), :])

        def conv_loads(ld, t):
            for j in range(4):
                ld(zs[:, j, :], z[ds(t * P + PADROWS - 3 + j, P), GX:GX + W3])

        def conv(link, out):
            for j in range(4):
                link(G_.tensor_tensor(zs[:, j, :], zs[:, j, :], cw[:, j, :], ALU.mult))
            link(G_.tensor_tensor(zs[:, 0, :], zs[:, 0, :], zs[:, 1, :], ALU.add))
            link(G_.tensor_tensor(zs[:, 2, :], zs[:, 2, :], zs[:, 3, :], ALU.add))
            link(G_.tensor_tensor(zs[:, 0, :], zs[:, 0, :], zs[:, 2, :], ALU.add), S("conved"))

        with ExitStack() as c2:
            def sb2(name, shape):
                return c2.enter_context(nc.sbuf_tensor(name, shape, F32))
            zg = sb2("r_zg", [P, 3, NT, 256])
            zsm = sb2("r_zsm", [P, 2, NT, 8])
            gains = sb2("r_gains", [P, 3, 256])
            sg = sb2("r_sg", [P, NT, 256])
            with nc.Block() as b:
                @b.sync
                def _(sp):
                    ld = Loads(sp, S("ld"))
                    for j, name in enumerate(("mlstm_b_i", "mlstm_b_f", "gdn_dt_bias", "gdn_A_log")):
                        ld(gates[:, 4 * j:4 * j + 4], io[name][ds(l, 1), :].rearrange("a n -> (a n)").partition_broadcast(P))
                    ld(zsm[:, 0], tiles(MI, 8))
                    ld(zsm[:, 1], tiles(GA, 8))
                    ld(upper[:], io["c_upper"])
                    ldc = Loads(sp, S("conv_in"))
                    ldc(cw[:].rearrange("p a n -> p (a n)"), io["gdn_conv_w"][ds(l, 1)].rearrange("a j n -> (a j n)").partition_broadcast(P))
                    conv_loads(ldc, 0)
                    ldg = Loads(sp, S("gates_in"))
                    for j, a in enumerate((RG, MO, GG)):
                        ldg(zg[:, j], tiles(a, 256))
                    for j, name in enumerate(("ret_norm", "mlstm_norm", "gdn_norm")):
                        ldg(gains[:, j, :], io[name][ds(l, 1), :].rearrange("a n -> (a n)").partition_broadcast(P))
                    ld2 = Loads(sp, S("ld2"))
                    ld2(retD[:].rearrange("p h n -> p (h n)"), io["c_retD"])
                    ld2(xi[:].rearrange("p a h -> p (a h)"), io["c_xi"])
                    ld2(mask[:], io["c_mask"])
                    ld2(maskT[:], io["c_maskT"])
                    ld2(last[:], io["c_last"])
                    ld2(lev[:], io["c_lev"][:, 0:P])
                    ld2(levT[:].rearrange("p a n -> p (a n)"), io["c_levT"])
                    ld2(qkscale[:], io["c_qkscale"])
                    loads(ld2, 0, slice(0, 1))
                    for x in (ld, ldc, ldg, ld2):
                        x.all_in()
                    ldn = Loads(sp, S("beside_in"))
                    beside(ldn)
                    ldn.all_in()

                @b.gpsimd
                def _(pool):
                    link = Link(pool, S("p"))
                    pool.wait_ge(S("conv_in"), 16 * 5)
                    conv(link, 0)

                @b.scalar
                def _(act):
                    link = Link(act, S("a"))
                    act.wait_ge(S("ld"), 16 * 7)
                    link(A.activation(gates[:, 12:16], gates[:, 12:16], ACT.Exp))
                    link(A.activation(qa[:, BETA], zsm[:, 1, :, 4:8], ACT.Exp, scale=-1.0))
                    act.wait_ge(S("abs"), 1)
                    link(A.activation(qa[:, AB:AB2 + 1], qa[:, AB:AB2 + 1], ACT.Exp, scale=-1.0))
                    link(A.activation(qa[:, AB:AB2 + 1], qa[:, AB:AB2 + 1], ACT.Ln, bias=1.0), S("softplus"))
                    act.wait_ge(S("cols"), 1)
                    link(A.activation(qa[:, EG:WE + 1], qa[:, EG:WE + 1], ACT.Exp), S("exps"))
                    act.wait_ge(S("gates_in"), 16 * 6)
                    for j, dst in ((1, smo[:]), (0, gain[:, :, 0, :]), (2, gain[:, :, 2, :])):
                        link(A.activation(dst, zg[:, j], ACT.Tanh, scale=0.5), S("tanh"))
                    act.wait_ge(S("conved"), 1)
                    link(A.activation(xc[:, 0, :], zs[:, 0, :], ACT.Tanh, scale=0.5), S("xtanh"))

                @b.tensor
                def _(pe):
                    pe.wait_ge(S("lf_g"), 1)
                    nc.tensor.matmul(ps[:, 0, 0:64], upper[:], qa[:, LF:G + 1].rearrange("p a t h -> p (a t h)"), start=True, stop=True)
                    nc.tensor.matmul(ps[:, 0, 64:96], ones[:], qa[:, G].rearrange("p t h -> p (t h)"), start=True, stop=True).then_inc(S("sums"), 1)

                @b.vector
                def _(dve):
                    link = Link(dve, S("v"))
                    for x in (Sret, Caug, Sgdn, mprev):
                        link(V.memset(x[:], 0.0))
                    link(V.memset(ones[:], 1.0))
                    dve.wait_ge(S("ld"), 16 * 7)

                    def bias(j):
                        return gates[:, 4 * j:4 * j + 4].unsqueeze(1).to_broadcast([P, NT, H])
                    dve.wait_ge(S("a"), 2)
                    link(V.tensor_tensor(qa[:, IC], zsm[:, 0, :, 0:4], bias(0), ALU.add))
                    link(V.tensor_tensor(qa[:, LF], zsm[:, 0, :, 4:8], bias(1), ALU.add))
                    link(V.tensor_tensor(qa[:, G], zsm[:, 1, :, 0:4], bias(2), ALU.add))
                    link(V.tensor_scalar(qa[:, MN], qa[:, LF], 0.0, None, ALU.min))
                    link(V.tensor_scalar(qa[:, MX], qa[:, G], 0.0, None, ALU.max))
                    link(V.scalar_tensor_tensor(qa[:, AB:AB2 + 1], qa[:, LF:G + 1], -1.0, qa[:, LF:G + 1], ALU.mult, ALU.max), S("abs"))
                    link(V.tensor_scalar(qa[:, BETA], qa[:, BETA], 1.0, None, ALU.add))
                    link(V.reciprocal(qa[:, BETA], qa[:, BETA]))
                    link(V.tensor_scalar(qa[:, BETAH], qa[:, BETA], 0.5, None, ALU.mult))
                    dve.wait_ge(S("softplus"), 1)
                    link(V.tensor_tensor(qa[:, LF], qa[:, MN], qa[:, AB], ALU.subtract))
                    link(V.tensor_tensor(qa[:, G], qa[:, MX], qa[:, AB2], ALU.add))
                    link(V.scalar_tensor_tensor(qa[:, G], qa[:, G], -1.0, bias(3), ALU.mult, ALU.mult), S("lf_g"))
                    link(V.tensor_scalar(qa[:, NEGG], qa[:, G], -1.0, None, ALU.mult))
                    dve.wait_ge(S("sums"), 1)
                    link(V.tensor_copy(qa[:, BC:GC + 1].rearrange("p a t h -> p (a t h)"), ps[:, 0, 0:64]))
                    link(V.tensor_copy(qa[:, EGE].rearrange("p t h -> p (t h)"), ps[:, 0, 64:96]))
                    link(V.tensor_tensor(qa[:, CC], qa[:, IC], qa[:, BC], ALU.subtract))
                    link(V.tensor_copy(qa[:, EG], qa[:, GC]))
                    link(V.tensor_tensor(qa[:, WE], qa[:, EGE], qa[:, GC], ALU.subtract), S("cols"))
                    dve.wait_ge(S("tanh"), 1)
                    link(V.tensor_scalar(smo[:], smo[:], 0.5, 0.5, ALU.mult, ALU.add))
                    for n, j in ((2, 0), (3, 2)):
                        dve.wait_ge(S("tanh"), n)
                        gj = gains[:, j, :].unsqueeze(1).to_broadcast([P, NT, 256])
                        link(V.tensor_scalar(sg[:], gain[:, :, j, :], 0.5, 0.5, ALU.mult, ALU.add))
                        link(V.tensor_tensor(sg[:], sg[:], zg[:, j], ALU.mult))
                        link(V.tensor_tensor(gain[:, :, j, :], sg[:], gj, ALU.mult))
                    link(V.tensor_copy(gain[:, :, 1, :], gains[:, 1, :].unsqueeze(1).to_broadcast([P, NT, 256])))
                    dve.wait_ge(S("xtanh"), 1)
                    link(V.scalar_tensor_tensor(xc[:, 0, :], xc[:, 0, :], 1.0, zs[:, 0, :], ALU.add, ALU.mult))
            kit.clear()

        qk = sb("r_qk", [P, 2 * H, HD])
        qkw = sb("r_qkw", [P, 2, 2 * H, HD // 2])
        qkm = sb("r_qkm", [P, 2 * H, HD])
        qkg = sb("r_qkg", [P, 2 * H, HD])
        kb = sb("r_kb", [P, H, HD])
        qTr, kTr, qTm, kTm, qTg, kTg, kbT, wTn = [sb(f"r_T{i}", [HD, H, P]) for i in range(8)]
        vr = sb("r_vr", [P, H, HD])
        vm = sb("r_vm", [P, H, HD + 1])
        pTr, pTm, pTg, w1, w2, wm, dgm, dgg, dmu = [sb(f"r_W{i}", [P, H, P]) for i in range(9)]
        kzr, kzm, kzg, rk, rv, dl = [sb(f"r_K{i}", [P, H, HD]) for i in range(6)]
        om = sb("r_om", [P, H, HD + 1])
        o3 = sb("r_o3", [P, 3, H, HD])
        sq = sb("r_sq", [P, 3, H, HD])
        y = sb("r_y", [P, 3 * H, HD])
        sm = sb("r_sm", [P, 12, H])
        ss8 = sb("r_ss8", [P, 2, 8])
        ss12 = sb("r_ss12", [P, 2, 3 * H])
        X = sb("r_X", [P, H, P])
        XT = sb("r_XT", [P, H, P])
        NLT = sb("r_NT", [P, H, P])
        NM = [sb(f"r_NM{i}", [P, H, P]) for i in range(1, LEV)]
        Y = sb("r_Y", [P, H, P])
        with nc.Block() as b:
            @b.vector
            def _(dve):
                V.memset(vm[:], 1.0).then_inc(S("v"), 1)
        kit.clear()

        with nc.Fori(0, NT) as t:
            par = ds(t % 2, 1)
            nxt = ds((t + 1) % 2, 1)
            MXM, MU, MM, GIN, WEND, GEND, EM, MEND, DEN, RD = range(10)

            def gq(i, n=H):
                return qa[:, i, ds(t, 1), :].rearrange("p a h -> p (a h)")

            def heads(a, n=H):
                return zt[:, par, a:a + n * HD].rearrange("p a (h d) -> p (a h) d", d=HD)

            def s4(i):
                return sm[:, i, :]

            def b64(ap):
                return bc(ap, H, [P, H, HD])

            def b128(ap):
                return bc(ap, H, [P, H, P])

            def flat(ap):
                return ap.rearrange("p h n -> p (h n)")

            def bank(i):
                return ps[:, i, :].rearrange("p (h n) -> p h n", h=H)

            def bank64(i, n=HD, rows_=P):
                return ps[0:rows_, i, 0:H * n].rearrange("p (h d) -> p h d", d=n)

            def b512(ap):
                return ap.unsqueeze(1).to_broadcast([P, H, P])

            xh = xc[:, par, :].rearrange("p a (h d) -> p (a h) d", d=HD)
            halves = ((0, 1), (2, 3))

            def half(ap, k):
                return ap[:, 2 * k:2 * k + 2, :]

            with nc.Block(no_gpsimd_drain=True) as b:
                @b.sync
                def _(sp):
                    ldc = Loads(sp, S("conv_in"))
                    conv_loads(ldc, (t + 1) % NT)
                    ld = Loads(sp, S("next_z"))
                    loads(ld, (t + 1) % NT, nxt)
                    sp.wait_ge(S("y_ready"), 1)
                    st = Loads(sp, S("y_stored"))
                    st(y_mix[rows(t), 0:768], y[:].rearrange("p a n -> p (a n)"))
                    ldc.all_in()
                    ld.all_in()
                    st.all_in()

                @b.gpsimd
                def _(pool):
                    link = Link(pool, S("p"))
                    link(G_.tensor_tensor(dgm[:], b512(ident[:]), b128(gq(CC)), ALU.mult), S("m_diag"))
                    link(G_.tensor_tensor(dgg[:], b512(upper[:]), b128(gq(NEGG)), ALU.mult), S("g_diag"))
                    pool.wait_ge(S("g_squares"), 1)
                    link(G_.tensor_tensor(ss8[:, 1, :], ss8[:, 0, :], mhalf[:, 0:8], ALU.pow), S("g_r"))
                    pool.wait_ge(S("g_nlt"), 1)
                    for s in range(1, LEV):
                        link(G_.tensor_tensor(NM[s - 1][:], NLT[:], b512(levT[:, s, :]), ALU.mult), S("g_nm"))
                    pool.wait_ge(S("conv_in"), 16 * 4)
                    conv(link, nxt)
                    pool.wait_ge(S("squares"), 1)
                    link(G_.tensor_tensor(ss12[:, 1, :], ss12[:, 0, :], mhalf[:, 0:12], ALU.pow), S("r_all"))

                @b.tensor
                def _(pe):
                    def turn(n, src, signal):
                        for h in range(H):
                            m = nc.tensor.transpose(ps[0:HD, n, h * P:h * P + P], src[:, h, :], ident[:])
                        m.then_inc(signal, 1)

                    def mm4(out, lhs, rhs, signal, hs=range(H)):
                        for h in hs:
                            m = nc.tensor.matmul(out(h), lhs(h), rhs(h), start=True, stop=True)
                        m.then_inc(signal, 1)

                    def at(n, w=P, rows_=P):
                        return lambda h: ps[0:rows_, n, h * w:h * w + w]

                    def of(x, w=None):
                        return lambda h: x[:, h, :] if w is None else x[:, h, 0:w]

                    pe.wait_ge(S("m_qk"), 1)
                    turn(2, qkm[:, 0:4, :], S("m_turned"))
                    turn(3, qkm[:, 4:8, :], S("m_turned"))
                    pe.wait_ge(S("m_diag"), 1)
                    nc.tensor.matmul(ps[:, 4, :], ones[:], flat(dgm[:]), start=True, stop=True).then_inc(S("m_crow"), 1)
                    pe.wait_ge(S("g_diag"), 1)
                    nc.tensor.matmul(ps[:, 5, :], ones[:], flat(dgg[:]), start=True, stop=False)
                    nc.tensor.matmul(ps[:, 5, :], upper[:], b128(gq(G)), start=False, stop=True).then_inc(S("g_square"), 1)
                    pe.wait_ge(S("r_roped"), 1)
                    turn(0, qk[:, 0:4, :], S("r_turned"))
                    turn(1, qk[:, 4:8, :], S("r_turned"))
                    pe.wait_ge(S("g_qk"), 1)
                    pe.wait_ge(S("r_T"), 1)
                    turn(0, qkg[:, 0:4, :], S("g_turned"))
                    pe.wait_ge(S("r_T"), 2)
                    turn(1, qkg[:, 4:8, :], S("g_turned"))
                    pe.wait_ge(S("m_T"), 1)
                    turn(2, kb, S("g_turned"))
                    pe.wait_ge(S("m_T"), 2)
                    mm4(at(3), of(kTr), of(qTr), S("r_scores"))
                    pe.wait_ge(S("m_mu"), 1)
                    nc.tensor.matmul(ps[:, 4, :], ones[:], flat(dmu[:]), start=True, stop=False)
                    nc.tensor.matmul(ps[:, 4, :], ident[:], b128(gq(CC)), start=False, stop=True).then_inc(S("m_square"), 1)
                    nc.tensor.matmul(ps[:, 6, 0:8], last[:], sm[:, MU:MM + 1, :].rearrange("p a h -> p (a h)"), start=True, stop=True).then_inc(S("m_end"), 1)
                    pe.wait_ge(S("g_T"), 3)
                    pe.wait_ge(S("g_shifted"), 1)
                    mm4(at(5), of(kbT), of(kTg), S("g_nn"))
                    mm4(at(7), of(kTg), of(kbT), S("g_nn"))
                    mm4(at(0), of(kTg), of(qTg), S("g_nn"))

                    def level(s):
                        for k in range(2):
                            pe.wait_ge(S("g_x"), 2 * (s - 1) + k + 1)
                            if k == 0:
                                pe.wait_ge(S("g_nm"), s)
                            mm4(lambda h: ps[:, 1 + k, (h % 2) * P:(h % 2) * P + P], of(NM[s - 1]), of(X), S("g_y"), halves[k])
                        for k, n in ((0, 5), (1, 7)):
                            pe.wait_ge(S("g_ysb"), 2 * (s - 1) + k + 1)
                            if s < LEV - 1:
                                for h in halves[k]:
                                    nc.tensor.matmul(ps[:, n, (h % 2) * P:(h % 2) * P + P], XT[:, h, :], Y[:, h, :], start=True, stop=True)
                            for h in halves[k]:
                                m = nc.tensor.matmul(ps[:, n, 256 + (h % 2) * P:256 + (h % 2) * P + P], Y[:, h, :], XT[:, h, :], start=True, stop=True)
                            m.then_inc(S("g_xy"), 1)

                    level(1)
                    mm4(at(0, HD), of(qTr), of(Sret), S("r_inter"))
                    pe.wait_ge(S("m_end_read"), 1)
                    mm4(at(6, HD, HD), of(kzr), of(vr), S("r_dstate"))
                    level(2)
                    pe.wait_ge(S("r_p"), 1)
                    mm4(at(3, HD), of(pTr), of(vr), S("r_intra"))
                    pe.wait_ge(S("m_shifted"), 1)
                    mm4(at(4), of(kTm), of(qTm), S("m_scores"))
                    level(3)
                    pe.wait_ge(S("r_state"), 1)
                    mm4(at(0, HD + 1), of(qTm), of(Caug), S("m_inter"))
                    pe.wait_ge(S("m_kz"), 1)
                    mm4(at(6, HD + 1, HD), of(kzm), of(vm), S("m_dstate"))
                    level(4)
                    pe.wait_ge(S("m_p"), 1)
                    mm4(at(3, HD + 1), of(pTm), of(vm), S("m_intra"))
                    level(5)
                    pe.wait_ge(S("m_state"), 1)
                    mm4(at(0, HD), of(qTg), of(Sgdn), S("g_inter"))
                    level(6)
                    pe.wait_ge(S("g_x"), 2 * LEV)
                    mm4(at(4, P, HD), of(rk), of(XT), S("g_wt"))
                    pe.wait_ge(S("g_wtn"), 1)
                    for h in range(H):
                        nc.tensor.matmul(ps[:, 1, h * HD:h * HD + HD], XT[:, h, :], rv[:, h, :], start=True, stop=False)
                        m = nc.tensor.matmul(ps[:, 1, h * HD:h * HD + HD], wTn[:, h, :], Sgdn[:, h, :], start=False, stop=True)
                    m.then_inc(S("g_delta"), 1)
                    pe.wait_ge(S("g_dl"), 1)
                    pe.wait_ge(S("m_o"), 1)
                    mm4(at(3, HD), of(pTg), of(dl), S("g_intra"))
                    mm4(at(6, HD, HD), of(kzg), of(dl), S("g_dstate"))

                @b.scalar
                def _(act):
                    link = Link(act, S("a"))

                    def turned(dst, n, signal, at_, done):
                        act.wait_ge(signal, at_)
                        A.activation(flat(dst[:]), ps[0:HD, n, :], ACT.Copy).then_inc(done, 1)
                    A.activation(qkm[:], heads(768, 8), ACT.Copy).then_inc(S("m_qk"), 1)
                    A.activation(vr[:], heads(512), ACT.Copy).then_inc(S("v_ready"), 1)
                    A.activation(vm[:, :, 0:HD], heads(1280), ACT.Copy).then_inc(S("v_ready"), 1)
                    turned(qTm, 2, S("m_turned"), 1, S("m_T"))
                    turned(kTm, 3, S("m_turned"), 2, S("m_T"))
                    turned(qTr, 0, S("r_turned"), 1, S("r_T"))
                    turned(kTr, 1, S("r_turned"), 2, S("r_T"))
                    for i, x in enumerate((qTg, kTg, kbT)):
                        turned(x, i, S("g_turned"), i + 1, S("g_T"))
                    act.wait_ge(S("g_shifted"), 1)
                    A.activation(w1[:], w1[:], ACT.Exp).then_inc(S("g_weights"), 1)
                    A.activation(w2[:], w2[:], ACT.Exp).then_inc(S("g_weights"), 1)
                    act.wait_ge(S("m_exp_in"), 1)
                    A.activation(sm[:, GIN:EM + 1, :], sm[:, GIN:EM + 1, :], ACT.Exp).then_inc(S("m_exps"), 1)
                    act.wait_ge(S("m_shifted"), 1)
                    A.activation(wm[:], wm[:], ACT.Exp).then_inc(S("m_weights"), 1)
                    for s in range(1, LEV):
                        for k in range(2):
                            act.wait_ge(S("g_y"), 2 * (s - 1) + k + 1)
                            A.activation(flat(half(Y[:], k)), ps[:, 1 + k, 0:2 * P], ACT.Copy).then_inc(S("g_ysb"), 1)
                    act.wait_ge(S("g_wt"), 1)
                    A.activation(flat(wTn[:]), ps[0:HD, 4, :], ACT.Copy, scale=-1.0).then_inc(S("g_wtn"), 1)
                    act.wait_ge(S("g_delta"), 1)
                    A.activation(flat(dl[:]), ps[:, 1, 0:256], ACT.Copy).then_inc(S("g_dl"), 1)
                    act.wait_ge(S("conved"), 1)
                    A.activation(xc[:, nxt, :].rearrange("p a n -> p (a n)"), zs[:, 0, :], ACT.Tanh, scale=0.5).then_inc(S("xtanh"), 1)

                @b.vector
                def _(dve):
                    link = Link(dve, S("v"))
                    sq8 = sq[:, 0:2].rearrange("p a h d -> p (a h) d")
                    link(V.tensor_tensor(sq8, xh[:, 0:8, :], xh[:, 0:8, :], ALU.mult))
                    link(V.tensor_reduce(ss8[:, 0, :], sq8, AX.X, ALU.add))
                    link(V.tensor_scalar(ss8[:, 0, :], ss8[:, 0, :], 0.25, EPS, ALU.mult, ALU.add), S("g_squares"))
                    x12 = heads(0, 8)
                    cos = rope[:, par, 0:32].to_broadcast([P, 8, 32])
                    sin = rope[:, par, 32:64].to_broadcast([P, 8, 32])
                    lo, hi = slice(0, 32), slice(32, 64)
                    link(V.tensor_tensor(qkw[:, 0], x12[:, :, lo], cos, ALU.mult))
                    link(V.tensor_tensor(qkw[:, 1], x12[:, :, hi], sin, ALU.mult))
                    link(V.tensor_tensor(qk[:, :, lo], qkw[:, 0], qkw[:, 1], ALU.subtract))
                    link(V.tensor_tensor(qkw[:, 0], x12[:, :, lo], sin, ALU.mult))
                    link(V.tensor_tensor(qkw[:, 1], x12[:, :, hi], cos, ALU.mult))
                    link(V.tensor_tensor(qk[:, :, hi], qkw[:, 0], qkw[:, 1], ALU.add), S("r_roped"))
                    dve.wait_ge(S("g_r"), 1)
                    link(V.tensor_tensor(ss8[:, 1, :], ss8[:, 1, :], qkscale[:], ALU.mult))
                    link(V.tensor_tensor(qkg[:], xh[:, 0:8, :], bc(ss8[:, 1, :], 8, [P, 8, HD]), ALU.mult))
                    link(V.tensor_tensor(kb[:], qkg[:, 4:8, :], b64(gq(BETA)), ALU.mult), S("g_qk"))
                    dve.wait_ge(S("m_crow"), 1)
                    link(V.tensor_tensor(wm[:], bank(4), b512(mask[:]), ALU.add))
                    link(V.tensor_reduce(s4(MXM), wm[:], AX.X, ALU.max))
                    link(V.tensor_tensor(s4(MU), s4(MXM), mprev[:], ALU.max))
                    link(V.tensor_tensor(s4(MM), s4(MU), gq(BC), ALU.add))
                    link(V.scalar_tensor_tensor(dmu[:], b128(s4(MU)), -1.0, b512(ident[:]), ALU.mult, ALU.mult), S("m_mu"))
                    dve.wait_ge(S("g_square"), 1)
                    link(V.tensor_tensor(w1[:], bank(5), b512(mask[:]), ALU.add))
                    link(V.scalar_tensor_tensor(w2[:], bank(5), -1.0, b512(maskT[:]), ALU.mult, ALU.add), S("g_shifted"))
                    link(V.tensor_tensor(rk[:], kb[:], b64(gq(EG)), ALU.mult))
                    link(V.tensor_tensor(rv[:], xh[:, 8:12, :], b64(gq(BETAH)), ALU.mult))
                    link(V.tensor_tensor(kzg[:], qkg[:, 4:8, :], b64(gq(WE)), ALU.mult))
                    link(V.tensor_tensor(kzr[:], qk[:, 4:8, :], b64(xi[:, 1, :]), ALU.mult))
                    dve.wait_ge(S("m_end"), 1)
                    link(V.tensor_tensor(s4(GIN), mprev[:], s4(MU), ALU.subtract))
                    link(V.tensor_tensor(s4(WEND), gq(CC), ps[:, 6, 0:4], ALU.subtract))
                    link(V.tensor_tensor(s4(GEND), mprev[:], ps[:, 6, 0:4], ALU.subtract))
                    link(V.tensor_scalar(s4(EM), s4(MM), -1.0, None, ALU.mult), S("m_exp_in"))
                    link(V.tensor_copy(mprev[:], ps[:, 6, 4:8]), S("m_end_read"))
                    dve.wait_ge(S("m_square"), 1)
                    link(V.tensor_tensor(wm[:], bank(4), b512(maskT[:]), ALU.add), S("m_shifted"))
                    dve.wait_ge(S("g_weights"), 2)
                    dve.wait_ge(S("g_nn"), 2)
                    link(V.tensor_tensor(NLT[:], bank(7), w2[:], ALU.mult), S("g_nlt"))
                    link(V.tensor_tensor(w1[:], bank(5), w1[:], ALU.mult))
                    link(V.tensor_tensor(X[:], w1[:], b512(lev[:]), ALU.mult))
                    link(V.tensor_tensor(X[:], b512(ident[:]), X[:], ALU.subtract))
                    link(V.tensor_tensor(XT[:], NLT[:], b512(levT[:, 0, :]), ALU.mult))
                    dve.wait_ge(S("g_nn"), 3)
                    link(V.tensor_tensor(pTg[:], bank(0), w2[:], ALU.mult))
                    V.tensor_tensor(half(XT[:], 0), b512(ident[:])[:, 0:2, :], half(XT[:], 0), ALU.subtract).then_inc(S("g_x"), 1)
                    V.tensor_tensor(half(XT[:], 1), b512(ident[:])[:, 0:2, :], half(XT[:], 1), ALU.subtract).then_inc(S("g_x"), 1)

                    def level(s):
                        for k, n in ((0, 5), (1, 7)):
                            dve.wait_ge(S("g_xy"), 2 * (s - 1) + k + 1)
                            dve.wait_ge(S("g_x"), 2 * (s - 1) + k + 1)
                            if s < LEV - 1:
                                link(V.tensor_tensor(half(X[:], k), half(X[:], k), ps[:, n, 0:256].rearrange("p (h n) -> p h n", h=2), ALU.subtract))
                            V.tensor_tensor(half(XT[:], k), half(XT[:], k), ps[:, n, 256:512].rearrange("p (h n) -> p h n", h=2), ALU.subtract).then_inc(S("g_x"), 1)

                    link(V.tensor_tensor(pTr[:], bank(3), retD[:], ALU.mult), S("r_p"))
                    level(1)
                    dve.wait_ge(S("r_inter"), 1)
                    link(V.tensor_tensor(o3[:, 0], bank64(0), b64(xi[:, 0, :]), ALU.mult))
                    link(V.tensor_tensor(Sret[:], Sret[:], bc(xi[0:HD, 2, :], H, [HD, H, HD]), ALU.mult))
                    dve.wait_ge(S("m_exps"), 1)
                    link(V.scalar_tensor_tensor(kzm[:], qkm[:, 4:8, :], 0.125, b64(s4(WEND)), ALU.mult, ALU.mult), S("m_kz"))
                    level(2)
                    dve.wait_ge(S("r_dstate"), 1)
                    link(V.tensor_tensor(Sret[:], Sret[:], bank64(6, HD, HD), ALU.add), S("r_state"))
                    dve.wait_ge(S("r_intra"), 1)
                    link(V.tensor_tensor(o3[:, 0], o3[:, 0], bank64(3), ALU.add))
                    level(3)
                    dve.wait_ge(S("m_scores"), 1)
                    dve.wait_ge(S("m_weights"), 1)
                    link(V.scalar_tensor_tensor(pTm[:], bank(4), 0.125, wm[:], ALU.mult, ALU.mult), S("m_p"))
                    level(4)
                    dve.wait_ge(S("m_inter"), 1)
                    link(V.tensor_tensor(om[:], bank64(0, HD + 1), bc(s4(GIN), H, [P, H, HD + 1]), ALU.mult))
                    link(V.tensor_tensor(Caug[:], Caug[:], bc(sm[0:HD, GEND, :], H, [HD, H, HD + 1]), ALU.mult))
                    dve.wait_ge(S("m_dstate"), 1)
                    link(V.tensor_tensor(Caug[:], Caug[:], bank64(6, HD + 1, HD), ALU.add), S("m_state"))
                    level(5)
                    dve.wait_ge(S("m_intra"), 1)
                    link(V.tensor_tensor(om[:], om[:], bank64(3, HD + 1), ALU.add), S("m_o"))
                    link(V.scalar_tensor_tensor(s4(DEN), om[:, :, HD], -1.0, om[:, :, HD], ALU.mult, ALU.max))
                    link(V.tensor_tensor(s4(DEN), s4(DEN), s4(EM), ALU.max))
                    link(V.reciprocal(s4(RD), s4(DEN)))
                    link(V.tensor_tensor(o3[:, 1], om[:, :, 0:HD], b64(s4(RD)), ALU.mult))
                    link(V.tensor_tensor(o3[:, 1], o3[:, 1], smo[:, ds(t, 1), :].rearrange("p a (h d) -> p (a h) d", d=HD), ALU.mult))
                    level(6)
                    dve.wait_ge(S("g_inter"), 1)
                    link(V.tensor_tensor(o3[:, 2], bank64(0), b64(gq(EG)), ALU.mult))
                    link(V.tensor_tensor(sq[:, 0:2], o3[:, 0:2], o3[:, 0:2], ALU.mult))
                    link(V.tensor_reduce(ss12[:, 0, 0:8], sq[:, 0:2].rearrange("p a h d -> p (a h) d"), AX.X, ALU.add))
                    dve.wait_ge(S("g_delta"), 1)
                    link(V.tensor_tensor(Sgdn[:], Sgdn[:], qa[0:HD, EGE, ds(t, 1), :].rearrange("p a h -> p (a h)").unsqueeze(2).to_broadcast([HD, H, HD]), ALU.mult))
                    dve.wait_ge(S("g_intra"), 1)
                    link(V.tensor_tensor(o3[:, 2], o3[:, 2], bank64(3), ALU.add))
                    link(V.tensor_tensor(sq[:, 2], o3[:, 2], o3[:, 2], ALU.mult))
                    link(V.tensor_reduce(ss12[:, 0, 8:12], sq[:, 2], AX.X, ALU.add))
                    link(V.tensor_scalar(ss12[:, 0, :], ss12[:, 0, :], 1.0 / HD, EPS, ALU.mult, ALU.add), S("squares"))
                    dve.wait_ge(S("g_dstate"), 1)
                    link(V.tensor_tensor(Sgdn[:], Sgdn[:], bank64(6, HD, HD), ALU.add))
                    dve.wait_ge(S("r_all"), 1)
                    o12 = o3[:].rearrange("p a h d -> p (a h) d")
                    link(V.tensor_tensor(y[:], o12, bc(ss12[:, 1, :], 12, [P, 12, HD]), ALU.mult))
                    link(V.tensor_tensor(y[:].rearrange("p a d -> p (a d)"), y[:].rearrange("p a d -> p (a d)"),
                                         gain[:, ds(t, 1)].rearrange("p a j n -> p (a j n)"), ALU.mult), S("y_ready"))
                    dve.wait_ge(S("xtanh"), 1)
                    xn = xc[:, nxt, :].rearrange("p a n -> p (a n)")
                    link(V.scalar_tensor_tensor(xn, xn, 1.0, zs[:, 0, :], ALU.add, ALU.mult))
            kit.clear()

        with nc.Block() as b:
            @b.sync
            def _(sp):
                st = Loads(sp, S("st"))
                st(io["p_ret"][ds(l, 1), 0].rearrange("a h d e -> d (a h) e"), Sret[:])
                st(io["p_C"][ds(l, 1), 0].rearrange("a h d e -> d (a h) e"), Caug[:, :, 0:HD])
                st(io["p_n"][ds(l, 1), 0].rearrange("a h (d o) -> d (a h) o", o=1), Caug[:, :, HD:HD + 1], slow=True)
                st(io["p_gdn"][ds(l, 1), 0].rearrange("a h d e -> d (a h) e"), Sgdn[:])
                st(io["p_m"][ds(l, 1), 0], mprev[0:1, :])
                st.all_in()
        kit.clear()


def copy_states(kit, io, z, l, sp):
    st = Loads(sp, kit.sem("states_copied"))
    p0, s0 = PADROWS, PADROWS + SEQ
    st(io["p_nsa"][ds(l, 1), 0].rearrange("a t r d -> (a t) (r d)"), z[p0:p0 + SEQ, NKV:NKV + 256])
    st(io["p_swa"][ds(l, 1), 0].rearrange("a t r d -> (a t) (r d)"), z[p0 + SEQ - WIN:p0 + SEQ, NKV + 256:NKV + 384])
    st(io["p_gconv"][ds(l, 1), 0].rearrange("a r n -> (a r) n"), z[p0 + SEQ - 3:p0 + SEQ, GX:GX + 768])
    st(io["s_nsa"][ds(l, 1), :, 0].rearrange("a b r d -> (a b) (r d)"), z[s0:s0 + NB, NKV:NKV + 256])
    st(io["s_swa"][ds(l, 1), :, WIN - 1].rearrange("a b r d -> (a b) (r d)"), z[s0:s0 + NB, NKV + 256:NKV + 384])
    st(io["s_swa"][ds(l, 1), :, 0:WIN - 1].rearrange("a b t r d -> (a b) (t r d)"),
       io["cache_swa_kv"][ds(l, 1), :, 1:WIN].rearrange("a b t r d -> (a b) (t r d)"))
    st(io["s_gconv"][ds(l, 1), :, 2].rearrange("a b n -> (a b) n"), z[s0:s0 + NB, GX:GX + 768])
    st(io["s_gconv"][ds(l, 1), :, 0:2], io["state_gdn_conv"][ds(l, 1), :, 1:3])
    st.all_in()


def sample_heads(ld, io, z, dst, a, groups, pitch=256):
    s0 = PADROWS + SEQ
    for h in range(H):
        src = z[s0:s0 + NB, a + h * HD:a + h * HD + pitch * (groups - 1) + HD] if groups == 1 else \
            z[s0:s0 + NB, a:a + pitch * groups].rearrange("b (g n) -> b g n", n=pitch)[:, :, h * HD:h * HD + HD]
        ld(dst[h * NB:h * NB + NB], src)


class SampleData:

    def __init__(self, nc, ctx):
        def sb(name, shape):
            return ctx.enter_context(nc.sbuf_tensor(name, shape, F32))
        R = H * NB
        self.rz = sb("d_rz", [R, 4, HD])
        self.mz = sb("d_mz", [R, 3, HD])
        self.mo = sb("d_mo", [R, HD])
        self.taps = sb("d_taps", [R, 4, 3, HD])
        self.cw = sb("d_cw", [R, 4, 3, HD])
        self.gg = sb("d_gg", [R, HD])
        self.sc = sb("d_sc", [R, 4])
        self.par = sb("d_par", [R, 4])
        self.gains = sb("d_gains", [R, 3, HD])
        self.rope = sb("d_rope", [R, HD])
        self.dec = sb("d_dec", [R, 1])
        self.nst = sb("d_n", [R, HD])
        self.mst = sb("d_m", [R, 1])

    def load(self, io, z, l, ld):
        rz, mz, mo, taps, cw, gg, sc, par = self.rz, self.mz, self.mo, self.taps, self.cw, self.gg, self.sc, self.par
        gains, rope, dec, nst, mst = self.gains, self.rope, self.dec, self.nst, self.mst
        R = H * NB
        s0 = PADROWS + SEQ
        sample_heads(ld, io, z, rz, RQ, 4)
        sample_heads(ld, io, z, mz, MQ, 3)
        sample_heads(ld, io, z, mo, MO, 1)
        sample_heads(ld, io, z, taps[:, 3], GX, 3)
        sample_heads(ld, io, z, gg, GG, 1)
        for h in range(H):
            hb = slice(h * NB, h * NB + NB)
            for j, a in enumerate((MI, MF, GA, GB)):
                ld(sc[hb, j:j + 1], z[s0:s0 + NB, a + h:a + h + 1], slow=True)
            for j, name in enumerate(("mlstm_b_i", "mlstm_b_f", "gdn_dt_bias", "gdn_A_log")):
                ld(par[hb, j:j + 1], io[name][ds(l, 1), h:h + 1].rearrange("a n -> (a n)").partition_broadcast(NB))
            for j, name in enumerate(("ret_norm", "mlstm_norm", "gdn_norm")):
                ld(gains[hb, j], io[name][ds(l, 1), h * HD:h * HD + HD].rearrange("a n -> (a n)").partition_broadcast(NB))
            ld(cw[hb].rearrange("p j g n -> p (j g) n"), io["gdn_conv_w"][ds(l, 1)]
               .rearrange("a j (g n) -> (a j g) n", g=3)[:, h * HD:h * HD + HD].partition_broadcast(NB))
            ld(taps[hb, 0:3].rearrange("p j g n -> p (j g) n"), io["state_gdn_conv"][ds(l, 1)]
               .rearrange("a b j (g n) -> (a b) (j g) n", g=3)[:, :, h * HD:h * HD + HD])
            ld(nst[hb], io["state_mlstm_n"][ds(l, 1), :, h].rearrange("a b d -> (a b) d"))
            ld(mst[hb], io["state_mlstm_m"][ds(l, 1), :, h:h + 1].rearrange("a b d -> (a b) d"), slow=True)
        ld(rope[:], io["c_rope"][SEQ:SEQ + 1, :].rearrange("a n -> (a n)").partition_broadcast(R))
        ld(dec[:], io["c_dec"])


def recurrent_sample(kit, env, io, l, data):
    nc, S, mhalf = kit.nc, kit.sem, env["mhalf"]
    z, y_mix = env["z"], env["y_mix"]
    V, A = nc.vector, nc.scalar
    R = H * NB
    rz, mz, mo, taps, cw, gg, sc, par = data.rz, data.mz, data.mo, data.taps, data.cw, data.gg, data.sc, data.par
    gains, rope, dec, nst, mst = data.gains, data.rope, data.dec, data.nst, data.mst
    with ExitStack() as c:
        def sb(name, shape):
            return c.enter_context(nc.sbuf_tensor(name, shape, F32))
        st3 = [sb(f"d_st{j}", [R, HD, HD]) for j in range(3)]
        tmp = sb("d_tmp", [R, HD, HD])
        q = sb("d_q", [R, HD])
        k = sb("d_k", [R, HD])
        xc = sb("d_xc", [R, 3, HD])
        xe = sb("d_xe", [R, 3, HD])
        sg = sb("d_sg", [R, 3, HD])
        t4 = sb("d_t4", [R, 4, HD])
        o = sb("d_o", [R, HD])
        col = sb("d_col", [R, 24])
        y = sb("d_y", [R, 3, HD])

        with nc.Block() as b:
            LFC, ABS, MN, E1, MT, WI, GI, EM, DEN, SS, RR, GD, BT, EGD, SS2, RR2, EA, IP = range(18)

            def cc(i, n=1):
                return col[:, i:i + n]

            @b.sync
            def _(sp):
                for j, name in enumerate(("state_ret", "state_mlstm_C", "state_gdn")):
                    ld = Loads(sp, S(f"state{j}_in"))
                    for h in range(H):
                        ld(st3[j][h * NB:h * NB + NB], io[name][ds(l, 1), :, h].rearrange("a b d e -> (a b) d e"))
                copy_states(kit, io, z, l, sp)

            @b.gpsimd
            def _(pool):
                for j, (src, dst, n) in enumerate(((SS, RR, 1), (SS, RR, 1), (18, 20, 2), (SS, RR, 1))):
                    pool.wait_ge(S("squares"), j + 1)
                    nc.gpsimd.tensor_tensor(cc(dst, n), cc(src, n), mhalf[0:R, 0:n], ALU.pow).then_inc(S("r_ready"), 1)

            @b.scalar
            def _(act):
                link = Link(act, S("a"))
                for j, src in enumerate((rz[:, 3, :], mo[:], gg[:])):
                    link(A.activation(sg[:, j], src, ACT.Exp, scale=-1.0))
                link(A.activation(cc(EA), par[:, 3:4], ACT.Exp))
                link(A.activation(cc(BT), sc[:, 3:4], ACT.Exp, scale=-1.0), S("sig_exp"))
                act.wait_ge(S("abs"), 1)
                link(A.activation(cc(E1), cc(ABS), ACT.Exp, scale=-1.0))
                link(A.activation(cc(E1), cc(E1), ACT.Ln, bias=1.0), S("softplus"))
                act.wait_ge(S("mt"), 1)
                link(A.activation(cc(WI), cc(WI), ACT.Exp))
                link(A.activation(cc(GI), cc(GI), ACT.Exp))
                link(A.activation(cc(EM), cc(MT), ACT.Exp, scale=-1.0), S("mexp"))
                act.wait_ge(S("conved"), 1)
                link(A.activation(xe[:], xc[:], ACT.Exp, scale=-1.0), S("silu_exp"))
                act.wait_ge(S("abs"), 2)
                link(A.activation(cc(E1), cc(ABS), ACT.Exp, scale=-1.0))
                link(A.activation(cc(E1), cc(E1), ACT.Ln, bias=1.0), S("softplus"))
                act.wait_ge(S("gd"), 1)
                link(A.activation(cc(EGD), cc(GD), ACT.Exp), S("gexp"))

            @b.vector
            def _(dve):
                link = Link(dve, S("v"))

                def outer(kk, vv):
                    link(V.tensor_tensor(tmp[:], kk.unsqueeze(2).to_broadcast([R, HD, HD]),
                                         vv.unsqueeze(1).to_broadcast([R, HD, HD]), ALU.mult))

                def dot(out, vec, st):
                    link(V.tensor_tensor(tmp[:], st[:], vec.unsqueeze(2).to_broadcast([R, HD, HD]), ALU.mult))
                    link(V.tensor_reduce(out, tmp[:].rearrange("p d e -> p e d"), AX.X, ALU.add))

                def head_norm(j, gate, n):
                    link(V.tensor_tensor_reduce(t4[:, 0], o[:], o[:], 1.0, 0.0, ALU.mult, ALU.add, cc(SS)))
                    link(V.tensor_scalar(cc(SS), cc(SS), 1.0 / HD, EPS, ALU.mult, ALU.add), S("squares"))
                    dve.wait_ge(S("r_ready"), n)
                    link(V.scalar_tensor_tensor(y[:, j], o[:], cc(RR), gains[:, j], ALU.mult, ALU.mult))
                    if gate is not None:
                        link(V.tensor_tensor(y[:, j], y[:, j], gate, ALU.mult))

                dve.wait_ge(S("sig_exp"), 1)
                link(V.tensor_scalar(sg[:], sg[:], 1.0, None, ALU.add))
                link(V.reciprocal(sg[:], sg[:]))
                link(V.tensor_tensor(sg[:, 0], sg[:, 0], rz[:, 3], ALU.mult))
                link(V.tensor_tensor(sg[:, 2], sg[:, 2], gg[:], ALU.mult))
                link(V.tensor_scalar(cc(BT), cc(BT), 1.0, None, ALU.add))
                link(V.reciprocal(cc(BT), cc(BT)))
                lo, hi = slice(0, 32), slice(32, 64)
                for j, out in ((0, q), (1, k)):
                    link(V.tensor_tensor(t4[:, 0, 0:32], rz[:, j, lo], rope[:, lo], ALU.mult))
                    link(V.tensor_tensor(t4[:, 1, 0:32], rz[:, j, hi], rope[:, hi], ALU.mult))
                    link(V.tensor_tensor(out[:, lo], t4[:, 0, 0:32], t4[:, 1, 0:32], ALU.subtract))
                    link(V.tensor_tensor(t4[:, 0, 0:32], rz[:, j, lo], rope[:, hi], ALU.mult))
                    link(V.tensor_tensor(t4[:, 1, 0:32], rz[:, j, hi], rope[:, lo], ALU.mult))
                    link(V.tensor_tensor(out[:, hi], t4[:, 0, 0:32], t4[:, 1, 0:32], ALU.add))
                link(V.tensor_scalar(k[:], k[:], 0.125, None, ALU.mult))
                outer(k[:], rz[:, 2])
                dve.wait_ge(S("state0_in"), 16 * H)
                link(V.scalar_tensor_tensor(st3[0][:], st3[0][:], dec[:, 0:1], tmp[:], ALU.mult, ALU.add))
                dot(o[:], q[:], st3[0])
                head_norm(0, sg[:, 0], 1)
                link(V.tensor_tensor(cc(LFC), sc[:, 1:2], par[:, 1:2], ALU.add))
                link(V.tensor_tensor(cc(IP), sc[:, 0:1], par[:, 0:1], ALU.add))
                link(V.tensor_scalar(cc(MN), cc(LFC), 0.0, None, ALU.min))
                link(V.scalar_tensor_tensor(cc(ABS), cc(LFC), -1.0, cc(LFC), ALU.mult, ALU.max), S("abs"))
                dve.wait_ge(S("softplus"), 1)
                link(V.tensor_tensor(cc(LFC), cc(MN), cc(E1), ALU.subtract))
                link(V.tensor_tensor(cc(LFC), cc(LFC), mst[:], ALU.add))
                link(V.tensor_tensor(cc(MT), cc(LFC), cc(IP), ALU.max))
                link(V.tensor_tensor(cc(WI), cc(IP), cc(MT), ALU.subtract))
                link(V.tensor_tensor(cc(GI), cc(LFC), cc(MT), ALU.subtract), S("mt"))
                dve.wait_ge(S("mexp"), 1)
                link(V.tensor_scalar(k[:], mz[:, 1], cc(WI), 0.125, ALU.mult, ALU.mult))
                outer(k[:], mz[:, 2])
                dve.wait_ge(S("state1_in"), 16 * H)
                link(V.scalar_tensor_tensor(st3[1][:], st3[1][:], cc(GI), tmp[:], ALU.mult, ALU.add))
                link(V.scalar_tensor_tensor(nst[:], nst[:], cc(GI), k[:], ALU.mult, ALU.add))
                dot(o[:], mz[:, 0], st3[1])
                link(V.tensor_tensor_reduce(t4[:, 0], mz[:, 0], nst[:], 1.0, 0.0, ALU.mult, ALU.add, cc(DEN)))
                link(V.scalar_tensor_tensor(cc(DEN), cc(DEN), -1.0, cc(DEN), ALU.mult, ALU.max))
                link(V.tensor_tensor(cc(DEN), cc(DEN), cc(EM), ALU.max))
                link(V.reciprocal(cc(DEN), cc(DEN)))
                link(V.scalar_tensor_tensor(o[:], o[:], cc(DEN), sg[:, 1], ALU.mult, ALU.mult))
                head_norm(1, None, 2)
                link(V.tensor_tensor(taps[:], taps[:], cw[:], ALU.mult))
                link(V.tensor_tensor(taps[:, 0], taps[:, 0], taps[:, 1], ALU.add))
                link(V.tensor_tensor(taps[:, 2], taps[:, 2], taps[:, 3], ALU.add))
                link(V.tensor_tensor(xc[:], taps[:, 0], taps[:, 2], ALU.add), S("conved"))
                link(V.tensor_tensor(cc(GD), sc[:, 2:3], par[:, 2:3], ALU.add))
                link(V.tensor_scalar(cc(MN), cc(GD), 0.0, None, ALU.max))
                link(V.scalar_tensor_tensor(cc(ABS), cc(GD), -1.0, cc(GD), ALU.mult, ALU.max), S("abs"))
                dve.wait_ge(S("silu_exp"), 1)
                link(V.tensor_scalar(xe[:], xe[:], 1.0, None, ALU.add))
                link(V.reciprocal(xe[:], xe[:]))
                link(V.tensor_tensor(xc[:], xc[:], xe[:], ALU.mult))
                for j in range(2):
                    link(V.tensor_tensor_reduce(t4[:, 0], xc[:, j], xc[:, j], 1.0, 0.0, ALU.mult, ALU.add, cc(18 + j)))
                link(V.tensor_scalar(cc(18, 2), cc(18, 2), EPS, None, ALU.add), S("squares"))
                dve.wait_ge(S("softplus"), 2)
                link(V.tensor_tensor(cc(GD), cc(MN), cc(E1), ALU.add))
                link(V.scalar_tensor_tensor(cc(GD), cc(GD), -1.0, cc(EA), ALU.mult, ALU.mult), S("gd"))
                dve.wait_ge(S("r_ready"), 3)
                link(V.tensor_scalar(q[:], xc[:, 0], cc(20), 0.125, ALU.mult, ALU.mult))
                link(V.tensor_scalar(k[:], xc[:, 1], cc(21), None, ALU.mult))
                dve.wait_ge(S("gexp"), 1)
                dve.wait_ge(S("state2_in"), 16 * H)
                link(V.tensor_scalar(st3[2][:], st3[2][:], cc(EGD), None, ALU.mult))
                dot(o[:], k[:], st3[2])
                link(V.tensor_tensor(o[:], xc[:, 2], o[:], ALU.subtract))
                link(V.tensor_scalar(o[:], o[:], cc(BT), None, ALU.mult))
                outer(k[:], o[:])
                link(V.tensor_tensor(st3[2][:], st3[2][:], tmp[:], ALU.add))
                dot(o[:], q[:], st3[2])
                head_norm(2, sg[:, 2], 4)
        kit.clear()

        with nc.Block() as b:
            @b.sync
            def _(sp):
                st = Loads(sp, S("st"))
                for h in range(H):
                    hb = slice(h * NB, h * NB + NB)
                    for j, name in enumerate(("s_ret", "s_C", "s_gdn")):
                        st(io[name][ds(l, 1), :, h].rearrange("a b d e -> (a b) d e"), st3[j][hb])
                    st(io["s_n"][ds(l, 1), :, h].rearrange("a b d -> (a b) d"), nst[hb])
                    st(io["s_m"][ds(l, 1), :, h:h + 1].rearrange("a b d -> (a b) d"), col[hb, 4:5], slow=True)
                    st(y_mix[SEQ:TOK, 0:768].rearrange("b (j n) -> b j n", j=3)[:, :, h * HD:h * HD + HD], y[hb])
                st.all_in()
        kit.clear()


TL = 1152
WL = 768
TWC = TL + WL


def bias_tables(kit, env, io):
    nc, S, ps = kit.nc, kit.sem, env["ps"]
    V, A = nc.vector, nc.scalar
    with ExitStack() as c:
        def sb(name, shape):
            return c.enter_context(nc.sbuf_tensor(name, shape, F32))
        rel = sb("b_rel", [33, H])
        relb = sb("b_relb", [33, H, P])
        oneh = sb("b_oneh", [33, TWC])
        rows_sb = sb("b_rows", [P, H, TWC])
        with nc.Block() as b:
            @b.sync
            def _(sp):
                ld = Loads(sp, S("ld"))
                ld(rel[0:32, :], io["rel_bias"])
                ld(oneh[:], io["c_onehot"])
                sp.wait_ge(S("rows_ready"), H)
                ld(env["wdist"].rearrange("h p n -> p h n"), rows_sb[:])
                ld.all_in()

            @b.vector
            def _(dve):
                link = Link(dve, S("v"))
                link(V.memset(relb[:], 1.0))
                dve.wait_ge(S("ld"), 32)
                link(V.tensor_copy(relb[0:32], bc(rel[0:32, :], H, [32, H, P])), S("rel_ready"))
                for h in range(H):
                    dve.wait_ge(S("looked_up"), h + 1)
                    link(V.tensor_copy(rows_sb[:, h, :].rearrange("p (a n) -> p a n", a=4), ps[:, 0:4, 0:TWC // 4]), S("rows_ready"))

            @b.tensor
            def _(pe):
                pe.wait_ge(S("rel_ready"), 1)
                for h in range(H):
                    if h:
                        pe.wait_ge(S("rows_ready"), h)
                    for a in range(4):
                        m = nc.tensor.matmul(ps[:, a, 0:TWC // 4], relb[:, h, :], oneh[:, a * (TWC // 4):(a + 1) * (TWC // 4)],
                                             start=True, stop=True)
                    m.then_inc(S("looked_up"), 1)
        kit.clear()


def compress_weights(kit, env, io, l, wb, peadd, c):
    nc, S, ps, ident = kit.nc, kit.sem, env["ps"], env["ident"]
    V, A = nc.vector, nc.scalar
    with ExitStack() as c2:
        pe_in = c2.enter_context(nc.sbuf_tensor("cw_pe", [32, P], F32))
        peT = c2.enter_context(nc.sbuf_tensor("cw_peT", [P, 32], F32))
        with nc.Block() as b:
            @b.sync
            def _(sp):
                ld = Loads(sp, S("pe_in"))
                ld(pe_in[:], io["nsa_cmp_pe"][ds(l, 1)].rearrange("a j c d -> (a j) (c d)"))
                ld.all_in()
                ld2 = Loads(sp, S("wb_in"))
                sp.wait_ge(S("wb_zero"), 1)
                for cc in range(2):
                    ld2(wb[cc * HD:cc * HD + HD, :, cc * HD:cc * HD + HD],
                        io["nsa_cmp_w"][ds(l, 1), cc].rearrange("a j d e -> d (a j) e"))
                ld2.all_in()

            @b.vector
            def _(dve):
                V.memset(wb[:], 0.0).then_inc(S("wb_zero"), 1)
                dve.wait_ge(S("turned"), 1)
                V.tensor_copy(peT[:], ps[:, 0, 0:32]).then_inc(S("peT"), 1)
                dve.wait_ge(S("pe_summed"), 1)
                V.tensor_copy(peadd[:], ps[:, 1, 0:1]).then_inc(S("v"), 1)

            @b.tensor
            def _(pe):
                pe.wait_ge(S("pe_in"), 16)
                nc.tensor.transpose(ps[:, 0, 0:32], pe_in[:], ident[0:32, 0:32]).then_inc(S("turned"), 1)
                pe.wait_ge(S("peT"), 1)
                pe.wait_ge(S("wb_in"), 32)
                for j in range(32):
                    m = nc.tensor.matmul(ps[:, 1, 0:1], wb[:, j, :], peT[:, j:j + 1], start=(j == 0), stop=(j == 31))
                m.then_inc(S("pe_summed"), 1)
        kit.clear()


def nsa_prompt(kit, env, io, l, wb, peadd):
    nc, S, ps, ident = kit.nc, kit.sem, env["ps"], env["ident"]
    z, y_mix = env["z"], env["y_mix"]
    V, A = nc.vector, nc.scalar
    NC = SEQ // 16 - 1
    WT = WIN // P
    with ExitStack() as c:
        def sb(name, shape):
            return c.enter_context(nc.sbuf_tensor(name, shape, F32))
        kTs = sb("p_kTs", [HD, SEQ])
        kTw = sb("p_kTw", [HD, SEQ])
        qT = sb("p_qT", [HD, H, SEQ])
        kc = sb("p_kc", [P, 64])
        vc = sb("p_vc", [64, HD])
        zk = sb("p_zk", [P, NT, 384])
        ng = sb("p_ng", [P, NT, H, 3])
        T = sb("p_T", [P, H, SEQ])
        TW = sb("p_TW", [P, H, WIN + P])
        valid = sb("p_valid", [P, NT])
        y = sb("p_y", [P, 2, 256])
        with ExitStack() as c2:
            zq = c2.enter_context(nc.sbuf_tensor("p_zq", [P, NT, 256], F32))
            cT = c2.enter_context(nc.sbuf_tensor("p_cT", [P, SEQ], F32))
            with nc.Block() as b:
                @b.sync
                def _(sp):
                    ld = Loads(sp, S("ld"))
                    zr = z[PADROWS:PADROWS + SEQ, :]
                    ld(zk[:], zr[:, NKV:NKV + 384].rearrange("(t p) n -> p t n", p=P))
                    ld(zq[:], zr[:, NQ:NQ + 256].rearrange("(t p) n -> p t n", p=P))
                    ld2 = Loads(sp, S("ld2"))
                    ld2(ng[:].rearrange("p t h b -> p t (h b)"), zr[:, NG:NG + 12].rearrange("(t p) n -> p t n", p=P))
                    wt = env["wdist"].tensor
                    for h in range(H):
                        base = h * P * TWC + P - 1
                        ld2(T[:, h, :], bass.AP(wt, base, [[TWC - 1, P], [1, SEQ]]))
                        ld2(TW[:, h, :], bass.AP(wt, base + TL, [[TWC - 1, P], [1, WIN + P]]))
                    ld2(valid[:], io["c_valid"])
                    ld2.all_in()

                @b.tensor
                def _(pe):
                    pe.wait_ge(S("ld"), 32)
                    g = 0
                    for kind in range(3 + H):
                        for half in range(2):
                            if g >= 4:
                                pe.wait_ge(S("even" if g % 2 == 0 else "odd"), (g - 4) // 2 + 1)
                            for i in range(4):
                                t = 4 * half + i
                                if kind == 0:
                                    m = nc.tensor.transpose(ps[:, g % 4, i * P:i * P + P], zk[:, t, 0:P], ident[:])
                                else:
                                    src = zk[:, t, P:P + HD] if kind == 1 else zk[:, t, 256:256 + HD] if kind == 2 else \
                                        zq[:, t, (kind - 3) * HD:(kind - 2) * HD]
                                    m = nc.tensor.transpose(ps[0:HD, g % 4, i * P:i * P + P], src, ident[:])
                            m.then_inc(S("turned"), 1)
                            g += 1
                    pe.wait_ge(S("even"), 1)
                    pe.wait_ge(S("odd"), 1)
                    for j in range(32):
                        m = nc.tensor.matmul(ps[:, 4, 0:NC], wb[:, j, :], cT[:, j:j + 16 * (NC - 1) + 1:16],
                                             start=(j == 0), stop=(j == 31))
                    m.then_inc(S("compressed"), 1)
                    pe.wait_ge(S("kc"), 1)
                    nc.tensor.transpose(ps[0:64, 5, 0:P], kc[:], ident[:]).then_inc(S("vc_turned"), 1)

                def dests():
                    out = []
                    for kind in range(3 + H):
                        for half in range(2):
                            cols = slice(512 * half, 512 * half + 512)
                            out.append((cT[:, cols], P) if kind == 0 else (kTs[:, cols], HD) if kind == 1 else
                                       (kTw[:, cols], HD) if kind == 2 else (qT[:, kind - 3, cols], HD))
                    return out

                @b.scalar
                def _(act):
                    for g, (dst, n) in enumerate(dests()):
                        if g % 2 == 0:
                            act.wait_ge(S("turned"), g + 1)
                            A.activation(dst, ps[0:n, g % 4, :], ACT.Copy, scale=0.125 if g >= 6 else 1.0).then_inc(S("even"), 1)
                    act.wait_ge(S("ld2"), 16 * 10)
                    A.activation(ng[:], ng[:], ACT.Exp, scale=-1.0).then_inc(S("gexp"), 1)

                @b.vector
                def _(dve):
                    link = Link(dve, S("v"))
                    link(V.memset(kc[:], 0.0))
                    for g, (dst, n) in enumerate(dests()):
                        if g % 2 == 1:
                            dve.wait_ge(S("turned"), g + 1)
                            V.tensor_scalar(dst, ps[0:n, g % 4, :], 0.125 if g >= 6 else 1.0, None, ALU.mult).then_inc(S("odd"), 1)
                    dve.wait_ge(S("gexp"), 1)
                    link(V.tensor_scalar(ng[:], ng[:], 1.0, None, ALU.add))
                    link(V.reciprocal(ng[:], ng[:]))
                    dve.wait_ge(S("compressed"), 1)
                    link(V.tensor_scalar(kc[:, 0:NC], ps[:, 4, 0:NC], peadd[:, 0:1], None, ALU.add), S("kc"))
                    dve.wait_ge(S("vc_turned"), 1)
                    link(V.tensor_copy(vc[:], ps[0:64, 5, HD:P]))
            kit.clear()

        CW, CC = SEQ, SEQ + 640
        s = sb("p_s", [P, 2, CC + 64])
        pT = sb("p_pT", [P, 2, 14, P])
        stat = sb("p_stat", [P, 2, 4, 3])
        bits = sb("p_bits", [P, HD])
        for t in range(NT):
            nk = (t + 1) * P
            w0 = max(0, t - WT) * P
            nw = nk - w0
            ncm = 8 * t + 7
            blocks = [(1, i * P, P, zk[:, i, 192:256]) for i in range(t + 1)]
            blocks += [(2, CW + i * P, P, zk[:, w0 // P + i, 320:384]) for i in range(nw // P)]
            blocks += [(0, CC, ncm, vc[0:ncm, :])]
            groups = [blocks[i:i + 4] for i in range(0, len(blocks), 4)]
            NGr = len(groups)

            def turn_wait(eng, g):
                eng.wait_ge(S("even" if g % 2 == 0 else "odd"), g // 2 + 1)

            def copy_group(op, h, gi, grp, g, name):
                k = len(grp)
                whole = k if grp[-1][0] != 0 else k - 1
                m = None
                if whole:
                    m = op(pT[:, h % 2, 4 * gi:4 * gi + whole, :].rearrange("p a n -> p (a n)"), ps[:, 4 + g % 2, 0:whole * P])
                if whole < k:
                    n = grp[-1][2]
                    m = op(pT[0:n, h % 2, 4 * gi + whole, :], ps[0:n, 4 + g % 2, whole * P:k * P])
                m.then_inc(S(name), 1)

            with nc.Block(no_gpsimd_drain=True) as b:
                @b.tensor
                def _(pe):
                    def scores(h):
                        if h:
                            pe.wait_ge(S("biased"), h)
                        q = qT[:, h, t * P:t * P + P]
                        for n0 in range(0, nk, 512):
                            n = min(512, nk - n0)
                            nc.tensor.matmul(ps[:, n0 // 512, 0:n], q, kTs[:, n0:n0 + n], start=True, stop=True)
                        n = min(512, nw)
                        nc.tensor.matmul(ps[:, 2, 0:n], q, kTw[:, w0:w0 + n], start=True, stop=True)
                        if nw > 512:
                            nc.tensor.matmul(ps[:, 3, 0:P], q, kTw[:, w0 + 512:w0 + nw], start=True, stop=True)
                        nc.tensor.matmul(ps[:, 3, P:P + ncm], q, kc[0:HD, 0:ncm], start=True, stop=True).then_inc(S("scored"), 1)

                    scores(0)
                    for h in range(H):
                        if h + 1 < H:
                            scores(h + 1)
                        pe.wait_ge(S("exped"), h + 1)
                        for gi, grp in enumerate(groups):
                            g = h * NGr + gi
                            if g >= 2:
                                turn_wait(pe, g - 2)
                            for i, (br, col, n, v) in enumerate(grp):
                                m = nc.tensor.transpose(ps[0:n, 4 + g % 2, i * P:i * P + P], s[:, h % 2, col:col + n], ident[:])
                            m.then_inc(S("turned"), 1)
                        for g in (h * NGr + NGr - 2, h * NGr + NGr - 1):
                            if g >= 0:
                                turn_wait(pe, g)
                        if h >= 2:
                            pe.wait_ge(S("combined"), h - 1)
                        first = set()
                        for bi, (br, col, n, v) in enumerate(blocks):
                            lastb = bi + 1 == len(blocks) or blocks[bi + 1][0] != br
                            m = nc.tensor.matmul(ps[:, 6 + h % 2, br * HD:br * HD + HD], pT[0:n, h % 2, bi, :], v,
                                                 start=br not in first, stop=lastb)
                            first.add(br)
                        m.then_inc(S("pv"), 1)

                @b.vector
                def _(dve):
                    link = Link(dve, S("v"))

                    def biases(h):
                        dve.wait_ge(S("scored"), h + 1)
                        if h >= 2:
                            dve.wait_ge(S("turned"), (h - 1) * NGr)
                        sp_, hp = s[:, h % 2], h % 2
                        off = SEQ - nk
                        for n0 in range(0, nk, 512):
                            n = min(512, nk - n0)
                            link(V.tensor_tensor(sp_[:, n0:n0 + n], ps[:, n0 // 512, 0:n], T[:, h, off + n0:off + n0 + n], ALU.add))
                        wo = WIN + P - nw
                        n = min(512, nw)
                        link(V.tensor_tensor(sp_[:, CW:CW + n], ps[:, 2, 0:n], TW[:, h, wo:wo + n], ALU.add))
                        if nw > 512:
                            link(V.tensor_tensor(sp_[:, CW + 512:CW + nw], ps[:, 3, 0:P], TW[:, h, 512:512 + P], ALU.add))
                        co = 927 - P * t
                        link(V.tensor_tensor(sp_[:, CC:CC + ncm], ps[:, 3, P:P + ncm], T[:, h, co:co + 16 * (ncm - 1) + 1:16], ALU.add), S("biased"))
                        for br, (a, n) in enumerate(((CC, ncm), (0, nk), (CW, nw))):
                            link(V.tensor_reduce(stat[:, hp, 0, br:br + 1], sp_[:, a:a + n], AX.X, ALU.max, negate=True), S("maxed") if br == 2 else None)

                    def copies(h):
                        if h >= 2:
                            dve.wait_ge(S("pv"), h - 1)
                        for gi, grp in enumerate(groups):
                            g = h * NGr + gi
                            if g % 2 == 1:
                                dve.wait_ge(S("turned"), g + 1)
                                copy_group(nc.vector.tensor_copy, h, gi, grp, g, "odd")

                    def combine(h):
                        hp = h % 2
                        dve.wait_ge(S("exped"), h + 1)
                        link(V.reciprocal(stat[:, hp, 2, :], stat[:, hp, 1, :]))
                        link(V.tensor_tensor(stat[:, hp, 3, :], stat[:, hp, 2, :], ng[:, t, h, :], ALU.mult))
                        link(V.tensor_tensor(stat[:, hp, 3, 0:1], stat[:, hp, 3, 0:1], valid[:, t:t + 1], ALU.mult))
                        dve.wait_ge(S("pv"), h + 1)
                        yh = y[:, t % 2, h * HD:h * HD + HD]
                        link(V.tensor_scalar(yh, ps[:, 6 + hp, 0:HD], stat[:, hp, 3, 0:1], None, ALU.mult))
                        link(V.scalar_tensor_tensor(yh, ps[:, 6 + hp, HD:2 * HD], stat[:, hp, 3, 1:2], yh, ALU.mult, ALU.add))
                        link(V.scalar_tensor_tensor(yh, ps[:, 6 + hp, 2 * HD:3 * HD], stat[:, hp, 3, 2:3], yh, ALU.mult, ALU.add), S("combined"))

                    biases(0)
                    for h in range(H):
                        if h + 1 < H:
                            biases(h + 1)
                        copies(h)
                        combine(h)

                @b.scalar
                def _(act):
                    def exps(h):
                        act.wait_ge(S("maxed"), h + 1)
                        hp = h % 2
                        if h >= 2:
                            act.wait_ge(S("combined"), h - 1)
                        for br, (a, n) in enumerate(((CC, ncm), (0, nk), (CW, nw))):
                            m = A.activation(s[:, hp, a:a + n], s[:, hp, a:a + n], ACT.Exp, bias=stat[:, hp, 0, br:br + 1],
                                             accum_out=stat[:, hp, 1, br:br + 1])
                        m.then_inc(S("exped"), 1)

                    exps(0)
                    for h in range(H):
                        if h + 1 < H:
                            exps(h + 1)
                        if h >= 2:
                            act.wait_ge(S("pv"), h - 1)
                        for gi, grp in enumerate(groups):
                            g = h * NGr + gi
                            if g % 2 == 0:
                                act.wait_ge(S("turned"), g + 1)
                                copy_group(lambda o_, i_: A.activation(o_, i_, ACT.Copy), h, gi, grp, g, "even")

                @b.sync
                def _(sp):
                    sp.wait_ge(S("combined"), H)
                    st = Loads(sp, S("st"))
                    st(y_mix[t * P:t * P + P, 768:1024], y[:, t % 2, :])
                    st.all_in()
            kit.clear()


def nsa(kit, env, io, l):
    nc = kit.nc
    with ExitStack() as c:
        wb = c.enter_context(nc.sbuf_tensor("c_wb", [P, 32, P], F32))
        peadd = c.enter_context(nc.sbuf_tensor("c_peadd", [P, 1], F32))
        compress_weights(kit, env, io, l, wb, peadd, c)
        nsa_prompt(kit, env, io, l, wb, peadd)
        if NSA_SAMPLE:
            nsa_sample(kit, env, io, l, wb, peadd)


NSA_SAMPLE = True


SL, SCM, SWN, SNW = 0, PAST, PAST + 256, PAST + 256 + WIN
NDEC = SNW + 8


def nsa_sample(kit, env, io, l, wb, peadd):
    nc, S, ps, ident = kit.nc, kit.sem, env["ps"], env["ident"]
    z, y_mix = env["z"], env["y_mix"]
    V, A = nc.vector, nc.scalar
    R = H * NB
    s0 = PADROWS + SEQ
    G4 = 4
    NCH = PAGES // G4
    with ExitStack() as c:
        def sb(name, shape, dt=F32):
            return c.enter_context(nc.sbuf_tensor(name, shape, dt))
        q = sb("e_q", [R, HD])
        qT = sb("e_qT", [HD, R])
        qpad = sb("e_qpad", [HD, NB, R])
        qb = sb("e_qb", [HD, 2, R])
        kvn = sb("e_kvn", [R, 6, HD])
        ng = sb("e_ng", [R, 3])
        same = sb("e_same", [R, R])
        own = sb("e_own", [R, NB])
        new = sb("e_new", [R, 16])
        sall = sb("e_sall", [R, PAST + 4])
        scm = sb("e_scm", [R, 256])
        ptab = sb("e_ptab", [1, NB * PAGES], I32)
        t64 = sb("e_t64", [R, HD])
        st = sb("e_st", [R, 16])
        ob = sb("e_ob", [R, NB, HD])
        o = sb("e_o", [R, 3, HD])
        y = sb("e_y", [R, HD])

        with ExitStack() as c2:
            vall = c2.enter_context(nc.sbuf_tensor("e_vall", [P, NB, PAGES, HD], F32))
            vcm = c2.enter_context(nc.sbuf_tensor("e_vcm", [P, NB, 2, HD], F32))
            with ExitStack() as c3:
                first_pages = c3.enter_context(nc.sbuf_tensor("e_pg0", [P, PAGES, 256], F32))
                kvT = c3.enter_context(nc.sbuf_tensor("e_kvT", [P, 256], F32))

                U = 8

                def load_pages(eng, buf, bb, sem, first=0, last=PAGES):
                    def group(i):
                        page = [eng.value_load(ptab[0:1, ds(bb * PAGES + i * U + u, 1)], min_val=0, max_val=NPOOL - 1)
                                for u in range(U)]
                        for u in range(U):
                            eng.dma_start(buf[:, ds(i * U + u, 1), :] if last - first > U else buf[:, first + u:first + u + 1, :],
                                          io["cache_nsa_kv"][ds(l, 1), ds(page[u], 1)].rearrange("a g t r d -> t (a g) (r d)")).then_inc(sem, 16)

                    if last - first > U:
                        with eng.Fori(first // U, last // U) as i:
                            group(i)
                    else:
                        group(first // U)

                with ExitStack() as c4:
                    def sb2(name, shape):
                        return c4.enter_context(nc.sbuf_tensor(name, shape, F32))
                    win = sb2("e_win", [P, NB, WIN // P, P])
                    kTw = sb2("e_kTw", [HD, NB, WIN])
                    swn = sb2("e_swn", [R, WIN + 1])
                    pTw = sb2("e_pTw", [P, WIN // P, R])
                    oneh = sb2("e_oneh", [33, NDEC])
                    rel = sb2("e_rel", [33, H])
                    relq = sb2("e_relq", [33, H, NB])
                    with nc.Block() as b:
                        @b.sync
                        def _(sp):
                            ld = Loads(sp, S("ld"))
                            sample_heads(ld, io, z, q, NQ, 1)
                            for h in range(H):
                                hb = slice(h * NB, h * NB + NB)
                                ld(kvn[hb].rearrange("p a n -> p (a n)"), z[s0:s0 + NB, NKV:NKV + 384])
                                ld(ng[hb], z[s0:s0 + NB, NG + 3 * h:NG + 3 * h + 3])
                            ld(rel[0:32, :], io["rel_bias"])
                            ld(oneh[:], io["c_onehot_dec"])
                            ld(same[:], io["c_same"])
                            ld(own[:], io["c_own"])
                            ld2 = Loads(sp, S("win_in"))
                            for bb in range(NB):
                                ld2(win[:, bb], io["cache_swa_kv"][ds(l, 1), bb].rearrange("a (t p) r d -> p (a t) (r d)", p=P))
                            table = Loads(sp, S("ptab_in"))
                            table(ptab[:], io["page_table"].rearrange("b n -> (b n)").rearrange("(a n) -> a n", a=1))
                            table.all_in()
                            load_pages(sp, first_pages, 0, S("pages_in"))
                            ld.all_in()
                            ld2.all_in()
                            sp.wait_ge(S("pages_in"), 16 * PAGES)

                        @b.vector
                        def _(dve):
                            link = Link(dve, S("v"))
                            link(V.memset(qpad[:], 0.0))
                            link(V.memset(kvT[:], 0.0))
                            link(V.memset(relq[:], 1.0))
                            dve.wait_ge(S("ld"), 16 * 16)
                            link(V.tensor_scalar(q[:], q[:], 0.125, None, ALU.mult), S("q_ready"))
                            link(V.tensor_copy(relq[0:32], bc(rel[0:32, :], H, [32, H, NB])), S("rel_ready"))
                            dve.wait_ge(S("q_turned"), 1)
                            link(V.tensor_copy(qT[:], ps[0:HD, 0, 0:R]))
                            for bb in range(NB):
                                link(V.tensor_copy(qpad[:, bb, bb::NB], qT[:, bb::NB]), S("qpad") if bb == NB - 1 else None)
                            for bb in range(NB):
                                dve.wait_ge(S("kw_turned"), bb + 1)
                                link(V.tensor_copy(kTw[:, bb, :], ps[0:HD, 1 + bb % 2, :]), S("kw_ready"))
                            dve.wait_ge(S("biases"), 1)
                            link(V.tensor_copy(scm[:], ps[0:R, 4, 0:256]))
                            link(V.tensor_copy(swn[:, 0:WIN], ps[0:R, 5, :]))
                            link(V.tensor_copy(new[:, 0:1], ps[0:R, 6, 0:1]), S("bias_read"))
                            for ch in range(NCH):
                                dve.wait_ge(S("slc_bias"), ch + 1)
                                link(V.tensor_copy(sall[:, ch * 512:ch * 512 + 512], ps[0:R, 4 + ch % 2, :]), S("bias_read"))
                            for j, r in enumerate((2, 4)):
                                link(V.tensor_tensor_reduce(t64[:], q[:], kvn[:, r, :], 1.0, 0.0, ALU.mult, ALU.add, new[:, 1 + j:2 + j]))
                                link(V.tensor_tensor(new[:, 1 + j:2 + j], new[:, 1 + j:2 + j], new[:, 0:1], ALU.add))
                            link(V.tensor_copy(sall[:, PAST:PAST + 1], new[:, 1:2]))
                            link(V.tensor_copy(swn[:, WIN:WIN + 1], new[:, 2:3]))
                            dve.wait_ge(S("gexp"), 1)
                            link(V.tensor_scalar(ng[:], ng[:], 1.0, None, ALU.add))
                            link(V.reciprocal(ng[:], ng[:]))
                            dve.wait_ge(S("w_scored"), 1)
                            link(V.tensor_tensor(swn[:, 0:WIN], swn[:, 0:WIN], ps[0:R, 7, :], ALU.add))
                            link(V.tensor_reduce(st[:, 0:1], swn[:], AX.X, ALU.max, negate=True), S("w_max"))
                            dve.wait_ge(S("pw_turned"), 1)
                            link(V.tensor_copy(pTw[:].rearrange("p a n -> p (a n)"), ps[:, 0, 0:4 * R]), S("pw_ready"))
                            dve.wait_ge(S("w_pv"), 1)
                            link(V.tensor_tensor(ob[:], ps[0:R, 1, :].rearrange("p (b d) -> p b d", b=NB), bc(own[:], NB, [R, NB, HD]), ALU.mult))
                            link(V.tensor_reduce(o[:, 2, :], ob[:].rearrange("p b d -> p d b"), AX.X, ALU.add))
                            link(V.scalar_tensor_tensor(o[:, 2, :], kvn[:, 5, :], swn[:, WIN:WIN + 1], o[:, 2, :], ALU.mult, ALU.add))
                            link(V.reciprocal(st[:, 8:9], st[:, 1:2]))
                            link(V.tensor_scalar(o[:, 2, :], o[:, 2, :], st[:, 8:9], ng[:, 2:3], ALU.mult, ALU.mult))

                        @b.scalar
                        def _(act):
                            act.wait_ge(S("ld"), 16 * 16)
                            A.activation(ng[:], ng[:], ACT.Exp, scale=-1.0).then_inc(S("gexp"), 1)
                            act.wait_ge(S("w_max"), 1)
                            A.activation(swn[:], swn[:], ACT.Exp, bias=st[:, 0:1], accum_out=st[:, 1:2]).then_inc(S("w_exp"), 1)

                        @b.tensor
                        def _(pe):
                            pe.wait_ge(S("q_ready"), 1)
                            nc.tensor.transpose(ps[0:HD, 0, 0:R], q[:], ident[0:R, 0:R]).then_inc(S("q_turned"), 1)
                            pe.wait_ge(S("win_in"), 16 * NB)
                            for bb in range(NB):
                                if bb >= 2:
                                    pe.wait_ge(S("kw_ready"), bb - 1)
                                for i in range(4):
                                    m = nc.tensor.transpose(ps[0:HD, 1 + bb % 2, i * P:i * P + P], win[:, bb, i, 0:HD], ident[:])
                                m.then_inc(S("kw_turned"), 1)
                            pe.wait_ge(S("rel_ready"), 1)
                            rq = relq[:].rearrange("p h b -> p (h b)")
                            nc.tensor.matmul(ps[0:R, 4, 0:256], rq, oneh[:, SCM:SCM + 256], start=True, stop=True)
                            nc.tensor.matmul(ps[0:R, 5, :], rq, oneh[:, SWN:SWN + WIN], start=True, stop=True)
                            nc.tensor.matmul(ps[0:R, 6, 0:8], rq, oneh[:, SNW:SNW + 8], start=True, stop=True).then_inc(S("biases"), 1)
                            for ch in range(NCH):
                                pe.wait_ge(S("bias_read"), max(1, ch))
                                nc.tensor.matmul(ps[0:R, 4 + ch % 2, :], rq, oneh[:, ch * 512:ch * 512 + 512], start=True, stop=True).then_inc(S("slc_bias"), 1)
                            pe.wait_ge(S("qpad"), 1)
                            pe.wait_ge(S("kw_ready"), NB)
                            for bb in range(NB):
                                m = nc.tensor.matmul(ps[0:R, 7, :], qpad[:, bb, :], kTw[:, bb, :], start=(bb == 0), stop=(bb == NB - 1))
                            m.then_inc(S("w_scored"), 1)
                            pe.wait_ge(S("w_exp"), 1)
                            for i in range(4):
                                m = nc.tensor.transpose(ps[:, 0, i * R:i * R + R], swn[:, i * P:i * P + P], ident[0:R, 0:R])
                            m.then_inc(S("pw_turned"), 1)
                            pe.wait_ge(S("pw_ready"), 1)
                            for i in range(4):
                                m = nc.tensor.matmul(ps[0:R, 1, :], pTw[:, i, :], win[:, :, i, HD:P], start=(i == 0), stop=(i == 3))
                            m.then_inc(S("w_pv"), 1)
                    kit.clear()

                pages = [first_pages, c3.enter_context(nc.sbuf_tensor("e_pg1", [P, PAGES, 256], F32))]
                pT = c3.enter_context(nc.sbuf_tensor("e_pT", [P, PAST], F32))
                kT = c3.enter_context(nc.sbuf_tensor("e_kT", [HD, 2, 512], F32))

                with nc.Fori(0, NB // 2) as g:
                    with nc.Block(no_gpsimd_drain=True) as b:
                        @b.sync
                        def _(sp):
                            load_pages(sp, pages[1], g * 2 + 1, S("odd_in"))
                            sp.wait_ge(S("k_turned"), NCH)
                            sp.wait_ge(S("v_kept"), 1)
                            load_pages(sp, pages[0], (g * 2 + 2) % NB, S("next_in"), U)
                            sp.wait_ge(S("odd_in"), 16 * PAGES)
                            sp.wait_ge(S("next_in"), 16 * (PAGES - U))
                            sp.wait_ge(S("next_in_act"), 16 * U)

                        @b.tensor
                        def _(pe):
                            def score(pe, j, ch):
                                n = NCH * j + ch
                                pe.wait_ge(S("qb"), j + 1)
                                pe.wait_ge(S("kT"), n + 1)
                                if n >= 2:
                                    pe.wait_ge(S("added"), n - 1)
                                nc.tensor.matmul(ps[0:R, 4 + ch % 2, :], qb[:, j, :], kT[:, ch % 2, :], start=True, stop=True).then_inc(S("scored"), 1)

                            for j in range(2):
                                pg = pages[j]
                                if j:
                                    pe.wait_ge(S("odd_in"), 16 * PAGES)
                                for ch in range(NCH):
                                    n = NCH * j + ch
                                    if n >= 2:
                                        pe.wait_ge(S("pT"), n - 1)
                                    for i in range(G4):
                                        m = nc.tensor.transpose(ps[:, ch % 2, i * P:i * P + P], pg[:, ch * G4 + i, 0:P], ident[:])
                                    m.then_inc(S("kv_turned"), 1)
                                    if n >= 2:
                                        pe.wait_ge(S("kT"), n - 1)
                                    for i in range(G4):
                                        m = nc.tensor.transpose(ps[0:HD, 2 + ch % 2, i * P:i * P + P], pg[:, ch * G4 + i, P:P + HD], ident[:])
                                    m.then_inc(S("k_turned"), 1)
                                    if ch:
                                        score(pe, j, ch - 1)
                                score(pe, j, NCH - 1)
                                if j:
                                    pe.wait_ge(S("c_added"), 1)
                                pe.wait_ge(S("pT"), NCH * (j + 1))
                                for k in range(32):
                                    m = nc.tensor.matmul(ps[:, 6, 0:255], wb[:, k, :], pT[:, k:k + 16 * 254 + 1:16],
                                                         start=(k == 0), stop=(k == 31))
                                m.then_inc(S("compressed"), 1)
                                pe.wait_ge(S("kvT"), j + 1)
                                for i in range(2):
                                    m = nc.tensor.transpose(ps[:, 7, i * P:i * P + P], kvT[:, i * P:i * P + P], ident[:])
                                m.then_inc(S("vc_turned"), 1)
                                nc.tensor.matmul(ps[0:R, 6, 0:255], qb[:, j, :], kvT[0:HD, 0:255], start=True, stop=True).then_inc(S("c_scored"), 1)

                        @b.scalar
                        def _(act):
                            for j in range(2):
                                for ch in range(NCH):
                                    n = NCH * j + ch
                                    act.wait_ge(S("kv_turned"), n + 1)
                                    if n == NCH:
                                        act.wait_ge(S("compressed"), 1)
                                    A.activation(pT[:, ch * 512:ch * 512 + 512], ps[:, ch % 2, :], ACT.Copy).then_inc(S("pT"), 1)
                                A.activation(vall[:, ds(2 * g + j, 1)].rearrange("p a n d -> p (a n) d"), pages[j][:, :, 192:256], ACT.Copy).then_inc(S("v_kept"), 1)
                                if j == 0:
                                    act.wait_ge(S("k_turned"), NCH)
                                    act.wait_ge(S("v_kept"), 1)
                                    load_pages(act, pages[0], (g * 2 + 2) % NB, S("next_in_act"), 0, U)

                        @b.vector
                        def _(dve):
                            link = Link(dve, S("v"))
                            for j in range(2):
                                link(V.tensor_copy(qb[:, j, :], qpad[:, ds(2 * g + j, 1), :].rearrange("p a n -> p (a n)")), S("qb"))
                                for ch in range(NCH + 1):
                                    n = NCH * j + ch
                                    if ch < NCH:
                                        dve.wait_ge(S("k_turned"), n + 1)
                                        if n >= 2:
                                            dve.wait_ge(S("scored"), n - 1)
                                        link(V.tensor_copy(kT[:, ch % 2, :], ps[0:HD, 2 + ch % 2, :]), S("kT"))
                                    if ch:
                                        dve.wait_ge(S("scored"), n)
                                        sc = sall[:, (ch - 1) * 512:ch * 512]
                                        link(V.tensor_tensor(sc, sc, ps[0:R, 4 + (ch - 1) % 2, :], ALU.add), S("added"))
                                dve.wait_ge(S("compressed"), j + 1)
                                link(V.tensor_scalar(kvT[:, 0:255], ps[:, 6, 0:255], peadd[:, 0:1], None, ALU.add), S("kvT"))
                                dve.wait_ge(S("vc_turned"), j + 1)
                                link(V.tensor_copy(vcm[:, ds(2 * g + j, 1)].rearrange("p a n d -> p (a n) d"),
                                                   ps[:, 7, 0:256].rearrange("p (n d) -> p n d", n=2)[:, :, HD:P]))
                                dve.wait_ge(S("c_scored"), j + 1)
                                link(V.tensor_tensor(scm[:, 0:255], scm[:, 0:255], ps[0:R, 6, 0:255], ALU.add), S("c_added"))
                    kit.clear()

            with ExitStack() as c3:
                def sb3(name, shape):
                    return c3.enter_context(nc.sbuf_tensor(name, shape, F32))
                pcT = sb3("e_pcT", [P, 2, R])
                psT = sb3("e_psT", [P, PAGES, R])
                imp = sb3("e_imp", [R, 64])
                score_ = sb3("e_score", [R, 72])
                top = sb3("e_top", [R, 16])
                with nc.Block() as b:
                    @b.vector
                    def _(dve):
                        link = Link(dve, S("v"))
                        link(V.tensor_reduce(st[:, 2:3], scm[:], AX.X, ALU.max, negate=True), S("c_max"))
                        dve.wait_ge(S("c_exp"), 1)
                        link(V.reciprocal(st[:, 4:5], st[:, 3:4]))
                        link(V.tensor_scalar(scm[:], scm[:], st[:, 4:5], None, ALU.mult), S("p_c"))
                        link(V.tensor_reduce(imp[:], scm[:].rearrange("p (j n) -> p j n", n=4), AX.X, ALU.add))
                        link(V.tensor_tensor(imp[:, 1:64], imp[:, 1:64], scm[:, 3:252:4], ALU.add), S("imp"))
                        link(V.memset(score_[:], 1.0e30))
                        dve.wait_ge(S("imp_summed"), 1)
                        link(V.tensor_copy(score_[:, 1:63], ps[0:R, 0, 1:63]))
                        link(V.max(top[:, 0:8], score_[:, 0:65]))
                        link(V.match_replace(score_[:, 0:65], top[:, 0:8], score_[:, 0:65], -1.0e30))
                        link(V.max(top[:, 8:16], score_[:, 0:65]))
                        link(V.match_replace(score_[:, 0:65], top[:, 8:16], score_[:, 0:65], -1.0e30))
                        link(V.tensor_scalar(score_[:, 0:65], score_[:, 0:65], -5.0e29, NEG, ALU.is_gt, ALU.mult))
                        s3 = sall[:, 0:PAST].rearrange("p (j n) -> p j n", n=HD)
                        link(V.tensor_tensor(s3, s3, score_[:, 0:64].unsqueeze(2).to_broadcast([R, 64, HD]), ALU.add))
                        link(V.tensor_reduce(st[:, 5:6], sall[:, 0:PAST + 1], AX.X, ALU.max, negate=True), S("s_max"))
                        dve.wait_ge(S("pc_turned"), 1)
                        link(V.tensor_copy(pcT[:].rearrange("p a n -> p (a n)"), ps[:, 1, 0:2 * R]), S("pcT"))
                        for k in range(2):
                            dve.wait_ge(S("ps_turned"), k + 1)
                            link(V.tensor_copy(psT[:, 16 * k:16 * k + 16, :].rearrange("p a n -> p (a n)"), ps[:, 2 + k, :]), S("psT"))

                        def own_part(acc, br):
                            link(V.tensor_tensor(ob[:], acc.rearrange("p (b d) -> p b d", b=NB), bc(own[:], NB, [R, NB, HD]), ALU.mult))
                            link(V.tensor_reduce(o[:, br, :], ob[:].rearrange("p b d -> p d b"), AX.X, ALU.add))

                        dve.wait_ge(S("c_pv"), 1)
                        own_part(ps[0:R, 4, :], 0)
                        dve.wait_ge(S("s_pv"), 1)
                        own_part(ps[0:R, 5, :], 1)
                        link(V.scalar_tensor_tensor(o[:, 1, :], kvn[:, 3, :], sall[:, PAST:PAST + 1], o[:, 1, :], ALU.mult, ALU.add))
                        link(V.reciprocal(st[:, 7:8], st[:, 6:7]))
                        link(V.tensor_tensor(st[:, 7:8], st[:, 7:8], ng[:, 1:2], ALU.mult))
                        link(V.scalar_tensor_tensor(y[:], o[:, 1, :], st[:, 7:8], o[:, 2, :], ALU.mult, ALU.add))
                        link(V.scalar_tensor_tensor(y[:], o[:, 0, :], ng[:, 0:1], y[:], ALU.mult, ALU.add), S("y_ready"))

                    @b.scalar
                    def _(act):
                        act.wait_ge(S("c_max"), 1)
                        A.activation(scm[:], scm[:], ACT.Exp, bias=st[:, 2:3], accum_out=st[:, 3:4]).then_inc(S("c_exp"), 1)
                        act.wait_ge(S("s_max"), 1)
                        A.activation(sall[:, 0:PAST + 1], sall[:, 0:PAST + 1], ACT.Exp, bias=st[:, 5:6], accum_out=st[:, 6:7]).then_inc(S("s_exp"), 1)

                    @b.tensor
                    def _(pe):
                        pe.wait_ge(S("imp"), 1)
                        nc.tensor.matmul(ps[0:R, 0, 0:64], same[:], imp[:], start=True, stop=True).then_inc(S("imp_summed"), 1)
                        for i in range(2):
                            m = nc.tensor.transpose(ps[:, 1, i * R:i * R + R], scm[:, i * P:i * P + P], ident[0:R, 0:R])
                        m.then_inc(S("pc_turned"), 1)
                        pe.wait_ge(S("pcT"), 1)
                        for i in range(2):
                            m = nc.tensor.matmul(ps[0:R, 4, :], pcT[:, i, :], vcm[:, :, i, :], start=(i == 0), stop=(i == 1))
                        m.then_inc(S("c_pv"), 1)
                        pe.wait_ge(S("s_exp"), 1)
                        for k in range(2):
                            for i in range(16):
                                m = nc.tensor.transpose(ps[:, 2 + k, i * R:i * R + R], sall[:, (16 * k + i) * P:(16 * k + i) * P + P], ident[0:R, 0:R])
                            m.then_inc(S("ps_turned"), 1)
                        pe.wait_ge(S("psT"), 2)
                        for i in range(PAGES):
                            m = nc.tensor.matmul(ps[0:R, 5, :], psT[:, i, :], vall[:, :, i, :], start=(i == 0), stop=(i == PAGES - 1))
                        m.then_inc(S("s_pv"), 1)

                    @b.sync
                    def _(sp):
                        sp.wait_ge(S("y_ready"), 1)
                        so = Loads(sp, S("st"))
                        for h in range(H):
                            so(y_mix[SEQ:TOK, 768 + h * HD:768 + h * HD + HD], y[h * NB:h * NB + NB, :])
                        so.all_in()
                kit.clear()


def mixers(kit, env, io, l):
    with ExitStack() as c:
        data = SampleData(kit.nc, c)
        recurrent_prompt(kit, env, io, l, lambda ld: data.load(io, env["z"], l, ld))
        kit.next_stage()
        recurrent_sample(kit, env, io, l, data)
        kit.next_stage()
    nsa(kit, env, io, l)
    kit.next_stage()


OUTS = [("y_prompt", (1, SEQ, D)), ("y_sample", (NB, 1, D)),
        ("p_nsa", (2, 1, SEQ, 4, HD)), ("p_swa", (2, 1, WIN, 2, HD)), ("p_ret", (2, 1, 4, HD, HD)),
        ("p_C", (2, 1, 4, HD, HD)), ("p_n", (2, 1, 4, HD)), ("p_m", (2, 1, 4)), ("p_gdn", (2, 1, 4, HD, HD)),
        ("p_gconv", (2, 1, 3, 768)), ("p_ffn_conv", (2, 1, 2, DFF)),
        ("s_nsa", (2, NB, 1, 4, HD)), ("s_swa", (2, NB, WIN, 2, HD)), ("s_ret", (2, NB, 4, HD, HD)),
        ("s_C", (2, NB, 4, HD, HD)), ("s_n", (2, NB, 4, HD)), ("s_m", (2, NB, 4)), ("s_gdn", (2, NB, 4, HD, HD)),
        ("s_gconv", (2, NB, 3, 768)), ("s_ffn_conv", (2, NB, 2, DFF))]


def buckets(n):
    f = np.float32
    big = 16 + (np.log(np.maximum(n, 1).astype(f) / f(16)) / f(math.log(64)) * f(16)).astype(np.int32)
    return np.where(n < 16, n, np.minimum(big, 31))


def onehot(dist, ok):
    out = np.zeros((33, len(dist)), np.float32)
    out[buckets(np.maximum(dist, 0)), np.arange(len(dist))] = ok
    out[32] = np.where(ok, 0.0, NEG)
    return out


def constants():
    f = np.float32
    i = np.arange(P)
    lo = i[:, None] >= i[None, :]
    pos = np.concatenate([np.arange(SEQ), [PAST]]).astype(f)
    inv = f(10000.0) ** (-np.linspace(0.0, 1.0, HD // 2, dtype=f))
    ang = (pos[:, None] * inv[None, :]).astype(f).astype(np.float64)
    log_g = np.log(1.0 - 2.0 ** (-5.0 - np.arange(H)))
    dist = (i[None, :] - i[:, None])
    ret = np.where(dist[:, None, :] >= 0, np.exp(log_g[None, :, None] * np.maximum(dist, 0)[:, None, :]), 0.0) * 0.125
    xi = np.stack([np.exp(log_g[None] * (i[:, None] + 1.0)), 0.125 * np.exp(log_g[None] * (P - 1.0 - i[:, None])),
                   np.broadcast_to(np.exp(log_g * P), (P, H))], 1)
    lev = []
    for s in range(7):
        w = 1 << s
        lev.append((i[:, None] // (2 * w) == i[None, :] // (2 * w)) & (i[:, None] // w % 2 == 1) & (i[None, :] // w % 2 == 0))
    lev = np.stack(lev, 1)
    last = np.zeros((P, P), f)
    last[P - 1] = 1.0
    d1, d2 = 1023 - np.arange(TL), 639 - np.arange(WL)
    return {
        "c_ident": np.eye(P, dtype=f),
        "c_rope": np.concatenate([np.cos(ang), np.sin(ang)], 1).astype(f),
        "c_retD": ret.astype(f).reshape(P, H * P),
        "c_xi": xi.astype(f).reshape(P, 3 * H),
        "c_dec": np.repeat(1.0 - 2.0 ** (-5.0 - np.arange(H)), NB).astype(f)[:, None],
        "c_onehot": np.concatenate([onehot(d1, d1 >= 0), onehot(d2, (d2 >= 0) & (d2 < WIN))], 1),
        "c_onehot_dec": np.concatenate([onehot(x, ok) for x, ok in (
            (PAST - np.arange(PAST), np.arange(PAST) >= 0),
            (PAST - (16 * np.arange(256) + 31), np.arange(256) < 255),
            (WIN - np.arange(WIN), np.arange(WIN) > 0),
            (np.zeros(8, int), np.arange(8) < 8))], 1),
        "c_same": (np.arange(H * NB)[:, None] % NB == np.arange(H * NB)[None] % NB).astype(f),
        "c_own": (np.arange(H * NB)[:, None] % NB == np.arange(NB)[None]).astype(f),
        "c_qkscale": np.broadcast_to(np.repeat(np.array([0.0625, 0.5], f), H), (P, 8)).copy(),
        "c_valid": (np.arange(SEQ) >= 31).astype(f).reshape(NT, P).T.copy(),
        "c_upper": lo.T.astype(f),
        "c_mask": np.where(lo, 0.0, NEG).astype(f),
        "c_maskT": np.where(lo.T, 0.0, NEG).astype(f),
        "c_last": last,
        "c_lev": lev.astype(f).reshape(P, 7 * P),
        "c_levT": lev.transpose(2, 1, 0).astype(f).reshape(P, 7 * P),
    }


def kernel(**inputs):
    import concourse.bacc as bacc
    from concourse.bass_utils import run_bass_kernel_spmd

    nc = bacc.Bacc("TRN2", target_bir_lowering=False, num_devices=1)
    arrays, io = {}, {}
    for name, a in {**inputs, **constants()}.items():
        arrays[name] = np.ascontiguousarray(a)
        io[name] = nc.dram_tensor(name, a.shape, mybir.dt.from_np(np.asarray(a).dtype), kind="ExternalInput").ap()
    for name, shape in OUTS:
        io[name] = nc.dram_tensor(name, shape, F32, kind="ExternalOutput").ap()
    program(nc, io)
    r = run_bass_kernel_spmd(nc, [arrays], core_ids=[0])
    return tuple(r.results[0][name] for name, _ in OUTS)
```
